# Optimizing a Trainium2 kernel written in Bass

```python
import math, functools
import jax, jax.numpy as jnp
from jax import lax
import numpy as np
import math
import jax
import jax.numpy as jnp

D_MODEL = 1024
BATCH = 1
SEQ = 512
DEPTH = 1

HEAD_DIM = 64
N_MIX_HEADS = D_MODEL // HEAD_DIM
HEADS_PER_MIXER = N_MIX_HEADS // 4
GROUP_WIDTH = HEADS_PER_MIXER * HEAD_DIM
Q_BLOCK = 128
MOBA_BLOCK = 256
MOBA_TOPK = 3
MLA_Q_RANK = D_MODEL // 4
MLA_KV_RANK = D_MODEL // 8
MLA_NOPE = HEAD_DIM
MLA_ROPE = HEAD_DIM // 2
MLA_V = HEAD_DIM
ROPE_THETA = 10000.0
DILATED_BRANCHES = ((128, 1), (512, 4), (2048, 16))
SWA_WINDOW = 128
SWA_KV_HEADS = 2
SWA_KV_WIDTH = SWA_KV_HEADS * HEAD_DIM
D_FF = 4 * D_MODEL
EPS = 1e-6
NEG = -1e30
COL_WIDTHS = (GROUP_WIDTH, GROUP_WIDTH, GROUP_WIDTH,
              MLA_Q_RANK, MLA_KV_RANK, MLA_ROPE,
              GROUP_WIDTH, GROUP_WIDTH, GROUP_WIDTH,
              GROUP_WIDTH, SWA_KV_WIDTH, SWA_KV_WIDTH)
IN_COLS = sum(COL_WIDTHS)


def rms_norm(x, g):
    xf = x.astype(jnp.float32)
    y = xf * lax.rsqrt(jnp.mean(xf * xf, axis=-1, keepdims=True) + EPS)
    return (y * g.astype(jnp.float32)).astype(x.dtype)

def split_columns(h):
    parts, off = [], 0
    for wdt in COL_WIDTHS:
        parts.append(h[..., off:off + wdt])
        off += wdt
    return parts

def alibi_slopes():
    n = 3 * HEADS_PER_MIXER
    idx = np.arange(1, n + 1, dtype=np.float32).reshape(HEADS_PER_MIXER, 3)
    s = jnp.asarray(np.exp2(-8.0 * idx / n), dtype=jnp.float32)
    return s[:, 0], s[:, 1], s[:, 2]

def rope_tables(S):
    inv = 1.0 / (ROPE_THETA ** (jnp.arange(0, MLA_ROPE, 2, dtype=jnp.float32) / MLA_ROPE))
    ang = jnp.arange(S, dtype=jnp.float32)[:, None] * inv[None, :]
    return jnp.cos(ang), jnp.sin(ang)

def apply_rope(x, cos, sin):
    x1, x2 = jnp.split(x.astype(jnp.float32), 2, axis=-1)
    c, s = cos[None, :, None, :], sin[None, :, None, :]
    return jnp.concatenate([x1 * c - x2 * s, x1 * s + x2 * c], axis=-1).astype(x.dtype)

def moba_attention(q, k, v, slopes):
    B, H, S, dh = q.shape
    nb = -(-S // MOBA_BLOCK)
    Sp = nb * MOBA_BLOCK
    topk = min(MOBA_TOPK, nb)
    pad = ((0, 0), (0, 0), (0, Sp - S), (0, 0))
    qp, kp, vp = jnp.pad(q, pad), jnp.pad(k, pad), jnp.pad(v, pad)
    kb = kp.reshape(B, H, nb, MOBA_BLOCK, dh)
    vb = vp.reshape(B, H, nb, MOBA_BLOCK, dh)
    kmean = jnp.mean(kb.astype(jnp.float32), axis=3)
    scale = dh ** -0.5
    bi = jnp.arange(B)[:, None, None, None]
    hi = jnp.arange(H)[None, :, None, None]
    slope_b = slopes.astype(jnp.float32)

    def chunk(c):
        t0 = c * Q_BLOCK
        qc = lax.dynamic_slice_in_dim(qp, t0, Q_BLOCK, axis=2)
        tpos = t0 + jnp.arange(Q_BLOCK)
        qblk = tpos // MOBA_BLOCK
        own = t0 // MOBA_BLOCK
        gate = jnp.einsum('bhqd,bhnd->bhqn', qc.astype(jnp.float32), kmean)
        past = jnp.arange(nb)[None, :] < qblk[:, None]
        gate = jnp.where(past, gate, NEG)
        _, sel = lax.top_k(gate, topk)
        sel_ok = sel < qblk[:, None]
        ksel = kb[bi, hi, sel]
        vsel = vb[bi, hi, sel]
        kpos_sel = sel[..., None] * MOBA_BLOCK + jnp.arange(MOBA_BLOCK)
        dist_sel = (tpos[:, None, None] - kpos_sel).astype(jnp.float32)
        s_sel = (jnp.einsum('bhqd,bhqjkd->bhqjk', qc, ksel).astype(jnp.float32) * scale
                 - slope_b[None, :, None, None, None] * dist_sel)
        s_sel = jnp.where(sel_ok[..., None], s_sel, NEG).reshape(B, H, Q_BLOCK, topk * MOBA_BLOCK)
        kown = lax.dynamic_slice_in_dim(kb, own, 1, axis=2)[:, :, 0]
        vown = lax.dynamic_slice_in_dim(vb, own, 1, axis=2)[:, :, 0]
        dist_own = tpos[:, None] - (own * MOBA_BLOCK + jnp.arange(MOBA_BLOCK))[None, :]
        s_own = (jnp.einsum('bhqd,bhkd->bhqk', qc, kown).astype(jnp.float32) * scale
                 - slope_b[None, :, None, None] * dist_own.astype(jnp.float32))
        s_own = jnp.where(dist_own >= 0, s_own, NEG)
        p = jax.nn.softmax(jnp.concatenate([s_sel, s_own], axis=-1), axis=-1)
        p_sel = p[..., :topk * MOBA_BLOCK].reshape(B, H, Q_BLOCK, topk, MOBA_BLOCK)
        p_own = p[..., topk * MOBA_BLOCK:]
        return (jnp.einsum('bhqjk,bhqjkd->bhqd', p_sel.astype(v.dtype), vsel)
                + jnp.einsum('bhqk,bhkd->bhqd', p_own.astype(v.dtype), vown))

    out = lax.map(chunk, jnp.arange(Sp // Q_BLOCK))
    return out.transpose(1, 2, 0, 3, 4).reshape(B, H, Sp, dh)[:, :, :S]

def causal_dense_attention(q, k, v, scale):
    B, H, S, _ = q.shape
    kpos = jnp.arange(S)

    def blk(c):
        qc = lax.dynamic_slice_in_dim(q, c * Q_BLOCK, Q_BLOCK, axis=2)
        s = jnp.einsum('bhqd,bhkd->bhqk', qc, k).astype(jnp.float32) * scale
        tpos = c * Q_BLOCK + jnp.arange(Q_BLOCK)
        s = jnp.where(kpos[None, :] <= tpos[:, None], s, NEG)
        p = jax.nn.softmax(s, axis=-1)
        return jnp.einsum('bhqk,bhkd->bhqd', p.astype(v.dtype), v)

    out = lax.map(blk, jnp.arange(S // Q_BLOCK))
    return out.transpose(1, 2, 0, 3, 4).reshape(B, H, S, -1)

def mla_attention(q_lat, kv_lat, k_rope, g_qlat, g_kvlat, w_uq, w_ukv, g_q, g_k):
    B, S, _ = q_lat.shape
    H = HEADS_PER_MIXER
    qk_dim = MLA_NOPE + MLA_ROPE
    q = (rms_norm(q_lat, g_qlat) @ w_uq).reshape(B, S, H, qk_dim)
    kv = (rms_norm(kv_lat, g_kvlat) @ w_ukv).reshape(B, S, H, MLA_NOPE + MLA_V)
    k_nope, v = kv[..., :MLA_NOPE], kv[..., MLA_NOPE:]
    k = jnp.concatenate([k_nope, jnp.broadcast_to(k_rope[:, :, None, :], (B, S, H, MLA_ROPE))], axis=-1)
    q, k = rms_norm(q, g_q), rms_norm(k, g_k)
    cos, sin = rope_tables(S)
    q = jnp.concatenate([q[..., :MLA_NOPE], apply_rope(q[..., MLA_NOPE:], cos, sin)], axis=-1)
    k = jnp.concatenate([k[..., :MLA_NOPE], apply_rope(k[..., MLA_NOPE:], cos, sin)], axis=-1)
    t = lambda a: a.transpose(0, 2, 1, 3)
    return causal_dense_attention(t(q), t(k), t(v), qk_dim ** -0.5)

def dilated_branch(q, k, v, slopes, window, dilation):
    B, H, S, dh = q.shape
    span = dilation * Q_BLOCK
    Sp = -(-S // span) * span
    L = Sp // dilation
    nb = L // Q_BLOCK
    steps = window // dilation

    def to_sub(t):
        t = jnp.pad(t, ((0, 0), (0, 0), (0, Sp - S), (0, 0)))
        return t.reshape(B, H, L, dilation, dh).transpose(0, 1, 3, 2, 4).reshape(B, H, dilation, nb, Q_BLOCK, dh)

    def with_prev(t):
        prev = jnp.pad(t, ((0, 0), (0, 0), (0, 0), (1, 0), (0, 0), (0, 0)))[:, :, :, :-1]
        return jnp.concatenate([prev, t], axis=4)

    qs = to_sub(q)
    kk, vv = with_prev(to_sub(k)), with_prev(to_sub(v))
    qi = jnp.arange(Q_BLOCK)[:, None]
    kidx = jnp.arange(2 * Q_BLOCK)[None, :]
    rel = qi + Q_BLOCK - kidx
    blk = jnp.arange(nb)[:, None, None]
    valid = (rel >= 0) & (rel <= steps) & (blk * Q_BLOCK + kidx[None] - Q_BLOCK >= 0)
    s = (jnp.einsum('bhrnqd,bhrnkd->bhrnqk', qs, kk).astype(jnp.float32) * (dh ** -0.5)
         - slopes.astype(jnp.float32)[None, :, None, None, None, None] * (dilation * rel).astype(jnp.float32))
    s = jnp.where(valid, s, NEG)
    m = jnp.max(s, axis=-1, keepdims=True)
    e = jnp.exp(s - m)
    l = jnp.sum(e, axis=-1, keepdims=True)
    o = jnp.einsum('bhrnqk,bhrnkd->bhrnqd', e, vv.astype(jnp.float32))
    back = lambda t: t.reshape(B, H, dilation, L, -1).transpose(0, 1, 3, 2, 4).reshape(B, H, Sp, -1)[:, :, :S]
    return back(o), back(m), back(l)

def dilated_mixture(q, k, v, slopes):
    branches = [dilated_branch(q, k, v, slopes, w, d) for (w, d) in DILATED_BRANCHES]
    M = functools.reduce(jnp.maximum, [b[1] for b in branches])
    num = jnp.zeros(q.shape, jnp.float32)
    den = jnp.zeros(q.shape[:-1] + (1,), jnp.float32)
    for o, m, l in branches:
        w = jnp.exp(m - M)
        num = num + w * o
        den = den + w * l
    return (num / den).astype(q.dtype)

def swa_sink_attention(q, k, v, sinks, slopes):
    B, H, S, dh = q.shape
    G = H // SWA_KV_HEADS
    nb = S // Q_BLOCK
    qb = q.reshape(B, SWA_KV_HEADS, G, nb, Q_BLOCK, dh)

    def with_prev(t):
        t = t.reshape(B, SWA_KV_HEADS, nb, Q_BLOCK, dh)
        prev = jnp.pad(t, ((0, 0), (0, 0), (1, 0), (0, 0), (0, 0)))[:, :, :-1]
        return jnp.concatenate([prev, t], axis=3)

    kk, vv = with_prev(k), with_prev(v)
    qi = jnp.arange(Q_BLOCK)[:, None]
    kidx = jnp.arange(2 * Q_BLOCK)[None, :]
    rel = qi + Q_BLOCK - kidx
    blk = jnp.arange(nb)[:, None, None]
    valid = (rel >= 0) & (rel < SWA_WINDOW) & (blk * Q_BLOCK + kidx[None] - Q_BLOCK >= 0)
    sl = slopes.astype(jnp.float32).reshape(SWA_KV_HEADS, G)[None, :, :, None, None, None]
    s = jnp.einsum('bkgnqd,bkncd->bkgnqc', qb, kk).astype(jnp.float32) * (dh ** -0.5) - sl * rel.astype(jnp.float32)
    s = jnp.where(valid, s, NEG)
    sink = jnp.broadcast_to(sinks.astype(jnp.float32).reshape(SWA_KV_HEADS, G)[None, :, :, None, None, None],
                            s.shape[:-1] + (1,))
    p = jax.nn.softmax(jnp.concatenate([s, sink], axis=-1), axis=-1)[..., :-1]
    o = jnp.einsum('bkgnqc,bkncd->bkgnqd', p.astype(v.dtype), vv)
    return o.reshape(B, H, S, dh)

def hybrid_layer(x, attn_norm_g, w_in, moba_q_g, moba_k_g, mla_qlat_g, mla_kvlat_g,
                 mla_w_uq, mla_w_ukv, mla_q_g, mla_k_g, dil_q_g, dil_k_g, swa_q_g, swa_k_g,
                 swa_sinks, group_out_g, w_o, mlp_norm_g, w_up, w_down):
    B, S, _ = x.shape
    H = HEADS_PER_MIXER
    slope_a, slope_c, slope_d = alibi_slopes()
    h = rms_norm(x, attn_norm_g) @ w_in
    a_q, a_k, a_v, b_ql, b_kvl, b_kr, c_q, c_k, c_v, d_q, d_k, d_v = split_columns(h)
    heads = lambda t, n: t.reshape(B, S, n, HEAD_DIM)
    tr = lambda t: t.transpose(0, 2, 1, 3)
    oa = moba_attention(tr(rms_norm(heads(a_q, H), moba_q_g)), tr(rms_norm(heads(a_k, H), moba_k_g)),
                        tr(heads(a_v, H)), slope_a)
    ob = mla_attention(b_ql, b_kvl, b_kr, mla_qlat_g, mla_kvlat_g, mla_w_uq, mla_w_ukv, mla_q_g, mla_k_g)
    oc = dilated_mixture(tr(rms_norm(heads(c_q, H), dil_q_g)), tr(rms_norm(heads(c_k, H), dil_k_g)),
                         tr(heads(c_v, H)), slope_c)
    od = swa_sink_attention(tr(rms_norm(heads(d_q, H), swa_q_g)),
                            tr(rms_norm(heads(d_k, SWA_KV_HEADS), swa_k_g)),
                            tr(heads(d_v, SWA_KV_HEADS)), swa_sinks, slope_d)
    groups = [tr(o).reshape(B, S, GROUP_WIDTH) for o in (oa, ob, oc, od)]
    mixed = jnp.concatenate([rms_norm(gr, group_out_g[i]) for i, gr in enumerate(groups)], axis=-1)
    x = x + mixed @ w_o
    u = jax.nn.relu(rms_norm(x, mlp_norm_g) @ w_up)
    return x + (u * u) @ w_down

def first_inputs(seed: int = 0) -> dict:
    key = jax.random.key(seed)
    ks = jax.random.split(key, 24)
    f = jnp.float32
    H = HEADS_PER_MIXER
    w = lambda k, shape, fan_in: jax.random.normal(k, shape, f) * (fan_in ** -0.5)
    g = lambda k, shape: 1.0 + 0.02 * jax.random.normal(k, shape, f)
    return {
        "x": jax.random.normal(ks[0], (BATCH, SEQ, D_MODEL), f),
        "attn_norm_g": g(ks[1], (DEPTH, D_MODEL)),
        "w_in": w(ks[2], (DEPTH, D_MODEL, IN_COLS), D_MODEL),
        "moba_q_g": g(ks[3], (DEPTH, HEAD_DIM)),
        "moba_k_g": g(ks[4], (DEPTH, HEAD_DIM)),
        "mla_qlat_g": g(ks[5], (DEPTH, MLA_Q_RANK)),
        "mla_kvlat_g": g(ks[6], (DEPTH, MLA_KV_RANK)),
        "mla_w_uq": w(ks[7], (DEPTH, MLA_Q_RANK, H * (MLA_NOPE + MLA_ROPE)), MLA_Q_RANK),
        "mla_w_ukv": w(ks[8], (DEPTH, MLA_KV_RANK, H * (MLA_NOPE + MLA_V)), MLA_KV_RANK),
        "mla_q_g": g(ks[9], (DEPTH, MLA_NOPE + MLA_ROPE)),
        "mla_k_g": g(ks[10], (DEPTH, MLA_NOPE + MLA_ROPE)),
        "dil_q_g": g(ks[11], (DEPTH, HEAD_DIM)),
        "dil_k_g": g(ks[12], (DEPTH, HEAD_DIM)),
        "swa_q_g": g(ks[13], (DEPTH, HEAD_DIM)),
        "swa_k_g": g(ks[14], (DEPTH, HEAD_DIM)),
        "swa_sinks": 0.5 * jax.random.normal(ks[15], (DEPTH, H), f),
        "group_out_g": g(ks[16], (DEPTH, 4, GROUP_WIDTH)),
        "w_o": w(ks[17], (DEPTH, D_MODEL, D_MODEL), D_MODEL),
        "mlp_norm_g": g(ks[18], (DEPTH, D_MODEL)),
        "w_up": w(ks[19], (DEPTH, D_MODEL, D_FF), D_MODEL),
        "w_down": w(ks[20], (DEPTH, D_FF, D_MODEL), D_FF),
    }

def first_block(x, attn_norm_g, w_in, moba_q_g, moba_k_g, mla_qlat_g, mla_kvlat_g, mla_w_uq,
              mla_w_ukv, mla_q_g, mla_k_g, dil_q_g, dil_k_g, swa_q_g, swa_k_g, swa_sinks,
              group_out_g, w_o, mlp_norm_g, w_up, w_down):
    for l in range(DEPTH):
        x = hybrid_layer(x, attn_norm_g[l], w_in[l], moba_q_g[l], moba_k_g[l], mla_qlat_g[l],
                         mla_kvlat_g[l], mla_w_uq[l], mla_w_ukv[l], mla_q_g[l], mla_k_g[l],
                         dil_q_g[l], dil_k_g[l], swa_q_g[l], swa_k_g[l], swa_sinks[l],
                         group_out_g[l], w_o[l], mlp_norm_g[l], w_up[l], w_down[l])
    return x


DEPTH_2 = 2

GRID_W = 64
CTX_LEN = 256
N_MIXERS = 4
NEG_INF = -1e30
F32 = jnp.float32

HY_ORDER = 2
HY_SHORT = 3
HY_EMB = 33
HY_FFN = 64
HY_FAST_DECAY = 0.3
HY_SLOW_DECAY = 1.5
HY_TARGET = 1e-2
HY_SHIFT = 0.05

SW_HQ = 16
SW_HKV = 4
SW_REP = SW_HQ // SW_HKV
SW_HD = 64
SW_WINDOW = 128
SW_BLOCK = SW_WINDOW
ROPE_BASE = 10000.0

GD_H = 8
GD_DK = 128
GD_DV = 128
GD_QK = GD_H * GD_DK
GD_V = GD_H * GD_DV
GD_CONV = 3
GD_CHUNK = 64

HG_DK = 128
HG_H = D_MODEL // HG_DK
HG_DV = D_MODEL // HG_H
HG_CHUNK = 64

N_EXPERTS = 16
EXPERT_FF = 1024
EC_CAPACITY = 2


def rms_norm_2(x, w):
    xf = x.astype(F32)
    y = xf * lax.rsqrt(jnp.mean(xf * xf, axis=-1, keepdims=True) + EPS)
    return (y * w.astype(F32)).astype(x.dtype)

def l2_normalize(x):
    xf = x.astype(F32)
    return xf * lax.rsqrt(jnp.sum(xf * xf, axis=-1, keepdims=True) + EPS)

def orient(t, direction):
    return jnp.flip(t, axis=1) if direction == 1 else t

def centred_depthwise_conv(x, w, b=None):
    K, C = w.shape
    y = lax.conv_general_dilated(x, w[:, None, :].astype(x.dtype), window_strides=(1,),
                                 padding=[(K // 2, K // 2)],
                                 dimension_numbers=('NWC', 'WIO', 'NWC'), feature_group_count=C)
    return y if b is None else y + b

def hyena_positional_features(L):
    t = jnp.linspace(0.0, 1.0, L, dtype=F32)[:, None]
    bands = (HY_EMB - 1) // 2
    w = 2.0 * math.pi * jnp.arange(L, dtype=F32)[:, None] / L
    f = jnp.linspace(1e-4, bands - 1, bands, dtype=F32)[None, :]
    z = jnp.concatenate([t, jnp.cos(f * w), -jnp.sin(f * w)], axis=-1)
    return t, z

def hyena_filters(L, w1, b1, w2, b2, w3, freq):
    t, z = hyena_positional_features(L)
    h = jnp.sin(freq[0].astype(F32) * (z @ w1.astype(F32) + b1.astype(F32)))
    h = jnp.sin(freq[1].astype(F32) * (h @ w2.astype(F32) + b2.astype(F32)))
    h = (h @ w3.astype(F32)).reshape(L, HY_ORDER, 2, D_MODEL)
    max_decay = math.log(HY_TARGET) / HY_FAST_DECAY
    min_decay = math.log(HY_TARGET) / HY_SLOW_DECAY
    deltas = jnp.abs(jnp.linspace(min_decay, max_decay, D_MODEL, dtype=F32))
    window = jnp.exp(-t * deltas) + HY_SHIFT
    return h * window[:, None, None, :]

def two_sided_fft_conv(u, h_fwd, h_bwd, bias):
    L = u.shape[1]
    kern = jnp.concatenate([h_fwd, jnp.zeros((1, h_fwd.shape[1]), F32), h_bwd[:0:-1]], axis=0)
    uf = u.astype(F32)
    spec = jnp.fft.rfft(uf, n=2 * L, axis=1) * jnp.fft.rfft(kern, n=2 * L, axis=0)[None]
    y = jnp.fft.irfft(spec, n=2 * L, axis=1)[:, :L]
    return (y + uf * bias.astype(F32)).astype(u.dtype)

def hyena_mixer(h, w_in, b_in, short_w, short_b, w1, b1, w2, b2, w3, freq, filt_bias, w_out, b_out):
    L = h.shape[1]
    u = centred_depthwise_conv(h @ w_in + b_in, short_w, short_b)
    v, x1, x2 = jnp.split(u, 3, axis=-1)
    filt = hyena_filters(L, w1, b1, w2, b2, w3, freq)
    z = x1 * two_sided_fft_conv(v, filt[:, 0, 0], filt[:, 0, 1], filt_bias[0])
    z = x2 * two_sided_fft_conv(z, filt[:, 1, 0], filt[:, 1, 1], filt_bias[1])
    return z @ w_out + b_out

def axial_rope_tables(L):
    rows = L // GRID_W
    row = jnp.repeat(jnp.arange(rows, dtype=F32), GRID_W)
    col = jnp.tile(jnp.arange(GRID_W, dtype=F32), rows)
    nf = SW_HD // 4
    inv = ROPE_BASE ** (-jnp.arange(nf, dtype=F32) / nf)
    ang = jnp.concatenate([row[:, None] * inv, col[:, None] * inv], axis=-1)
    return jnp.cos(ang), jnp.sin(ang)

def apply_rope_2(x, cos, sin):
    shape = (1, cos.shape[0]) + (1,) * (x.ndim - 3) + (cos.shape[1],)
    cos = cos.reshape(shape).astype(x.dtype)
    sin = sin.reshape(shape).astype(x.dtype)
    x1, x2 = jnp.split(x, 2, axis=-1)
    return jnp.concatenate([x1 * cos - x2 * sin, x2 * cos + x1 * sin], axis=-1)

def sink_softmax(s, sink):
    sk = jnp.broadcast_to(sink.astype(F32).reshape(SW_HKV, SW_REP, 1, 1), s.shape[:-1] + (1,))
    return jax.nn.softmax(jnp.concatenate([s, sk], axis=-1), axis=-1)[..., :-1]

def swa_mixer(h_ctx, h_lat, w_in, sink, w_out, with_ctx_out):
    B, L, _ = h_lat.shape
    scale = SW_HD ** -0.5

    def project(h):
        n = h.shape[1]
        u = h @ w_in
        q = u[..., :SW_HQ * SW_HD].reshape(B, n, SW_HKV, SW_REP, SW_HD)
        k = u[..., SW_HQ * SW_HD:(SW_HQ + SW_HKV) * SW_HD].reshape(B, n, SW_HKV, SW_HD)
        v = u[..., (SW_HQ + SW_HKV) * SW_HD:].reshape(B, n, SW_HKV, SW_HD)
        return q, k, v

    q_c, k_c, v_c = project(h_ctx)
    q_l, k_l, v_l = project(h_lat)
    cos, sin = axial_rope_tables(L)
    q_l = apply_rope_2(q_l, cos, sin)
    k_l = apply_rope_2(k_l, cos, sin)
    n_ctx = k_c.shape[1]
    nb = L // SW_BLOCK

    def band(t):
        tp = jnp.pad(t, ((0, 0), (SW_BLOCK, SW_BLOCK), (0, 0), (0, 0)))
        tp = tp.reshape(B, nb + 2, SW_BLOCK, SW_HKV, SW_HD)
        return jnp.concatenate([tp[:, :-2], tp[:, 1:-1], tp[:, 2:]], axis=2).swapaxes(0, 1)

    blk = jnp.arange(nb)[:, None, None]
    qpos = blk * SW_BLOCK + jnp.arange(SW_BLOCK)[None, :, None]
    kpos = (blk - 1) * SW_BLOCK + jnp.arange(3 * SW_BLOCK)[None, None, :]
    band_mask = (jnp.abs(qpos - kpos) <= SW_WINDOW) & (kpos >= 0) & (kpos < L)
    q_blocks = q_l.reshape(B, nb, SW_BLOCK, SW_HKV, SW_REP, SW_HD).swapaxes(0, 1)

    def block_attention(xs):
        q_b, k_b, v_b, m_b = xs
        s_ctx = jnp.einsum('bqgrd,bkgd->bgrqk', q_b, k_c).astype(F32) * scale
        s_loc = jnp.einsum('bqgrd,bkgd->bgrqk', q_b, k_b).astype(F32) * scale
        s_loc = jnp.where(m_b, s_loc, NEG_INF)
        p = sink_softmax(jnp.concatenate([s_ctx, s_loc], axis=-1), sink).astype(v_b.dtype)
        return (jnp.einsum('bgrqk,bkgd->bqgrd', p[..., :n_ctx], v_c)
                + jnp.einsum('bgrqk,bkgd->bqgrd', p[..., n_ctx:], v_b))

    o_l = lax.map(block_attention, (q_blocks, band(k_l), band(v_l), band_mask))
    y_lat = o_l.swapaxes(0, 1).reshape(B, L, SW_HQ * SW_HD) @ w_out
    y_ctx = None
    if with_ctx_out:
        s = jnp.einsum('bqgrd,bkgd->bgrqk', q_c, k_c).astype(F32) * scale
        p = sink_softmax(s, sink).astype(v_c.dtype)
        y_ctx = jnp.einsum('bgrqk,bkgd->bqgrd', p, v_c).reshape(B, n_ctx, SW_HQ * SW_HD) @ w_out
    return y_ctx, y_lat

def to_chunks(t, size):
    B, L, H = t.shape[:3]
    t = t.reshape((B, L // size, size, H) + t.shape[3:])
    return jnp.moveaxis(t, (1, 3), (0, 2))

def from_chunks(t):
    t = jnp.moveaxis(t, (0, 2), (1, 3))
    return t.reshape((t.shape[0], t.shape[1] * t.shape[2]) + t.shape[3:])

def chunk_gated_delta(q, k, v, g, beta, S0):
    dv = v.shape[-1]
    C = GD_CHUNK
    qc, kc, vc = to_chunks(q, C), to_chunks(k, C), to_chunks(v, C)
    gc, bc = to_chunks(g, C), to_chunks(beta, C)
    G = jnp.cumsum(gc, axis=-1)
    incl = jnp.tril(jnp.ones((C, C), bool))
    strict = jnp.tril(jnp.ones((C, C), bool), -1)
    decay = jnp.exp(jnp.where(incl, G[..., :, None] - G[..., None, :], -jnp.inf))
    kb = kc * bc[..., None]
    A = jnp.where(strict, jnp.einsum('nbhid,nbhjd->nbhij', kb, kc) * decay, 0.0)
    rhs = jnp.concatenate([vc * bc[..., None], kb * jnp.exp(G)[..., None]], axis=-1)
    uw = lax.linalg.triangular_solve(jnp.eye(C, dtype=F32) + A, rhs, left_side=True, lower=True,
                                     unit_diagonal=True)
    u, w = uw[..., :dv], uw[..., dv:]

    def step(S, xs):
        q_i, k_i, u_i, w_i, G_i, dec_i = xs
        v_new = u_i - jnp.einsum('bhck,bhkv->bhcv', w_i, S)
        attn = jnp.einsum('bhik,bhjk->bhij', q_i, k_i) * dec_i
        o = (jnp.einsum('bhck,bhkv->bhcv', q_i * jnp.exp(G_i)[..., None], S)
             + jnp.einsum('bhij,bhjv->bhiv', attn, v_new))
        g_last = G_i[..., -1:]
        S = (S * jnp.exp(g_last)[..., None]
             + jnp.einsum('bhck,bhcv->bhkv', k_i * jnp.exp(g_last - G_i)[..., None], v_new))
        return S, o

    S, o = lax.scan(step, S0, (qc, kc, u, w, G, decay))
    return from_chunks(o), S

def chunk_gla(q, k, v, logf, S0):
    C = HG_CHUNK
    qc, kc, vc, gc = to_chunks(q, C), to_chunks(k, C), to_chunks(v, C), to_chunks(logf, C)
    G = jnp.cumsum(gc, axis=-2)
    incl = jnp.tril(jnp.ones((C, C), bool))[:, :, None]

    def step(S, xs):
        q_i, k_i, v_i, G_i = xs
        dec = jnp.exp(jnp.where(incl, G_i[:, :, :, None, :] - G_i[:, :, None, :, :], -jnp.inf))
        attn = jnp.einsum('bhtk,bhtsk->bhts', q_i, dec * k_i[:, :, None, :, :])
        o = (jnp.einsum('bhtk,bhkv->bhtv', q_i * jnp.exp(G_i), S)
             + jnp.einsum('bhts,bhsv->bhtv', attn, v_i))
        g_last = G_i[:, :, -1:, :]
        S = (S * jnp.exp(g_last[:, :, 0, :])[..., None]
             + jnp.einsum('bhsk,bhsv->bhkv', k_i * jnp.exp(g_last - G_i), v_i))
        return S, o

    S, o = lax.scan(step, S0, (qc, kc, vc, G))
    return from_chunks(o), S

def gdn_mixer(h_ctx, h_lat, w_in, conv_w, a_log, dt_bias, norm_w, w_out, with_ctx_out):
    n_qkv = 2 * GD_QK + GD_V

    def project(h):
        B, n, _ = h.shape
        u = h @ w_in
        qkv = jax.nn.silu(centred_depthwise_conv(u[..., :n_qkv], conv_w))
        q = l2_normalize(qkv[..., :GD_QK].reshape(B, n, GD_H, GD_DK)) * GD_DK ** -0.5
        k = l2_normalize(qkv[..., GD_QK:2 * GD_QK].reshape(B, n, GD_H, GD_DK))
        v = qkv[..., 2 * GD_QK:].astype(F32).reshape(B, n, GD_H, GD_DV)
        z = u[..., n_qkv:n_qkv + GD_V]
        ba = u[..., n_qkv + GD_V:].astype(F32).reshape(B, n, 2, 2, GD_H)
        beta = jax.nn.sigmoid(ba[:, :, 0])
        g = -jnp.exp(a_log.astype(F32)) * jax.nn.softplus(ba[:, :, 1] + dt_bias.astype(F32))
        return q, k, v, z, beta, g

    qc, kc, vc, zc, bc, gc = project(h_ctx)
    ql, kl, vl, zl, bl, gl = project(h_lat)
    S0 = jnp.zeros((h_lat.shape[0], GD_H, GD_DK, GD_DV), F32)
    o_c = 0.0
    o_l = 0.0
    for d in range(2):
        oc_d, S_c = chunk_gated_delta(orient(qc, d), orient(kc, d), orient(vc, d),
                                      orient(gc[:, :, d], d), orient(bc[:, :, d], d), S0)
        ol_d, _ = chunk_gated_delta(orient(ql, d), orient(kl, d), orient(vl, d),
                                    orient(gl[:, :, d], d), orient(bl[:, :, d], d), S_c)
        o_c = o_c + orient(oc_d, d)
        o_l = o_l + orient(ol_d, d)

    def readout(o, z):
        B, n = o.shape[:2]
        y = rms_norm_2(o, norm_w) * jax.nn.silu(z.astype(F32)).reshape(B, n, GD_H, GD_DV)
        return y.reshape(B, n, GD_V).astype(z.dtype) @ w_out

    y_ctx = readout(o_c, zc) if with_ctx_out else None
    return y_ctx, readout(o_l, zl)

def hgrn2_mixer(h_ctx, h_lat, w_in, lb, norm_w, w_out, with_ctx_out):
    lbh = lb.reshape(HG_H, HG_DK)

    def project(h):
        B, n, _ = h.shape
        q, f_fw, f_bw, i, g = jnp.split(h @ w_in, 5, axis=-1)
        q = jax.nn.silu(q).astype(F32).reshape(B, n, HG_H, HG_DK)
        f = jnp.stack([f_fw, f_bw], axis=2).astype(F32).reshape(B, n, 2, HG_H, HG_DK)
        logf = jnp.log(lbh + (1.0 - lbh) * jax.nn.sigmoid(f))
        k = (1.0 - lbh) * jax.nn.sigmoid(-f)
        v = i.astype(F32).reshape(B, n, HG_H, HG_DV)
        return q, k, v, logf, g

    qc, kc, vc, fc, gc = project(h_ctx)
    ql, kl, vl, fl, gl = project(h_lat)
    S0 = jnp.zeros((h_lat.shape[0], HG_H, HG_DK, HG_DV), F32)
    o_c = 0.0
    o_l = 0.0
    for d in range(2):
        oc_d, S_c = chunk_gla(orient(qc, d), orient(kc[:, :, d], d), orient(vc, d),
                              orient(fc[:, :, d], d), S0)
        ol_d, _ = chunk_gla(orient(ql, d), orient(kl[:, :, d], d), orient(vl, d),
                            orient(fl[:, :, d], d), S_c)
        o_c = o_c + orient(oc_d, d)
        o_l = o_l + orient(ol_d, d)

    def readout(o, g):
        B, n = o.shape[:2]
        y = rms_norm_2(o, norm_w) * jax.nn.silu(g.astype(F32)).reshape(B, n, HG_H, HG_DV)
        return y.reshape(B, n, D_MODEL).astype(g.dtype) @ w_out

    y_ctx = readout(o_c, gc) if with_ctx_out else None
    return y_ctx, readout(o_l, gl)

def expert_choice_ffn(h, router_w, w_gate, w_up, w_down):
    B, n, D = h.shape
    cap = EC_CAPACITY * n // N_EXPERTS
    aff = jax.nn.softmax((h @ router_w).astype(F32), axis=-1)
    gate, idx = lax.top_k(jnp.swapaxes(aff, 1, 2), cap)
    xe = jax.vmap(lambda hb, ib: hb[ib])(h, idx)
    a = jnp.einsum('becd,edf->becf', xe, w_gate)
    u = jnp.einsum('becd,edf->becf', xe, w_up)
    ye = jnp.einsum('becf,efd->becd', jax.nn.silu(a) * u, w_down) * gate[..., None].astype(h.dtype)
    return jax.vmap(lambda ib, yb: jnp.zeros((n, D), h.dtype).at[ib.reshape(-1)].add(yb.reshape(-1, D)))(idx, ye)

def second_inputs(seed: int = 0) -> dict:
    key = jax.random.key(seed)
    keys = iter(jax.random.split(key, 48))

    def nrm(shape, std):
        return std * jax.random.normal(next(keys), shape, F32)

    def gain(shape):
        return 1.0 + nrm(shape, 0.02)

    D = D_MODEL
    gd_cols = 2 * GD_QK + 2 * GD_V + 4 * GD_H
    gd_a_log = jnp.log(jax.random.uniform(next(keys), (2, GD_H), F32, 1.0, 16.0))
    dt = jnp.exp(jax.random.uniform(next(keys), (2, GD_H), F32, math.log(1e-3), math.log(1e-1)))
    gd_dt_bias = jnp.log(jnp.expm1(dt))
    return {
        'x': nrm((BATCH, SEQ, D), 1.0),
        'c': nrm((BATCH, D), 1.0),
        'ctx': nrm((BATCH, CTX_LEN, D), 1.0),
        'c_ctx': nrm((D,), 1.0),
        'ada_w': nrm((DEPTH_2, D, 6 * D), 0.5 * D ** -0.5),
        'ada_b': nrm((DEPTH_2, 6 * D), 0.02),
        'norm1_w': gain((DEPTH_2, D)),
        'norm2_w': gain((DEPTH_2, D)),
        'final_norm_w': gain((D,)),
        'hy_w_in': nrm((D, 3 * D), D ** -0.5),
        'hy_b_in': nrm((3 * D,), 0.02),
        'hy_short_w': nrm((HY_SHORT, 3 * D), HY_SHORT ** -0.5),
        'hy_short_b': nrm((3 * D,), 0.02),
        'hy_ffn_w1': nrm((HY_EMB, HY_FFN), HY_EMB ** -0.5),
        'hy_ffn_b1': nrm((HY_FFN,), 0.02),
        'hy_ffn_w2': nrm((HY_FFN, HY_FFN), HY_FFN ** -0.5),
        'hy_ffn_b2': nrm((HY_FFN,), 0.02),
        'hy_ffn_w3': nrm((HY_FFN, HY_ORDER * 2 * D), 0.01),
        'hy_sin_freq': gain((2, HY_FFN)),
        'hy_filter_bias': nrm((HY_ORDER, D), 0.5),
        'hy_w_out': nrm((D, D), D ** -0.5),
        'hy_b_out': nrm((D,), 0.02),
        'sw_w_in': nrm((D, (SW_HQ + 2 * SW_HKV) * SW_HD), D ** -0.5),
        'sw_sink': nrm((SW_HQ,), 0.5),
        'sw_w_out': nrm((SW_HQ * SW_HD, D), (SW_HQ * SW_HD) ** -0.5),
        'gd_w_in': nrm((D, gd_cols), D ** -0.5),
        'gd_conv_w': nrm((GD_CONV, 2 * GD_QK + GD_V), GD_CONV ** -0.5),
        'gd_a_log': gd_a_log,
        'gd_dt_bias': gd_dt_bias,
        'gd_norm_w': gain((GD_DV,)),
        'gd_w_out': nrm((GD_V, D), GD_V ** -0.5),
        'hg_w_in': nrm((D, 5 * D), D ** -0.5),
        'hg_lb': nrm((DEPTH_2, D), 1.0),
        'hg_norm_w': gain((HG_DV,)),
        'hg_w_out': nrm((D, D), D ** -0.5),
        'moe_router': nrm((DEPTH_2, D, N_EXPERTS), D ** -0.5),
        'moe_w_gate': nrm((DEPTH_2, N_EXPERTS, D, EXPERT_FF), D ** -0.5),
        'moe_w_up': nrm((DEPTH_2, N_EXPERTS, D, EXPERT_FF), D ** -0.5),
        'moe_w_down': nrm((DEPTH_2, N_EXPERTS, EXPERT_FF, D), EXPERT_FF ** -0.5),
    }

def second_block(x, c, ctx, c_ctx, ada_w, ada_b, norm1_w, norm2_w, final_norm_w,
              hy_w_in, hy_b_in, hy_short_w, hy_short_b, hy_ffn_w1, hy_ffn_b1, hy_ffn_w2, hy_ffn_b2,
              hy_ffn_w3, hy_sin_freq, hy_filter_bias, hy_w_out, hy_b_out,
              sw_w_in, sw_sink, sw_w_out,
              gd_w_in, gd_conv_w, gd_a_log, gd_dt_bias, gd_norm_w, gd_w_out,
              hg_w_in, hg_lb, hg_norm_w, hg_w_out,
              moe_router, moe_w_gate, moe_w_up, moe_w_down):
    lat, cx = x, ctx
    lb_all = jnp.cumsum(jax.nn.softmax(hg_lb.astype(F32), axis=0), axis=0)
    for layer in range(DEPTH_2):
        kind = layer % N_MIXERS
        keep_ctx = layer < DEPTH_2 - 1
        mod_l = [m[:, None, :] for m in jnp.split(jax.nn.silu(c) @ ada_w[layer] + ada_b[layer], 6, axis=-1)]
        mod_c = jnp.split(jax.nn.silu(c_ctx) @ ada_w[layer] + ada_b[layer], 6, axis=-1)
        h_l = rms_norm_2(lat, norm1_w[layer]) * (1.0 + mod_l[1]) + mod_l[0]
        h_c = rms_norm_2(cx, norm1_w[layer]) * (1.0 + mod_c[1]) + mod_c[0]
        if kind == 0:
            hy_args = (hy_w_in, hy_b_in, hy_short_w, hy_short_b, hy_ffn_w1, hy_ffn_b1, hy_ffn_w2,
                       hy_ffn_b2, hy_ffn_w3, hy_sin_freq, hy_filter_bias, hy_w_out, hy_b_out)
            y_l = hyena_mixer(h_l, *hy_args)
            y_c = hyena_mixer(h_c, *hy_args) if keep_ctx else None
        elif kind == 1:
            y_c, y_l = swa_mixer(h_c, h_l, sw_w_in, sw_sink, sw_w_out, keep_ctx)
        elif kind == 2:
            y_c, y_l = gdn_mixer(h_c, h_l, gd_w_in, gd_conv_w, gd_a_log, gd_dt_bias, gd_norm_w,
                                 gd_w_out, keep_ctx)
        else:
            lb = lb_all[layer] - lb_all[0]
            y_c, y_l = hgrn2_mixer(h_c, h_l, hg_w_in, lb, hg_norm_w, hg_w_out, keep_ctx)
        lat = lat + mod_l[2] * y_l
        h_l = rms_norm_2(lat, norm2_w[layer]) * (1.0 + mod_l[4]) + mod_l[3]
        lat = lat + mod_l[5] * expert_choice_ffn(h_l, moe_router[layer], moe_w_gate[layer],
                                                 moe_w_up[layer], moe_w_down[layer])
        if keep_ctx:
            cx = cx + mod_c[2] * y_c
            h_c = rms_norm_2(cx, norm2_w[layer]) * (1.0 + mod_c[4]) + mod_c[3]
            cx = cx + mod_c[5] * expert_choice_ffn(h_c, moe_router[layer], moe_w_gate[layer],
                                                   moe_w_up[layer], moe_w_down[layer])
    return rms_norm_2(lat, final_norm_w)


def setup_inputs(seed=0):
    out = dict(first_inputs(seed))
    for name, value in second_inputs(seed + 1).items():
        if name != "x":
            out[name + "_2"] = value
    return out


def reference(
    x, attn_norm_g, w_in, moba_q_g, moba_k_g, mla_qlat_g, mla_kvlat_g, mla_w_uq, mla_w_ukv,
    mla_q_g, mla_k_g, dil_q_g, dil_k_g, swa_q_g, swa_k_g, swa_sinks, group_out_g, w_o,
    mlp_norm_g, w_up, w_down, c_2, ctx_2, c_ctx_2, ada_w_2, ada_b_2, norm1_w_2, norm2_w_2,
    final_norm_w_2, hy_w_in_2, hy_b_in_2, hy_short_w_2, hy_short_b_2, hy_ffn_w1_2, hy_ffn_b1_2,
    hy_ffn_w2_2, hy_ffn_b2_2, hy_ffn_w3_2, hy_sin_freq_2, hy_filter_bias_2, hy_w_out_2,
    hy_b_out_2, sw_w_in_2, sw_sink_2, sw_w_out_2, gd_w_in_2, gd_conv_w_2, gd_a_log_2,
    gd_dt_bias_2, gd_norm_w_2, gd_w_out_2, hg_w_in_2, hg_lb_2, hg_norm_w_2, hg_w_out_2,
    moe_router_2, moe_w_gate_2, moe_w_up_2, moe_w_down_2,
):
    x = first_block(
        x, attn_norm_g, w_in, moba_q_g, moba_k_g, mla_qlat_g, mla_kvlat_g, mla_w_uq, mla_w_ukv,
        mla_q_g, mla_k_g, dil_q_g, dil_k_g, swa_q_g, swa_k_g, swa_sinks, group_out_g, w_o,
        mlp_norm_g, w_up, w_down,
    )
    return second_block(
        x, c_2, ctx_2, c_ctx_2, ada_w_2, ada_b_2, norm1_w_2, norm2_w_2, final_norm_w_2,
        hy_w_in_2, hy_b_in_2, hy_short_w_2, hy_short_b_2, hy_ffn_w1_2, hy_ffn_b1_2, hy_ffn_w2_2,
        hy_ffn_b2_2, hy_ffn_w3_2, hy_sin_freq_2, hy_filter_bias_2, hy_w_out_2, hy_b_out_2,
        sw_w_in_2, sw_sink_2, sw_w_out_2, gd_w_in_2, gd_conv_w_2, gd_a_log_2, gd_dt_bias_2,
        gd_norm_w_2, gd_w_out_2, hg_w_in_2, hg_lb_2, hg_norm_w_2, hg_w_out_2, moe_router_2,
        moe_w_gate_2, moe_w_up_2, moe_w_down_2,
    )


_drawn_inputs = setup_inputs


def setup_inputs(seed=0):
    import zlib

    import numpy as np

    out = dict(_drawn_inputs(seed))
    spreads = {}
    factors = {'moba_q_g': 8.0,
     'moba_k_g': 8.0,
     'mla_qlat_g': 6.769,
     'mla_kvlat_g': 4.285,
     'mla_q_g': 6.448,
     'mla_k_g': 6.579,
     'dil_q_g': 8.0,
     'dil_k_g': 8.0,
     'swa_q_g': 8.0,
     'swa_k_g': 8.0,
     'swa_sinks': 200.0,
     'group_out_g': 3.55,
     'mlp_norm_g': 3.678,
     'ctx_2': 4.925,
     'ada_b_2': 3.053,
     'norm1_w_2': 8.0,
     'norm2_w_2': 40.684,
     'final_norm_w_2': 24.833,
     'hy_b_in_2': 7.391,
     'hy_short_b_2': 6.934,
     'hy_ffn_b1_2': 3.607,
     'hy_sin_freq_2': 8.0,
     'hy_b_out_2': 64.0,
     'sw_sink_2': 8.0,
     'c_ctx_2': 2.953}
    for name, (base, spread) in spreads.items():
        noise = np.random.default_rng([zlib.crc32(name.encode()), seed]).standard_normal(out[name].shape)
        drawn = base * np.exp(spread * noise) if base else spread * noise
        out[name] = jnp.asarray(drawn.astype(out[name].dtype))
    for name, factor in factors.items():
        out[name] = (out[name] * factor).astype(out[name].dtype)
    return out
```

```python
from contextlib import ExitStack

import numpy as np

import concourse.bass as bass
from concourse import mybir

ALU = mybir.AluOpType
ACT = mybir.ActivationFunctionType
F32 = mybir.dt.float32
AX_X = mybir.AxisListType.X

P = 128
D = 1024
KD = D // P
SEQ = 512
CTX = 256
TOK = SEQ + CTX
LT, CT = SEQ // P, CTX // P
FF = 4096
EPS = 1e-6
NEG = -1e30
HD = 64
IN_COLS = 2464
HEADS = 4
MLA_DIM = 96
N_EXP = 16
CAP_L, CAP_C = 2 * SEQ // N_EXP, 2 * CTX // N_EXP
NS = 3
CW = 512
TWO_PI = 2.0 * np.pi
TWO_PI_HI = float(np.float32(TWO_PI))
TWO_PI_LO = float(TWO_PI - np.float64(np.float32(TWO_PI)))
ROUND_MAGIC = float(1.5 * 2 ** 23)
SIN_MAX = 3.1415925

A_Q, A_K, A_V, B_QL, B_KVL, B_KR, C_Q, C_K, C_V, D_Q, D_K, D_V = (
    0, 256, 512, 768, 1024, 1152, 1184, 1440, 1696, 1952, 2208, 2336)

VEC_ROWS = [
    [("ada_b_2", 96), ("c_2", 8), ("c_ctx_2", 8), ("attn_norm_g", 8), ("group_out_g", 8)],
    [("hy_b_in_2", 24), ("hy_short_w_2", 72), ("hy_short_b_2", 24), ("hy_b_out_2", 8)],
    [("norm1_w_2", 16), ("norm2_w_2", 16), ("final_norm_w_2", 8), ("mlp_norm_g", 8),
     ("hy_filter_bias_2", 16), ("mla_qlat_g", 2), ("mla_kvlat_g", 1)],
]
VEC_AT = {}
for _t, _rows in enumerate(VEC_ROWS):
    _r = 0
    for _name, _n in _rows:
        VEC_AT[_name] = (_t * P + _r, _n)
        _r += _n


class Counter:

    def __init__(self, handle):
        self.handle = handle
        self.base = 0

    def at(self, n):
        return n + self.base


class Link:

    def __init__(self, eng, signal, start=0):
        self.eng, self.counter, self.start, self.n = eng, signal, start, 0

    def __call__(self, ins):
        self.n += 1
        ins.then_inc(self.counter.handle, 1)
        self.eng.wait_ge(self.counter.handle, self.counter.at(self.start + self.n))


class Stage:

    def __init__(self, core, name):
        core.stages += 1
        self.core, self.name = core, f"{name}{core.stages}"
        self.mem = ExitStack()
        self.used = []

    def sb(self, name, shape, dt=F32):
        return self.mem.enter_context(self.core.nc.sbuf_tensor(f"{self.name}_{name}", shape, dt))

    def ps(self, name, banks=1):
        return self.mem.enter_context(self.core.nc.psum_tensor(f"{self.name}_{name}", [P, banks * 512], F32))

    def counter(self, name, total):
        s = self.core.counter(name)
        self.used.append((s, total))
        return s

    def __enter__(self):
        return self

    def run(self):
        return self.core.nc.Block()

    def __exit__(self, *e):
        self.mem.__exit__(*e)
        for s, total in self.used:
            s.base += total


class Core:

    def __init__(self, nc, ins, consts, ctx):
        self.nc, self.ins, self.consts, self.ctx = nc, ins, consts, ctx
        self.counters = {}
        self.stages = 0
        sb = lambda n, s: ctx.enter_context(nc.sbuf_tensor(n, s, F32))
        self.x = sb("residual", [P, KD, TOK])
        self.h = sb("normed", [P, KD, TOK])
        self.ring = [sb(f"ring{i}", [P, KD * CW]) for i in range(NS)]
        self.ident = sb("ident", [P, P])
        self.ones = sb("ones", [P, P])
        self.vec = sb("vec", [P, 3 * P])
        self.mod = sb("mod", [P, 96, 2])
        self.loaded = [self.counter(f"ring_loaded{i}") for i in range(NS)]
        self.freed = self.counter("ring_freed")
        self.chunks = []
        self.issued = 0
        self.used = 0

    def counter(self, name):
        if name not in self.counters:
            self.counters[name] = Counter(self.ctx.enter_context(self.nc.semaphore(name)))
        return self.counters[name]

    def col(self, name, i=0, n=None):
        at, size = VEC_AT[name]
        return self.vec[:, at + i:at + i + (size - i if n is None else n)]

    def slot(self, n):
        return self.ring[n % NS]

    def set_chunks(self, chunks):
        self.chunks = chunks
        self.arrival, so_far = [], [0] * NS
        for n, place in enumerate(chunks):
            so_far[n % NS] += 16 * len(place(self.slot(n)))
            self.arrival.append(so_far[n % NS])

    def issue(self, sp, n, place):
        for dst, src in place(self.slot(n)):
            sp.dma_start(dst, src).then_inc(self.loaded[n % NS].handle, 16)

    def load_chunk(self, sp, n):
        if n >= NS:
            sp.wait_ge(self.freed.handle, n - NS + 1)
        self.issue(sp, n, self.chunks[n])

    def stream(self, sp, used):
        while self.issued < min(used + NS, len(self.chunks)):
            self.load_chunk(sp, self.issued)
            self.issued += 1

    def await_chunk(self, eng, n, it=0, per=0):
        if per:
            each = self.arrival[n + per] - self.arrival[n]
            eng.wait_ge(self.loaded[n % NS].handle, it * each + self.arrival[n])
            return
        eng.wait_ge(self.loaded[n % NS].handle, self.arrival[n])


def column_chunk(w, c0, width):
    def place(slot):
        return [(slot[:, 0:KD * width].rearrange("p (k n) -> p k n", k=KD),
                 w[:, c0:c0 + width].rearrange("(k p) n -> p k n", p=P))]
    return place


def row_chunk(w, r0, tiles=4):
    def place(slot):
        return [(slot[:, 0:tiles * D].rearrange("p (k n) -> p k n", k=tiles),
                 w[r0:r0 + tiles * P, :].rearrange("(k p) n -> p k n", p=P))]
    return place


def by_k(slot, width=CW, k=KD):
    return slot[:, 0:k * width].rearrange("p (k n) -> p k n", k=k)


def load_stage(core):
    nc, ins = core.nc, core.ins
    with Stage(core, "load") as st:
        rows = st.sb("rows", [P, 3, P])
        tok = core.h[:].rearrange("p k n -> p (k n)").rearrange("p (t d) -> p t d", d=D)
        pv = st.ps("pv")
        px = [st.ps(f"px{i}") for i in range(2)]
        pc = [st.ps(f"pc{i}") for i in range(2)]
        rows_loaded = st.counter("rows_loaded", 16 * sum(len(r) for r in VEC_ROWS))
        x_loaded = st.counter("x_loaded", 32)
        id_loaded = st.counter("id_loaded", 16)
        vec_turned = st.counter("vec_turned", 1)
        lat_turned = st.counter("lat_turned", KD)
        ctx_turned = st.counter("ctx_turned", KD)
        lat_kept = st.counter("lat_kept", KD)
        ctx_kept = st.counter("ctx_kept", KD)
        with st.run() as block:
            @block.sync
            def _(sp):
                sp.dma_start(core.ident[:], core.consts["ident"]).then_inc(id_loaded.handle, 16)
                sp.dma_start(tok[:, 0:LT], ins["x"][0].rearrange("(t p) d -> p t d", p=P)).then_inc(x_loaded.handle, 16)
                sp.dma_start(tok[:, LT:LT + CT], ins["ctx_2"][0].rearrange("(t p) d -> p t d", p=P)).then_inc(x_loaded.handle, 16)
                core.stream(sp, core.used)

            @block.gpsimd
            def _(pool):
                nc.gpsimd.memset(core.ones[:], 1.0 / D)

            @block.scalar
            def _(act):
                for t, group in enumerate(VEC_ROWS):
                    r = 0
                    for name, n in group:
                        a = ins[name]
                        while len(a.shape) > 1:
                            a = a.rearrange("a b ... -> (a b) ...") if len(a.shape) > 2 else a.rearrange("a b -> (a b)")
                        act.dma_start(rows[r:r + n, t, :], a.rearrange("(r c) -> r c", c=P)).then_inc(rows_loaded.handle, 16)
                        r += n
                for k in range(KD):
                    act.wait_ge(ctx_turned.handle, ctx_turned.at(k + 1))
                    nc.scalar.copy(core.x[:, k, SEQ:TOK], pc[k % 2][:, 0:CTX]).then_inc(ctx_kept.handle, 1)

            @block.tensor
            def _(pe):
                pe.wait_ge(id_loaded.handle, id_loaded.at(16))
                pe.wait_ge(x_loaded.handle, x_loaded.at(32))
                for k in range(KD):
                    if k >= 2:
                        pe.wait_ge(lat_kept.handle, lat_kept.at(k - 1))
                        pe.wait_ge(ctx_kept.handle, ctx_kept.at(k - 1))
                    for t in range(LT):
                        last = nc.tensor.transpose(px[k % 2][:, t * P:(t + 1) * P], tok[:, t, k * P:(k + 1) * P], core.ident[:])
                    last.then_inc(lat_turned.handle, 1)
                    for t in range(CT):
                        last = nc.tensor.transpose(pc[k % 2][:, t * P:(t + 1) * P], tok[:, LT + t, k * P:(k + 1) * P], core.ident[:])
                    last.then_inc(ctx_turned.handle, 1)
                pe.wait_ge(rows_loaded.handle, rows_loaded.at(16 * sum(len(r) for r in VEC_ROWS)))
                for t, group in enumerate(VEC_ROWS):
                    n = sum(c for _, c in group)
                    last = nc.tensor.transpose(pv[:, t * P:t * P + n], rows[0:n, t, :], core.ident[0:n, 0:n])
                last.then_inc(vec_turned.handle, 1)

            @block.vector
            def _(dve):
                for k in range(KD):
                    dve.wait_ge(lat_turned.handle, lat_turned.at(k + 1))
                    nc.vector.tensor_copy(core.x[:, k, 0:SEQ], px[k % 2][:]).then_inc(lat_kept.handle, 1)
                dve.wait_ge(vec_turned.handle, vec_turned.at(1))
                n = 2 * P + sum(c for _, c in VEC_ROWS[2])
                nc.vector.tensor_copy(core.vec[:, 0:n], pv[:, 0:n])


def modulation_stage(core):
    nc = core.nc
    n0 = core.used
    per = 6
    turns = 24 // per
    with Stage(core, "mod") as st:
        cs = st.sb("cs", [P, KD, 2])
        row = st.sb("row", [2, 2, CW])
        pr = [st.ps(f"pr{i}") for i in range(2)]
        pt = [st.ps(f"pt{i}") for i in range(2)]
        silu_done = st.counter("silu_done", 2)
        row_done = st.counter("row_done", 24)
        row_kept = st.counter("row_kept", 24)
        row_turned = st.counter("row_turned", 24)
        col_kept = st.counter("col_kept", 24 + 2)
        row_free = st.counter("row_free", 24 + 2)
        with st.run() as block:
            @block.sync
            def _(sp):
                core.used = n0 + 24
                core.stream(sp, core.used)

            @block.scalar
            def _(act):
                nc.scalar.activation(cs[:, :, 0], core.col("c_2"), ACT.Silu).then_inc(silu_done.handle, 1)
                nc.scalar.activation(cs[:, :, 1], core.col("c_ctx_2"), ACT.Silu).then_inc(silu_done.handle, 1)
                with act.Fori(0, turns) as it:
                    for r in range(per):
                        act.wait_ge(row_done.handle, it * per + row_done.at(r + 1))
                        act.wait_ge(row_free.handle, it * per + row_free.at(r + 1))
                        nc.scalar.copy(row[:, r % 2, :], pr[r % 2][0:2, 0:CW]).then_inc(row_kept.handle, 1)

            @block.tensor
            def _(pe):
                def turn(it, r):
                    pe.wait_ge(row_kept.handle, it * per + row_kept.at(r + 1))
                    pe.wait_ge(col_kept.handle, it * per + col_kept.at(r + 1))
                    for j in range(4):
                        last = nc.tensor.matmul(pt[r % 2][:, 2 * j:2 * j + 2], row[:, r % 2, j * P:(j + 1) * P], core.ident[0:2, 0:2], start=True, stop=True)
                    last.then_inc(row_turned.handle, 1)

                pe.wait_ge(silu_done.handle, silu_done.at(2))
                with pe.Fori(0, turns) as it:
                    for r in range(per):
                        n = n0 + r
                        core.await_chunk(pe, n, it, per)
                        w = by_k(core.slot(n))
                        for k in range(KD):
                            last = nc.tensor.matmul(pr[r % 2][0:2, 0:CW], cs[:, k, :], w[:, k, :], start=(k == 0), stop=(k == KD - 1))
                        last.then_inc(row_done.handle, 1)
                        if r:
                            turn(it, r - 1)
                    turn(it, per - 1)

            @block.vector
            def _(dve):
                dve.sem_inc(col_kept.handle, 2)
                with dve.Fori(0, turns) as it:
                    for r in range(per):
                        dve.wait_ge(row_turned.handle, it * per + row_turned.at(r + 1))
                        nc.vector.tensor_copy(core.mod[:, bass.ds(it * (per * 4) + r * 4, 4), :],
                                              pt[r % 2][:, 0:8].rearrange("p (j s) -> p j s", s=2)).then_inc(col_kept.handle, 1)
                dve.wait_ge(col_kept.handle, col_kept.at(26))
                nc.vector.tensor_tensor(core.mod[:], core.mod[:], core.col("ada_b_2").unsqueeze(2).to_broadcast([P, 96, 2]), ALU.add)

            @block.gpsimd
            def _(pool):
                pool.sem_inc(row_free.handle, 2)
                with pool.Fori(0, turns) as it:
                    for r in range(per):
                        pool.wait_ge(row_turned.handle, it * per + row_turned.at(r + 1))
                        pool.sem_inc(row_free.handle, 1)
                        pool.sem_inc(core.freed.handle, 1)


def norm_stage(core, name, streams, dst=None):
    nc = core.nc
    x, h = core.x, core.h
    with Stage(core, name) as st:
        ms = [st.ps(f"ms{i}") for i in range(2)]
        var = st.sb("var", [P, 2, 512])
        rstd = st.sb("rstd", [P, 2, 512])
        gain = st.sb("gain", [P, 2, KD])
        total = KD * len(streams)
        squared = st.counter("norm_squared", total)
        summed = st.counter("norm_summed", len(streams))
        inverted = st.counter("norm_inverted", len(streams))
        rooted = st.counter("norm_rooted", len(streams))
        scaled = st.counter("norm_scaled", total)
        chain = st.counter("norm_chain", 4 * len(streams))
        with st.run() as block:
            @block.sync
            def _(sp):
                core.stream(sp, core.used)

            @block.scalar
            def _(act):
                for i, (c0, n, g, sc, sh) in enumerate(streams):
                    for k in range(KD):
                        nc.scalar.activation(h[:, k, c0:c0 + n], x[:, k, c0:c0 + n], ACT.Square).then_inc(squared.handle, 1)
                for i, (c0, n, g, sc, sh) in enumerate(streams):
                    act.wait_ge(inverted.handle, inverted.at(i + 1))
                    nc.scalar.activation(rstd[:, i, 0:n], var[:, i, 0:n], ACT.Sqrt).then_inc(rooted.handle, 1)
                for i, (c0, n, g, sc, sh) in enumerate(streams):
                    if sh is not None:
                        for k in range(KD):
                            act.wait_ge(scaled.handle, scaled.at(i * KD + k + 1))
                            nc.scalar.activation(h[:, k, c0:c0 + n], h[:, k, c0:c0 + n], ACT.Identity, bias=sh[:, k:k + 1])

            @block.tensor
            def _(pe):
                for i, (c0, n, g, sc, sh) in enumerate(streams):
                    for k in range(KD):
                        pe.wait_ge(squared.handle, squared.at(i * KD + k + 1))
                        last = nc.tensor.matmul(ms[i][:, 0:n], core.ones[:], h[:, k, c0:c0 + n], start=(k == 0), stop=(k == KD - 1))
                    last.then_inc(summed.handle, 1)

            @block.vector
            def _(dve):
                link = Link(dve, chain)
                for i, (c0, n, g, sc, sh) in enumerate(streams):
                    if sc is None:
                        link(nc.vector.tensor_copy(gain[:, i, :], g))
                    else:
                        link(nc.vector.scalar_tensor_tensor(out=gain[:, i, :], in0=sc, scalar=1.0, in1=g, op0=ALU.add, op1=ALU.mult))
                for i, (c0, n, g, sc, sh) in enumerate(streams):
                    dve.wait_ge(summed.handle, summed.at(i + 1))
                    link(nc.vector.tensor_scalar(var[:, i, 0:n], ms[i][:, 0:n], EPS, None, ALU.add))
                    nc.vector.reciprocal(var[:, i, 0:n], var[:, i, 0:n]).then_inc(inverted.handle, 1)
                for i, (c0, n, g, sc, sh) in enumerate(streams):
                    dve.wait_ge(rooted.handle, rooted.at(i + 1))
                    for k in range(KD):
                        nc.vector.scalar_tensor_tensor(out=h[:, k, c0:c0 + n], in0=x[:, k, c0:c0 + n], scalar=gain[:, i, k:k + 1],
                                                       in1=rstd[:, i, 0:n], op0=ALU.mult, op1=ALU.mult).then_inc(scaled.handle, 1)
        st.used[-1] = (chain, 2 * len(streams))


def project_stage(core, name, tiles, widths, keep):
    nc = core.nc
    n0 = core.used
    todo = [(c, t) for c in range(len(widths)) for t in tiles[c]]
    with Stage(core, name) as st:
        acc = [st.ps(f"acc{i}") for i in range(4)]
        done = st.counter("proj_done", len(todo))
        kept = [st.counter("proj_kept_act", (len(todo) + 1) // 2), st.counter("proj_kept_dve", len(todo) // 2)]
        with st.run() as block:
            @block.sync
            def _(sp):
                core.used = n0 + len(widths)
                core.stream(sp, core.used)

            @block.tensor
            def _(pe):
                for i, (c, t) in enumerate(todo):
                    if t == tiles[c][0]:
                        core.await_chunk(pe, n0 + c)
                    if i >= 4:
                        pe.wait_ge(kept[i % 2].handle, kept[i % 2].at((i - 4) // 2 + 1))
                    w = by_k(core.slot(n0 + c), widths[c])
                    for k in range(KD):
                        last = nc.tensor.matmul(acc[i % 4][:, 0:widths[c]], core.h[:, k, t * P:(t + 1) * P], w[:, k, :],
                                                start=(k == 0), stop=(k == KD - 1))
                    last.then_inc(done.handle, 1)

            @block.scalar
            def _(act):
                for i, (c, t) in enumerate(todo):
                    if i % 2 == 0:
                        act.wait_ge(done.handle, done.at(i + 1))
                        nc.scalar.copy(keep(t, c), acc[i % 4][:, 0:widths[c]]).then_inc(kept[0].handle, 1)

            @block.vector
            def _(dve):
                for i, (c, t) in enumerate(todo):
                    if i % 2 == 1:
                        dve.wait_ge(done.handle, done.at(i + 1))
                        nc.vector.tensor_copy(keep(t, c), acc[i % 4][:, 0:widths[c]]).then_inc(kept[1].handle, 1)

            @block.gpsimd
            def _(pool):
                for c in range(len(widths)):
                    pool.wait_ge(done.handle, done.at(sum(len(t) for t in tiles[:c + 1])))
                    pool.sem_inc(core.freed.handle, 1)


def residual_stage(core, name, gate=None):
    nc = core.nc
    n0 = core.used
    with Stage(core, name) as st:
        acc = [st.ps(f"acc{i}") for i in range(2)]
        done = st.counter("res_done", KD)
        added = st.counter("res_added", KD)
        with st.run() as block:
            @block.sync
            def _(sp):
                core.used = n0 + 2
                core.stream(sp, core.used)

            @block.tensor
            def _(pe):
                for j in range(KD):
                    c, o = j // 4, (j % 4) * P
                    if j % 4 == 0:
                        core.await_chunk(pe, n0 + c)
                    if j >= 2:
                        pe.wait_ge(added.handle, added.at(j - 1))
                    w = by_k(core.slot(n0 + c))
                    for k in range(KD):
                        last = nc.tensor.matmul(acc[j % 2][:], w[:, k, o:o + P], core.h[:, k, 0:SEQ], start=(k == 0), stop=(k == KD - 1))
                    last.then_inc(done.handle, 1)

            @block.vector
            def _(dve):
                for j in range(KD):
                    dve.wait_ge(done.handle, done.at(j + 1))
                    if gate is None:
                        ins = nc.vector.tensor_tensor(core.x[:, j, 0:SEQ], acc[j % 2][:], core.x[:, j, 0:SEQ], ALU.add)
                    else:
                        ins = nc.vector.scalar_tensor_tensor(out=core.x[:, j, 0:SEQ], in0=acc[j % 2][:], scalar=gate[:, j:j + 1],
                                                             in1=core.x[:, j, 0:SEQ], op0=ALU.mult, op1=ALU.add)
                    ins.then_inc(added.handle, 1)

            @block.gpsimd
            def _(pool):
                for c in range(2):
                    pool.wait_ge(done.handle, done.at(4 * c + 4))
                    pool.sem_inc(core.freed.handle, 1)


def mlp_stage(core):
    nc = core.nc
    n_up = FF // CW
    n0 = core.used
    with Stage(core, "mlp") as outer:
        u = outer.sb("u", [P, FF // P, SEQ])
        with Stage(core, "up") as st:
            acc = [st.ps(f"acc{i}") for i in range(2)]
            tiles = FF // P
            done = st.counter("up_done", tiles)
            rectified = st.counter("up_rectified", tiles)
            with st.run() as block:
                @block.sync
                def _(sp):
                    core.used = n0 + n_up
                    core.stream(sp, core.used)

                @block.tensor
                def _(pe):
                    for f in range(tiles):
                        c, o = f // 4, (f % 4) * P
                        if f % 4 == 0:
                            core.await_chunk(pe, n0 + c)
                        if f >= 2:
                            pe.wait_ge(rectified.handle, rectified.at(f - 1))
                        w = by_k(core.slot(n0 + c))
                        for k in range(KD):
                            last = nc.tensor.matmul(acc[f % 2][:], w[:, k, o:o + P], core.h[:, k, 0:SEQ], start=(k == 0), stop=(k == KD - 1))
                        last.then_inc(done.handle, 1)

                @block.scalar
                def _(act):
                    for f in range(tiles):
                        act.wait_ge(done.handle, done.at(f + 1))
                        nc.scalar.activation(u[:, f, :], acc[f % 2][:], ACT.Relu).then_inc(rectified.handle, 1)

                @block.vector
                def _(dve):
                    for f in range(tiles):
                        dve.wait_ge(rectified.handle, rectified.at(f + 1))
                        nc.vector.tensor_tensor(u[:, f, :], u[:, f, :], u[:, f, :], ALU.mult)

                @block.gpsimd
                def _(pool):
                    for c in range(n_up):
                        pool.wait_ge(done.handle, done.at(4 * c + 4))
                        pool.sem_inc(core.freed.handle, 1)
        n1 = n0 + n_up
        with Stage(core, "down") as st:
            acc = [st.ps(f"acc{i}") for i in range(KD)]
            done = st.counter("down_done", n_up + KD - 1)
            with st.run() as block:
                @block.sync
                def _(sp):
                    core.used = n1 + n_up
                    core.stream(sp, core.used)

                @block.tensor
                def _(pe):
                    for c in range(n_up):
                        core.await_chunk(pe, n1 + c)
                        w = by_k(core.slot(n1 + c), D, 4)
                        for j in range(KD):
                            for f in range(4):
                                last = nc.tensor.matmul(acc[j][:], w[:, f, j * P:(j + 1) * P], u[:, 4 * c + f, :],
                                                        start=(c == 0 and f == 0), stop=(c == n_up - 1 and f == 3))
                            if c == n_up - 1 or j == KD - 1:
                                last.then_inc(done.handle, 1)

                @block.gpsimd
                def _(pool):
                    for c in range(n_up):
                        pool.wait_ge(done.handle, done.at(c + 1 if c < n_up - 1 else n_up + KD - 1))
                        pool.sem_inc(core.freed.handle, 1)

                @block.vector
                def _(dve):
                    for j in range(KD):
                        dve.wait_ge(done.handle, done.at(n_up + j))
                        nc.vector.tensor_tensor(core.x[:, j, 0:SEQ], acc[j][:], core.x[:, j, 0:SEQ], ALU.add)


def rms_rows(nc, act, squares, x, scratch, signal):
    nc.scalar.activation(scratch, x, ACT.Square).then_inc(signal.handle, 1)


def head_norm_stage(core, cols):
    nc = core.nc
    spans = [(A_Q, 8, HD), (C_Q, 8, HD), (D_Q, 6, HD), (B_QL, 1, 256), (B_KVL, 1, 128)]
    with Stage(core, "heads") as st:
        square = st.sb("square", [P, 2, 512])
        ss = st.sb("ss", [P, LT, 24])
        rstd = st.sb("rstd", [P, LT, 24])
        n = LT * len(spans)
        squared = st.counter("head_squared", n)
        reduced = st.counter("head_reduced", n)
        inverted = st.counter("head_inverted", 1)
        rooted = st.counter("head_rooted", 1)
        chain = st.counter("head_chain", 2)
        at, offs = 0, []
        for _, heads, _ in spans:
            offs.append(at)
            at += heads
        todo = [(t, s) for t in range(LT) for s in range(len(spans))]
        with st.run() as block:
            @block.scalar
            def _(act):
                for i, (t, s) in enumerate(todo):
                    c, heads, w = spans[s]
                    if i >= 2:
                        act.wait_ge(reduced.handle, reduced.at(i - 1))
                    nc.scalar.activation(square[:, i % 2, 0:heads * w], cols[:, t, c:c + heads * w], ACT.Square,
                                         scale=float(w) ** -0.5).then_inc(squared.handle, 1)
                act.wait_ge(inverted.handle, inverted.at(1))
                nc.scalar.activation(rstd[:], ss[:], ACT.Sqrt).then_inc(rooted.handle, 1)

            @block.vector
            def _(dve):
                link = Link(dve, chain)
                for i, (t, s) in enumerate(todo):
                    c, heads, w = spans[s]
                    dve.wait_ge(squared.handle, squared.at(i + 1))
                    nc.vector.tensor_reduce(ss[:, t, offs[s]:offs[s] + heads],
                                            square[:, i % 2, 0:heads * w].rearrange("p (h w) -> p h w", w=w),
                                            AX_X, ALU.add).then_inc(reduced.handle, 1)
                dve.wait_ge(reduced.handle, reduced.at(n))
                link(nc.vector.tensor_scalar(ss[:], ss[:], EPS, None, ALU.add))
                nc.vector.reciprocal(ss[:], ss[:]).then_inc(inverted.handle, 1)
                dve.wait_ge(rooted.handle, rooted.at(1))
                for t, s in todo:
                    c, heads, w = spans[s]
                    v = cols[:, t, c:c + heads * w].rearrange("p (h w) -> p h w", w=w)
                    nc.vector.tensor_tensor(v, v, rstd[:, t, offs[s]:offs[s] + heads].unsqueeze(2).to_broadcast([P, heads, w]), ALU.mult)
        st.used[-1] = (chain, 1)


def mla_stage(core, cols, q, kf, ukv):
    nc, ins = core.nc, core.ins
    with Stage(core, "mla") as st:
        uq = st.sb("uq", [P, 2, HEADS * MLA_DIM])
        uk = st.sb("uk", [P, 512])
        gains = st.sb("gains", [P, 2, MLA_DIM])
        rope = st.sb("rope", [P, 2, LT, 16])
        lat = st.sb("lat", [P, 3, SEQ])
        square = st.sb("square", [P, 16 * MLA_DIM])
        ss = st.sb("ss", [P, 2, 16])
        rstd = st.sb("rstd", [P, 2, 16])
        tmp = st.sb("tmp", [P, 4, LT, HEADS, 16])
        pl = [st.ps(f"pl{i}") for i in range(3)]
        pq = [st.ps(f"pq{i}") for i in range(2)]
        pk = [st.ps(f"pk{i}") for i in range(2)]
        loaded = st.counter("mla_loaded", 16 * 6)
        turned = st.counter("mla_turned", 3)
        lat_kept = st.counter("mla_lat_kept", 3)
        up_q = st.counter("mla_up_q", LT)
        up_k = st.counter("mla_up_k", LT)
        q_kept = st.counter("mla_q_kept", LT)
        k_kept = st.counter("mla_k_kept", LT)
        k_built = st.counter("mla_k_built", 2 * LT)
        squared = st.counter("mla_squared", 2)
        inverted = st.counter("mla_inverted", 1)
        rooted = st.counter("mla_rooted", 1)
        reduced = st.counter("mla_reduced", 2)
        chain = st.counter("mla_chain", 8 + 3)
        with st.run() as block:
            @block.sync
            def _(sp):
                sp.dma_start(uq[:], ins["mla_w_uq"][0].rearrange("(k p) n -> p k n", p=P)).then_inc(loaded.handle, 16)
                sp.dma_start(uk[:], ins["mla_w_ukv"][0]).then_inc(loaded.handle, 16)
                sp.dma_start(gains[:, 0, :], ins["mla_q_g"][0].partition_broadcast(P)).then_inc(loaded.handle, 16)
                sp.dma_start(gains[:, 1, :], ins["mla_k_g"][0].partition_broadcast(P)).then_inc(loaded.handle, 16)
                sp.dma_start(rope[:, 0], core.consts["rope_cos"]).then_inc(loaded.handle, 16)
                sp.dma_start(rope[:, 1], core.consts["rope_sin"]).then_inc(loaded.handle, 16)

            @block.tensor
            def _(pe):
                for j, c in enumerate((B_QL, B_QL + P, B_KVL)):
                    for t in range(LT):
                        last = nc.tensor.transpose(pl[j][:, t * P:(t + 1) * P], cols[:, t, c:c + P], core.ident[:])
                    last.then_inc(turned.handle, 1)
                pe.wait_ge(loaded.handle, loaded.at(96))
                pe.wait_ge(lat_kept.handle, lat_kept.at(3))
                for t in range(LT):
                    if t >= 2:
                        pe.wait_ge(q_kept.handle, q_kept.at(t - 1))
                        pe.wait_ge(k_kept.handle, k_kept.at(t - 1))
                    for j in range(2):
                        last = nc.tensor.matmul(pq[t % 2][:, 0:HEADS * MLA_DIM], lat[:, j, t * P:(t + 1) * P], uq[:, j, :], start=(j == 0), stop=(j == 1))
                    last.then_inc(up_q.handle, 1)
                    nc.tensor.matmul(pk[t % 2][:], lat[:, 2, t * P:(t + 1) * P], uk[:], start=True, stop=True).then_inc(up_k.handle, 1)

            @block.scalar
            def _(act):
                for t in range(LT):
                    act.wait_ge(up_k.handle, up_k.at(t + 1))
                    nc.scalar.copy(ukv[:, t, :], pk[t % 2][:]).then_inc(k_kept.handle, 1)
                for i, (v, ready, n) in enumerate(((q, q_kept, LT), (kf, k_built, 2 * LT))):
                    act.wait_ge(ready.handle, ready.at(n))
                    if i:
                        act.wait_ge(reduced.handle, reduced.at(1))
                    nc.scalar.activation(square[:], v[:].rearrange("p t h w -> p (t h w)"), ACT.Square, scale=float(MLA_DIM) ** -0.5).then_inc(squared.handle, 1)
                act.wait_ge(inverted.handle, inverted.at(1))
                nc.scalar.activation(rstd[:], ss[:], ACT.Sqrt).then_inc(rooted.handle, 1)

            @block.gpsimd
            def _(pool):
                for t in range(LT):
                    pool.wait_ge(k_kept.handle, k_kept.at(t + 1))
                    nc.gpsimd.tensor_copy(kf[:, t, :, 0:HD], ukv[:, t, :].rearrange("p (h w) -> p h w", h=HEADS)[:, :, 0:HD]).then_inc(k_built.handle, 1)
                    nc.gpsimd.tensor_copy(kf[:, t, :, HD:MLA_DIM], cols[:, t, B_KR:B_KR + 32].unsqueeze(1).to_broadcast([P, HEADS, 32])).then_inc(k_built.handle, 1)

            @block.vector
            def _(dve):
                link = Link(dve, chain)
                for j, g in enumerate((core.col("mla_qlat_g", 0, 1), core.col("mla_qlat_g", 1, 1), core.col("mla_kvlat_g"))):
                    dve.wait_ge(turned.handle, turned.at(j + 1))
                    nc.vector.tensor_scalar(lat[:, j, :], pl[j][:], g, None, ALU.mult).then_inc(lat_kept.handle, 1)
                for t in range(LT):
                    dve.wait_ge(up_q.handle, up_q.at(t + 1))
                    nc.vector.tensor_copy(q[:, t].rearrange("p h w -> p (h w)"), pq[t % 2][:, 0:HEADS * MLA_DIM]).then_inc(q_kept.handle, 1)
                for i in range(2):
                    dve.wait_ge(squared.handle, squared.at(i + 1))
                    nc.vector.tensor_reduce(ss[:, i, :], square[:].rearrange("p (g w) -> p g w", w=MLA_DIM), AX_X, ALU.add).then_inc(reduced.handle, 1)
                dve.wait_ge(reduced.handle, reduced.at(2))
                link(nc.vector.tensor_scalar(ss[:], ss[:], EPS, None, ALU.add))
                nc.vector.reciprocal(ss[:], ss[:]).then_inc(inverted.handle, 1)
                dve.wait_ge(rooted.handle, rooted.at(1))
                for i, v in enumerate((q, kf)):
                    flat = v[:].rearrange("p t h w -> p (t h) w")
                    link(nc.vector.tensor_tensor(flat, flat, rstd[:, i, :].unsqueeze(2).to_broadcast([P, 16, MLA_DIM]), ALU.mult))
                    link(nc.vector.tensor_tensor(flat, flat, gains[:, i, :].unsqueeze(1).to_broadcast([P, 16, MLA_DIM]), ALU.mult))
                    x1, x2 = v[:, :, :, HD:HD + 16], v[:, :, :, HD + 16:MLA_DIM]
                    cos, sin = (rope[:, j].unsqueeze(2).to_broadcast([P, LT, HEADS, 16]) for j in range(2))
                    nc.vector.tensor_tensor(tmp[:, 0], x1, cos, ALU.mult)
                    nc.vector.tensor_tensor(tmp[:, 1], x2, sin, ALU.mult)
                    nc.vector.tensor_tensor(tmp[:, 2], x1, sin, ALU.mult)
                    link(nc.vector.tensor_tensor(tmp[:, 3], x2, cos, ALU.mult))
                    nc.vector.tensor_tensor(x1, tmp[:, 0], tmp[:, 1], ALU.subtract)
                    link(nc.vector.tensor_tensor(x2, tmp[:, 2], tmp[:, 3], ALU.add))
        st.used[-1] = (chain, 9)


def turn_heads_stage(core, name, jobs, zero=(), extra=None):
    nc = core.nc
    with Stage(core, name) as st:
        bank = [st.ps(f"bank{i}", 2) for i in range(2)]
        turned = st.counter("turn_turned", len(jobs))
        kept = st.counter("turn_kept", sum(len(j[3]) for j in jobs))
        ends, n = [], 0
        for j in jobs:
            n += len(j[3])
            ends.append(n)
        loaded = st.counter("turn_loaded", 16 * (0 if extra is None else extra(None, None)))
        with st.run() as block:
            if extra is not None:
                @block.sync
                def _(sp):
                    extra(sp, loaded)

            @block.tensor
            def _(pe):
                for i, (src, tiles, w, dsts, gain, scale) in enumerate(jobs):
                    if i >= 2:
                        pe.wait_ge(kept.handle, kept.at(ends[i - 2]))
                    for t in range(tiles):
                        last = nc.tensor.transpose(bank[i % 2][0:w, t * P:(t + 1) * P], src(t), core.ident[:])
                    last.then_inc(turned.handle, 1)

            @block.vector
            def _(dve):
                if extra is not None:
                    dve.wait_ge(loaded.handle, loaded.at(16 * extra(None, None)))
                for z in zero:
                    nc.vector.memset(z, 0.0)
                for i, (src, tiles, w, dsts, gain, scale) in enumerate(jobs):
                    dve.wait_ge(turned.handle, turned.at(i + 1))
                    for d in dsts:
                        s = bank[i % 2][0:w, 0:tiles * P]
                        if gain is None:
                            ins_ = nc.vector.tensor_scalar(d, s, scale, None, ALU.mult)
                        else:
                            ins_ = nc.vector.tensor_scalar(d, s, gain, scale, ALU.mult, ALU.mult)
                        ins_.then_inc(kept.handle, 1)


def attention_stage(core, name, turns, per, dim, q_tiles, keys, q, k_of, v_of, bias_of, out_of, sink_of=None):
    nc = core.nc
    steps = per * q_tiles
    pieces = [keys(i) for i in range(q_tiles)]
    width = max(sum(n for _, n, _ in p) for p in pieces)
    npc = max(len(p) for p in pieces)
    with Stage(core, name) as st:
        q_now = st.sb("q_now", [dim, 2, q_tiles * P])
        s = st.sb("s", [P, 2, width + 1])
        p = st.sb("p", [P, 2, width + 1])
        pt = st.sb("pt", [P, 2, width])
        top = st.sb("top", [P, 2])
        total = st.sb("total", [P, 2])
        inv = st.sb("inv", [P, 2])
        ps_s = [st.ps(f"scores{i}", npc) for i in range(2)]
        ps_t = st.ps("turned", 2)
        ps_o = [st.ps(f"out{i}") for i in range(2)]
        N = turns * steps
        q_staged = st.counter("att_q_staged", turns * per)
        held = 2 * q_tiles
        scored = st.counter("att_scored", N + held)
        biased = st.counter("att_biased", N + 2)
        topped = st.counter("att_topped", N)
        raised = st.counter("att_raised", N + 2)
        turned = st.counter("att_turned", N)
        copied = st.counter("att_copied", N + 1)
        weighed = st.counter("att_weighed", N + 2)
        normed = st.counter("att_normed", N + 2)
        summed = st.counter("att_summed", N)
        off = 0 if sink_of is None else 1
        n_of = [sum(n for _, n, _ in pc) for pc in pieces]

        with st.run() as block:
            @block.sync
            def _(sp):
                core.stream(sp, core.used)

            @block.gpsimd
            def _(pool):
                with pool.Fori(0, turns) as it:
                    for r in range(per):
                        pool.wait_ge(scored.handle, it * steps + scored.at((r + 1) * q_tiles))
                        nc.gpsimd.tensor_copy(q_now[:, r % 2, :], q[:, bass.ds(it * per + r, 1), :].rearrange("p a n -> p (a n)")).then_inc(q_staged.handle, 1)

            @block.tensor
            def _(pe):
                def score(it, g):
                    r, i = divmod(g, q_tiles)
                    if i == 0:
                        pe.wait_ge(q_staged.handle, it * per + q_staged.at(r + 1))
                    pe.wait_ge(biased.handle, it * steps + biased.at(g + 1))
                    for b, (k0, n, _) in enumerate(pieces[i]):
                        last = nc.tensor.matmul(ps_s[g % 2][:, b * 512:b * 512 + n], q_now[:, r % 2, i * P:(i + 1) * P], k_of(it, r, k0, n), start=True, stop=True)
                    last.then_inc(scored.handle, 1)

                def turn(it, g):
                    i = g % q_tiles
                    pe.wait_ge(raised.handle, it * steps + raised.at(g + 3))
                    pe.wait_ge(copied.handle, it * steps + copied.at(g + 1))
                    for j in range(n_of[i] // P):
                        last = nc.tensor.transpose(ps_t[:, j * P:(j + 1) * P], p[:, g % 2, off + j * P:off + (j + 1) * P], core.ident[:])
                    last.then_inc(turned.handle, 1)

                def weigh(it, g):
                    r, i = divmod(g, q_tiles)
                    pe.wait_ge(copied.handle, it * steps + copied.at(g + 2))
                    pe.wait_ge(normed.handle, it * steps + normed.at(g + 1))
                    tiles = [(k0 + j * P) // P for k0, n, _ in pieces[i] for j in range(n // P)]
                    for j, kt in enumerate(tiles):
                        last = nc.tensor.matmul(ps_o[g % 2][:, 0:HD], pt[:, g % 2, j * P:(j + 1) * P], v_of(it, r, kt), start=(j == 0), stop=(j == len(tiles) - 1))
                    last.then_inc(weighed.handle, 1)

                pe.sem_inc(scored.handle, held)
                pe.sem_inc(weighed.handle, 2)
                with pe.Fori(0, turns) as it:
                    score(it, 0)
                    for g in range(steps):
                        if g + 1 < steps:
                            score(it, g + 1)
                        turn(it, g)
                        if g:
                            weigh(it, g - 1)
                    weigh(it, steps - 1)

            @block.vector
            def _(dve):
                def bias(it, g):
                    r, i = divmod(g, q_tiles)
                    dve.wait_ge(scored.handle, it * steps + scored.at(g + 1 + held))
                    dve.wait_ge(raised.handle, it * steps + raised.at(g + 1))
                    at = off
                    if off:
                        nc.vector.tensor_scalar(s[:, g % 2, 0:1], sink_of(it, r), 1.0, None, ALU.mult)
                    for b, (k0, n, bs) in enumerate(pieces[i]):
                        src = ps_s[g % 2][:, b * 512:b * 512 + n]
                        if bs is None:
                            last = nc.vector.tensor_copy(s[:, g % 2, at:at + n], src)
                        else:
                            last = nc.vector.tensor_tensor(s[:, g % 2, at:at + n], src, bias_of(it, r, *bs), ALU.add)
                        at += n
                    last.then_inc(biased.handle, 1)
                    dve.wait_ge(biased.handle, it * steps + biased.at(g + 3))
                    nc.vector.tensor_reduce(top[:, g % 2:g % 2 + 1], s[:, g % 2, 0:at], AX_X, ALU.max, negate=True).then_inc(topped.handle, 1)

                def norm(it, g):
                    r, i = divmod(g, q_tiles)
                    dve.wait_ge(weighed.handle, it * steps + weighed.at(g + 3))
                    dve.wait_ge(raised.handle, it * steps + raised.at(g + 3))
                    nc.vector.reciprocal(inv[:, g % 2:g % 2 + 1], total[:, g % 2:g % 2 + 1]).then_inc(summed.handle, 1)
                    dve.wait_ge(summed.handle, it * steps + summed.at(g + 1))
                    nc.vector.tensor_scalar(out_of(it, r, i), ps_o[g % 2][:, 0:HD], inv[:, g % 2:g % 2 + 1], None, ALU.mult).then_inc(normed.handle, 1)

                dve.sem_inc(biased.handle, 2)
                dve.sem_inc(normed.handle, 2)
                with dve.Fori(0, turns) as it:
                    for g in range(steps):
                        bias(it, g)
                        if g:
                            norm(it, g - 1)
                    norm(it, steps - 1)

            @block.scalar
            def _(act):
                act.sem_inc(copied.handle, 1)
                act.sem_inc(raised.handle, 2)
                with act.Fori(0, turns) as it:
                    for g in range(steps):
                        i = g % q_tiles
                        n = n_of[i] + off
                        act.wait_ge(topped.handle, it * steps + topped.at(g + 1))
                        act.wait_ge(normed.handle, it * steps + normed.at(g + 1))
                        nc.scalar.activation(p[:, g % 2, 0:n], s[:, g % 2, 0:n], ACT.Exp, bias=top[:, g % 2:g % 2 + 1],
                                             accum_out=total[:, g % 2:g % 2 + 1]).then_inc(raised.handle, 1)
                        act.wait_ge(turned.handle, it * steps + turned.at(g + 1))
                        act.wait_ge(weighed.handle, it * steps + weighed.at(g + 1))
                        nc.scalar.copy(pt[:, g % 2, 0:n_of[i]], ps_t[:, 0:n_of[i]]).then_inc(copied.handle, 1)


def group_norm_stage(core, o):
    nc = core.nc
    G, W = 4, 256
    with Stage(core, "groups") as st:
        square = st.sb("square", [P, LT * G, W])
        ss = st.sb("ss", [P, LT * G])
        rstd = st.sb("rstd", [P, LT * G])
        bank = [st.ps(f"bank{i}") for i in range(2)]
        squared = st.counter("group_squared", 1)
        inverted = st.counter("group_inverted", 1)
        rooted = st.counter("group_rooted", 1)
        scaled = st.counter("group_scaled", LT * G)
        turned = st.counter("group_turned", KD)
        kept = st.counter("group_kept", KD)
        chain = st.counter("group_chain", 1)
        with st.run() as block:
            @block.scalar
            def _(act):
                for t in range(LT):
                    for g in range(G):
                        last = nc.scalar.activation(square[:, t * G + g, :], o[:, t, g * W:(g + 1) * W], ACT.Square, scale=float(W) ** -0.5,
                                                    accum_out=ss[:, t * G + g:t * G + g + 1])
                last.then_inc(squared.handle, 1)
                act.wait_ge(inverted.handle, inverted.at(1))
                nc.scalar.activation(rstd[:], ss[:], ACT.Sqrt).then_inc(rooted.handle, 1)

            @block.vector
            def _(dve):
                link = Link(dve, chain)
                dve.wait_ge(squared.handle, squared.at(1))
                link(nc.vector.tensor_scalar(ss[:], ss[:], EPS, None, ALU.add))
                nc.vector.reciprocal(ss[:], ss[:]).then_inc(inverted.handle, 1)
                dve.wait_ge(rooted.handle, rooted.at(1))
                for g in range(G):
                    for t in range(LT):
                        v = o[:, t, g * W:(g + 1) * W]
                        nc.vector.tensor_scalar(v, v, rstd[:, t * G + g:t * G + g + 1], None, ALU.mult).then_inc(scaled.handle, 1)
                for k in range(KD):
                    dve.wait_ge(turned.handle, turned.at(k + 1))
                    nc.vector.tensor_scalar(core.h[:, k, 0:SEQ], bank[k % 2][:], core.col("group_out_g", k, 1), None, ALU.mult).then_inc(kept.handle, 1)

            @block.tensor
            def _(pe):
                for k in range(KD):
                    pe.wait_ge(scaled.handle, scaled.at(LT * (k // 2 + 1)))
                    if k >= 2:
                        pe.wait_ge(kept.handle, kept.at(k - 1))
                    for t in range(LT):
                        last = nc.tensor.transpose(bank[k % 2][:, t * P:(t + 1) * P], o[:, t, k * P:(k + 1) * P], core.ident[:])
                    last.then_inc(turned.handle, 1)


def turn_tokens_stage(core, name, src, dst, tiles):
    nc = core.nc
    with Stage(core, name) as st:
        bank = [st.ps(f"bank{i}") for i in range(4)]
        todo = [(t, j) for t in tiles for j in range(2)]
        turned = st.counter("back_turned", len(todo))
        kept = [st.counter("back_kept_act", len(todo) // 2), st.counter("back_kept_dve", len(todo) // 2)]
        with st.run() as block:
            @block.tensor
            def _(pe):
                for i, (t, j) in enumerate(todo):
                    if i >= 4:
                        pe.wait_ge(kept[i % 2].handle, kept[i % 2].at((i - 4) // 2 + 1))
                    for k in range(4):
                        last = nc.tensor.transpose(bank[i % 4][:, k * P:(k + 1) * P], src[:, 4 * j + k, t * P:(t + 1) * P], core.ident[:])
                    last.then_inc(turned.handle, 1)

            @block.scalar
            def _(act):
                for i, (t, j) in enumerate(todo):
                    if i % 2 == 0:
                        act.wait_ge(turned.handle, turned.at(i + 1))
                        nc.scalar.copy(dst[:, t, j * 512:(j + 1) * 512], bank[i % 4][:]).then_inc(kept[0].handle, 1)

            @block.vector
            def _(dve):
                for i, (t, j) in enumerate(todo):
                    if i % 2 == 1:
                        dve.wait_ge(turned.handle, turned.at(i + 1))
                        nc.vector.tensor_copy(dst[:, t, j * 512:(j + 1) * 512], bank[i % 4][:]).then_inc(kept[1].handle, 1)


def first_block(core):
    nc, ins = core.nc, core.ins
    norm_stage(core, "norm_a", [(0, SEQ, core.col("attn_norm_g"), None, None)])
    with Stage(core, "mixers") as mx:
        cols = mx.sb("cols", [P, LT, IN_COLS])
        o = mx.sb("o", [P, LT, D])
        widths = [CW] * 4 + [IN_COLS - 4 * CW]
        project_stage(core, "w_in", [range(LT)] * len(widths), widths, lambda t, c: cols[:, t, c * CW:c * CW + widths[c]])
        head_norm_stage(core, cols)
        spare = core.h[:].rearrange("p k n -> p (k n)")
        n = HEADS * MLA_DIM
        q96 = spare[:, 0:LT * n].rearrange("p (t h w) -> p t h w", t=LT, h=HEADS)
        k96 = spare[:, LT * n:2 * LT * n].rearrange("p (t h w) -> p t h w", t=LT, h=HEADS)
        ukv = spare[:, 2 * LT * n:2 * LT * n + LT * 512].rearrange("p (t w) -> p t w", t=LT)
        mla_stage(core, cols, q96, k96, ukv)
        for g, (name, dim) in enumerate((("moba", HD), ("mla", MLA_DIM), ("dil", HD), ("swa", HD))):
            with Stage(core, f"g_{name}") as gs:
                qT = gs.sb("qT", [MLA_DIM, HEADS, SEQ])
                kv = 2 if name == "swa" else HEADS
                kT = gs.sb("kT", [MLA_DIM, kv, SEQ])
                table = gs.sb("table", [P, HEADS, SEQ])
                gain = gs.sb("gain", [HD, 2])
                sink = gs.sb("sink", [P, HEADS])

                def extra(sp, loaded, name=name, g=g, gain=gain, table=table, sink=sink):
                    todo = [(table[:], core.consts["bias"][g])]
                    if name != "mla":
                        for j in range(2):
                            todo.append((gain[:, j:j + 1], ins[f"{name}_{'qk'[j]}_g"][0].unsqueeze(1)))
                    if name == "swa":
                        todo.append((sink[:], ins["swa_sinks"][0].partition_broadcast(P)))
                    if sp is not None:
                        for d, s in todo:
                            sp.dma_start(d, s).then_inc(loaded.handle, 16)
                    return len(todo)

                jobs = []
                for dst, at, heads, j in ((qT, (A_Q, 0, C_Q, D_Q)[g], HEADS, 0), (kT, (A_K, 0, C_K, D_K)[g], kv, 1)):
                    for hd in range(heads):
                        if name == "mla":
                            src = lambda t, v=(q96, k96)[j], hd=hd: v[:, t, hd, :]
                            jobs.append((src, LT, dim, [dst[0:dim, hd, :]], None, float(dim) ** -0.5 if j == 0 else 1.0))
                        else:
                            src = lambda t, c=at + hd * HD: cols[:, t, c:c + HD]
                            jobs.append((src, LT, dim, [dst[0:dim, hd, :]], gain[:, j:j + 1], float(dim) ** -0.5 if j == 0 else 1.0))
                turn_heads_stage(core, f"turn_{name}", jobs, zero=[] if dim == MLA_DIM else [qT[dim:MLA_DIM], kT[dim:MLA_DIM]], extra=extra)
                per = 2

                def k_of(it, r, k0, n, kT=kT, name=name):
                    head = it if name == "swa" else it * per + r
                    return kT[:, bass.ds(head, 1), k0:k0 + n].rearrange("p a n -> p (a n)")

                def v_of(it, r, kt, name=name):
                    if name == "mla":
                        return ukv[:, kt, bass.ds(it * (2 * per * HD) + (r * 2 * HD + HD), HD)]
                    if name == "swa":
                        return cols[:, kt, bass.ds(it * HD + D_V, HD)]
                    return cols[:, kt, bass.ds(it * (per * HD) + ((A_V if name == "moba" else C_V) + r * HD), HD)]

                attention_stage(
                    core, f"att_{name}", HEADS // per, per, MLA_DIM, LT,
                    lambda i: [(0, (i + 1) * P, (SEQ - (i + 1) * P, SEQ))], qT, k_of, v_of,
                    lambda it, r, a, b, table=table: table[:, bass.ds(it * per + r, 1), a:b].rearrange("p a n -> p (a n)"),
                    lambda it, r, i, g=g: o[:, i, bass.ds(it * (per * HD) + (g * 256 + r * HD), HD)],
                    (lambda it, r, sink=sink: sink[:, bass.ds(it * per + r, 1)]) if name == "swa" else None)
        group_norm_stage(core, o)
    residual_stage(core, "w_o")
    norm_stage(core, "norm_m", [(0, SEQ, core.col("mlp_norm_g"), None, None)])
    mlp_stage(core)


QC = 256
TURNS = D // QC
UP = 772
CTX_AT = SEQ + 2


def filter_net_stage(core, h2):
    nc, ins = core.nc, core.ins
    with Stage(core, "fnet") as st:
        z = st.sb("z", [33, TOK])
        w1 = st.sb("w1", [33, 64])
        w2 = st.sb("w2", [64, 64])
        col = st.sb("col", [64, 4])
        arg = st.sb("arg", [64, TOK])
        turns = st.sb("turns", [64, TOK])
        h1 = st.sb("h1", [64, TOK])
        acc = [st.ps(f"acc{i}", 2) for i in range(2)]
        loaded = st.counter("fnet_loaded", 16 * 7)
        done = st.counter("fnet_done", 2)
        reduced = st.counter("fnet_reduced", 2)
        bent = st.counter("fnet_bent", 2)
        chain = st.counter("fnet_chain", 12)
        spans = ((0, SEQ), (SEQ, CTX))
        with st.run() as block:
            @block.sync
            def _(sp):
                sp.dma_start(z[:], core.consts["filter_z"]).then_inc(loaded.handle, 16)
                sp.dma_start(w1[:], ins["hy_ffn_w1_2"]).then_inc(loaded.handle, 16)
                sp.dma_start(w2[:], ins["hy_ffn_w2_2"]).then_inc(loaded.handle, 16)
                sp.dma_start(col[:, 0:1], ins["hy_ffn_b1_2"].unsqueeze(1)).then_inc(loaded.handle, 16)
                sp.dma_start(col[:, 1:2], ins["hy_ffn_b2_2"].unsqueeze(1)).then_inc(loaded.handle, 16)
                sp.dma_start(col[:, 2:3], ins["hy_sin_freq_2"][0].unsqueeze(1)).then_inc(loaded.handle, 16)
                sp.dma_start(col[:, 3:4], ins["hy_sin_freq_2"][1].unsqueeze(1)).then_inc(loaded.handle, 16)

            @block.tensor
            def _(pe):
                pe.wait_ge(loaded.handle, loaded.at(112))
                for layer, (w, x) in enumerate(((w1, z), (w2, h1))):
                    if layer:
                        pe.wait_ge(bent.handle, bent.at(1))
                    for c0, n in spans:
                        last = nc.tensor.matmul(acc[layer][0:64, c0:c0 + n], w[:], x[:, c0:c0 + n], start=True, stop=True)
                    last.then_inc(done.handle, 1)

            @block.vector
            def _(dve):
                link = Link(dve, chain)
                dve.wait_ge(loaded.handle, loaded.at(112))
                for layer in range(2):
                    dve.wait_ge(done.handle, done.at(layer + 1))
                    link(nc.vector.tensor_scalar(arg[:], acc[layer][0:64, 0:TOK], col[:, layer:layer + 1], col[:, 2 + layer:3 + layer], ALU.add, ALU.mult))
                    link(nc.vector.tensor_scalar(turns[:], arg[:], 1.0 / TWO_PI, ROUND_MAGIC, ALU.mult, ALU.add))
                    link(nc.vector.tensor_scalar(turns[:], turns[:], -ROUND_MAGIC, None, ALU.add))
                    link(nc.vector.scalar_tensor_tensor(out=arg[:], in0=turns[:], scalar=-TWO_PI_HI, in1=arg[:], op0=ALU.mult, op1=ALU.add))
                    link(nc.vector.scalar_tensor_tensor(out=arg[:], in0=turns[:], scalar=-TWO_PI_LO, in1=arg[:], op0=ALU.mult, op1=ALU.add))
                    nc.vector.tensor_scalar(arg[:], arg[:], SIN_MAX, -SIN_MAX, ALU.min, ALU.max).then_inc(reduced.handle, 1)
                    dve.wait_ge(bent.handle, bent.at(layer + 1))

            @block.scalar
            def _(act):
                for layer, dst in enumerate((h1, h2)):
                    act.wait_ge(reduced.handle, reduced.at(layer + 1))
                    nc.scalar.activation(dst[:], arg[:], ACT.Sin).then_inc(bent.handle, 1)
        st.used[-1] = (chain, 10)


def hyena_chunks(core):
    w = core.ins["hy_w_in_2"].rearrange("(k p) (s c) -> p k s c", p=P, s=3)
    out = core.ins["hy_w_out_2"].rearrange("(q k p) n -> q p k n", p=P, k=2)

    def first(q):
        return lambda slot: [(slot[:].rearrange("p (k s c) -> p k s c", k=KD, s=2)[:, :, s], w[:, :, s, bass.ds(q * QC, QC)]) for s in range(2)]

    def second(q):
        return lambda slot: [(slot[:, 0:KD * QC].rearrange("p (k c) -> p k c", k=KD), w[:, :, 2, bass.ds(q * QC, QC)])]

    def third(q):
        return lambda slot: [(slot[:, 0:2 * D].rearrange("p (k n) -> p k n", k=2), out[bass.ds(q, 1)].rearrange("a p k n -> (a p) k n"))]
    return [first, second, third]


def hyena_stage(core, gate):
    nc, ins = core.nc, core.ins
    n0 = core.used
    x, h = core.x, core.h
    with Stage(core, "hyena") as st:
        h2 = st.sb("h2", [64, TOK])
        filter_net_stage(core, h2)
        tables = {n: st.sb(n, [P, 4, k, w]) for n, k, w in (("dft_l", 2, 256), ("idft_l", 2, 256), ("dft_c", 1, P), ("idft_c", 1, P))}
        raw = st.sb("raw", [P, 2, UP])
        u = st.sb("u", [P, 6, UP])
        v_tok = st.sb("v_tok", [P, 6, QC])
        ab = st.sb("ab", [P, 2, 2, 3, QC])
        taps = ab[:].rearrange("p a b c n -> p a (b c) n")
        pq = st.sb("pq", [P, 2, 2, 3, QC])
        win = st.sb("win", [P, 6, 2, QC])
        w3 = st.sb("w3", [64, 4, QC])
        even = st.sb("even", [P, 2, QC])
        t1 = st.sb("t1", [P, TOK])
        t2 = st.sb("t2", [P, TOK])
        lat = [st.ps(f"lat{i}") for i in range(2)]
        ctx = [st.ps(f"ctx{i}") for i in range(2)]
        spec = [st.ps(f"spec{i}") for i in range(4)]

        IP = ["act"] * 6 + ["act"] * 2 + ["dve"] * 2 + ["act"] * 2 + ["dve"] * 2 + ["dve"] * 8
        NI, NA, ND = len(IP), IP.count("act"), IP.count("dve")
        SP = 36
        rank = [IP[:i].count(IP[i]) for i in range(NI)]
        ip_done = st.counter("hy_ip_done", NI * TURNS)
        ip_act = st.counter("hy_ip_act", NA * TURNS)
        ip_dve = st.counter("hy_ip_dve", ND * TURNS + 2)
        sp_done = st.counter("hy_sp_done", SP * TURNS)
        sp_free = st.counter("hy_sp_free", SP * TURNS + 4)
        even_kept = st.counter("hy_even_kept", 24 * TURNS)
        raw_kept = st.counter("hy_raw_kept", 6 * TURNS)
        convolved = st.counter("hy_convolved", 6 * TURNS + 2)
        taps_made = st.counter("hy_taps_made", 12 * TURNS)
        tok_kept = st.counter("hy_tok_kept", 2 * TURNS)
        combined = st.counter("hy_combined", 2 * TURNS)
        gated = st.counter("hy_gated", 2 * TURNS)
        win_loaded = st.counter("hy_win_loaded", 32 * TURNS)
        tab_loaded = st.counter("hy_tab_loaded", 64)
        pads = st.counter("hy_pads", 1)
        chain = st.counter("hy_chain", 0)

        def parity(tile, c0, n):
            return tile[:, c0:c0 + n].rearrange("p (i a) -> p a i", a=2)

        with st.run() as block:
            @block.sync
            def _(sp):
                def load_filters(q):
                    sp.dma_start(win[:], core.consts["window"][:, :, :, bass.ds(q * QC, QC)]).then_inc(win_loaded.handle, 16)
                    sp.dma_start(w3[:], ins["hy_ffn_w3_2"].rearrange("a (o c) -> a o c", o=4)[:, :, bass.ds(q * QC, QC)]).then_inc(win_loaded.handle, 16)

                load_filters(0)
                for name, t in tables.items():
                    sp.dma_start(t[:], core.consts[name]).then_inc(tab_loaded.handle, 16)
                with sp.Fori(0, TURNS - 1) as it:
                    for j, place in enumerate(hyena_chunks(core)):
                        n = n0 + 3 + j
                        sp.wait_ge(core.freed.handle, it * 3 + (n - NS + 1))
                        core.issue(sp, n, place(it + 1))
                        if j == 1:
                            sp.wait_ge(taps_made.handle, it * 12 + taps_made.at(12))
                            load_filters(it + 1)
                core.used = core.issued = n0 + 3 * TURNS
                core.stream(sp, core.used)

            @block.tensor
            def _(pe):
                def take(it, i):
                    j = i - 2
                    if j < 0:
                        pe.wait_ge(ip_dve.handle, it * ND + ip_dve.at(rank[j] + 1 - ND + 2))
                    elif IP[j] == "act":
                        pe.wait_ge(ip_act.handle, it * NA + ip_act.at(rank[j] + 1))
                    else:
                        pe.wait_ge(ip_dve.handle, it * ND + ip_dve.at(rank[j] + 3))
                    return lat[i % 2], ctx[i % 2]

                def take_spec(it, m):
                    pe.wait_ge(sp_free.handle, it * SP + sp_free.at(m + 1))
                    return spec[m % 4]

                def filters(it, o):
                    for t in range(6):
                        b = take_spec(it, 18 * o + t)
                        for d in range(2):
                            last = nc.tensor.matmul(b[:, d * QC:(d + 1) * QC], h2[:, t * P:(t + 1) * P], w3[:, 2 * o + d, :], start=True, stop=True)
                        last.then_inc(sp_done.handle, 1)

                def transform(it, m0, src):
                    for a in range(2):
                        for f in range(3):
                            b = take_spec(it, m0 + 3 * a + f)
                            table, o, base, kn = (tables["dft_l"], f * P, 0, 2) if f < 2 else (tables["dft_c"], 0, 4, 1)
                            for par in range(2):
                                for k in range(kn):
                                    last = nc.tensor.matmul(b[:, par * QC:(par + 1) * QC], table[:, 2 * a + par, k, o:o + P],
                                                            src(a)[:, base + kn * par + k, :], start=(k == 0), stop=(k == kn - 1))
                            last.then_inc(sp_done.handle, 1)

                def turn_tokens(it, i0):
                    for j in range(2):
                        bl, bc = take(it, i0 + j)
                        for par in range(2):
                            for k in range(2):
                                nc.tensor.transpose(bl[:, (2 * par + k) * P:(2 * par + k + 1) * P],
                                                    parity(u[:, j], 0, SEQ)[:, par, k * P:(k + 1) * P], core.ident[:])
                            last = nc.tensor.transpose(bc[:, par * P:(par + 1) * P], parity(u[:, j], CTX_AT, CTX)[:, par, :], core.ident[:])
                        last.then_inc(ip_done.handle, 1)

                def back(it, o, i0):
                    pe.wait_ge(combined.handle, it * 2 + combined.at(o + 1))
                    for j in range(2):
                        bl, bc = take(it, i0 + j)
                        for b, table, tiles, n in ((bl, tables["idft_l"], (0, 1), 256), (bc, tables["idft_c"], (2,), P)):
                            for par in range(2):
                                steps = [(a, k, f) for a in range(2) for k, f in enumerate(tiles)]
                                for s, (a, k, f) in enumerate(steps):
                                    last = nc.tensor.matmul(b[:, par * n:(par + 1) * n], pq[:, a, par, f, j * P:(j + 1) * P],
                                                            table[:, 2 * a + par, k, :], start=(s == 0), stop=(s == len(steps) - 1))
                        last.then_inc(ip_done.handle, 1)

                pe.wait_ge(tab_loaded.handle, tab_loaded.at(64))
                with pe.Fori(0, TURNS) as it:
                    pe.wait_ge(win_loaded.handle, it * 32 + win_loaded.at(32))
                    filters(it, 0)
                    for i in range(6):
                        c = 0 if i < 4 else 1
                        n = n0 + c
                        if i in (0, 4):
                            core.await_chunk(pe, n, it, 3)
                        w = by_k(core.slot(n), CW if c == 0 else QC)
                        bl, bc = take(it, i)
                        col = (i if c == 0 else i - 4) * P
                        for k in range(KD):
                            nc.tensor.matmul(bl[:], w[:, k, col:col + P], h[:, k, 0:SEQ], start=(k == 0), stop=(k == KD - 1))
                        for k in range(KD):
                            last = nc.tensor.matmul(bc[:, 0:CTX], w[:, k, col:col + P], h[:, k, SEQ:TOK], start=(k == 0), stop=(k == KD - 1))
                        last.then_inc(ip_done.handle, 1)
                    for o in range(2):
                        if o:
                            filters(it, 1)
                        pe.wait_ge(taps_made.handle, it * 12 + taps_made.at(6 * o + 6))
                        transform(it, 18 * o + 6, lambda a: taps[:, a])
                        if o == 0:
                            pe.wait_ge(convolved.handle, it * 6 + convolved.at(2 + 2))
                        else:
                            pe.wait_ge(gated.handle, it * 2 + gated.at(1))
                        turn_tokens(it, 6 if o == 0 else 10)
                        pe.wait_ge(tok_kept.handle, it * 2 + tok_kept.at(o + 1))
                        transform(it, 18 * o + 12, lambda a: v_tok[:])
                        back(it, o, 8 if o == 0 else 12)
                    n = n0 + 2
                    core.await_chunk(pe, n, it, 3)
                    pe.wait_ge(gated.handle, it * 2 + gated.at(2))
                    w = by_k(core.slot(n), D, 2)
                    for j in range(KD):
                        bl, bc = take(it, 14 + j)
                        for k in range(2):
                            nc.tensor.matmul(bl[:], w[:, k, j * P:(j + 1) * P], u[:, k, 0:SEQ], start=(k == 0), stop=(k == 1))
                        for k in range(2):
                            last = nc.tensor.matmul(bc[:, 0:CTX], w[:, k, j * P:(j + 1) * P], u[:, k, CTX_AT:CTX_AT + CTX], start=(k == 0), stop=(k == 1))
                        last.then_inc(ip_done.handle, 1)

            @block.gpsimd
            def _(pool):
                nc.gpsimd.memset(raw[:], 0.0).then_inc(pads.handle, 1)
                with pool.Fori(0, TURNS) as it:
                    for i in (4, 6, NI):
                        pool.wait_ge(ip_done.handle, it * NI + ip_done.at(i))
                        pool.sem_inc(core.freed.handle, 1)

            @block.scalar
            def _(act):
                def keep_even(it, m0, e0):
                    for s in range(6):
                        act.wait_ge(sp_done.handle, it * SP + sp_done.at(m0 + s + 1))
                        act.wait_ge(sp_free.handle, it * SP + sp_free.at(m0 + s - 2 + 1 + 4))
                        nc.scalar.copy(even[:, s % 2, :], spec[(m0 + s) % 4][:, 0:QC]).then_inc(even_kept.handle, 1)

                def keep_tokens(it, i0):
                    for j in range(2):
                        act.wait_ge(ip_done.handle, it * NI + ip_done.at(i0 + j + 1))
                        nc.scalar.copy(v_tok[:, 0:4, j * P:(j + 1) * P], lat[(i0 + j) % 2][:].rearrange("p (t n) -> p t n", n=P))
                        last = nc.scalar.copy(v_tok[:, 4:6, j * P:(j + 1) * P], ctx[(i0 + j) % 2][:, 0:CTX].rearrange("p (t n) -> p t n", n=P))
                        last.then_inc(ip_act.handle, 1)
                    act.wait_ge(ip_act.handle, it * NA + ip_act.at(rank[i0 + 1] + 1))
                    act.sem_inc(tok_kept.handle, 1)

                act.wait_ge(pads.handle, pads.at(1))
                with act.Fori(0, TURNS) as it:
                    for i in range(6):
                        act.wait_ge(ip_done.handle, it * NI + ip_done.at(i + 1))
                        act.wait_ge(convolved.handle, it * 6 + convolved.at(i + 1))
                        b = core.vec[:, bass.ds(it * 2 + (VEC_AT["hy_b_in_2"][0] + (i // 2) * KD + i % 2), 1)]
                        nc.scalar.activation(raw[:, i % 2, 1:1 + SEQ], lat[i % 2][:], ACT.Identity, bias=b).then_inc(raw_kept.handle, 1)
                        nc.scalar.activation(raw[:, i % 2, SEQ + 3:UP - 1], ctx[i % 2][:, 0:CTX], ACT.Identity, bias=b).then_inc(ip_act.handle, 1)
                    for o in range(2):
                        keep_even(it, 18 * o + 6, 12 * o)
                        keep_tokens(it, 6 if o == 0 else 10)
                        keep_even(it, 18 * o + 12, 12 * o + 6)

            @block.vector
            def _(dve):
                per_turn = 2 * (6 + 16) + 12 + 8
                links = []

                def combine(it, link, m0, e0, dst):
                    for a in range(2):
                        for f in range(3):
                            s = 3 * a + f
                            m = m0 + s
                            dve.wait_ge(sp_done.handle, it * SP + sp_done.at(m + 1))
                            dve.wait_ge(even_kept.handle, it * 24 + even_kept.at(e0 + s + 1))
                            odd = spec[m % 4][:, QC:2 * QC]
                            nc.vector.tensor_tensor(dst[:, a, 0, f, :], even[:, s % 2, :], odd, ALU.add)
                            if a == 0:
                                last = nc.vector.tensor_tensor(dst[:, a, 1, f, :], even[:, s % 2, :], odd, ALU.subtract)
                            else:
                                last = nc.vector.tensor_tensor(dst[:, a, 1, f, :], odd, even[:, s % 2, :], ALU.subtract)
                            last.then_inc(sp_free.handle, 1)

                def make_taps(it, link, o):
                    for t in range(6):
                        m = 18 * o + t
                        dve.wait_ge(sp_done.handle, it * SP + sp_done.at(m + 1))
                        link(nc.vector.tensor_tensor(t1[:, 0:2 * QC], spec[m % 4][:], win[:, t].rearrange("p d n -> p (d n)"), ALU.mult))
                        nc.vector.tensor_tensor(taps[:, 0, t, :], t1[:, 0:QC], t1[:, QC:2 * QC], ALU.add).then_inc(sp_free.handle, 1)
                        nc.vector.tensor_tensor(taps[:, 1, t, :], t1[:, 0:QC], t1[:, QC:2 * QC], ALU.subtract).then_inc(taps_made.handle, 1)
                        dve.wait_ge(taps_made.handle, it * 12 + taps_made.at(6 * o + t + 1))

                def flat(v):
                    return v.rearrange("p f n -> p (f n)")

                def products(it, link, o):
                    for s in range(2):
                        A, B = flat(ab[:, 0, s]), flat(ab[:, 1, s])
                        Pc, Qs = flat(pq[:, 0, s]), flat(pq[:, 1, s])
                        nc.vector.tensor_tensor(t1[:], A, Pc, ALU.mult)
                        link(nc.vector.tensor_tensor(t2[:], B, Qs, ALU.mult))
                        nc.vector.tensor_tensor(A, A, Qs, ALU.mult)
                        link(nc.vector.tensor_tensor(B, B, Pc, ALU.mult))
                        nc.vector.tensor_tensor(B, A, B, ALU.add)
                        link(nc.vector.tensor_tensor(t1[:], t1[:], t2[:], ALU.subtract))
                        link(nc.vector.tensor_copy(A, t1[:]))
                    lo, hi = [flat(ab[:, a, 0]) for a in range(2)], [flat(ab[:, a, 1]) for a in range(2)]
                    nc.vector.tensor_tensor(flat(pq[:, 0, 0]), lo[0], hi[0], ALU.add)
                    nc.vector.tensor_tensor(flat(pq[:, 0, 1]), lo[0], hi[0], ALU.subtract)
                    nc.vector.tensor_tensor(flat(pq[:, 1, 0]), lo[1], hi[1], ALU.subtract)
                    nc.vector.tensor_tensor(flat(pq[:, 1, 1]), lo[1], hi[1], ALU.add).then_inc(combined.handle, 1)

                def gates(it, link, o, i0):
                    for j in range(2):
                        i = i0 + j
                        dve.wait_ge(ip_done.handle, it * NI + ip_done.at(i + 1))
                        b = core.vec[:, bass.ds(it * 2 + (VEC_AT["hy_filter_bias_2"][0] + o * KD + j), 1)]
                        y = lambda tile, n: tile[:, 0:n].rearrange("p (a i) -> p a i", a=2)
                        nc.vector.scalar_tensor_tensor(out=y(t1[:], SEQ), in0=parity(u[:, j], 0, SEQ), scalar=b, in1=y(lat[i % 2][:], SEQ), op0=ALU.mult, op1=ALU.add)
                        ins_ = nc.vector.scalar_tensor_tensor(out=y(t2[:], CTX), in0=parity(u[:, j], CTX_AT, CTX), scalar=b, in1=y(ctx[i % 2][:], CTX), op0=ALU.mult, op1=ALU.add)
                        ins_.then_inc(ip_dve.handle, 1)
                        dve.wait_ge(ip_dve.handle, it * ND + ip_dve.at(rank[i] + 1 + 2))
                        xo = u[:, 2 + 2 * o + j]
                        nc.vector.tensor_tensor(parity(u[:, j], 0, SEQ), y(t1[:], SEQ), parity(xo, 0, SEQ), ALU.mult)
                        last = nc.vector.tensor_tensor(parity(u[:, j], CTX_AT, CTX), y(t2[:], CTX), parity(xo, CTX_AT, CTX), ALU.mult)
                        if j == 0:
                            link(last)
                        else:
                            last.then_inc(gated.handle, 1)
                            dve.wait_ge(gated.handle, it * 2 + gated.at(o + 1))

                gb = t2[:, 0:2 * KD].rearrange("p (s k) -> p s k", s=2)
                pre = Link(dve, chain)
                for s in range(2):
                    pre(nc.vector.tensor_tensor(gb[:, s], gate[s], core.col("hy_b_out_2"), ALU.mult))
                for s, (c0, n) in enumerate(((0, SEQ), (SEQ, CTX))):
                    for k in range(KD):
                        last = nc.vector.tensor_scalar(x[:, k, c0:c0 + n], x[:, k, c0:c0 + n], gb[:, s, k:k + 1], None, ALU.add)
                pre(last)
                dve.sem_inc(ip_dve.handle, 2)
                dve.sem_inc(sp_free.handle, 4)
                dve.sem_inc(convolved.handle, 2)
                n_pre = pre.n
                with dve.Fori(0, TURNS) as it:
                    dve.wait_ge(win_loaded.handle, it * 32 + win_loaded.at(32))
                    link = Link(dve, chain, it * LINKS_PER_TURN + n_pre)
                    make_taps(it, link, 0)
                    for i in range(6):
                        dve.wait_ge(ip_act.handle, it * NA + ip_act.at(i + 1))
                        r = raw[:, i % 2]
                        col = lambda name, tap=0: core.vec[:, bass.ds(it * 2 + (VEC_AT[name][0] + tap * 24 + (i // 2) * KD + i % 2), 1)]
                        m = UP - 2
                        dst = u[:, i, 0:m]
                        link(nc.vector.tensor_scalar(dst, r[:, 1:1 + m], col("hy_short_w_2", 1), col("hy_short_b_2"), ALU.mult, ALU.add))
                        link(nc.vector.scalar_tensor_tensor(out=dst, in0=r[:, 0:m], scalar=col("hy_short_w_2", 0), in1=dst, op0=ALU.mult, op1=ALU.add))
                        nc.vector.scalar_tensor_tensor(out=dst, in0=r[:, 2:2 + m], scalar=col("hy_short_w_2", 2), in1=dst, op0=ALU.mult, op1=ALU.add).then_inc(convolved.handle, 1)
                    dve.wait_ge(convolved.handle, it * 6 + convolved.at(8))
                    for o in range(2):
                        if o:
                            make_taps(it, link, 1)
                        combine(it, link, 18 * o + 6, 12 * o, pq)
                        combine(it, link, 18 * o + 12, 12 * o + 6, ab)
                        dve.wait_ge(sp_free.handle, it * SP + sp_free.at(18 * o + 18 + 4))
                        products(it, link, o)
                        gates(it, link, o, 8 if o == 0 else 12)
                    for j in range(KD):
                        i = 14 + j
                        dve.wait_ge(ip_done.handle, it * NI + ip_done.at(i + 1))
                        dve.wait_ge(ip_dve.handle, it * ND + ip_dve.at(rank[i] + 2))
                        nc.vector.scalar_tensor_tensor(out=x[:, j, 0:SEQ], in0=lat[i % 2][:], scalar=gate[0][:, j:j + 1], in1=x[:, j, 0:SEQ], op0=ALU.mult, op1=ALU.add)
                        nc.vector.scalar_tensor_tensor(out=x[:, j, SEQ:TOK], in0=ctx[i % 2][:, 0:CTX], scalar=gate[1][:, j:j + 1], in1=x[:, j, SEQ:TOK], op0=ALU.mult, op1=ALU.add).then_inc(ip_dve.handle, 1)
                    links.append(link.n)
                assert links == [LINKS_PER_TURN], links
        st.used = [(s, n) if s is not chain else (chain, 3 + TURNS * LINKS_PER_TURN) for s, n in st.used]


LINKS_PER_TURN = 2 * (6 + 2 * 4 + 1) + 12


def route_stage(core, layer, ctx, xe_l, xe_c, sp_l, sp_c):
    nc, ins = core.nc, core.ins
    tiles = LT + (CT if ctx else 0)
    cols = tiles * P
    E = N_EXP
    with Stage(core, "route") as st:
        tok = st.sb("tok", [P, tiles, D])
        turn_tokens_stage(core, "back", core.h, tok, range(tiles))
        router = st.sb("router", [P, KD, E])
        number = st.sb("number", [P, CAP_L])
        aff = st.sb("aff", [P, tiles, E])
        top = st.sb("top", [P, tiles])
        total = st.sb("total", [P, tiles])
        rows = st.sb("rows", [E, cols])
        work = st.sb("work", [E, cols])
        best = st.sb("best", [E, 8])
        sel = rows
        pos = st.sb("pos", [E, cols])
        one = st.sb("one", [E, SEQ])
        at = st.sb("at", [P, tiles, E])
        pick_l = st.sb("pick_l", [P, LT, E, CAP_L])
        pick_c = st.sb("pick_c", [P, CT, E, CAP_C]) if ctx else None
        pl = st.ps("logits")
        pr = st.ps("by_expert", 2)
        pa = st.ps("places")
        bank = [st.ps(f"bank{i}") for i in range(4)]
        loaded = st.counter("route_loaded", 32)
        scored = st.counter("route_scored", 1)
        shifted = st.counter("route_shifted", 1)
        raised = st.counter("route_raised", 1)
        softmaxed = st.counter("route_softmaxed", 1)
        rowed = st.counter("route_rowed", 1)
        placed = st.counter("route_placed", 1)
        turned = st.counter("route_turned", 1)
        picked = st.counter("route_picked", 1)
        gathers = [(d, c, "l") for d in range(KD) for c in range(2)] + ([(d, 0, "c") for d in range(KD)] if ctx else [])
        ng = len(gathers)
        gathered = st.counter("route_gathered", ng)
        kept = [st.counter("route_kept_act", ng // 2), st.counter("route_kept_dve", ng // 2)]
        gated = st.counter("route_gated", 1)
        scatters = [("l", j) for j in range(E // 2)] + ([("c", j) for j in range(E // 4)] if ctx else [])
        spread = st.counter("route_spread", len(scatters))
        spread_kept = st.counter("route_spread_kept", len(scatters))
        chain = st.counter("route_chain", 0)
        spans = [(0, SEQ, CAP_L)] + ([(SEQ, CTX, CAP_C)] if ctx else [])
        n_links = []
        with st.run() as block:
            @block.sync
            def _(sp):
                sp.dma_start(router[:], ins["moe_router_2"][layer].rearrange("(k p) e -> p k e", p=P)).then_inc(loaded.handle, 16)
                sp.dma_start(number[:], core.consts["slot_number"]).then_inc(loaded.handle, 16)

            @block.tensor
            def _(pe):
                pe.wait_ge(loaded.handle, loaded.at(32))
                for t in range(tiles):
                    for k in range(KD):
                        last = nc.tensor.matmul(pl[:, t * E:(t + 1) * E], core.h[:, k, t * P:(t + 1) * P], router[:, k, :], start=(k == 0), stop=(k == KD - 1))
                last.then_inc(scored.handle, 1)
                pe.wait_ge(softmaxed.handle, softmaxed.at(1))
                for t in range(tiles):
                    last = nc.tensor.transpose(pr[0:E, t * P:(t + 1) * P], aff[:, t, :], core.ident[:])
                last.then_inc(rowed.handle, 1)
                pe.wait_ge(placed.handle, placed.at(1))
                for t in range(tiles):
                    last = nc.tensor.transpose(pa[:, t * E:(t + 1) * E], pos[:, t * P:(t + 1) * P], core.ident[0:E, 0:E])
                last.then_inc(turned.handle, 1)
                pe.wait_ge(picked.handle, picked.at(1))
                for i, (d, c, s) in enumerate(gathers):
                    if i >= 4:
                        pe.wait_ge(kept[i % 2].handle, kept[i % 2].at((i - 4) // 2 + 1))
                    tt = range(LT) if s == "l" else range(CT)
                    for t in tt:
                        rhs = pick_l[:, t, 8 * c:8 * c + 8, :] if s == "l" else pick_c[:, t]
                        src = tok[:, t if s == "l" else LT + t, d * P:(d + 1) * P]
                        last = nc.tensor.matmul(bank[i % 4][:], src, rhs.rearrange("p e s -> p (e s)"), start=(t == 0), stop=(t == tt[-1]))
                    last.then_inc(gathered.handle, 1)
                pe.wait_ge(gated.handle, gated.at(1))
                for i in (0, 1):
                    pe.wait_ge(kept[i].handle, kept[i].at(ng // 2))
                for i, (s, j) in enumerate(scatters):
                    if i >= 4:
                        pe.wait_ge(spread_kept.handle, spread_kept.at(i - 3))
                    for t in range(LT if s == "l" else CT):
                        src = pick_l[:, t, 2 * j:2 * j + 2, :] if s == "l" else pick_c[:, t, 4 * j:4 * j + 4, :]
                        last = nc.tensor.transpose(bank[i % 4][:, t * P:(t + 1) * P], src.rearrange("p e s -> p (e s)"), core.ident[:])
                    last.then_inc(spread.handle, 1)

            def keep(i):
                d, c, s = gathers[i]
                if s == "l":
                    return xe_l[:, 8 * c:8 * c + 8, d, :], bank[i % 4][:].rearrange("p (e s) -> p e s", s=CAP_L)
                return xe_c[:, :, d, :], bank[i % 4][:].rearrange("p (e s) -> p e s", s=CAP_C)

            @block.scalar
            def _(act):
                act.wait_ge(shifted.handle, shifted.at(1))
                nc.scalar.activation(aff[:], aff[:], ACT.Exp).then_inc(raised.handle, 1)
                for i in range(0, ng, 2):
                    act.wait_ge(gathered.handle, gathered.at(i + 1))
                    dst, src = keep(i)
                    nc.scalar.copy(dst, src).then_inc(kept[0].handle, 1)

            @block.vector
            def _(dve):
                link = Link(dve, chain)
                dve.wait_ge(scored.handle, scored.at(1))
                logits = pl[:, 0:tiles * E].rearrange("p (t e) -> p t e", e=E)
                link(nc.vector.tensor_reduce(top[:], logits, AX_X, ALU.max))
                nc.vector.tensor_tensor(aff[:], logits, top[:].unsqueeze(2).to_broadcast([P, tiles, E]), ALU.subtract).then_inc(shifted.handle, 1)
                dve.wait_ge(raised.handle, raised.at(1))
                link(nc.vector.tensor_reduce(total[:], aff[:], AX_X, ALU.add))
                link(nc.vector.reciprocal(total[:], total[:]))
                nc.vector.tensor_tensor(aff[:], aff[:], total[:].unsqueeze(2).to_broadcast([P, tiles, E]), ALU.mult).then_inc(softmaxed.handle, 1)
                nc.vector.memset(one[:], 1.0)
                dve.wait_ge(rowed.handle, rowed.at(1))
                link(nc.vector.tensor_copy(rows[:], pr[0:E, 0:cols]))
                for c0, n, cap in spans:
                    src = rows
                    for _r in range(cap // 8):
                        link(nc.vector.max(best[:], src[:, c0:c0 + n]))
                        link(nc.vector.match_replace(work[:, c0:c0 + n], best[:], src[:, c0:c0 + n], -1.0))
                        src = work
                link(nc.vector.tensor_scalar(sel[:], work[:], 0.0, None, ALU.is_lt))
                for c0, n, cap in spans:
                    last = nc.vector.tensor_tensor_scan(pos[:, c0:c0 + n], one[:, 0:n], sel[:, c0:c0 + n], 0.0, ALU.mult, ALU.add)
                link(last)
                nc.vector.tensor_tensor(pos[:], pos[:], sel[:], ALU.mult).then_inc(placed.handle, 1)
                dve.wait_ge(turned.handle, turned.at(1))
                link(nc.vector.tensor_copy(at[:], pa[:, 0:tiles * E].rearrange("p (t e) -> p t e", e=E)))
                dve.wait_ge(loaded.handle, loaded.at(32))
                sets = [(pick_l[:, t], t, CAP_L) for t in range(LT)] + ([(pick_c[:, t], LT + t, CAP_C) for t in range(CT)] if ctx else [])
                for v, t, cap in sets:
                    last = nc.vector.tensor_tensor(v, number[:, 0:cap].unsqueeze(1).to_broadcast([P, E, cap]),
                                                   at[:, t, :].unsqueeze(2).to_broadcast([P, E, cap]), ALU.is_equal)
                last.then_inc(picked.handle, 1)
                for i in range(1, ng, 2):
                    dve.wait_ge(gathered.handle, gathered.at(i + 1))
                    dst, src = keep(i)
                    nc.vector.tensor_copy(dst, src).then_inc(kept[1].handle, 1)
                dve.wait_ge(picked.handle, picked.at(1))
                dve.wait_ge(gathered.handle, gathered.at(ng))
                for v, t, cap in sets:
                    last = nc.vector.tensor_tensor(v, v, aff[:, t, :].unsqueeze(2).to_broadcast([P, E, cap]), ALU.mult)
                last.then_inc(gated.handle, 1)
                for i, (s, j) in enumerate(scatters):
                    dve.wait_ge(spread.handle, spread.at(i + 1))
                    dst = sp_l[:, j, :] if s == "l" else sp_c[:, j, :]
                    nc.vector.tensor_copy(dst, bank[i % 4][:, 0:SEQ if s == "l" else CTX]).then_inc(spread_kept.handle, 1)
                n_links.append(link.n)
        st.used = [(s, n) if s is not chain else (chain, n_links[0]) for s, n in st.used]


EXPERTS_PER_TURN = 4
EXPERT_ORDER = []
for _r in range(EXPERTS_PER_TURN):
    EXPERT_ORDER += [(_r, "gate", 0), (_r, "up", 0)] + ([(_r - 1, "down", 1)] if _r else []) + [(_r, "gate", 1), (_r, "up", 1), (_r, "down", 0)]
EXPERT_ORDER.append((EXPERTS_PER_TURN - 1, "down", 1))


def expert_chunks(core, layer):
    def place(r, what, half):
        w = core.ins[f"moe_w_{what}_2"][layer]

        def of(first):
            def at(slot):
                a = w[bass.ds(first + r, 1)]
                if what == "down":
                    return [(slot[:].rearrange("p (k n) -> p k n", k=4),
                             a.rearrange("e (h k p) n -> h p (e k) n", p=P, h=2)[half])]
                return [(slot[:].rearrange("p (k n) -> p k n", k=KD),
                         a.rearrange("e (k p) n -> p (e k) n", p=P)[:, :, half * CW:(half + 1) * CW])]
            return at
        return of
    return [place(*c) for c in EXPERT_ORDER]


def experts_stage(core, layer, ctx, xe_l, xe_c, sp_l, sp_c, gate):
    nc = core.nc
    n0 = core.used
    E, H = EXPERTS_PER_TURN, N_EXP // EXPERTS_PER_TURN
    S = CAP_L + (CAP_C if ctx else 0)
    NC = len(EXPERT_ORDER)
    M = 24 if ctx else 16
    nb = 3 if ctx else 2
    x = core.x
    with Stage(core, "experts") as st:
        xe = st.sb("xe", [P, 2, KD, S])
        act_ = st.sb("act", [S, 2, CW])
        hid = st.sb("hid", [S, 2, CW])
        hidT = st.sb("hidT", [P, 2, KD, S])
        y_l = st.sb("y_l", [P, 2, D])
        y_c = st.sb("y_c", [P, D])
        pg, pu, pt = st.ps("pg"), st.ps("pu"), st.ps("pt")
        py = st.ps("py", 2)
        psc = [st.ps(f"psc{i}") for i in range(nb)]
        staged = st.counter("ex_staged", E * H)
        c_up, c_silu, c_hid, c_turn, c_copy, c_y, c_yl, c_sc, c_add = 4, 1, 2, 2, 1, 2, 1, M, nb
        gate_done = st.counter("ex_gate_done", 2 * E * H)
        up_done = st.counter("ex_up_done", 2 * E * H + c_up)
        down_half = st.counter("ex_down_half", E * H)
        silu_done = st.counter("ex_silu_done", 2 * E * H + c_silu)
        hid_made = st.counter("ex_hid_made", 2 * E * H + c_hid)
        hid_turned = st.counter("ex_hid_turned", 2 * E * H + c_turn)
        hid_copied = st.counter("ex_hid_copied", 2 * E * H + c_copy)
        y_done = st.counter("ex_y_done", E * H + c_y)
        yl_kept = st.counter("ex_yl_kept", E * H + c_yl)
        yc_kept = st.counter("ex_yc_kept", E * H + c_yl)
        sc_done = st.counter("ex_sc_done", M * H + c_sc)
        sc_added = st.counter("ex_sc_added", M * H + c_add)
        place = expert_chunks(core, layer)
        with st.run() as block:
            @block.sync
            def _(sp):
                def used(it, j):
                    r, what, half = EXPERT_ORDER[j]
                    if what == "gate":
                        sp.wait_ge(gate_done.handle, it * (2 * E) + gate_done.at(2 * r + half + 1))
                    elif what == "up":
                        sp.wait_ge(up_done.handle, it * (2 * E) + up_done.at(2 * r + half + 1 + c_up))
                    elif half == 0:
                        sp.wait_ge(down_half.handle, it * E + down_half.at(r + 1))
                    else:
                        sp.wait_ge(y_done.handle, it * E + y_done.at(r + 1 + c_y))
                    sp.sem_inc(core.freed.handle, 1)

                def load(first, j):
                    core.issue(sp, n0 + j, place[j % NC](first + j // NC * E))

                with sp.Fori(0, H - 1) as it:
                    first = sp.snap(it * E)
                    for j in range(NC):
                        used(it, j)
                        load(first, j + NS)
                for j in range(NC):
                    used(H - 1, j)
                    if j + NS < NC:
                        load((H - 1) * E, j + NS)
                core.used = core.issued = n0 + NC * H
                core.stream(sp, core.used)

            @block.gpsimd
            def _(pool):
                with pool.Fori(0, H) as it:
                    for r in range(E):
                        pool.wait_ge(up_done.handle, it * (2 * E) + up_done.at(2 * r + 2))
                        last = nc.gpsimd.tensor_copy(xe[:, r % 2, :, 0:CAP_L], xe_l[:, bass.ds(it * E + r, 1)].rearrange("p e k s -> p (e k) s"))
                        if ctx:
                            last.then_inc(staged.handle, 1)
                            last = nc.gpsimd.tensor_copy(xe[:, r % 2, :, CAP_L:S], xe_c[:, bass.ds(it * E + r, 1)].rearrange("p e k s -> p (e k) s"))
                        last.then_inc(staged.handle, 1)

            per_stage = 2 if ctx else 1

            @block.tensor
            def _(pe):
                def chunk(it, r, what, half):
                    n = n0 + EXPERT_ORDER.index((r, what, half))
                    core.await_chunk(pe, n, it, NC)
                    return by_k(core.slot(n), D, 4) if what == "down" else by_k(core.slot(n))

                def gate_half(it, r, c):
                    w = chunk(it, r, "gate", c)
                    pe.wait_ge(silu_done.handle, it * (2 * E) + silu_done.at(2 * r + c + c_silu))
                    for k in range(KD):
                        last = nc.tensor.matmul(pg[0:S, :], xe[:, r % 2, k, :], w[:, k, :], start=(k == 0), stop=(k == KD - 1))
                    last.then_inc(gate_done.handle, 1)

                def up_half(it, r, c):
                    w = chunk(it, r, "up", c)
                    pe.wait_ge(hid_made.handle, it * (2 * E) + hid_made.at(2 * r + c + c_hid))
                    for k in range(KD):
                        last = nc.tensor.matmul(pu[0:S, :], xe[:, r % 2, k, :], w[:, k, :], start=(k == 0), stop=(k == KD - 1))
                    last.then_inc(up_done.handle, 1)

                def turn(it, r, c):
                    s = 2 * r + c
                    pe.wait_ge(hid_made.handle, it * (2 * E) + hid_made.at(s + 1 + c_hid))
                    pe.wait_ge(hid_copied.handle, it * (2 * E) + hid_copied.at(s + c_copy))
                    for f in range(4):
                        last = nc.tensor.matmul(pt[:, f * S:(f + 1) * S], hid[:, c, f * P:(f + 1) * P], core.ident[0:S, 0:S], start=True, stop=True)
                    last.then_inc(hid_turned.handle, 1)

                def down_of(it, r, c):
                    w = chunk(it, r, "down", c)
                    pe.wait_ge(hid_copied.handle, it * (2 * E) + hid_copied.at(2 * r + c + 1 + c_copy))
                    if c == 0:
                        pe.wait_ge(yl_kept.handle, it * E + yl_kept.at(r + c_yl))
                        if ctx:
                            pe.wait_ge(yc_kept.handle, it * E + yc_kept.at(r + c_yl))
                    for f in range(4):
                        for half in range(2):
                            last = nc.tensor.matmul(py[0:S, half * CW:(half + 1) * CW], hidT[:, r % 2, 4 * c + f, :], w[:, f, half * CW:(half + 1) * CW],
                                                    start=(c == 0 and f == 0), stop=(c == 1 and f == 3))
                    last.then_inc((down_half if c == 0 else y_done).handle, 1)

                def scatter(it, m0, m1):
                    for m in range(m0, m1):
                        if m in (0, 8):
                            pe.wait_ge(yl_kept.handle, it * E + yl_kept.at(2 * (m // 8) + 2 + c_yl))
                        if m == 16:
                            pe.wait_ge(yc_kept.handle, it * E + yc_kept.at(E + c_yl))
                        pe.wait_ge(sc_added.handle, it * M + sc_added.at(m + 1))
                        d = m % 8
                        if m < 16:
                            rhs = sp_l[:, bass.ds(it * 2 + m // 8, 1), :].rearrange("p a n -> p (a n)")
                            last = nc.tensor.matmul(psc[m % nb][:], y_l[:, m // 8, d * P:(d + 1) * P], rhs, start=True, stop=True)
                        else:
                            rhs = sp_c[:, bass.ds(it, 1), :].rearrange("p a n -> p (a n)")
                            last = nc.tensor.matmul(psc[m % nb][:, 0:CTX], y_c[:, d * P:(d + 1) * P], rhs, start=True, stop=True)
                        last.then_inc(sc_done.handle, 1)

                pe.sem_inc(up_done.handle, c_up)
                pe.sem_inc(hid_turned.handle, c_turn)
                pe.sem_inc(y_done.handle, c_y)
                pe.sem_inc(sc_done.handle, c_sc)
                with pe.Fori(0, H) as it:
                    for r in range(E):
                        pe.wait_ge(staged.handle, it * (E * per_stage) + staged.at((r + 1) * per_stage))
                        gate_half(it, r, 0)
                        up_half(it, r, 0)
                        if r:
                            down_of(it, r - 1, 1)
                        gate_half(it, r, 1)
                        if r == 2:
                            scatter(it, 0, 2)
                        turn(it, r, 0)
                        up_half(it, r, 1)
                        if r == 2:
                            scatter(it, 2, 5)
                        down_of(it, r, 0)
                        if r == 2:
                            scatter(it, 5, 8)
                        turn(it, r, 1)
                    down_of(it, E - 1, 1)
                    scatter(it, 8, M)

            @block.scalar
            def _(act):
                def silu(it, r, c):
                    s = 2 * r + c
                    act.wait_ge(gate_done.handle, it * (2 * E) + gate_done.at(s + 1))
                    act.wait_ge(hid_made.handle, it * (2 * E) + hid_made.at(s + 1))
                    nc.scalar.activation(act_[:, c, :], pg[0:S, :], ACT.Silu).then_inc(silu_done.handle, 1)

                def copy(it, r, c):
                    s = 2 * r + c
                    act.wait_ge(hid_turned.handle, it * (2 * E) + hid_turned.at(s + 1 + c_turn))
                    act.wait_ge(y_done.handle, it * E + y_done.at(r + 1))
                    nc.scalar.copy(hidT[:, r % 2, 4 * c:4 * c + 4, :], pt[:, 0:4 * S].rearrange("p (f s) -> p f s", f=4)).then_inc(hid_copied.handle, 1)

                def keep(it, r):
                    act.wait_ge(y_done.handle, it * E + y_done.at(r + 1 + c_y))
                    act.wait_ge(sc_done.handle, it * M + sc_done.at(8 * (r // 2) + 8))
                    o = (r % 2) * CAP_L
                    nc.scalar.copy(y_l[o:o + CAP_L, r // 2, :], py[0:CAP_L, :]).then_inc(yl_kept.handle, 1)

                act.sem_inc(silu_done.handle, c_silu)
                act.sem_inc(hid_copied.handle, c_copy)
                act.sem_inc(yl_kept.handle, c_yl)
                with act.Fori(0, H) as it:
                    for r in range(E):
                        silu(it, r, 0)
                        if r:
                            keep(it, r - 1)
                        silu(it, r, 1)
                        copy(it, r, 0)
                        copy(it, r, 1)
                    keep(it, E - 1)

            @block.vector
            def _(dve):
                def product(it, r, c):
                    s = 2 * r + c
                    dve.wait_ge(up_done.handle, it * (2 * E) + up_done.at(s + 1 + c_up))
                    dve.wait_ge(silu_done.handle, it * (2 * E) + silu_done.at(s + 1 + c_silu))
                    dve.wait_ge(hid_turned.handle, it * (2 * E) + hid_turned.at(s + 1))
                    nc.vector.tensor_tensor(hid[:, c, :], act_[:, c, :], pu[0:S, :], ALU.mult).then_inc(hid_made.handle, 1)

                def keep(it, r):
                    if ctx:
                        dve.wait_ge(y_done.handle, it * E + y_done.at(r + 1 + c_y))
                        dve.wait_ge(sc_done.handle, it * M + sc_done.at(M))
                        dve.wait_ge(yl_kept.handle, it * E + yl_kept.at(r + 1 + c_yl))
                        nc.vector.tensor_copy(y_c[r * CAP_C:(r + 1) * CAP_C, :], py[CAP_L:S, :]).then_inc(yc_kept.handle, 1)

                def add(it, m0, m1):
                    for m in range(m0, m1):
                        dve.wait_ge(sc_done.handle, it * M + sc_done.at(m + 1 + c_sc))
                        dve.wait_ge(sc_added.handle, it * M + sc_added.at(m + c_add))
                        d = m % 8
                        c0, n, s = (0, SEQ, 0) if m < 16 else (SEQ, CTX, 1)
                        nc.vector.scalar_tensor_tensor(out=x[:, d, c0:c0 + n], in0=psc[m % nb][:, 0:n], scalar=gate[s][:, d:d + 1], in1=x[:, d, c0:c0 + n],
                                                       op0=ALU.mult, op1=ALU.add).then_inc(sc_added.handle, 1)

                dve.sem_inc(hid_made.handle, c_hid)
                dve.sem_inc(yc_kept.handle, c_yl)
                dve.sem_inc(sc_added.handle, c_add)
                with dve.Fori(0, H) as it:
                    for r in range(E):
                        product(it, r, 0)
                        if r:
                            keep(it, r - 1)
                        if r == 2:
                            add(it, 0, 2)
                        product(it, r, 1)
                        if r == 2:
                            add(it, 2, 8)
                    keep(it, E - 1)
                    add(it, 8, M)
        st.used = [(s, n * per_stage) if s is staged else (s, n) for s, n in st.used]
        if not ctx:
            st.used = [(s, c_yl) if s is yc_kept else (s, n) for s, n in st.used]


def moe(core, layer, ctx, gate):
    with Stage(core, "moe") as st:
        xe_l = st.sb("xe_l", [P, N_EXP, KD, CAP_L])
        sp_l = st.sb("sp_l", [P, N_EXP // 2, SEQ])
        sp_c = st.sb("sp_c", [P, N_EXP // 4, CTX]) if ctx else None
        spare = core.h[:].rearrange("p k n -> p (k n)")[:, 0:N_EXP * KD * CAP_C]
        xe_c = spare.rearrange("p (e k s) -> p e k s", e=N_EXP, k=KD) if ctx else None
        route_stage(core, layer, ctx, xe_l, xe_c, sp_l, sp_c)
        experts_stage(core, layer, ctx, xe_l, xe_c, sp_l, sp_c, gate)


def axial_rope_stage(core, cols):
    nc = core.nc
    H = 20
    with Stage(core, "axial") as st:
        rope = st.sb("rope", [P, 2, LT, 32])
        tmp = [st.sb(f"tmp{i}", [P, H, 32]) for i in range(4)]
        loaded = st.counter("axial_loaded", 32)
        chain = st.counter("axial_chain", 2 * LT)
        with st.run() as block:
            @block.sync
            def _(sp):
                sp.dma_start(rope[:, 0], core.consts["axial_cos"]).then_inc(loaded.handle, 16)
                sp.dma_start(rope[:, 1], core.consts["axial_sin"]).then_inc(loaded.handle, 16)

            @block.vector
            def _(dve):
                link = Link(dve, chain)
                dve.wait_ge(loaded.handle, loaded.at(32))
                for t in range(LT):
                    v = cols[:, t, 0:H * HD].rearrange("p (h w) -> p h w", w=HD)
                    x1, x2 = v[:, :, 0:32], v[:, :, 32:HD]
                    cos, sin = (rope[:, j, t, :].unsqueeze(1).to_broadcast([P, H, 32]) for j in range(2))
                    nc.vector.tensor_tensor(tmp[0][:], x1, cos, ALU.mult)
                    nc.vector.tensor_tensor(tmp[1][:], x2, sin, ALU.mult)
                    nc.vector.tensor_tensor(tmp[2][:], x2, cos, ALU.mult)
                    link(nc.vector.tensor_tensor(tmp[3][:], x1, sin, ALU.mult))
                    nc.vector.tensor_tensor(x1, tmp[0][:], tmp[1][:], ALU.subtract)
                    link(nc.vector.tensor_tensor(x2, tmp[2][:], tmp[3][:], ALU.add))


def attention_layer(core, gate):
    nc, ins = core.nc, core.ins
    KV, REP, W = 4, 4, 1536
    with Stage(core, "swa2") as st:
        cols = st.sb("cols", [P, LT + CT, W])
        o = st.sb("o", [P, LT, D])
        lat, both = list(range(LT)), list(range(LT + CT))
        project_stage(core, "w_in2", [lat, lat, both], [CW] * 3, lambda t, c: cols[:, t, c * CW:(c + 1) * CW])
        axial_rope_stage(core, cols)
        qT = st.sb("qT", [MLA_DIM, KV * REP, SEQ])
        kT = core.h[0:MLA_DIM].rearrange("p k n -> p (k n)")[:, 0:KV * TOK].rearrange("p (h n) -> p h n", h=KV)
        band = st.sb("band", [P, 3 * P])
        sink = st.sb("sink", [P, KV * REP])
        jobs = [(lambda t, c=hd * HD: cols[:, t, c:c + HD], LT, HD, [qT[0:HD, hd, :]], None, HD ** -0.5) for hd in range(KV * REP)]
        order = [LT, LT + 1, 0, 1, 2, 3]
        jobs += [(lambda t, c=D + hd * HD: cols[:, order[t], c:c + HD], 6, HD, [kT[0:HD, hd, :]], None, 1.0) for hd in range(KV)]

        def extra(sp, loaded):
            if sp is not None:
                sp.dma_start(band[:], core.consts["band"]).then_inc(loaded.handle, 16)
                sp.dma_start(sink[:], ins["sw_sink_2"].partition_broadcast(P)).then_inc(loaded.handle, 16)
            return 2

        turn_heads_stage(core, "turn2", jobs, zero=[qT[HD:MLA_DIM], kT[HD:MLA_DIM]], extra=extra)

        def keys(i):
            lo, hi = max(0, i - 1), min(LT, i + 2)
            return [(0, CTX, None), (CTX + lo * P, (hi - lo) * P, ((lo - i + 1) * P, (hi - i + 1) * P))]

        attention_stage(
            core, "att2", KV, REP, MLA_DIM, LT, keys, qT,
            lambda it, r, k0, n: kT[:, bass.ds(it, 1), k0:k0 + n].rearrange("p a n -> p (a n)"),
            lambda it, r, kt: cols[:, order[kt], bass.ds(it * HD + D + KV * HD, HD)],
            lambda it, r, a, b: band[:, a:b],
            lambda it, r, i: o[:, i, bass.ds(it * (REP * HD) + r * HD, HD)],
            lambda it, r: sink[:, bass.ds(it * REP + r, 1)])
        turn_heads_stage(core, "turn3", [(lambda t, k=k: o[:, t, k * P:(k + 1) * P], LT, P, [core.h[:, k, 0:SEQ]], None, 1.0) for k in range(KD)])
    residual_stage(core, "w_out2", gate)


def store_stage(core, out):
    with Stage(core, "final") as st:
        tok = st.sb("tok", [P, LT, D])
        turn_tokens_stage(core, "last", core.h, tok, range(LT))
        stored = st.counter("stored", 16)
        with st.run() as block:
            @block.sync
            def _(sp):
                sp.dma_start(out[0].rearrange("(t p) d -> p t d", p=P), tok[:]).then_inc(stored.handle, 16)
                sp.wait_ge(stored.handle, stored.at(16))


def second_block(core, out, debug):
    def mod(layer, i, s):
        at = layer * 48 + i * KD
        return core.mod[:, at:at + KD, s]

    def streams(layer, gain, i, both):
        g = lambda: core.col(gain, layer * KD, KD)
        lat = [(0, SEQ, g(), mod(layer, i + 1, 0), mod(layer, i, 0))]
        return lat + ([(SEQ, CTX, g(), mod(layer, i + 1, 1), mod(layer, i, 1))] if both else [])

    norm_stage(core, "norm_h", streams(0, "norm1_w_2", 0, True))
    hyena_stage(core, [mod(0, 2, 0), mod(0, 2, 1)])
    if debug: debug(core, 'hyena')
    norm_stage(core, "norm_e", streams(0, "norm2_w_2", 3, True))
    moe(core, 0, True, [mod(0, 5, 0), mod(0, 5, 1)])
    if debug: debug(core, 'moe0')
    norm_stage(core, "norm_s", streams(1, "norm1_w_2", 0, True))
    attention_layer(core, mod(1, 2, 0))
    if debug: debug(core, 'swa')
    norm_stage(core, "norm_f", streams(1, "norm2_w_2", 3, False))
    moe(core, 1, False, [mod(1, 5, 0)])
    if debug: debug(core, 'moe1')
    norm_stage(core, "norm_l", [(0, SEQ, core.col("final_norm_w_2"), None, None)])
    store_stage(core, out)


def build(nc, ins, consts, out, debug=None):
    with ExitStack() as ctx:
        core = Core(nc, ins, consts, ctx)
        chunks = []
        for layer in range(2):
            chunks += [column_chunk(ins["ada_w_2"][layer], c * CW, CW) for c in range(12)]
        chunks += [column_chunk(ins["w_in"][0], c * CW, min(CW, IN_COLS - c * CW)) for c in range(5)]
        chunks += [column_chunk(ins["w_o"][0], c * CW, CW) for c in range(2)]
        chunks += [column_chunk(ins["w_up"][0], c * CW, CW) for c in range(FF // CW)]
        chunks += [row_chunk(ins["w_down"][0], c * CW) for c in range(FF // CW)]
        chunks += [place(q) for q in range(TURNS) for place in hyena_chunks(core)]
        experts = lambda layer: [place(first) for first in range(0, N_EXP, EXPERTS_PER_TURN) for place in expert_chunks(core, layer)]
        chunks += experts(0)
        chunks += [column_chunk(ins["sw_w_in_2"], c * CW, CW) for c in range(3)]
        chunks += [column_chunk(ins["sw_w_out_2"], c * CW, CW) for c in range(2)]
        chunks += experts(1)
        core.set_chunks(chunks)
        load_stage(core)
        modulation_stage(core)
        if debug: debug(core, 'load')
        first_block(core)
        if debug: debug(core, 'first')
        second_block(core, out, debug)


def constants():
    f = np.float32
    c = {"ident": np.eye(P, dtype=f)}
    inv = f(1.0) / (f(10000.0) ** (np.arange(0, 32, 2, dtype=f) / f(32)))
    ang = np.arange(SEQ, dtype=f)[:, None] * inv[None, :]
    tile = lambda a: np.ascontiguousarray(a.reshape(-1, P, a.shape[-1]).transpose(1, 0, 2))
    c["rope_cos"], c["rope_sin"] = tile(np.cos(ang)), tile(np.sin(ang))
    dist = np.arange(P)[:, None] + (SEQ - P) - np.arange(SEQ)[None, :]
    idx = np.arange(1, 3 * HEADS + 1, dtype=f).reshape(HEADS, 3)
    slopes = np.exp2(f(-8.0) * idx / f(3 * HEADS)).astype(f)
    causal = dist >= 0
    count = (dist <= 128).astype(f) + (dist % 4 == 0) + (dist % 16 == 0)
    bias = np.full((4, P, HEADS, SEQ), NEG, f)
    for h in range(HEADS):
        for g, (valid, col) in enumerate(((causal, 0), (causal, None), (causal & (count > 0), 1), (causal & (dist < 128), 2))):
            b = np.zeros_like(dist, dtype=f) if col is None else -slopes[h, col] * dist.astype(f)
            if g == 2:
                b = b + np.log(np.maximum(count, 1))
            bias[g, :, h, :] = np.where(valid, b, NEG)
    c["bias"] = bias
    deltas = np.abs(np.linspace(np.log(1e-2) / 1.5, np.log(1e-2) / 0.3, D, dtype=f))
    z_all, win_all = [], []
    for name, L in (("l", SEQ), ("c", CTX)):
        order = np.concatenate([np.arange(0, L, 2), np.arange(1, L, 2)])
        t = np.linspace(0.0, 1.0, L, dtype=f)[:, None]
        w = f(2.0 * np.pi) * np.arange(L, dtype=f)[:, None] / f(L)
        bands = np.linspace(1e-4, 15, 16, dtype=f)[None, :]
        z = np.concatenate([t, np.cos(bands * w), -np.sin(bands * w)], axis=-1).astype(f)
        z_all.append(z[order].T)
        window = np.exp(-t * deltas) + f(0.05)
        both = np.stack([window, window], axis=1)
        both[0, 1, :] = 0.0
        win_all.append(both[order].reshape(-1, P, 2, D).transpose(1, 0, 2, 3))
        half = L // 2
        freq = np.arange(half) + 0.5
        pos = [np.arange(0, L, 2), np.arange(1, L, 2)]
        fwd = [fn(np.pi * pos[par][:, None] * freq[None, :] / L) for fn in (np.cos, np.sin) for par in (0, 1)]
        inv = [m.T / L for m in fwd]
        pack = lambda ms: np.ascontiguousarray(np.stack([m.reshape(-1, P, half).transpose(1, 0, 2) for m in ms], axis=1)).astype(f)
        c["dft_" + name], c["idft_" + name] = pack(fwd), pack(inv)
    c["filter_z"] = np.ascontiguousarray(np.concatenate(z_all, axis=1)).astype(f)
    c["window"] = np.ascontiguousarray(np.concatenate(win_all, axis=1)).astype(f)
    row = np.repeat(np.arange(SEQ // 64, dtype=f), 64)
    col = np.tile(np.arange(64, dtype=f), SEQ // 64)
    inv = f(10000.0) ** (-np.arange(16, dtype=f) / f(16))
    ang = np.concatenate([row[:, None] * inv, col[:, None] * inv], axis=-1)
    c["axial_cos"], c["axial_sin"] = tile(np.cos(ang)), tile(np.sin(ang))
    gap = np.arange(P)[:, None] + P - np.arange(3 * P)[None, :]
    c["band"] = np.where(np.abs(gap) <= 128, f(0), f(NEG)).astype(f)
    c["slot_number"] = np.broadcast_to(np.arange(1, CAP_L + 1, dtype=f), (P, CAP_L)).copy()
    return c


_UNUSED = ("gd_", "hg_")


def kernel(**inputs):
    import concourse.bacc as bacc
    from concourse.bass_utils import run_bass_kernel_spmd

    nc = bacc.Bacc("TRN2", target_bir_lowering=False, num_devices=1)
    arrays, ins, consts = {}, {}, {}

    def place(name, a):
        a = np.ascontiguousarray(a)
        arrays[name] = a
        return nc.dram_tensor(name, a.shape, mybir.dt.from_np(a.dtype), kind="ExternalInput").ap()

    for name, a in inputs.items():
        if not name.startswith(_UNUSED):
            ins[name] = place("in_" + name, a)
    for name, a in constants().items():
        consts[name] = place("table_" + name, a)
    out = nc.dram_tensor("out", (1, SEQ, D), F32, kind="ExternalOutput").ap()
    build(nc, ins, consts, out)
    r = run_bass_kernel_spmd(nc, [arrays], core_ids=[0])
    return r.results[0]["out"]
```

```python
from contextlib import ExitStack

import numpy as np

import concourse.bass as bass
from concourse import mybir

ALU = mybir.AluOpType
ACT = mybir.ActivationFunctionType
F32 = mybir.dt.float32
F32R = mybir.dt.float32r
AX_X = mybir.AxisListType.X

P = 128
D = 1024
KD = D // P
SEQ = 512
CTX = 256
TOK = SEQ + CTX
LT, CT = SEQ // P, CTX // P
FF = 4096
EPS = 1e-6
NEG = -1e30
HD = 64
IN_COLS = 2464
HEADS = 4
MLA_DIM = 96
N_EXP = 16
CAP_L, CAP_C = 2 * SEQ // N_EXP, 2 * CTX // N_EXP
NS = 3
CW = 512
TWO_PI = 2.0 * np.pi
TWO_PI_HI = float(np.float32(TWO_PI))
TWO_PI_LO = float(TWO_PI - np.float64(np.float32(TWO_PI)))
ROUND_MAGIC = float(1.5 * 2 ** 23)
SIN_MAX = 3.1415925

A_Q, A_K, A_V, B_QL, B_KVL, B_KR, C_Q, C_K, C_V, D_Q, D_K, D_V = (
    0, 256, 512, 768, 1024, 1152, 1184, 1440, 1696, 1952, 2208, 2336)

VEC_ROWS = [
    [("ada_b_2", 96), ("c_2", 8), ("c_ctx_2", 8), ("attn_norm_g", 8), ("group_out_g", 8)],
    [("hy_b_in_2", 24), ("hy_short_w_2", 72), ("hy_short_b_2", 24), ("hy_b_out_2", 8)],
    [("norm1_w_2", 16), ("norm2_w_2", 16), ("final_norm_w_2", 8), ("mlp_norm_g", 8),
     ("hy_filter_bias_2", 16), ("mla_qlat_g", 2), ("mla_kvlat_g", 1)],
]
VEC_AT = {}
for _t, _rows in enumerate(VEC_ROWS):
    _r = 0
    for _name, _n in _rows:
        VEC_AT[_name] = (_t * P + _r, _n)
        _r += _n


class Counter:

    def __init__(self, handle):
        self.handle = handle
        self.base = 0

    def at(self, n):
        return n + self.base


class Link:

    def __init__(self, eng, signal, start=0):
        self.eng, self.counter, self.start, self.n = eng, signal, start, 0

    def __call__(self, ins):
        self.n += 1
        ins.then_inc(self.counter.handle, 1)
        self.eng.wait_ge(self.counter.handle, self.counter.at(self.start + self.n))


class Stage:

    def __init__(self, core, name):
        core.stages += 1
        self.core, self.name = core, f"{name}{core.stages}"
        self.mem = ExitStack()
        self.used = []

    def sb(self, name, shape, dt=F32):
        return self.mem.enter_context(self.core.nc.sbuf_tensor(f"{self.name}_{name}", shape, dt))

    def ps(self, name, banks=1):
        return self.mem.enter_context(self.core.nc.psum_tensor(f"{self.name}_{name}", [P, banks * 512], F32))

    def counter(self, name, total):
        s = self.core.counter(name)
        self.used.append((s, total))
        return s

    def __enter__(self):
        return self

    def run(self):
        return self.core.nc.Block()

    def __exit__(self, *e):
        self.mem.__exit__(*e)
        for s, total in self.used:
            s.base += total


class Core:

    def __init__(self, nc, ins, consts, ctx):
        self.nc, self.ins, self.consts, self.ctx = nc, ins, consts, ctx
        self.counters = {}
        self.stages = 0
        sb = lambda n, s: ctx.enter_context(nc.sbuf_tensor(n, s, F32))
        self.x = sb("residual", [P, KD, TOK])
        self.h = sb("normed", [P, KD, TOK])
        self.ring = [sb(f"ring{i}", [P, KD * CW]) for i in range(NS)]
        self.ident = sb("ident", [P, P])
        self.ones = sb("ones", [P, P])
        self.vec = sb("vec", [P, 3 * P])
        self.mod = sb("mod", [P, 96, 2])
        self.loaded = [self.counter(f"ring_loaded{i}") for i in range(NS)]
        self.freed = self.counter("ring_freed")
        self.chunks = []
        self.issued = 0
        self.used = 0

    def counter(self, name):
        if name not in self.counters:
            self.counters[name] = Counter(self.ctx.enter_context(self.nc.semaphore(name)))
        return self.counters[name]

    def col(self, name, i=0, n=None):
        at, size = VEC_AT[name]
        return self.vec[:, at + i:at + i + (size - i if n is None else n)]

    def slot(self, n):
        return self.ring[n % NS]

    def set_chunks(self, chunks):
        self.chunks = chunks
        self.arrival, so_far = [], [0] * NS
        for n, place in enumerate(chunks):
            so_far[n % NS] += 16 * len(place(self.slot(n)))
            self.arrival.append(so_far[n % NS])

    def issue(self, sp, n, place):
        for dst, src in place(self.slot(n)):
            sp.dma_start(dst, src).then_inc(self.loaded[n % NS].handle, 16)

    def load_chunk(self, sp, n):
        if n >= NS:
            sp.wait_ge(self.freed.handle, n - NS + 1)
        self.issue(sp, n, self.chunks[n])

    def stream(self, sp, used):
        while self.issued < min(used + NS, len(self.chunks)):
            self.load_chunk(sp, self.issued)
            self.issued += 1

    def await_chunk(self, eng, n, it=0, per=0):
        if per:
            each = self.arrival[n + per] - self.arrival[n]
            eng.wait_ge(self.loaded[n % NS].handle, it * each + self.arrival[n])
            return
        eng.wait_ge(self.loaded[n % NS].handle, self.arrival[n])


def column_chunk(w, c0, width):
    def place(slot):
        return [(slot[:, 0:KD * width].rearrange("p (k n) -> p k n", k=KD),
                 w[:, c0:c0 + width].rearrange("(k p) n -> p k n", p=P))]
    return place


def row_chunk(w, r0, tiles=4):
    def place(slot):
        return [(slot[:, 0:tiles * D].rearrange("p (k n) -> p k n", k=tiles),
                 w[r0:r0 + tiles * P, :].rearrange("(k p) n -> p k n", p=P))]
    return place


def by_k(slot, width=CW, k=KD):
    return slot[:, 0:k * width].rearrange("p (k n) -> p k n", k=k)


def load_stage(core):
    nc, ins = core.nc, core.ins
    with Stage(core, "load") as st:
        rows = st.sb("rows", [P, 3, P])
        tok = core.h[:].rearrange("p k n -> p (k n)").rearrange("p (t d) -> p t d", d=D)
        pv = st.ps("pv")
        px = [st.ps(f"px{i}") for i in range(2)]
        pc = [st.ps(f"pc{i}") for i in range(2)]
        rows_loaded = st.counter("rows_loaded", 16 * sum(len(r) for r in VEC_ROWS))
        x_loaded = st.counter("x_loaded", 32)
        id_loaded = st.counter("id_loaded", 16)
        vec_turned = st.counter("vec_turned", 1)
        lat_turned = st.counter("lat_turned", KD)
        ctx_turned = st.counter("ctx_turned", KD)
        lat_kept = st.counter("lat_kept", KD)
        ctx_kept = st.counter("ctx_kept", KD)
        with st.run() as block:
            @block.sync
            def _(sp):
                sp.dma_start(core.ident[:], core.consts["ident"]).then_inc(id_loaded.handle, 16)
                sp.dma_start(tok[:, 0:LT], ins["x"][0].rearrange("(t p) d -> p t d", p=P)).then_inc(x_loaded.handle, 16)
                sp.dma_start(tok[:, LT:LT + CT], ins["ctx_2"][0].rearrange("(t p) d -> p t d", p=P)).then_inc(x_loaded.handle, 16)
                core.stream(sp, core.used)

            @block.gpsimd
            def _(pool):
                nc.gpsimd.memset(core.ones[:], 1.0 / D)

            @block.scalar
            def _(act):
                for t, group in enumerate(VEC_ROWS):
                    r = 0
                    for name, n in group:
                        a = ins[name]
                        while len(a.shape) > 1:
                            a = a.rearrange("a b ... -> (a b) ...") if len(a.shape) > 2 else a.rearrange("a b -> (a b)")
                        act.dma_start(rows[r:r + n, t, :], a.rearrange("(r c) -> r c", c=P)).then_inc(rows_loaded.handle, 16)
                        r += n
                for k in range(KD):
                    act.wait_ge(ctx_turned.handle, ctx_turned.at(k + 1))
                    nc.scalar.copy(core.x[:, k, SEQ:TOK], pc[k % 2][:, 0:CTX]).then_inc(ctx_kept.handle, 1)

            @block.tensor
            def _(pe):
                pe.wait_ge(id_loaded.handle, id_loaded.at(16))
                pe.wait_ge(x_loaded.handle, x_loaded.at(32))
                for k in range(KD):
                    if k >= 2:
                        pe.wait_ge(lat_kept.handle, lat_kept.at(k - 1))
                        pe.wait_ge(ctx_kept.handle, ctx_kept.at(k - 1))
                    for t in range(LT):
                        last = nc.tensor.transpose(px[k % 2][:, t * P:(t + 1) * P], tok[:, t, k * P:(k + 1) * P], core.ident[:])
                    last.then_inc(lat_turned.handle, 1)
                    for t in range(CT):
                        last = nc.tensor.transpose(pc[k % 2][:, t * P:(t + 1) * P], tok[:, LT + t, k * P:(k + 1) * P], core.ident[:])
                    last.then_inc(ctx_turned.handle, 1)
                pe.wait_ge(rows_loaded.handle, rows_loaded.at(16 * sum(len(r) for r in VEC_ROWS)))
                for t, group in enumerate(VEC_ROWS):
                    n = sum(c for _, c in group)
                    last = nc.tensor.transpose(pv[:, t * P:t * P + n], rows[0:n, t, :], core.ident[0:n, 0:n])
                last.then_inc(vec_turned.handle, 1)

            @block.vector
            def _(dve):
                for k in range(KD):
                    dve.wait_ge(lat_turned.handle, lat_turned.at(k + 1))
                    nc.vector.tensor_copy(core.x[:, k, 0:SEQ], px[k % 2][:]).then_inc(lat_kept.handle, 1)
                dve.wait_ge(vec_turned.handle, vec_turned.at(1))
                n = 2 * P + sum(c for _, c in VEC_ROWS[2])
                nc.vector.tensor_copy(core.vec[:, 0:n], pv[:, 0:n])


def modulation_stage(core):
    nc = core.nc
    n0 = core.used
    per = 6
    turns = 24 // per
    with Stage(core, "mod") as st:
        cs = st.sb("cs", [P, KD, 2])
        row = st.sb("row", [2, 2, CW])
        pr = [st.ps(f"pr{i}") for i in range(2)]
        pt = [st.ps(f"pt{i}") for i in range(2)]
        silu_done = st.counter("silu_done", 2)
        row_done = st.counter("row_done", 24)
        row_kept = st.counter("row_kept", 24)
        row_turned = st.counter("row_turned", 24)
        col_kept = st.counter("col_kept", 24 + 2)
        row_free = st.counter("row_free", 24 + 2)
        with st.run() as block:
            @block.sync
            def _(sp):
                core.used = n0 + 24
                core.stream(sp, core.used)

            @block.scalar
            def _(act):
                nc.scalar.activation(cs[:, :, 0], core.col("c_2"), ACT.Silu).then_inc(silu_done.handle, 1)
                nc.scalar.activation(cs[:, :, 1], core.col("c_ctx_2"), ACT.Silu).then_inc(silu_done.handle, 1)
                with act.Fori(0, turns) as it:
                    for r in range(per):
                        act.wait_ge(row_done.handle, it * per + row_done.at(r + 1))
                        act.wait_ge(row_free.handle, it * per + row_free.at(r + 1))
                        nc.scalar.copy(row[:, r % 2, :], pr[r % 2][0:2, 0:CW]).then_inc(row_kept.handle, 1)

            @block.tensor
            def _(pe):
                def turn(it, r):
                    pe.wait_ge(row_kept.handle, it * per + row_kept.at(r + 1))
                    pe.wait_ge(col_kept.handle, it * per + col_kept.at(r + 1))
                    for j in range(4):
                        last = nc.tensor.matmul(pt[r % 2][:, 2 * j:2 * j + 2], row[:, r % 2, j * P:(j + 1) * P], core.ident[0:2, 0:2], start=True, stop=True)
                    last.then_inc(row_turned.handle, 1)

                pe.wait_ge(silu_done.handle, silu_done.at(2))
                with pe.Fori(0, turns) as it:
                    for r in range(per):
                        n = n0 + r
                        core.await_chunk(pe, n, it, per)
                        w = by_k(core.slot(n))
                        for k in range(KD):
                            last = nc.tensor.matmul(pr[r % 2][0:2, 0:CW], cs[:, k, :], w[:, k, :], start=(k == 0), stop=(k == KD - 1))
                        last.then_inc(row_done.handle, 1)
                        if r:
                            turn(it, r - 1)
                    turn(it, per - 1)

            @block.vector
            def _(dve):
                dve.sem_inc(col_kept.handle, 2)
                with dve.Fori(0, turns) as it:
                    for r in range(per):
                        dve.wait_ge(row_turned.handle, it * per + row_turned.at(r + 1))
                        nc.vector.tensor_copy(core.mod[:, bass.ds(it * (per * 4) + r * 4, 4), :],
                                              pt[r % 2][:, 0:8].rearrange("p (j s) -> p j s", s=2)).then_inc(col_kept.handle, 1)
                dve.wait_ge(col_kept.handle, col_kept.at(26))
                nc.vector.tensor_tensor(core.mod[:], core.mod[:], core.col("ada_b_2").unsqueeze(2).to_broadcast([P, 96, 2]), ALU.add)

            @block.gpsimd
            def _(pool):
                pool.sem_inc(row_free.handle, 2)
                with pool.Fori(0, turns) as it:
                    for r in range(per):
                        pool.wait_ge(row_turned.handle, it * per + row_turned.at(r + 1))
                        pool.sem_inc(row_free.handle, 1)
                        pool.sem_inc(core.freed.handle, 1)


def norm_stage(core, name, streams, dst=None):
    nc = core.nc
    x, h = core.x, core.h
    with Stage(core, name) as st:
        ms = [st.ps(f"ms{i}") for i in range(2)]
        var = st.sb("var", [P, 2, 512])
        rstd = st.sb("rstd", [P, 2, 512])
        gain = st.sb("gain", [P, 2, KD])
        total = KD * len(streams)
        squared = st.counter("norm_squared", total)
        summed = st.counter("norm_summed", len(streams))
        inverted = st.counter("norm_inverted", len(streams))
        rooted = st.counter("norm_rooted", len(streams))
        scaled = st.counter("norm_scaled", total)
        chain = st.counter("norm_chain", 4 * len(streams))
        with st.run() as block:
            @block.sync
            def _(sp):
                core.stream(sp, core.used)

            @block.scalar
            def _(act):
                for i, (c0, n, g, sc, sh) in enumerate(streams):
                    for k in range(KD):
                        nc.scalar.activation(h[:, k, c0:c0 + n], x[:, k, c0:c0 + n], ACT.Square).then_inc(squared.handle, 1)
                for i, (c0, n, g, sc, sh) in enumerate(streams):
                    act.wait_ge(inverted.handle, inverted.at(i + 1))
                    nc.scalar.activation(rstd[:, i, 0:n], var[:, i, 0:n], ACT.Sqrt).then_inc(rooted.handle, 1)
                for i, (c0, n, g, sc, sh) in enumerate(streams):
                    if sh is not None:
                        for k in range(KD):
                            act.wait_ge(scaled.handle, scaled.at(i * KD + k + 1))
                            nc.scalar.activation(h[:, k, c0:c0 + n], h[:, k, c0:c0 + n], ACT.Identity, bias=sh[:, k:k + 1])

            @block.tensor
            def _(pe):
                for i, (c0, n, g, sc, sh) in enumerate(streams):
                    for k in range(KD):
                        pe.wait_ge(squared.handle, squared.at(i * KD + k + 1))
                        last = nc.tensor.matmul(ms[i][:, 0:n], core.ones[:], h[:, k, c0:c0 + n], start=(k == 0), stop=(k == KD - 1))
                    last.then_inc(summed.handle, 1)

            @block.vector
            def _(dve):
                link = Link(dve, chain)
                for i, (c0, n, g, sc, sh) in enumerate(streams):
                    if sc is None:
                        link(nc.vector.tensor_copy(gain[:, i, :], g))
                    else:
                        link(nc.vector.scalar_tensor_tensor(out=gain[:, i, :], in0=sc, scalar=1.0, in1=g, op0=ALU.add, op1=ALU.mult))
                for i, (c0, n, g, sc, sh) in enumerate(streams):
                    dve.wait_ge(summed.handle, summed.at(i + 1))
                    link(nc.vector.tensor_scalar(var[:, i, 0:n], ms[i][:, 0:n], EPS, None, ALU.add))
                    nc.vector.reciprocal(var[:, i, 0:n], var[:, i, 0:n]).then_inc(inverted.handle, 1)
                for i, (c0, n, g, sc, sh) in enumerate(streams):
                    dve.wait_ge(rooted.handle, rooted.at(i + 1))
                    for k in range(KD):
                        nc.vector.scalar_tensor_tensor(out=h[:, k, c0:c0 + n], in0=x[:, k, c0:c0 + n], scalar=gain[:, i, k:k + 1],
                                                       in1=rstd[:, i, 0:n], op0=ALU.mult, op1=ALU.mult).then_inc(scaled.handle, 1)
        st.used[-1] = (chain, 2 * len(streams))


BUFS = 3


def product_stage(core, name, widths, tokens, tiles, move, by, take, then=None):
    nc = core.nc
    n0 = core.used
    items = [(c, t) for c in range(len(widths)) for t in tiles[c]]
    of = [[i for i, item in enumerate(items) if item[0] == c] for c in range(len(widths))]
    rank = [sum(by(j) == by(i) for j in range(i)) for i in range(len(items))]
    NB = 8
    amid = BUFS - 2
    with Stage(core, name) as st:
        h_hi = st.sb("h_hi", [P, KD, tokens], F32R)
        h_lo = st.sb("h_lo", [P, KD, tokens], F32R)
        w_hi = st.sb("w_hi", [P, BUFS, CW], F32R)
        w_lo = st.sb("w_lo", [P, BUFS, CW], F32R)
        acc = [st.ps(f"acc{i}") for i in range(NB)]
        pieces = KD * len(widths)
        h_high = st.counter("prod_h_high", KD)
        h_low = st.counter("prod_h_low", KD)
        w_high = st.counter("prod_w_high", pieces)
        w_low = st.counter("prod_w_low", pieces)
        w_used = st.counter("prod_w_used", pieces)
        kept = {e: st.counter(f"prod_kept_{e}", sum(by(i) == e for i in range(len(items)))) for e in ("act", "dve")}

        def await_kept(eng, i):
            eng.wait_ge(kept[by(i)].handle, kept[by(i)].at(rank[i] + 1))

        def bank(i):
            c, t = items[i]
            return acc[i % NB][:, 0:widths[c] if move else tokens]

        def await_outputs(eng, c):
            eng.wait_ge(w_used.handle, w_used.at(KD * (c + 1)))

        with st.run() as block:
            @block.sync
            def _(sp):
                core.used = n0 + len(widths)
                core.stream(sp, core.used)

            @block.gpsimd
            def _(pool):
                for c in range(len(widths)):
                    pool.wait_ge(w_low.handle, w_low.at(KD * (c + 1)))
                    pool.sem_inc(core.freed.handle, 1)

            @block.tensor
            def _(pe):
                for c, width in enumerate(widths):
                    for i in of[c]:
                        if i >= NB:
                            await_kept(pe, i - NB)
                    for k in range(KD):
                        n = KD * c + k
                        if c == 0:
                            pe.wait_ge(h_low.handle, h_low.at(k + 1))
                        pe.wait_ge(w_low.handle, w_low.at(n + 1))
                        for i in of[c]:
                            o = slice(items[i][1] * P, (items[i][1] + 1) * P)
                            if move:
                                s_hi, s_lo, m_hi, m_lo = h_hi[:, k, o], h_lo[:, k, o], w_hi[:, n % BUFS, 0:width], w_lo[:, n % BUFS, 0:width]
                            else:
                                s_hi, s_lo, m_hi, m_lo = w_hi[:, n % BUFS, o], w_lo[:, n % BUFS, o], h_hi[:, k, :], h_lo[:, k, :]
                            nc.tensor.matmul(bank(i), s_hi, m_hi, start=(k == 0), stop=False)
                            nc.tensor.matmul(bank(i), s_hi, m_lo, start=False, stop=False)
                            last = nc.tensor.matmul(bank(i), s_lo, m_hi, start=False, stop=(k == KD - 1))
                        last.then_inc(w_used.handle, 1)

            @block.scalar
            def _(act):
                def take_out(c):
                    if any(by(i) == "act" for i in of[c]):
                        await_outputs(act, c)
                    for i in of[c]:
                        if by(i) == "act":
                            take("act", *items[i], bank(i)).then_inc(kept["act"].handle, 1)

                for c, width in enumerate(widths):
                    for k in range(KD):
                        n = KD * c + k
                        if c == 0:
                            nc.scalar.copy(h_hi[:, k, :], core.h[:, k, 0:tokens]).then_inc(h_high.handle, 1)
                        if k == 0:
                            core.await_chunk(act, n0 + c)
                        if n >= BUFS:
                            act.wait_ge(w_used.handle, w_used.at(n - BUFS + 1))
                        nc.scalar.copy(w_hi[:, n % BUFS, 0:width], by_k(core.slot(n0 + c), width)[:, k, :]).then_inc(w_high.handle, 1)
                        if c and k == amid:
                            take_out(c - 1)
                take_out(len(widths) - 1)

            @block.vector
            def _(dve):
                def take_out(c):
                    if any(by(i) == "dve" for i in of[c]):
                        await_outputs(dve, c)
                    for i in of[c]:
                        if by(i) == "dve":
                            take("dve", *items[i], bank(i)).then_inc(kept["dve"].handle, 1)
                    if then is not None:
                        for i in of[c]:
                            await_kept(dve, i)
                            then(*items[i])

                for c, width in enumerate(widths):
                    for k in range(KD):
                        n = KD * c + k
                        if c == 0:
                            dve.wait_ge(h_high.handle, h_high.at(k + 1))
                            nc.vector.tensor_tensor(h_lo[:, k, :], core.h[:, k, 0:tokens], h_hi[:, k, :], ALU.subtract).then_inc(h_low.handle, 1)
                        dve.wait_ge(w_high.handle, w_high.at(n + 1))
                        nc.vector.tensor_tensor(w_lo[:, n % BUFS, 0:width], by_k(core.slot(n0 + c), width)[:, k, :], w_hi[:, n % BUFS, 0:width],
                                                ALU.subtract).then_inc(w_low.handle, 1)
                        if c and k == amid:
                            take_out(c - 1)
                take_out(len(widths) - 1)


def project_stage(core, name, tiles, widths, keep):
    nc = core.nc

    def take(engine, c, t, bank):
        return nc.scalar.copy(keep(t, c), bank) if engine == "act" else nc.vector.tensor_copy(keep(t, c), bank)

    product_stage(core, name, widths, P * (1 + max(max(t) for t in tiles)), tiles, True, lambda i: ("act", "dve")[i % 2], take)


def residual_stage(core, name, gate=None):
    nc = core.nc

    def take(engine, c, t, bank):
        j = 4 * c + t
        row = core.x[:, j, 0:SEQ]
        if gate is None:
            return nc.vector.tensor_tensor(row, bank, row, ALU.add)
        return nc.vector.scalar_tensor_tensor(out=row, in0=bank, scalar=gate[:, j:j + 1], in1=row, op0=ALU.mult, op1=ALU.add)

    product_stage(core, name, [CW] * 2, SEQ, [range(4)] * 2, False, lambda i: "dve", take)


def mlp_stage(core):
    nc = core.nc
    n_up = FF // CW
    with Stage(core, "mlp") as outer:
        u = outer.sb("u", [P, FF // P, SEQ])

        def take(engine, c, t, bank):
            return nc.scalar.activation(u[:, 4 * c + t, :], bank, ACT.Relu)

        def square(c, t):
            v = u[:, 4 * c + t, :]
            nc.vector.tensor_tensor(v, v, v, ALU.mult)

        product_stage(core, "up", [CW] * n_up, SEQ, [range(4)] * n_up, False, lambda i: "act", take, square)
        down_stage(core, u)


def down_stage(core, u):
    nc = core.nc
    n0 = core.used
    tiles = FF // P
    chunks = tiles // 4
    pieces = 2 * tiles
    B = 6
    with Stage(core, "down") as st:
        u_hi = st.sb("u_hi", [P, BUFS, SEQ], F32R)
        u_lo = st.sb("u_lo", [P, BUFS, SEQ], F32R)
        w_hi = st.sb("w_hi", [P, B, CW], F32R)
        w_lo = st.sb("w_lo", [P, B, CW], F32R)
        acc = [st.ps(f"acc{i}") for i in range(KD)]
        u_high = st.counter("prod_h_high", tiles)
        u_low = st.counter("prod_h_low", tiles)
        w_high = st.counter("prod_w_high", pieces)
        w_low = st.counter("prod_w_low", pieces)
        w_used = st.counter("prod_w_used", pieces)

        def raw(n):
            f, half = n // 2, n % 2
            return by_k(core.slot(n0 + f // 4), D, 4)[:, f % 4, half * CW:(half + 1) * CW]

        with st.run() as block:
            @block.sync
            def _(sp):
                core.used = n0 + chunks
                core.stream(sp, core.used)

            @block.gpsimd
            def _(pool):
                for c in range(chunks):
                    pool.wait_ge(w_low.handle, w_low.at(8 * (c + 1)))
                    pool.sem_inc(core.freed.handle, 1)

            @block.tensor
            def _(pe):
                for n in range(pieces):
                    f, half = n // 2, n % 2
                    if half == 0:
                        pe.wait_ge(u_low.handle, u_low.at(f + 1))
                    pe.wait_ge(w_low.handle, w_low.at(n + 1))
                    for j in range(4):
                        out, o = acc[4 * half + j][:], slice(j * P, (j + 1) * P)
                        nc.tensor.matmul(out, w_hi[:, n % B, o], u_hi[:, f % BUFS, :], start=(f == 0), stop=False)
                        nc.tensor.matmul(out, w_hi[:, n % B, o], u_lo[:, f % BUFS, :], start=False, stop=False)
                        last = nc.tensor.matmul(out, w_lo[:, n % B, o], u_hi[:, f % BUFS, :], start=False, stop=(f == tiles - 1))
                    last.then_inc(w_used.handle, 1)

            @block.scalar
            def _(act):
                for n in range(pieces):
                    f, half = n // 2, n % 2
                    if half == 0:
                        if f >= BUFS:
                            act.wait_ge(w_used.handle, w_used.at(2 * (f - BUFS + 1)))
                        nc.scalar.copy(u_hi[:, f % BUFS, :], u[:, f, :]).then_inc(u_high.handle, 1)
                    if n % 8 == 0:
                        core.await_chunk(act, n0 + n // 8)
                    if n >= B:
                        act.wait_ge(w_used.handle, w_used.at(n - B + 1))
                    nc.scalar.copy(w_hi[:, n % B, :], raw(n)).then_inc(w_high.handle, 1)

            @block.vector
            def _(dve):
                for n in range(pieces):
                    f, half = n // 2, n % 2
                    if half == 0:
                        dve.wait_ge(u_high.handle, u_high.at(f + 1))
                        nc.vector.tensor_tensor(u_lo[:, f % BUFS, :], u[:, f, :], u_hi[:, f % BUFS, :], ALU.subtract).then_inc(u_low.handle, 1)
                    dve.wait_ge(w_high.handle, w_high.at(n + 1))
                    nc.vector.tensor_tensor(w_lo[:, n % B, :], raw(n), w_hi[:, n % B, :], ALU.subtract).then_inc(w_low.handle, 1)
                for j in range(KD):
                    dve.wait_ge(w_used.handle, w_used.at(pieces - 1 + j // 4))
                    nc.vector.tensor_tensor(core.x[:, j, 0:SEQ], acc[j][:], core.x[:, j, 0:SEQ], ALU.add)


def rms_rows(nc, act, squares, x, scratch, signal):
    nc.scalar.activation(scratch, x, ACT.Square).then_inc(signal.handle, 1)


def head_norm_stage(core, cols):
    nc = core.nc
    spans = [(A_Q, 8, HD), (C_Q, 8, HD), (D_Q, 6, HD), (B_QL, 1, 256), (B_KVL, 1, 128)]
    with Stage(core, "heads") as st:
        square = st.sb("square", [P, 2, 512])
        ss = st.sb("ss", [P, LT, 24])
        rstd = st.sb("rstd", [P, LT, 24])
        n = LT * len(spans)
        squared = st.counter("head_squared", n)
        reduced = st.counter("head_reduced", n)
        inverted = st.counter("head_inverted", 1)
        rooted = st.counter("head_rooted", 1)
        chain = st.counter("head_chain", 2)
        at, offs = 0, []
        for _, heads, _ in spans:
            offs.append(at)
            at += heads
        todo = [(t, s) for t in range(LT) for s in range(len(spans))]
        with st.run() as block:
            @block.scalar
            def _(act):
                for i, (t, s) in enumerate(todo):
                    c, heads, w = spans[s]
                    if i >= 2:
                        act.wait_ge(reduced.handle, reduced.at(i - 1))
                    nc.scalar.activation(square[:, i % 2, 0:heads * w], cols[:, t, c:c + heads * w], ACT.Square,
                                         scale=float(w) ** -0.5).then_inc(squared.handle, 1)
                act.wait_ge(inverted.handle, inverted.at(1))
                nc.scalar.activation(rstd[:], ss[:], ACT.Sqrt).then_inc(rooted.handle, 1)

            @block.vector
            def _(dve):
                link = Link(dve, chain)
                for i, (t, s) in enumerate(todo):
                    c, heads, w = spans[s]
                    dve.wait_ge(squared.handle, squared.at(i + 1))
                    nc.vector.tensor_reduce(ss[:, t, offs[s]:offs[s] + heads],
                                            square[:, i % 2, 0:heads * w].rearrange("p (h w) -> p h w", w=w),
                                            AX_X, ALU.add).then_inc(reduced.handle, 1)
                dve.wait_ge(reduced.handle, reduced.at(n))
                link(nc.vector.tensor_scalar(ss[:], ss[:], EPS, None, ALU.add))
                nc.vector.reciprocal(ss[:], ss[:]).then_inc(inverted.handle, 1)
                dve.wait_ge(rooted.handle, rooted.at(1))
                for t, s in todo:
                    c, heads, w = spans[s]
                    v = cols[:, t, c:c + heads * w].rearrange("p (h w) -> p h w", w=w)
                    nc.vector.tensor_tensor(v, v, rstd[:, t, offs[s]:offs[s] + heads].unsqueeze(2).to_broadcast([P, heads, w]), ALU.mult)
        st.used[-1] = (chain, 1)


def mla_stage(core, cols, q, kf, ukv):
    nc, ins = core.nc, core.ins
    with Stage(core, "mla") as st:
        uq = st.sb("uq", [P, 2, HEADS * MLA_DIM])
        uk = st.sb("uk", [P, 512])
        gains = st.sb("gains", [P, 2, MLA_DIM])
        rope = st.sb("rope", [P, 2, LT, 16])
        lat = st.sb("lat", [P, 3, SEQ])
        square = st.sb("square", [P, 16 * MLA_DIM])
        ss = st.sb("ss", [P, 2, 16])
        rstd = st.sb("rstd", [P, 2, 16])
        tmp = st.sb("tmp", [P, 4, LT, HEADS, 16])
        pl = [st.ps(f"pl{i}") for i in range(3)]
        pq = [st.ps(f"pq{i}") for i in range(2)]
        pk = [st.ps(f"pk{i}") for i in range(2)]
        loaded = st.counter("mla_loaded", 16 * 6)
        turned = st.counter("mla_turned", 3)
        lat_kept = st.counter("mla_lat_kept", 3)
        up_q = st.counter("mla_up_q", LT)
        up_k = st.counter("mla_up_k", LT)
        q_kept = st.counter("mla_q_kept", LT)
        k_kept = st.counter("mla_k_kept", LT)
        k_built = st.counter("mla_k_built", 2 * LT)
        squared = st.counter("mla_squared", 2)
        inverted = st.counter("mla_inverted", 1)
        rooted = st.counter("mla_rooted", 1)
        reduced = st.counter("mla_reduced", 2)
        chain = st.counter("mla_chain", 8 + 3)
        with st.run() as block:
            @block.sync
            def _(sp):
                sp.dma_start(uq[:], ins["mla_w_uq"][0].rearrange("(k p) n -> p k n", p=P)).then_inc(loaded.handle, 16)
                sp.dma_start(uk[:], ins["mla_w_ukv"][0]).then_inc(loaded.handle, 16)
                sp.dma_start(gains[:, 0, :], ins["mla_q_g"][0].partition_broadcast(P)).then_inc(loaded.handle, 16)
                sp.dma_start(gains[:, 1, :], ins["mla_k_g"][0].partition_broadcast(P)).then_inc(loaded.handle, 16)
                sp.dma_start(rope[:, 0], core.consts["rope_cos"]).then_inc(loaded.handle, 16)
                sp.dma_start(rope[:, 1], core.consts["rope_sin"]).then_inc(loaded.handle, 16)

            @block.tensor
            def _(pe):
                for j, c in enumerate((B_QL, B_QL + P, B_KVL)):
                    for t in range(LT):
                        last = nc.tensor.transpose(pl[j][:, t * P:(t + 1) * P], cols[:, t, c:c + P], core.ident[:])
                    last.then_inc(turned.handle, 1)
                pe.wait_ge(loaded.handle, loaded.at(96))
                pe.wait_ge(lat_kept.handle, lat_kept.at(3))
                for t in range(LT):
                    if t >= 2:
                        pe.wait_ge(q_kept.handle, q_kept.at(t - 1))
                        pe.wait_ge(k_kept.handle, k_kept.at(t - 1))
                    for j in range(2):
                        last = nc.tensor.matmul(pq[t % 2][:, 0:HEADS * MLA_DIM], lat[:, j, t * P:(t + 1) * P], uq[:, j, :], start=(j == 0), stop=(j == 1))
                    last.then_inc(up_q.handle, 1)
                    nc.tensor.matmul(pk[t % 2][:], lat[:, 2, t * P:(t + 1) * P], uk[:], start=True, stop=True).then_inc(up_k.handle, 1)

            @block.scalar
            def _(act):
                for t in range(LT):
                    act.wait_ge(up_k.handle, up_k.at(t + 1))
                    nc.scalar.copy(ukv[:, t, :], pk[t % 2][:]).then_inc(k_kept.handle, 1)
                for i, (v, ready, n) in enumerate(((q, q_kept, LT), (kf, k_built, 2 * LT))):
                    act.wait_ge(ready.handle, ready.at(n))
                    if i:
                        act.wait_ge(reduced.handle, reduced.at(1))
                    nc.scalar.activation(square[:], v[:].rearrange("p t h w -> p (t h w)"), ACT.Square, scale=float(MLA_DIM) ** -0.5).then_inc(squared.handle, 1)
                act.wait_ge(inverted.handle, inverted.at(1))
                nc.scalar.activation(rstd[:], ss[:], ACT.Sqrt).then_inc(rooted.handle, 1)

            @block.gpsimd
            def _(pool):
                for t in range(LT):
                    pool.wait_ge(k_kept.handle, k_kept.at(t + 1))
                    nc.gpsimd.tensor_copy(kf[:, t, :, 0:HD], ukv[:, t, :].rearrange("p (h w) -> p h w", h=HEADS)[:, :, 0:HD]).then_inc(k_built.handle, 1)
                    nc.gpsimd.tensor_copy(kf[:, t, :, HD:MLA_DIM], cols[:, t, B_KR:B_KR + 32].unsqueeze(1).to_broadcast([P, HEADS, 32])).then_inc(k_built.handle, 1)

            @block.vector
            def _(dve):
                link = Link(dve, chain)
                for j, g in enumerate((core.col("mla_qlat_g", 0, 1), core.col("mla_qlat_g", 1, 1), core.col("mla_kvlat_g"))):
                    dve.wait_ge(turned.handle, turned.at(j + 1))
                    nc.vector.tensor_scalar(lat[:, j, :], pl[j][:], g, None, ALU.mult).then_inc(lat_kept.handle, 1)
                for t in range(LT):
                    dve.wait_ge(up_q.handle, up_q.at(t + 1))
                    nc.vector.tensor_copy(q[:, t].rearrange("p h w -> p (h w)"), pq[t % 2][:, 0:HEADS * MLA_DIM]).then_inc(q_kept.handle, 1)
                for i in range(2):
                    dve.wait_ge(squared.handle, squared.at(i + 1))
                    nc.vector.tensor_reduce(ss[:, i, :], square[:].rearrange("p (g w) -> p g w", w=MLA_DIM), AX_X, ALU.add).then_inc(reduced.handle, 1)
                dve.wait_ge(reduced.handle, reduced.at(2))
                link(nc.vector.tensor_scalar(ss[:], ss[:], EPS, None, ALU.add))
                nc.vector.reciprocal(ss[:], ss[:]).then_inc(inverted.handle, 1)
                dve.wait_ge(rooted.handle, rooted.at(1))
                for i, v in enumerate((q, kf)):
                    flat = v[:].rearrange("p t h w -> p (t h) w")
                    link(nc.vector.tensor_tensor(flat, flat, rstd[:, i, :].unsqueeze(2).to_broadcast([P, 16, MLA_DIM]), ALU.mult))
                    link(nc.vector.tensor_tensor(flat, flat, gains[:, i, :].unsqueeze(1).to_broadcast([P, 16, MLA_DIM]), ALU.mult))
                    x1, x2 = v[:, :, :, HD:HD + 16], v[:, :, :, HD + 16:MLA_DIM]
                    cos, sin = (rope[:, j].unsqueeze(2).to_broadcast([P, LT, HEADS, 16]) for j in range(2))
                    nc.vector.tensor_tensor(tmp[:, 0], x1, cos, ALU.mult)
                    nc.vector.tensor_tensor(tmp[:, 1], x2, sin, ALU.mult)
                    nc.vector.tensor_tensor(tmp[:, 2], x1, sin, ALU.mult)
                    link(nc.vector.tensor_tensor(tmp[:, 3], x2, cos, ALU.mult))
                    nc.vector.tensor_tensor(x1, tmp[:, 0], tmp[:, 1], ALU.subtract)
                    link(nc.vector.tensor_tensor(x2, tmp[:, 2], tmp[:, 3], ALU.add))
        st.used[-1] = (chain, 9)


def turn_heads_stage(core, name, jobs, zero=(), extra=None):
    nc = core.nc
    with Stage(core, name) as st:
        bank = [st.ps(f"bank{i}", 2) for i in range(2)]
        turned = st.counter("turn_turned", len(jobs))
        kept = st.counter("turn_kept", sum(len(j[3]) for j in jobs))
        ends, n = [], 0
        for j in jobs:
            n += len(j[3])
            ends.append(n)
        loaded = st.counter("turn_loaded", 16 * (0 if extra is None else extra(None, None)))
        with st.run() as block:
            if extra is not None:
                @block.sync
                def _(sp):
                    extra(sp, loaded)

            @block.tensor
            def _(pe):
                for i, (src, tiles, w, dsts, gain, scale) in enumerate(jobs):
                    if i >= 2:
                        pe.wait_ge(kept.handle, kept.at(ends[i - 2]))
                    for t in range(tiles):
                        last = nc.tensor.transpose(bank[i % 2][0:w, t * P:(t + 1) * P], src(t), core.ident[:])
                    last.then_inc(turned.handle, 1)

            @block.vector
            def _(dve):
                if extra is not None:
                    dve.wait_ge(loaded.handle, loaded.at(16 * extra(None, None)))
                for z in zero:
                    nc.vector.memset(z, 0.0)
                for i, (src, tiles, w, dsts, gain, scale) in enumerate(jobs):
                    dve.wait_ge(turned.handle, turned.at(i + 1))
                    for d in dsts:
                        s = bank[i % 2][0:w, 0:tiles * P]
                        if gain is None:
                            ins_ = nc.vector.tensor_scalar(d, s, scale, None, ALU.mult)
                        else:
                            ins_ = nc.vector.tensor_scalar(d, s, gain, scale, ALU.mult, ALU.mult)
                        ins_.then_inc(kept.handle, 1)


def attention_stage(core, name, turns, per, dim, q_tiles, keys, q, k_of, v_of, bias_of, out_of, sink_of=None):
    nc = core.nc
    steps = per * q_tiles
    pieces = [keys(i) for i in range(q_tiles)]
    width = max(sum(n for _, n, _ in p) for p in pieces)
    npc = max(len(p) for p in pieces)
    with Stage(core, name) as st:
        q_now = st.sb("q_now", [dim, 2, q_tiles * P])
        s = st.sb("s", [P, 2, width + 1])
        p = st.sb("p", [P, 2, width + 1])
        pt = st.sb("pt", [P, 2, width])
        top = st.sb("top", [P, 2])
        total = st.sb("total", [P, 4])
        inv = st.sb("inv", [P, 2])
        ps_s = [st.ps(f"scores{i}", npc) for i in range(2)]
        ps_t = st.ps("turned", 2)
        ps_o = [st.ps(f"out{i}") for i in range(2)]
        N = turns * steps
        q_staged = st.counter("att_q_staged", turns * per)
        held = 2 * q_tiles
        scored = st.counter("att_scored", N + held)
        biased = st.counter("att_biased", N + 2)
        topped = st.counter("att_topped", N)
        raised = st.counter("att_raised", N + 2)
        turned = st.counter("att_turned", N)
        copied = st.counter("att_copied", N + 1)
        weighed = st.counter("att_weighed", N + 2)
        normed = st.counter("att_normed", N + 4)
        summed = st.counter("att_summed", N)
        off = 0 if sink_of is None else 1
        n_of = [sum(n for _, n, _ in pc) for pc in pieces]

        with st.run() as block:
            @block.sync
            def _(sp):
                core.stream(sp, core.used)

            @block.gpsimd
            def _(pool):
                with pool.Fori(0, turns) as it:
                    for r in range(per):
                        pool.wait_ge(scored.handle, it * steps + scored.at((r + 1) * q_tiles))
                        nc.gpsimd.tensor_copy(q_now[:, r % 2, :], q[:, bass.ds(it * per + r, 1), :].rearrange("p a n -> p (a n)")).then_inc(q_staged.handle, 1)

            @block.tensor
            def _(pe):
                def score(it, g):
                    r, i = divmod(g, q_tiles)
                    if i == 0:
                        pe.wait_ge(q_staged.handle, it * per + q_staged.at(r + 1))
                    pe.wait_ge(biased.handle, it * steps + biased.at(g + 1))
                    for b, (k0, n, _) in enumerate(pieces[i]):
                        last = nc.tensor.matmul(ps_s[g % 2][:, b * 512:b * 512 + n], q_now[:, r % 2, i * P:(i + 1) * P], k_of(it, r, k0, n), start=True, stop=True)
                    last.then_inc(scored.handle, 1)

                def turn(it, g):
                    i = g % q_tiles
                    pe.wait_ge(raised.handle, it * steps + raised.at(g + 3))
                    pe.wait_ge(copied.handle, it * steps + copied.at(g + 1))
                    for j in range(n_of[i] // P):
                        last = nc.tensor.transpose(ps_t[:, j * P:(j + 1) * P], p[:, g % 2, off + j * P:off + (j + 1) * P], core.ident[:])
                    last.then_inc(turned.handle, 1)

                def weigh(it, g):
                    r, i = divmod(g, q_tiles)
                    pe.wait_ge(copied.handle, it * steps + copied.at(g + 2))
                    pe.wait_ge(normed.handle, it * steps + normed.at(g + 3))
                    tiles = [(k0 + j * P) // P for k0, n, _ in pieces[i] for j in range(n // P)]
                    for j, kt in enumerate(tiles):
                        last = nc.tensor.matmul(ps_o[g % 2][:, 0:HD], pt[:, g % 2, j * P:(j + 1) * P], v_of(it, r, kt), start=(j == 0), stop=(j == len(tiles) - 1))
                    last.then_inc(weighed.handle, 1)

                pe.sem_inc(scored.handle, held)
                pe.sem_inc(weighed.handle, 2)
                with pe.Fori(0, turns) as it:
                    score(it, 0)
                    score(it, 1)
                    for g in range(steps):
                        turn(it, g)
                        if g + 2 < steps:
                            score(it, g + 2)
                        if g:
                            weigh(it, g - 1)
                    weigh(it, steps - 1)

            @block.vector
            def _(dve):
                def bias(it, g):
                    r, i = divmod(g, q_tiles)
                    dve.wait_ge(scored.handle, it * steps + scored.at(g + 1 + held))
                    dve.wait_ge(raised.handle, it * steps + raised.at(g + 1))
                    at = off
                    if off:
                        nc.vector.tensor_scalar(s[:, g % 2, 0:1], sink_of(it, r), 1.0, None, ALU.mult)
                    for b, (k0, n, bs) in enumerate(pieces[i]):
                        src = ps_s[g % 2][:, b * 512:b * 512 + n]
                        if bs is None:
                            last = nc.vector.tensor_copy(s[:, g % 2, at:at + n], src)
                        else:
                            last = nc.vector.tensor_tensor(s[:, g % 2, at:at + n], src, bias_of(it, r, *bs), ALU.add)
                        at += n
                    last.then_inc(biased.handle, 1)
                    dve.wait_ge(biased.handle, it * steps + biased.at(g + 3))
                    nc.vector.tensor_reduce(top[:, g % 2:g % 2 + 1], s[:, g % 2, 0:at], AX_X, ALU.max, negate=True).then_inc(topped.handle, 1)

                def norm(it, g):
                    r, i = divmod(g, q_tiles)
                    dve.wait_ge(weighed.handle, it * steps + weighed.at(g + 3))
                    dve.wait_ge(raised.handle, it * steps + raised.at(g + 3))
                    nc.vector.reciprocal(inv[:, g % 2:g % 2 + 1], total[:, g % 4:g % 4 + 1]).then_inc(summed.handle, 1)
                    dve.wait_ge(summed.handle, it * steps + summed.at(g + 1))
                    nc.vector.tensor_scalar(out_of(it, r, i), ps_o[g % 2][:, 0:HD], inv[:, g % 2:g % 2 + 1], None, ALU.mult).then_inc(normed.handle, 1)

                dve.sem_inc(biased.handle, 2)
                dve.sem_inc(normed.handle, 4)
                with dve.Fori(0, turns) as it:
                    bias(it, 0)
                    bias(it, 1)
                    for g in range(steps):
                        if g + 2 < steps:
                            bias(it, g + 2)
                        if g:
                            norm(it, g - 1)
                    norm(it, steps - 1)

            @block.scalar
            def _(act):
                def exp(it, g):
                    n = n_of[g % q_tiles] + off
                    act.wait_ge(topped.handle, it * steps + topped.at(g + 1))
                    act.wait_ge(normed.handle, it * steps + normed.at(g + 1))
                    nc.scalar.activation(p[:, g % 2, 0:n], s[:, g % 2, 0:n], ACT.Exp, bias=top[:, g % 2:g % 2 + 1],
                                         accum_out=total[:, g % 4:g % 4 + 1]).then_inc(raised.handle, 1)

                act.sem_inc(copied.handle, 1)
                act.sem_inc(raised.handle, 2)
                with act.Fori(0, turns) as it:
                    exp(it, 0)
                    for g in range(steps):
                        if g + 1 < steps:
                            exp(it, g + 1)
                        n = n_of[g % q_tiles]
                        act.wait_ge(turned.handle, it * steps + turned.at(g + 1))
                        act.wait_ge(weighed.handle, it * steps + weighed.at(g + 1))
                        nc.scalar.copy(pt[:, g % 2, 0:n], ps_t[:, 0:n]).then_inc(copied.handle, 1)


def group_norm_stage(core, o):
    nc = core.nc
    G, W = 4, 256
    with Stage(core, "groups") as st:
        square = st.sb("square", [P, LT * G, W])
        ss = st.sb("ss", [P, LT * G])
        rstd = st.sb("rstd", [P, LT * G])
        bank = [st.ps(f"bank{i}") for i in range(2)]
        squared = st.counter("group_squared", 1)
        inverted = st.counter("group_inverted", 1)
        rooted = st.counter("group_rooted", 1)
        scaled = st.counter("group_scaled", LT * G)
        turned = st.counter("group_turned", KD)
        kept = st.counter("group_kept", KD)
        chain = st.counter("group_chain", 1)
        with st.run() as block:
            @block.scalar
            def _(act):
                for t in range(LT):
                    for g in range(G):
                        last = nc.scalar.activation(square[:, t * G + g, :], o[:, t, g * W:(g + 1) * W], ACT.Square, scale=float(W) ** -0.5,
                                                    accum_out=ss[:, t * G + g:t * G + g + 1])
                last.then_inc(squared.handle, 1)
                act.wait_ge(inverted.handle, inverted.at(1))
                nc.scalar.activation(rstd[:], ss[:], ACT.Sqrt).then_inc(rooted.handle, 1)

            @block.vector
            def _(dve):
                link = Link(dve, chain)
                dve.wait_ge(squared.handle, squared.at(1))
                link(nc.vector.tensor_scalar(ss[:], ss[:], EPS, None, ALU.add))
                nc.vector.reciprocal(ss[:], ss[:]).then_inc(inverted.handle, 1)
                dve.wait_ge(rooted.handle, rooted.at(1))
                for g in range(G):
                    for t in range(LT):
                        v = o[:, t, g * W:(g + 1) * W]
                        nc.vector.tensor_scalar(v, v, rstd[:, t * G + g:t * G + g + 1], None, ALU.mult).then_inc(scaled.handle, 1)
                for k in range(KD):
                    dve.wait_ge(turned.handle, turned.at(k + 1))
                    nc.vector.tensor_scalar(core.h[:, k, 0:SEQ], bank[k % 2][:], core.col("group_out_g", k, 1), None, ALU.mult).then_inc(kept.handle, 1)

            @block.tensor
            def _(pe):
                for k in range(KD):
                    pe.wait_ge(scaled.handle, scaled.at(LT * (k // 2 + 1)))
                    if k >= 2:
                        pe.wait_ge(kept.handle, kept.at(k - 1))
                    for t in range(LT):
                        last = nc.tensor.transpose(bank[k % 2][:, t * P:(t + 1) * P], o[:, t, k * P:(k + 1) * P], core.ident[:])
                    last.then_inc(turned.handle, 1)


def turn_tokens_stage(core, name, src, dst, tiles):
    nc = core.nc
    with Stage(core, name) as st:
        bank = [st.ps(f"bank{i}") for i in range(4)]
        todo = [(t, j) for t in tiles for j in range(2)]
        turned = st.counter("back_turned", len(todo))
        kept = [st.counter("back_kept_act", len(todo) // 2), st.counter("back_kept_dve", len(todo) // 2)]
        with st.run() as block:
            @block.tensor
            def _(pe):
                for i, (t, j) in enumerate(todo):
                    if i >= 4:
                        pe.wait_ge(kept[i % 2].handle, kept[i % 2].at((i - 4) // 2 + 1))
                    for k in range(4):
                        last = nc.tensor.transpose(bank[i % 4][:, k * P:(k + 1) * P], src[:, 4 * j + k, t * P:(t + 1) * P], core.ident[:])
                    last.then_inc(turned.handle, 1)

            @block.scalar
            def _(act):
                for i, (t, j) in enumerate(todo):
                    if i % 2 == 0:
                        act.wait_ge(turned.handle, turned.at(i + 1))
                        nc.scalar.copy(dst[:, t, j * 512:(j + 1) * 512], bank[i % 4][:]).then_inc(kept[0].handle, 1)

            @block.vector
            def _(dve):
                for i, (t, j) in enumerate(todo):
                    if i % 2 == 1:
                        dve.wait_ge(turned.handle, turned.at(i + 1))
                        nc.vector.tensor_copy(dst[:, t, j * 512:(j + 1) * 512], bank[i % 4][:]).then_inc(kept[1].handle, 1)


def first_block(core):
    nc, ins = core.nc, core.ins
    norm_stage(core, "norm_a", [(0, SEQ, core.col("attn_norm_g"), None, None)])
    with Stage(core, "mixers") as mx:
        cols = mx.sb("cols", [P, LT, IN_COLS])
        widths = [CW] * 4 + [IN_COLS - 4 * CW]
        project_stage(core, "w_in", [range(LT)] * len(widths), widths, lambda t, c: cols[:, t, c * CW:c * CW + widths[c]])
        o = mx.sb("o", [P, LT, D])
        head_norm_stage(core, cols)
        spare = core.h[:].rearrange("p k n -> p (k n)")
        n = HEADS * MLA_DIM
        q96 = spare[:, 0:LT * n].rearrange("p (t h w) -> p t h w", t=LT, h=HEADS)
        k96 = spare[:, LT * n:2 * LT * n].rearrange("p (t h w) -> p t h w", t=LT, h=HEADS)
        ukv = spare[:, 2 * LT * n:2 * LT * n + LT * 512].rearrange("p (t w) -> p t w", t=LT)
        mla_stage(core, cols, q96, k96, ukv)
        for g, (name, dim) in enumerate((("moba", HD), ("mla", MLA_DIM), ("dil", HD), ("swa", HD))):
            with Stage(core, f"g_{name}") as gs:
                qT = gs.sb("qT", [MLA_DIM, HEADS, SEQ])
                kv = 2 if name == "swa" else HEADS
                kT = gs.sb("kT", [MLA_DIM, kv, SEQ])
                table = gs.sb("table", [P, HEADS, SEQ])
                gain = gs.sb("gain", [HD, 2])
                sink = gs.sb("sink", [P, HEADS])

                def extra(sp, loaded, name=name, g=g, gain=gain, table=table, sink=sink):
                    todo = [(table[:], core.consts["bias"][g])]
                    if name != "mla":
                        for j in range(2):
                            todo.append((gain[:, j:j + 1], ins[f"{name}_{'qk'[j]}_g"][0].unsqueeze(1)))
                    if name == "swa":
                        todo.append((sink[:], ins["swa_sinks"][0].partition_broadcast(P)))
                    if sp is not None:
                        for d, s in todo:
                            sp.dma_start(d, s).then_inc(loaded.handle, 16)
                    return len(todo)

                jobs = []
                for dst, at, heads, j in ((qT, (A_Q, 0, C_Q, D_Q)[g], HEADS, 0), (kT, (A_K, 0, C_K, D_K)[g], kv, 1)):
                    for hd in range(heads):
                        if name == "mla":
                            src = lambda t, v=(q96, k96)[j], hd=hd: v[:, t, hd, :]
                            jobs.append((src, LT, dim, [dst[0:dim, hd, :]], None, float(dim) ** -0.5 if j == 0 else 1.0))
                        else:
                            src = lambda t, c=at + hd * HD: cols[:, t, c:c + HD]
                            jobs.append((src, LT, dim, [dst[0:dim, hd, :]], gain[:, j:j + 1], float(dim) ** -0.5 if j == 0 else 1.0))
                turn_heads_stage(core, f"turn_{name}", jobs, zero=[] if dim == MLA_DIM else [qT[dim:MLA_DIM], kT[dim:MLA_DIM]], extra=extra)
                per = 2

                def k_of(it, r, k0, n, kT=kT, name=name):
                    head = it if name == "swa" else it * per + r
                    return kT[:, bass.ds(head, 1), k0:k0 + n].rearrange("p a n -> p (a n)")

                def v_of(it, r, kt, name=name):
                    if name == "mla":
                        return ukv[:, kt, bass.ds(it * (2 * per * HD) + (r * 2 * HD + HD), HD)]
                    if name == "swa":
                        return cols[:, kt, bass.ds(it * HD + D_V, HD)]
                    return cols[:, kt, bass.ds(it * (per * HD) + ((A_V if name == "moba" else C_V) + r * HD), HD)]

                attention_stage(
                    core, f"att_{name}", HEADS // per, per, MLA_DIM, LT,
                    lambda i: [(0, (i + 1) * P, (SEQ - (i + 1) * P, SEQ))], qT, k_of, v_of,
                    lambda it, r, a, b, table=table: table[:, bass.ds(it * per + r, 1), a:b].rearrange("p a n -> p (a n)"),
                    lambda it, r, i, g=g: o[:, i, bass.ds(it * (per * HD) + (g * 256 + r * HD), HD)],
                    (lambda it, r, sink=sink: sink[:, bass.ds(it * per + r, 1)]) if name == "swa" else None)
        group_norm_stage(core, o)
    residual_stage(core, "w_o")
    norm_stage(core, "norm_m", [(0, SEQ, core.col("mlp_norm_g"), None, None)])
    mlp_stage(core)


QC = 256
TURNS = D // QC
UP = 772
CTX_AT = SEQ + 2


def filter_net_stage(core, h2):
    nc, ins = core.nc, core.ins
    with Stage(core, "fnet") as st:
        z = st.sb("z", [33, TOK])
        w1 = st.sb("w1", [33, 64])
        w2 = st.sb("w2", [64, 64])
        col = st.sb("col", [64, 4])
        arg = st.sb("arg", [64, TOK])
        turns = st.sb("turns", [64, TOK])
        h1 = st.sb("h1", [64, TOK])
        acc = [st.ps(f"acc{i}", 2) for i in range(2)]
        loaded = st.counter("fnet_loaded", 16 * 7)
        done = st.counter("fnet_done", 2)
        reduced = st.counter("fnet_reduced", 2)
        bent = st.counter("fnet_bent", 2)
        chain = st.counter("fnet_chain", 12)
        spans = ((0, SEQ), (SEQ, CTX))
        with st.run() as block:
            @block.sync
            def _(sp):
                sp.dma_start(z[:], core.consts["filter_z"]).then_inc(loaded.handle, 16)
                sp.dma_start(w1[:], ins["hy_ffn_w1_2"]).then_inc(loaded.handle, 16)
                sp.dma_start(w2[:], ins["hy_ffn_w2_2"]).then_inc(loaded.handle, 16)
                sp.dma_start(col[:, 0:1], ins["hy_ffn_b1_2"].unsqueeze(1)).then_inc(loaded.handle, 16)
                sp.dma_start(col[:, 1:2], ins["hy_ffn_b2_2"].unsqueeze(1)).then_inc(loaded.handle, 16)
                sp.dma_start(col[:, 2:3], ins["hy_sin_freq_2"][0].unsqueeze(1)).then_inc(loaded.handle, 16)
                sp.dma_start(col[:, 3:4], ins["hy_sin_freq_2"][1].unsqueeze(1)).then_inc(loaded.handle, 16)

            @block.tensor
            def _(pe):
                pe.wait_ge(loaded.handle, loaded.at(112))
                for layer, (w, x) in enumerate(((w1, z), (w2, h1))):
                    if layer:
                        pe.wait_ge(bent.handle, bent.at(1))
                    for c0, n in spans:
                        last = nc.tensor.matmul(acc[layer][0:64, c0:c0 + n], w[:], x[:, c0:c0 + n], start=True, stop=True)
                    last.then_inc(done.handle, 1)

            @block.vector
            def _(dve):
                link = Link(dve, chain)
                dve.wait_ge(loaded.handle, loaded.at(112))
                for layer in range(2):
                    dve.wait_ge(done.handle, done.at(layer + 1))
                    link(nc.vector.tensor_scalar(arg[:], acc[layer][0:64, 0:TOK], col[:, layer:layer + 1], col[:, 2 + layer:3 + layer], ALU.add, ALU.mult))
                    link(nc.vector.tensor_scalar(turns[:], arg[:], 1.0 / TWO_PI, ROUND_MAGIC, ALU.mult, ALU.add))
                    link(nc.vector.tensor_scalar(turns[:], turns[:], -ROUND_MAGIC, None, ALU.add))
                    link(nc.vector.scalar_tensor_tensor(out=arg[:], in0=turns[:], scalar=-TWO_PI_HI, in1=arg[:], op0=ALU.mult, op1=ALU.add))
                    link(nc.vector.scalar_tensor_tensor(out=arg[:], in0=turns[:], scalar=-TWO_PI_LO, in1=arg[:], op0=ALU.mult, op1=ALU.add))
                    nc.vector.tensor_scalar(arg[:], arg[:], SIN_MAX, -SIN_MAX, ALU.min, ALU.max).then_inc(reduced.handle, 1)
                    dve.wait_ge(bent.handle, bent.at(layer + 1))

            @block.scalar
            def _(act):
                for layer, dst in enumerate((h1, h2)):
                    act.wait_ge(reduced.handle, reduced.at(layer + 1))
                    nc.scalar.activation(dst[:], arg[:], ACT.Sin).then_inc(bent.handle, 1)
        st.used[-1] = (chain, 10)


def hyena_chunks(core):
    w = core.ins["hy_w_in_2"].rearrange("(k p) (s c) -> p k s c", p=P, s=3)
    out = core.ins["hy_w_out_2"].rearrange("(q k p) n -> q p k n", p=P, k=2)

    def first(q):
        return lambda slot: [(slot[:].rearrange("p (k s c) -> p k s c", k=KD, s=2)[:, :, s], w[:, :, s, bass.ds(q * QC, QC)]) for s in range(2)]

    def second(q):
        return lambda slot: [(slot[:, 0:KD * QC].rearrange("p (k c) -> p k c", k=KD), w[:, :, 2, bass.ds(q * QC, QC)])]

    def third(q):
        return lambda slot: [(slot[:, 0:2 * D].rearrange("p (k n) -> p k n", k=2), out[bass.ds(q, 1)].rearrange("a p k n -> (a p) k n"))]
    return [first, second, third]


def hyena_stage(core, gate):
    nc, ins = core.nc, core.ins
    n0 = core.used
    x, h = core.x, core.h
    with Stage(core, "hyena") as st:
        h2 = st.sb("h2", [64, TOK])
        filter_net_stage(core, h2)
        tables = {n: st.sb(n, [P, 4, k, w]) for n, k, w in (("dft_l", 2, 256), ("idft_l", 2, 256), ("dft_c", 1, P), ("idft_c", 1, P))}
        raw = st.sb("raw", [P, 2, UP])
        u = st.sb("u", [P, 6, UP])
        v_tok = st.sb("v_tok", [P, 6, QC])
        ab = st.sb("ab", [P, 2, 2, 3, QC])
        taps = ab[:].rearrange("p a b c n -> p a (b c) n")
        pq = st.sb("pq", [P, 2, 2, 3, QC])
        win = st.sb("win", [P, 6, 2, QC])
        w3 = st.sb("w3", [64, 4, QC])
        even = st.sb("even", [P, 2, QC])
        t1 = st.sb("t1", [P, TOK])
        t2 = st.sb("t2", [P, TOK])
        lat = [st.ps(f"lat{i}") for i in range(2)]
        ctx = [st.ps(f"ctx{i}") for i in range(2)]
        spec = [st.ps(f"spec{i}") for i in range(4)]

        IP = ["act"] * 6 + ["act"] * 2 + ["dve"] * 2 + ["act"] * 2 + ["dve"] * 2 + ["dve"] * 8
        NI, NA, ND = len(IP), IP.count("act"), IP.count("dve")
        SP = 36
        rank = [IP[:i].count(IP[i]) for i in range(NI)]
        ip_done = st.counter("hy_ip_done", NI * TURNS)
        ip_act = st.counter("hy_ip_act", NA * TURNS)
        ip_dve = st.counter("hy_ip_dve", ND * TURNS + 2)
        sp_done = st.counter("hy_sp_done", SP * TURNS)
        sp_free = st.counter("hy_sp_free", SP * TURNS + 4)
        even_kept = st.counter("hy_even_kept", 24 * TURNS)
        raw_kept = st.counter("hy_raw_kept", 6 * TURNS)
        convolved = st.counter("hy_convolved", 6 * TURNS + 2)
        taps_made = st.counter("hy_taps_made", 12 * TURNS)
        tok_kept = st.counter("hy_tok_kept", 2 * TURNS)
        combined = st.counter("hy_combined", 2 * TURNS)
        gated = st.counter("hy_gated", 2 * TURNS)
        win_loaded = st.counter("hy_win_loaded", 32 * TURNS)
        tab_loaded = st.counter("hy_tab_loaded", 64)
        pads = st.counter("hy_pads", 1)
        chain = st.counter("hy_chain", 0)

        def parity(tile, c0, n):
            return tile[:, c0:c0 + n].rearrange("p (i a) -> p a i", a=2)

        with st.run() as block:
            @block.sync
            def _(sp):
                def load_filters(q):
                    sp.dma_start(win[:], core.consts["window"][:, :, :, bass.ds(q * QC, QC)]).then_inc(win_loaded.handle, 16)
                    sp.dma_start(w3[:], ins["hy_ffn_w3_2"].rearrange("a (o c) -> a o c", o=4)[:, :, bass.ds(q * QC, QC)]).then_inc(win_loaded.handle, 16)

                load_filters(0)
                for name, t in tables.items():
                    sp.dma_start(t[:], core.consts[name]).then_inc(tab_loaded.handle, 16)
                with sp.Fori(0, TURNS - 1) as it:
                    for j, place in enumerate(hyena_chunks(core)):
                        n = n0 + 3 + j
                        sp.wait_ge(core.freed.handle, it * 3 + (n - NS + 1))
                        core.issue(sp, n, place(it + 1))
                        if j == 1:
                            sp.wait_ge(taps_made.handle, it * 12 + taps_made.at(12))
                            load_filters(it + 1)
                core.used = core.issued = n0 + 3 * TURNS
                core.stream(sp, core.used)

            @block.tensor
            def _(pe):
                def take(it, i):
                    j = i - 2
                    if j < 0:
                        pe.wait_ge(ip_dve.handle, it * ND + ip_dve.at(rank[j] + 1 - ND + 2))
                    elif IP[j] == "act":
                        pe.wait_ge(ip_act.handle, it * NA + ip_act.at(rank[j] + 1))
                    else:
                        pe.wait_ge(ip_dve.handle, it * ND + ip_dve.at(rank[j] + 3))
                    return lat[i % 2], ctx[i % 2]

                def take_spec(it, m):
                    pe.wait_ge(sp_free.handle, it * SP + sp_free.at(m + 1))
                    return spec[m % 4]

                def filters(it, o):
                    for t in range(6):
                        b = take_spec(it, 18 * o + t)
                        for d in range(2):
                            last = nc.tensor.matmul(b[:, d * QC:(d + 1) * QC], h2[:, t * P:(t + 1) * P], w3[:, 2 * o + d, :], start=True, stop=True)
                        last.then_inc(sp_done.handle, 1)

                def transform(it, m0, src):
                    for a in range(2):
                        for f in range(3):
                            b = take_spec(it, m0 + 3 * a + f)
                            table, o, base, kn = (tables["dft_l"], f * P, 0, 2) if f < 2 else (tables["dft_c"], 0, 4, 1)
                            for par in range(2):
                                for k in range(kn):
                                    last = nc.tensor.matmul(b[:, par * QC:(par + 1) * QC], table[:, 2 * a + par, k, o:o + P],
                                                            src(a)[:, base + kn * par + k, :], start=(k == 0), stop=(k == kn - 1))
                            last.then_inc(sp_done.handle, 1)

                def turn_tokens(it, i0):
                    for j in range(2):
                        bl, bc = take(it, i0 + j)
                        for par in range(2):
                            for k in range(2):
                                nc.tensor.transpose(bl[:, (2 * par + k) * P:(2 * par + k + 1) * P],
                                                    parity(u[:, j], 0, SEQ)[:, par, k * P:(k + 1) * P], core.ident[:])
                            last = nc.tensor.transpose(bc[:, par * P:(par + 1) * P], parity(u[:, j], CTX_AT, CTX)[:, par, :], core.ident[:])
                        last.then_inc(ip_done.handle, 1)

                def back(it, o, i0):
                    pe.wait_ge(combined.handle, it * 2 + combined.at(o + 1))
                    for j in range(2):
                        bl, bc = take(it, i0 + j)
                        for b, table, tiles, n in ((bl, tables["idft_l"], (0, 1), 256), (bc, tables["idft_c"], (2,), P)):
                            for par in range(2):
                                steps = [(a, k, f) for a in range(2) for k, f in enumerate(tiles)]
                                for s, (a, k, f) in enumerate(steps):
                                    last = nc.tensor.matmul(b[:, par * n:(par + 1) * n], pq[:, a, par, f, j * P:(j + 1) * P],
                                                            table[:, 2 * a + par, k, :], start=(s == 0), stop=(s == len(steps) - 1))
                        last.then_inc(ip_done.handle, 1)

                pe.wait_ge(tab_loaded.handle, tab_loaded.at(64))
                with pe.Fori(0, TURNS) as it:
                    pe.wait_ge(win_loaded.handle, it * 32 + win_loaded.at(32))
                    filters(it, 0)
                    for i in range(6):
                        c = 0 if i < 4 else 1
                        n = n0 + c
                        if i in (0, 4):
                            core.await_chunk(pe, n, it, 3)
                        w = by_k(core.slot(n), CW if c == 0 else QC)
                        bl, bc = take(it, i)
                        col = (i if c == 0 else i - 4) * P
                        for k in range(KD):
                            nc.tensor.matmul(bl[:], w[:, k, col:col + P], h[:, k, 0:SEQ], start=(k == 0), stop=(k == KD - 1))
                        for k in range(KD):
                            last = nc.tensor.matmul(bc[:, 0:CTX], w[:, k, col:col + P], h[:, k, SEQ:TOK], start=(k == 0), stop=(k == KD - 1))
                        last.then_inc(ip_done.handle, 1)
                    for o in range(2):
                        if o:
                            filters(it, 1)
                        pe.wait_ge(taps_made.handle, it * 12 + taps_made.at(6 * o + 6))
                        transform(it, 18 * o + 6, lambda a: taps[:, a])
                        if o == 0:
                            pe.wait_ge(convolved.handle, it * 6 + convolved.at(2 + 2))
                        else:
                            pe.wait_ge(gated.handle, it * 2 + gated.at(1))
                        turn_tokens(it, 6 if o == 0 else 10)
                        pe.wait_ge(tok_kept.handle, it * 2 + tok_kept.at(o + 1))
                        transform(it, 18 * o + 12, lambda a: v_tok[:])
                        back(it, o, 8 if o == 0 else 12)
                    n = n0 + 2
                    core.await_chunk(pe, n, it, 3)
                    pe.wait_ge(gated.handle, it * 2 + gated.at(2))
                    w = by_k(core.slot(n), D, 2)
                    for j in range(KD):
                        bl, bc = take(it, 14 + j)
                        for k in range(2):
                            nc.tensor.matmul(bl[:], w[:, k, j * P:(j + 1) * P], u[:, k, 0:SEQ], start=(k == 0), stop=(k == 1))
                        for k in range(2):
                            last = nc.tensor.matmul(bc[:, 0:CTX], w[:, k, j * P:(j + 1) * P], u[:, k, CTX_AT:CTX_AT + CTX], start=(k == 0), stop=(k == 1))
                        last.then_inc(ip_done.handle, 1)

            @block.gpsimd
            def _(pool):
                nc.gpsimd.memset(raw[:], 0.0).then_inc(pads.handle, 1)
                with pool.Fori(0, TURNS) as it:
                    for i in (4, 6, NI):
                        pool.wait_ge(ip_done.handle, it * NI + ip_done.at(i))
                        pool.sem_inc(core.freed.handle, 1)

            @block.scalar
            def _(act):
                def keep_even(it, m0, e0):
                    for s in range(6):
                        act.wait_ge(sp_done.handle, it * SP + sp_done.at(m0 + s + 1))
                        act.wait_ge(sp_free.handle, it * SP + sp_free.at(m0 + s - 2 + 1 + 4))
                        nc.scalar.copy(even[:, s % 2, :], spec[(m0 + s) % 4][:, 0:QC]).then_inc(even_kept.handle, 1)

                def keep_tokens(it, i0):
                    for j in range(2):
                        act.wait_ge(ip_done.handle, it * NI + ip_done.at(i0 + j + 1))
                        nc.scalar.copy(v_tok[:, 0:4, j * P:(j + 1) * P], lat[(i0 + j) % 2][:].rearrange("p (t n) -> p t n", n=P))
                        last = nc.scalar.copy(v_tok[:, 4:6, j * P:(j + 1) * P], ctx[(i0 + j) % 2][:, 0:CTX].rearrange("p (t n) -> p t n", n=P))
                        last.then_inc(ip_act.handle, 1)
                    act.wait_ge(ip_act.handle, it * NA + ip_act.at(rank[i0 + 1] + 1))
                    act.sem_inc(tok_kept.handle, 1)

                act.wait_ge(pads.handle, pads.at(1))
                with act.Fori(0, TURNS) as it:
                    for i in range(6):
                        act.wait_ge(ip_done.handle, it * NI + ip_done.at(i + 1))
                        act.wait_ge(convolved.handle, it * 6 + convolved.at(i + 1))
                        b = core.vec[:, bass.ds(it * 2 + (VEC_AT["hy_b_in_2"][0] + (i // 2) * KD + i % 2), 1)]
                        nc.scalar.activation(raw[:, i % 2, 1:1 + SEQ], lat[i % 2][:], ACT.Identity, bias=b).then_inc(raw_kept.handle, 1)
                        nc.scalar.activation(raw[:, i % 2, SEQ + 3:UP - 1], ctx[i % 2][:, 0:CTX], ACT.Identity, bias=b).then_inc(ip_act.handle, 1)
                    for o in range(2):
                        keep_even(it, 18 * o + 6, 12 * o)
                        keep_tokens(it, 6 if o == 0 else 10)
                        keep_even(it, 18 * o + 12, 12 * o + 6)

            @block.vector
            def _(dve):
                per_turn = 2 * (6 + 16) + 12 + 8
                links = []

                def combine(it, link, m0, e0, dst):
                    for a in range(2):
                        for f in range(3):
                            s = 3 * a + f
                            m = m0 + s
                            dve.wait_ge(sp_done.handle, it * SP + sp_done.at(m + 1))
                            dve.wait_ge(even_kept.handle, it * 24 + even_kept.at(e0 + s + 1))
                            odd = spec[m % 4][:, QC:2 * QC]
                            nc.vector.tensor_tensor(dst[:, a, 0, f, :], even[:, s % 2, :], odd, ALU.add)
                            if a == 0:
                                last = nc.vector.tensor_tensor(dst[:, a, 1, f, :], even[:, s % 2, :], odd, ALU.subtract)
                            else:
                                last = nc.vector.tensor_tensor(dst[:, a, 1, f, :], odd, even[:, s % 2, :], ALU.subtract)
                            last.then_inc(sp_free.handle, 1)

                def make_taps(it, link, o):
                    for t in range(6):
                        m = 18 * o + t
                        dve.wait_ge(sp_done.handle, it * SP + sp_done.at(m + 1))
                        link(nc.vector.tensor_tensor(t1[:, 0:2 * QC], spec[m % 4][:], win[:, t].rearrange("p d n -> p (d n)"), ALU.mult))
                        nc.vector.tensor_tensor(taps[:, 0, t, :], t1[:, 0:QC], t1[:, QC:2 * QC], ALU.add).then_inc(sp_free.handle, 1)
                        nc.vector.tensor_tensor(taps[:, 1, t, :], t1[:, 0:QC], t1[:, QC:2 * QC], ALU.subtract).then_inc(taps_made.handle, 1)
                        dve.wait_ge(taps_made.handle, it * 12 + taps_made.at(6 * o + t + 1))

                def flat(v):
                    return v.rearrange("p f n -> p (f n)")

                def products(it, link, o):
                    for s in range(2):
                        A, B = flat(ab[:, 0, s]), flat(ab[:, 1, s])
                        Pc, Qs = flat(pq[:, 0, s]), flat(pq[:, 1, s])
                        nc.vector.tensor_tensor(t1[:], A, Pc, ALU.mult)
                        link(nc.vector.tensor_tensor(t2[:], B, Qs, ALU.mult))
                        nc.vector.tensor_tensor(A, A, Qs, ALU.mult)
                        link(nc.vector.tensor_tensor(B, B, Pc, ALU.mult))
                        nc.vector.tensor_tensor(B, A, B, ALU.add)
                        link(nc.vector.tensor_tensor(t1[:], t1[:], t2[:], ALU.subtract))
                        link(nc.vector.tensor_copy(A, t1[:]))
                    lo, hi = [flat(ab[:, a, 0]) for a in range(2)], [flat(ab[:, a, 1]) for a in range(2)]
                    nc.vector.tensor_tensor(flat(pq[:, 0, 0]), lo[0], hi[0], ALU.add)
                    nc.vector.tensor_tensor(flat(pq[:, 0, 1]), lo[0], hi[0], ALU.subtract)
                    nc.vector.tensor_tensor(flat(pq[:, 1, 0]), lo[1], hi[1], ALU.subtract)
                    nc.vector.tensor_tensor(flat(pq[:, 1, 1]), lo[1], hi[1], ALU.add).then_inc(combined.handle, 1)

                def gates(it, link, o, i0):
                    for j in range(2):
                        i = i0 + j
                        dve.wait_ge(ip_done.handle, it * NI + ip_done.at(i + 1))
                        b = core.vec[:, bass.ds(it * 2 + (VEC_AT["hy_filter_bias_2"][0] + o * KD + j), 1)]
                        y = lambda tile, n: tile[:, 0:n].rearrange("p (a i) -> p a i", a=2)
                        nc.vector.scalar_tensor_tensor(out=y(t1[:], SEQ), in0=parity(u[:, j], 0, SEQ), scalar=b, in1=y(lat[i % 2][:], SEQ), op0=ALU.mult, op1=ALU.add)
                        ins_ = nc.vector.scalar_tensor_tensor(out=y(t2[:], CTX), in0=parity(u[:, j], CTX_AT, CTX), scalar=b, in1=y(ctx[i % 2][:], CTX), op0=ALU.mult, op1=ALU.add)
                        ins_.then_inc(ip_dve.handle, 1)
                        dve.wait_ge(ip_dve.handle, it * ND + ip_dve.at(rank[i] + 1 + 2))
                        xo = u[:, 2 + 2 * o + j]
                        nc.vector.tensor_tensor(parity(u[:, j], 0, SEQ), y(t1[:], SEQ), parity(xo, 0, SEQ), ALU.mult)
                        last = nc.vector.tensor_tensor(parity(u[:, j], CTX_AT, CTX), y(t2[:], CTX), parity(xo, CTX_AT, CTX), ALU.mult)
                        if j == 0:
                            link(last)
                        else:
                            last.then_inc(gated.handle, 1)
                            dve.wait_ge(gated.handle, it * 2 + gated.at(o + 1))

                gb = t2[:, 0:2 * KD].rearrange("p (s k) -> p s k", s=2)
                pre = Link(dve, chain)
                for s in range(2):
                    pre(nc.vector.tensor_tensor(gb[:, s], gate[s], core.col("hy_b_out_2"), ALU.mult))
                for s, (c0, n) in enumerate(((0, SEQ), (SEQ, CTX))):
                    for k in range(KD):
                        last = nc.vector.tensor_scalar(x[:, k, c0:c0 + n], x[:, k, c0:c0 + n], gb[:, s, k:k + 1], None, ALU.add)
                pre(last)
                dve.sem_inc(ip_dve.handle, 2)
                dve.sem_inc(sp_free.handle, 4)
                dve.sem_inc(convolved.handle, 2)
                n_pre = pre.n
                with dve.Fori(0, TURNS) as it:
                    dve.wait_ge(win_loaded.handle, it * 32 + win_loaded.at(32))
                    link = Link(dve, chain, it * LINKS_PER_TURN + n_pre)
                    make_taps(it, link, 0)
                    for i in range(6):
                        dve.wait_ge(ip_act.handle, it * NA + ip_act.at(i + 1))
                        r = raw[:, i % 2]
                        col = lambda name, tap=0: core.vec[:, bass.ds(it * 2 + (VEC_AT[name][0] + tap * 24 + (i // 2) * KD + i % 2), 1)]
                        m = UP - 2
                        dst = u[:, i, 0:m]
                        link(nc.vector.tensor_scalar(dst, r[:, 1:1 + m], col("hy_short_w_2", 1), col("hy_short_b_2"), ALU.mult, ALU.add))
                        link(nc.vector.scalar_tensor_tensor(out=dst, in0=r[:, 0:m], scalar=col("hy_short_w_2", 0), in1=dst, op0=ALU.mult, op1=ALU.add))
                        nc.vector.scalar_tensor_tensor(out=dst, in0=r[:, 2:2 + m], scalar=col("hy_short_w_2", 2), in1=dst, op0=ALU.mult, op1=ALU.add).then_inc(convolved.handle, 1)
                    dve.wait_ge(convolved.handle, it * 6 + convolved.at(8))
                    for o in range(2):
                        if o:
                            make_taps(it, link, 1)
                        combine(it, link, 18 * o + 6, 12 * o, pq)
                        combine(it, link, 18 * o + 12, 12 * o + 6, ab)
                        dve.wait_ge(sp_free.handle, it * SP + sp_free.at(18 * o + 18 + 4))
                        products(it, link, o)
                        gates(it, link, o, 8 if o == 0 else 12)
                    for j in range(KD):
                        i = 14 + j
                        dve.wait_ge(ip_done.handle, it * NI + ip_done.at(i + 1))
                        dve.wait_ge(ip_dve.handle, it * ND + ip_dve.at(rank[i] + 2))
                        nc.vector.scalar_tensor_tensor(out=x[:, j, 0:SEQ], in0=lat[i % 2][:], scalar=gate[0][:, j:j + 1], in1=x[:, j, 0:SEQ], op0=ALU.mult, op1=ALU.add)
                        nc.vector.scalar_tensor_tensor(out=x[:, j, SEQ:TOK], in0=ctx[i % 2][:, 0:CTX], scalar=gate[1][:, j:j + 1], in1=x[:, j, SEQ:TOK], op0=ALU.mult, op1=ALU.add).then_inc(ip_dve.handle, 1)
                    links.append(link.n)
                assert links == [LINKS_PER_TURN], links
        st.used = [(s, n) if s is not chain else (chain, 3 + TURNS * LINKS_PER_TURN) for s, n in st.used]


LINKS_PER_TURN = 2 * (6 + 2 * 4 + 1) + 12


def route_stage(core, layer, ctx, xe_l, xe_c, sp_l, sp_c):
    nc, ins = core.nc, core.ins
    tiles = LT + (CT if ctx else 0)
    cols = tiles * P
    E = N_EXP
    with Stage(core, "route") as st:
        tok = st.sb("tok", [P, tiles, D])
        turn_tokens_stage(core, "back", core.h, tok, range(tiles))
        router = st.sb("router", [P, KD, E])
        number = st.sb("number", [P, CAP_L])
        aff = st.sb("aff", [P, tiles, E])
        top = st.sb("top", [P, tiles])
        total = st.sb("total", [P, tiles])
        rows = st.sb("rows", [E, cols])
        work = st.sb("work", [E, cols])
        best = st.sb("best", [E, 8])
        sel = rows
        pos = st.sb("pos", [E, cols])
        one = st.sb("one", [E, SEQ])
        at = st.sb("at", [P, tiles, E])
        pick_l = st.sb("pick_l", [P, LT, E, CAP_L])
        pick_c = st.sb("pick_c", [P, CT, E, CAP_C]) if ctx else None
        pl = st.ps("logits")
        pr = st.ps("by_expert", 2)
        pa = st.ps("places")
        bank = [st.ps(f"bank{i}") for i in range(4)]
        loaded = st.counter("route_loaded", 32)
        scored = st.counter("route_scored", 1)
        shifted = st.counter("route_shifted", 1)
        raised = st.counter("route_raised", 1)
        softmaxed = st.counter("route_softmaxed", 1)
        rowed = st.counter("route_rowed", 1)
        placed = st.counter("route_placed", 1)
        turned = st.counter("route_turned", 1)
        picked = st.counter("route_picked", 1)
        gathers = [(d, c, "l") for d in range(KD) for c in range(2)] + ([(d, 0, "c") for d in range(KD)] if ctx else [])
        ng = len(gathers)
        gathered = st.counter("route_gathered", ng)
        kept = [st.counter("route_kept_act", ng // 2), st.counter("route_kept_dve", ng // 2)]
        gated = st.counter("route_gated", 1)
        scatters = [("l", j) for j in range(E // 2)] + ([("c", j) for j in range(E // 4)] if ctx else [])
        spread = st.counter("route_spread", len(scatters))
        spread_kept = st.counter("route_spread_kept", len(scatters))
        chain = st.counter("route_chain", 0)
        spans = [(0, SEQ, CAP_L)] + ([(SEQ, CTX, CAP_C)] if ctx else [])
        n_links = []
        with st.run() as block:
            @block.sync
            def _(sp):
                sp.dma_start(router[:], ins["moe_router_2"][layer].rearrange("(k p) e -> p k e", p=P)).then_inc(loaded.handle, 16)
                sp.dma_start(number[:], core.consts["slot_number"]).then_inc(loaded.handle, 16)

            @block.tensor
            def _(pe):
                pe.wait_ge(loaded.handle, loaded.at(32))
                for t in range(tiles):
                    for k in range(KD):
                        last = nc.tensor.matmul(pl[:, t * E:(t + 1) * E], core.h[:, k, t * P:(t + 1) * P], router[:, k, :], start=(k == 0), stop=(k == KD - 1))
                last.then_inc(scored.handle, 1)
                pe.wait_ge(softmaxed.handle, softmaxed.at(1))
                for t in range(tiles):
                    last = nc.tensor.transpose(pr[0:E, t * P:(t + 1) * P], aff[:, t, :], core.ident[:])
                last.then_inc(rowed.handle, 1)
                pe.wait_ge(placed.handle, placed.at(1))
                for t in range(tiles):
                    last = nc.tensor.transpose(pa[:, t * E:(t + 1) * E], pos[:, t * P:(t + 1) * P], core.ident[0:E, 0:E])
                last.then_inc(turned.handle, 1)
                pe.wait_ge(picked.handle, picked.at(1))
                for i, (d, c, s) in enumerate(gathers):
                    if i >= 4:
                        pe.wait_ge(kept[i % 2].handle, kept[i % 2].at((i - 4) // 2 + 1))
                    tt = range(LT) if s == "l" else range(CT)
                    for t in tt:
                        rhs = pick_l[:, t, 8 * c:8 * c + 8, :] if s == "l" else pick_c[:, t]
                        src = tok[:, t if s == "l" else LT + t, d * P:(d + 1) * P]
                        last = nc.tensor.matmul(bank[i % 4][:], src, rhs.rearrange("p e s -> p (e s)"), start=(t == 0), stop=(t == tt[-1]))
                    last.then_inc(gathered.handle, 1)
                pe.wait_ge(gated.handle, gated.at(1))
                for i in (0, 1):
                    pe.wait_ge(kept[i].handle, kept[i].at(ng // 2))
                for i, (s, j) in enumerate(scatters):
                    if i >= 4:
                        pe.wait_ge(spread_kept.handle, spread_kept.at(i - 3))
                    for t in range(LT if s == "l" else CT):
                        src = pick_l[:, t, 2 * j:2 * j + 2, :] if s == "l" else pick_c[:, t, 4 * j:4 * j + 4, :]
                        last = nc.tensor.transpose(bank[i % 4][:, t * P:(t + 1) * P], src.rearrange("p e s -> p (e s)"), core.ident[:])
                    last.then_inc(spread.handle, 1)

            def keep(i):
                d, c, s = gathers[i]
                if s == "l":
                    return xe_l[:, 8 * c:8 * c + 8, d, :], bank[i % 4][:].rearrange("p (e s) -> p e s", s=CAP_L)
                return xe_c[:, :, d, :], bank[i % 4][:].rearrange("p (e s) -> p e s", s=CAP_C)

            @block.scalar
            def _(act):
                act.wait_ge(shifted.handle, shifted.at(1))
                nc.scalar.activation(aff[:], aff[:], ACT.Exp).then_inc(raised.handle, 1)
                for i in range(0, ng, 2):
                    act.wait_ge(gathered.handle, gathered.at(i + 1))
                    dst, src = keep(i)
                    nc.scalar.copy(dst, src).then_inc(kept[0].handle, 1)

            @block.vector
            def _(dve):
                link = Link(dve, chain)
                dve.wait_ge(scored.handle, scored.at(1))
                logits = pl[:, 0:tiles * E].rearrange("p (t e) -> p t e", e=E)
                link(nc.vector.tensor_reduce(top[:], logits, AX_X, ALU.max))
                nc.vector.tensor_tensor(aff[:], logits, top[:].unsqueeze(2).to_broadcast([P, tiles, E]), ALU.subtract).then_inc(shifted.handle, 1)
                dve.wait_ge(raised.handle, raised.at(1))
                link(nc.vector.tensor_reduce(total[:], aff[:], AX_X, ALU.add))
                link(nc.vector.reciprocal(total[:], total[:]))
                nc.vector.tensor_tensor(aff[:], aff[:], total[:].unsqueeze(2).to_broadcast([P, tiles, E]), ALU.mult).then_inc(softmaxed.handle, 1)
                nc.vector.memset(one[:], 1.0)
                dve.wait_ge(rowed.handle, rowed.at(1))
                link(nc.vector.tensor_copy(rows[:], pr[0:E, 0:cols]))
                for c0, n, cap in spans:
                    src = rows
                    for _r in range(cap // 8):
                        link(nc.vector.max(best[:], src[:, c0:c0 + n]))
                        link(nc.vector.match_replace(work[:, c0:c0 + n], best[:], src[:, c0:c0 + n], -1.0))
                        src = work
                link(nc.vector.tensor_scalar(sel[:], work[:], 0.0, None, ALU.is_lt))
                for c0, n, cap in spans:
                    last = nc.vector.tensor_tensor_scan(pos[:, c0:c0 + n], one[:, 0:n], sel[:, c0:c0 + n], 0.0, ALU.mult, ALU.add)
                link(last)
                nc.vector.tensor_tensor(pos[:], pos[:], sel[:], ALU.mult).then_inc(placed.handle, 1)
                dve.wait_ge(turned.handle, turned.at(1))
                link(nc.vector.tensor_copy(at[:], pa[:, 0:tiles * E].rearrange("p (t e) -> p t e", e=E)))
                dve.wait_ge(loaded.handle, loaded.at(32))
                sets = [(pick_l[:, t], t, CAP_L) for t in range(LT)] + ([(pick_c[:, t], LT + t, CAP_C) for t in range(CT)] if ctx else [])
                for v, t, cap in sets:
                    last = nc.vector.tensor_tensor(v, number[:, 0:cap].unsqueeze(1).to_broadcast([P, E, cap]),
                                                   at[:, t, :].unsqueeze(2).to_broadcast([P, E, cap]), ALU.is_equal)
                last.then_inc(picked.handle, 1)
                for i in range(1, ng, 2):
                    dve.wait_ge(gathered.handle, gathered.at(i + 1))
                    dst, src = keep(i)
                    nc.vector.tensor_copy(dst, src).then_inc(kept[1].handle, 1)
                dve.wait_ge(picked.handle, picked.at(1))
                dve.wait_ge(gathered.handle, gathered.at(ng))
                for v, t, cap in sets:
                    last = nc.vector.tensor_tensor(v, v, aff[:, t, :].unsqueeze(2).to_broadcast([P, E, cap]), ALU.mult)
                last.then_inc(gated.handle, 1)
                for i, (s, j) in enumerate(scatters):
                    dve.wait_ge(spread.handle, spread.at(i + 1))
                    dst = sp_l[:, j, :] if s == "l" else sp_c[:, j, :]
                    nc.vector.tensor_copy(dst, bank[i % 4][:, 0:SEQ if s == "l" else CTX]).then_inc(spread_kept.handle, 1)
                n_links.append(link.n)
        st.used = [(s, n) if s is not chain else (chain, n_links[0]) for s, n in st.used]


EXPERTS_PER_TURN = 4
EXPERT_ORDER = []
for _r in range(EXPERTS_PER_TURN):
    EXPERT_ORDER += [(_r, "gate", 0), (_r, "up", 0)] + ([(_r - 1, "down", 1)] if _r else []) + [(_r, "gate", 1), (_r, "up", 1), (_r, "down", 0)]
EXPERT_ORDER.append((EXPERTS_PER_TURN - 1, "down", 1))


def expert_chunks(core, layer):
    def place(r, what, half):
        w = core.ins[f"moe_w_{what}_2"][layer]

        def of(first):
            def at(slot):
                a = w[bass.ds(first + r, 1)]
                if what == "down":
                    return [(slot[:].rearrange("p (k n) -> p k n", k=4),
                             a.rearrange("e (h k p) n -> h p (e k) n", p=P, h=2)[half])]
                return [(slot[:].rearrange("p (k n) -> p k n", k=KD),
                         a.rearrange("e (k p) n -> p (e k) n", p=P)[:, :, half * CW:(half + 1) * CW])]
            return at
        return of
    return [place(*c) for c in EXPERT_ORDER]


PIECES = 8
SPLIT_BUFS = 6
AMID = 5
POOL_PIECES = (2,)
DVE_PIECES = [q for q in range(PIECES) if q not in POOL_PIECES]


def experts_stage(core, layer, ctx, xe_l, xe_c, sp_l, sp_c, gate):
    nc = core.nc
    n0 = core.used
    E, H = EXPERTS_PER_TURN, N_EXP // EXPERTS_PER_TURN
    S = CAP_L + (CAP_C if ctx else 0)
    NC = len(EXPERT_ORDER)
    NP = NC * PIECES
    ND, NG = len(DVE_PIECES), len(POOL_PIECES)
    M = 24 if ctx else 16
    nb = 3 if ctx else 2
    x = core.x
    W = KD * CW // PIECES
    with Stage(core, "experts") as st:
        x_hi = st.sb("x_hi", [P, 2, KD, S], F32R)
        x_lo = st.sb("x_lo", [P, 2, KD, S], F32R)
        w_hi = st.sb("w_hi", [P, SPLIT_BUFS, W], F32R)
        w_lo = st.sb("w_lo", [P, SPLIT_BUFS, W], F32R)
        act_ = st.sb("act", [S, 2, CW])
        hid = st.sb("hid", [S, 2, CW])
        hid_hi = st.sb("hid_hi", [P, KD, S], F32R)
        hid_lo = st.sb("hid_lo", [P, KD, S], F32R)
        y_l = core.h[:].rearrange("p k n -> p (k n)")[:, N_EXP * KD * CAP_C:].rearrange("p (j d) -> p j d", j=2)
        y_c = st.sb("y_c", [P, D]) if ctx else None
        pg, pu, pt = st.ps("pg"), st.ps("pu"), st.ps("pt")
        py = st.ps("py", 2)
        psc = [st.ps(f"psc{i}") for i in range(nb)]
        per_stage = 2 if ctx else 1
        x_high = st.counter("ex_x_high", per_stage * E * H)
        x_high_seen = st.counter("ex_x_high_seen", per_stage * E * H)
        staged = st.counter("ex_staged", per_stage * E * H)
        c_used, c_silu, c_hid, c_turn, c_low, c_yl, c_sc, c_add = NP, 1, 2, 2, 1, 1, M, nb
        w_high = st.counter("ex_w_high", NP * H)
        w_low = st.counter("ex_w_low", len(DVE_PIECES) * NC * H)
        w_low_pool = st.counter("ex_w_low_pool", len(POOL_PIECES) * NC * H)
        w_used = st.counter("ex_w_used", NP * H + c_used)
        silu_done = st.counter("ex_silu_done", 2 * E * H + c_silu)
        hid_made = st.counter("ex_hid_made", 2 * E * H + c_hid)
        hid_turned = st.counter("ex_hid_turned", 2 * E * H + c_turn)
        hid_high = st.counter("ex_hid_high", 2 * E * H)
        hid_low = st.counter("ex_hid_low", 2 * E * H + c_low)
        yl_kept = st.counter("ex_yl_kept", E * H + c_yl)
        yc_kept = st.counter("ex_yc_kept", E * H + c_yl if ctx else c_yl)
        sc_done = st.counter("ex_sc_done", M * H + c_sc)
        sc_added = st.counter("ex_sc_added", M * H + c_add)
        place = expert_chunks(core, layer)

        def raw(j, q):
            return core.slot(n0 + j)[:, q * W:(q + 1) * W]

        def await_product(eng, it, r, what, half):
            j = EXPERT_ORDER.index((r % E, what, half)) - (NC if r < 0 else 0)
            eng.wait_ge(w_used.handle, it * NP + w_used.at(PIECES * (j + 1) + c_used))

        def in_order(it, piece, after):
            for j, c in enumerate(EXPERT_ORDER):
                for q in range(PIECES):
                    piece(it, j, q)
                    if q == AMID:
                        after(it, *c)

        with st.run() as block:
            @block.sync
            def _(sp):
                def split(it, j):
                    sp.wait_ge(w_low.handle, it * (ND * NC) + w_low.at(ND * (j + 1)))
                    sp.sem_inc(core.freed.handle, 1)

                def load(first, j):
                    core.issue(sp, n0 + j, place[j % NC](first + j // NC * E))

                with sp.Fori(0, H - 1) as it:
                    first = sp.snap(it * E)
                    for j in range(NC):
                        split(it, j)
                        load(first, j + NS)
                for j in range(NC):
                    split(H - 1, j)
                    if j + NS < NC:
                        load((H - 1) * E, j + NS)
                core.used = core.issued = n0 + NC * H
                core.stream(sp, core.used)

            @block.gpsimd
            def _(pool):
                def stage(it, r):
                    await_product(pool, it, r - 2, "up", 1)
                    for i, (part, c0, n) in enumerate(((xe_l, 0, CAP_L), (xe_c, CAP_L, CAP_C))[:per_stage]):
                        src = part[:, bass.ds(it * E + r, 1)].rearrange("p e k s -> p (e k) s")
                        nc.gpsimd.tensor_copy(x_hi[:, r % 2, :, c0:c0 + n], src).then_inc(x_high.handle, 1)
                        pool.wait_ge(x_high.handle, it * (E * per_stage) + x_high.at(r * per_stage + i + 1))
                        pool.sem_inc(x_high_seen.handle, 1)
                        nc.gpsimd.tensor_tensor(x_lo[:, r % 2, :, c0:c0 + n], src, x_hi[:, r % 2, :, c0:c0 + n], ALU.subtract).then_inc(staged.handle, 1)

                def low(it, j, q):
                    if q in POOL_PIECES:
                        b = (j * PIECES + q) % SPLIT_BUFS
                        pool.wait_ge(w_high.handle, it * NP + w_high.at(j * PIECES + q + 1))
                        nc.gpsimd.tensor_tensor(w_lo[:, b, :], raw(j, q), w_hi[:, b, :], ALU.subtract).then_inc(w_low_pool.handle, 1)

                def after(it, r, what, half):
                    if (what, half) == ("gate", 1) and r + 1 < E:
                        stage(it, r + 1)

                with pool.Fori(0, H) as it:
                    stage(it, 0)
                    in_order(it, low, after)

            @block.tensor
            def _(pe):
                def part(it, j, q):
                    if q in POOL_PIECES:
                        pe.wait_ge(w_low_pool.handle, it * (NG * NC) + w_low_pool.at(NG * j + POOL_PIECES.index(q) + 1))
                    else:
                        pe.wait_ge(w_low.handle, it * (ND * NC) + w_low.at(ND * j + DVE_PIECES.index(q) + 1))
                    b = (j * PIECES + q) % SPLIT_BUFS
                    return w_hi[:, b, :], w_lo[:, b, :]

                def product(out, hi, lo, w_h, w_l, start, stop):
                    nc.tensor.matmul(out, hi, w_h, start=start, stop=False)
                    nc.tensor.matmul(out, hi, w_l, start=False, stop=False)
                    return nc.tensor.matmul(out, lo, w_h, start=False, stop=stop)

                def into_hidden(it, r, what, c):
                    j = EXPERT_ORDER.index((r, what, c))
                    if what == "gate":
                        acc = pg
                        pe.wait_ge(silu_done.handle, it * (2 * E) + silu_done.at(2 * r + c + c_silu))
                    else:
                        acc = pu
                        pe.wait_ge(hid_made.handle, it * (2 * E) + hid_made.at(2 * r + c + c_hid))
                    for k in range(KD):
                        product(acc[0:S, :], x_hi[:, r % 2, k, :], x_lo[:, r % 2, k, :], *part(it, j, k), k == 0, k == KD - 1).then_inc(w_used.handle, 1)

                def turn(it, r, c):
                    s = 2 * r + c
                    pe.wait_ge(hid_made.handle, it * (2 * E) + hid_made.at(s + 1 + c_hid))
                    pe.wait_ge(hid_low.handle, it * (2 * E) + hid_low.at(s + c_low))
                    for f in range(4):
                        last = nc.tensor.matmul(pt[:, f * S:(f + 1) * S], hid[:, c, f * P:(f + 1) * P], core.ident[0:S, 0:S], start=True, stop=True)
                    last.then_inc(hid_turned.handle, 1)

                def down_of(it, r, c):
                    j = EXPERT_ORDER.index((r, "down", c))
                    pe.wait_ge(hid_low.handle, it * (2 * E) + hid_low.at(2 * r + c + 1 + c_low))
                    if c == 0:
                        pe.wait_ge(yl_kept.handle, it * E + yl_kept.at(r + c_yl))
                        if ctx:
                            pe.wait_ge(yc_kept.handle, it * E + yc_kept.at(r + c_yl))
                    for q in range(PIECES):
                        f, half = 4 * c + q // 2, q % 2
                        product(py[0:S, half * CW:(half + 1) * CW], hid_hi[:, f, :], hid_lo[:, f, :], *part(it, j, q), f == 0, f == KD - 1).then_inc(w_used.handle, 1)

                def scatter(it, m0, m1):
                    for m in range(m0, m1):
                        if m in (0, 8):
                            pe.wait_ge(yl_kept.handle, it * E + yl_kept.at(2 * (m // 8) + 2 + c_yl))
                        if m == 16:
                            pe.wait_ge(yc_kept.handle, it * E + yc_kept.at(E + c_yl))
                        pe.wait_ge(sc_added.handle, it * M + sc_added.at(m + 1))
                        d = m % 8
                        if m < 16:
                            rhs = sp_l[:, bass.ds(it * 2 + m // 8, 1), :].rearrange("p a n -> p (a n)")
                            last = nc.tensor.matmul(psc[m % nb][:], y_l[:, m // 8, d * P:(d + 1) * P], rhs, start=True, stop=True)
                        else:
                            rhs = sp_c[:, bass.ds(it, 1), :].rearrange("p a n -> p (a n)")
                            last = nc.tensor.matmul(psc[m % nb][:, 0:CTX], y_c[:, d * P:(d + 1) * P], rhs, start=True, stop=True)
                        last.then_inc(sc_done.handle, 1)

                pe.sem_inc(w_used.handle, c_used)
                pe.sem_inc(hid_turned.handle, c_turn)
                pe.sem_inc(sc_done.handle, c_sc)
                with pe.Fori(0, H) as it:
                    for r in range(E):
                        pe.wait_ge(staged.handle, it * (E * per_stage) + staged.at((r + 1) * per_stage))
                        into_hidden(it, r, "gate", 0)
                        if r == 3:
                            scatter(it, 6, 8)
                        into_hidden(it, r, "up", 0)
                        if r:
                            down_of(it, r - 1, 1)
                        into_hidden(it, r, "gate", 1)
                        if r == 2:
                            scatter(it, 0, 2)
                        turn(it, r, 0)
                        into_hidden(it, r, "up", 1)
                        if r == 2:
                            scatter(it, 2, 4)
                        down_of(it, r, 0)
                        if r == 2:
                            scatter(it, 4, 6)
                        turn(it, r, 1)
                    down_of(it, E - 1, 1)
                    scatter(it, 8, M)

            @block.scalar
            def _(act):
                def high(it, j, q):
                    i = j * PIECES + q
                    if q == 0:
                        core.await_chunk(act, n0 + j, it, NC)
                    act.wait_ge(w_used.handle, it * NP + w_used.at(i + 1 - SPLIT_BUFS + c_used))
                    nc.scalar.copy(w_hi[:, i % SPLIT_BUFS, :], raw(j, q)).then_inc(w_high.handle, 1)

                def silu(it, r, c):
                    s = 2 * r + c
                    await_product(act, it, r, "gate", c)
                    act.wait_ge(hid_made.handle, it * (2 * E) + hid_made.at(s + 1))
                    nc.scalar.activation(act_[:, c, :], pg[0:S, :], ACT.Silu).then_inc(silu_done.handle, 1)

                def turned(it, r, c):
                    act.wait_ge(hid_turned.handle, it * (2 * E) + hid_turned.at(2 * r + c + 1 + c_turn))
                    await_product(act, it, r - 1, "down", c)
                    nc.scalar.copy(hid_hi[:, 4 * c:4 * c + 4, :], pt[:, 0:4 * S].rearrange("p (f s) -> p f s", f=4)).then_inc(hid_high.handle, 1)

                def keep(it, r):
                    await_product(act, it, r, "down", 1)
                    act.wait_ge(sc_done.handle, it * M + sc_done.at(8 * (r // 2) + 8))
                    o = (r % 2) * CAP_L
                    nc.scalar.copy(y_l[o:o + CAP_L, r // 2, :], py[0:CAP_L, :]).then_inc(yl_kept.handle, 1)

                def after(it, r, what, half):
                    if (what, half) == ("up", 0):
                        silu(it, r, 0)
                    elif (what, half) == ("gate", 0) and r:
                        turned(it, r - 1, 1)
                    elif (what, half) == ("gate", 1) and r:
                        keep(it, r - 1)
                    elif (what, half) == ("up", 1):
                        silu(it, r, 1)
                        turned(it, r, 0)
                    elif (what, half) == ("down", 1) and r == E - 1:
                        turned(it, r, 1)

                act.sem_inc(silu_done.handle, c_silu)
                act.sem_inc(yl_kept.handle, c_yl)
                with act.Fori(0, H) as it:
                    in_order(it, high, after)
                    keep(it, E - 1)

            @block.vector
            def _(dve):
                def low(it, j, q):
                    if q in DVE_PIECES:
                        b = (j * PIECES + q) % SPLIT_BUFS
                        dve.wait_ge(w_high.handle, it * NP + w_high.at(j * PIECES + q + 1))
                        if q == PIECES - 1:
                            dve.wait_ge(w_low_pool.handle, it * (NG * NC) + w_low_pool.at(NG * (j + 1)))
                        nc.vector.tensor_tensor(w_lo[:, b, :], raw(j, q), w_hi[:, b, :], ALU.subtract).then_inc(w_low.handle, 1)

                def product(it, r, c):
                    s = 2 * r + c
                    await_product(dve, it, r, "up", c)
                    dve.wait_ge(silu_done.handle, it * (2 * E) + silu_done.at(s + 1 + c_silu))
                    dve.wait_ge(hid_turned.handle, it * (2 * E) + hid_turned.at(s + 1))
                    nc.vector.tensor_tensor(hid[:, c, :], act_[:, c, :], pu[0:S, :], ALU.mult).then_inc(hid_made.handle, 1)

                def turned(it, r, c):
                    dve.wait_ge(hid_high.handle, it * (2 * E) + hid_high.at(2 * r + c + 1))
                    at = slice(4 * c, 4 * c + 4)
                    nc.vector.tensor_tensor(hid_lo[:, at, :], pt[:, 0:4 * S].rearrange("p (f s) -> p f s", f=4), hid_hi[:, at, :], ALU.subtract).then_inc(hid_low.handle, 1)

                def keep(it, r):
                    if ctx:
                        await_product(dve, it, r, "down", 1)
                        dve.wait_ge(sc_done.handle, it * M + sc_done.at(M))
                        dve.wait_ge(yl_kept.handle, it * E + yl_kept.at(r + 1 + c_yl))
                        nc.vector.tensor_copy(y_c[r * CAP_C:(r + 1) * CAP_C, :], py[CAP_L:S, :]).then_inc(yc_kept.handle, 1)

                def add(it, m0, m1):
                    for m in range(m0, m1):
                        dve.wait_ge(sc_done.handle, it * M + sc_done.at(m + 1 + c_sc))
                        dve.wait_ge(sc_added.handle, it * M + sc_added.at(m + c_add))
                        d = m % 8
                        c0, n, s = (0, SEQ, 0) if m < 16 else (SEQ, CTX, 1)
                        nc.vector.scalar_tensor_tensor(out=x[:, d, c0:c0 + n], in0=psc[m % nb][:, 0:n], scalar=gate[s][:, d:d + 1], in1=x[:, d, c0:c0 + n],
                                                       op0=ALU.mult, op1=ALU.add).then_inc(sc_added.handle, 1)

                def after(it, r, what, half):
                    if (what, half) == ("gate", 0) and r:
                        turned(it, r - 1, 1)
                        if r == 3:
                            add(it, 4, 6)
                    elif (what, half) == ("up", 0) and r == 3:
                        add(it, 6, 8)
                    elif (what, half) == ("down", 1) and r < E - 1:
                        product(it, r + 1, 0)
                    elif (what, half) == ("gate", 1):
                        if r:
                            keep(it, r - 1)
                        else:
                            product(it, 0, 0)
                    elif (what, half) == ("up", 1):
                        turned(it, r, 0)
                        if r == 2:
                            add(it, 0, 2)
                    elif (what, half) == ("down", 0):
                        product(it, r, 1)
                        if r == 2:
                            add(it, 2, 4)
                    elif (what, half) == ("down", 1) and r == E - 1:
                        turned(it, r, 1)

                dve.sem_inc(hid_made.handle, c_hid)
                dve.sem_inc(hid_low.handle, c_low)
                dve.sem_inc(yc_kept.handle, c_yl)
                dve.sem_inc(sc_added.handle, c_add)
                with dve.Fori(0, H) as it:
                    in_order(it, low, after)
                    keep(it, E - 1)
                    add(it, 8, M)


def moe(core, layer, ctx, gate):
    with Stage(core, "moe") as st:
        xe_l = st.sb("xe_l", [P, N_EXP, KD, CAP_L])
        sp_l = st.sb("sp_l", [P, N_EXP // 2, SEQ])
        sp_c = st.sb("sp_c", [P, N_EXP // 4, CTX]) if ctx else None
        spare = core.h[:].rearrange("p k n -> p (k n)")[:, 0:N_EXP * KD * CAP_C]
        xe_c = spare.rearrange("p (e k s) -> p e k s", e=N_EXP, k=KD) if ctx else None
        route_stage(core, layer, ctx, xe_l, xe_c, sp_l, sp_c)
        experts_stage(core, layer, ctx, xe_l, xe_c, sp_l, sp_c, gate)


def axial_rope_stage(core, cols):
    nc = core.nc
    H = 20
    with Stage(core, "axial") as st:
        rope = st.sb("rope", [P, 2, LT, 32])
        tmp = [st.sb(f"tmp{i}", [P, H, 32]) for i in range(4)]
        loaded = st.counter("axial_loaded", 32)
        chain = st.counter("axial_chain", 2 * LT)
        with st.run() as block:
            @block.sync
            def _(sp):
                sp.dma_start(rope[:, 0], core.consts["axial_cos"]).then_inc(loaded.handle, 16)
                sp.dma_start(rope[:, 1], core.consts["axial_sin"]).then_inc(loaded.handle, 16)

            @block.vector
            def _(dve):
                link = Link(dve, chain)
                dve.wait_ge(loaded.handle, loaded.at(32))
                for t in range(LT):
                    v = cols[:, t, 0:H * HD].rearrange("p (h w) -> p h w", w=HD)
                    x1, x2 = v[:, :, 0:32], v[:, :, 32:HD]
                    cos, sin = (rope[:, j, t, :].unsqueeze(1).to_broadcast([P, H, 32]) for j in range(2))
                    nc.vector.tensor_tensor(tmp[0][:], x1, cos, ALU.mult)
                    nc.vector.tensor_tensor(tmp[1][:], x2, sin, ALU.mult)
                    nc.vector.tensor_tensor(tmp[2][:], x2, cos, ALU.mult)
                    link(nc.vector.tensor_tensor(tmp[3][:], x1, sin, ALU.mult))
                    nc.vector.tensor_tensor(x1, tmp[0][:], tmp[1][:], ALU.subtract)
                    link(nc.vector.tensor_tensor(x2, tmp[2][:], tmp[3][:], ALU.add))


def attention_layer(core, gate):
    nc, ins = core.nc, core.ins
    KV, REP, W = 4, 4, 1536
    with Stage(core, "swa2") as st:
        cols = st.sb("cols", [P, LT + CT, W])
        lat, both = list(range(LT)), list(range(LT + CT))
        project_stage(core, "w_in2", [lat, lat, both], [CW] * 3, lambda t, c: cols[:, t, c * CW:(c + 1) * CW])
        o = st.sb("o", [P, LT, D])
        axial_rope_stage(core, cols)
        qT = st.sb("qT", [MLA_DIM, KV * REP, SEQ])
        kT = core.h[0:MLA_DIM].rearrange("p k n -> p (k n)")[:, 0:KV * TOK].rearrange("p (h n) -> p h n", h=KV)
        band = st.sb("band", [P, 3 * P])
        sink = st.sb("sink", [P, KV * REP])
        jobs = [(lambda t, c=hd * HD: cols[:, t, c:c + HD], LT, HD, [qT[0:HD, hd, :]], None, HD ** -0.5) for hd in range(KV * REP)]
        order = [LT, LT + 1, 0, 1, 2, 3]
        jobs += [(lambda t, c=D + hd * HD: cols[:, order[t], c:c + HD], 6, HD, [kT[0:HD, hd, :]], None, 1.0) for hd in range(KV)]

        def extra(sp, loaded):
            if sp is not None:
                sp.dma_start(band[:], core.consts["band"]).then_inc(loaded.handle, 16)
                sp.dma_start(sink[:], ins["sw_sink_2"].partition_broadcast(P)).then_inc(loaded.handle, 16)
            return 2

        turn_heads_stage(core, "turn2", jobs, zero=[qT[HD:MLA_DIM], kT[HD:MLA_DIM]], extra=extra)

        def keys(i):
            lo, hi = max(0, i - 1), min(LT, i + 2)
            return [(0, CTX, None), (CTX + lo * P, (hi - lo) * P, ((lo - i + 1) * P, (hi - i + 1) * P))]

        attention_stage(
            core, "att2", KV, REP, MLA_DIM, LT, keys, qT,
            lambda it, r, k0, n: kT[:, bass.ds(it, 1), k0:k0 + n].rearrange("p a n -> p (a n)"),
            lambda it, r, kt: cols[:, order[kt], bass.ds(it * HD + D + KV * HD, HD)],
            lambda it, r, a, b: band[:, a:b],
            lambda it, r, i: o[:, i, bass.ds(it * (REP * HD) + r * HD, HD)],
            lambda it, r: sink[:, bass.ds(it * REP + r, 1)])
        turn_heads_stage(core, "turn3", [(lambda t, k=k: o[:, t, k * P:(k + 1) * P], LT, P, [core.h[:, k, 0:SEQ]], None, 1.0) for k in range(KD)])
    residual_stage(core, "w_out2", gate)


def store_stage(core, out):
    with Stage(core, "final") as st:
        tok = st.sb("tok", [P, LT, D])
        turn_tokens_stage(core, "last", core.h, tok, range(LT))
        stored = st.counter("stored", 16)
        with st.run() as block:
            @block.sync
            def _(sp):
                sp.dma_start(out[0].rearrange("(t p) d -> p t d", p=P), tok[:]).then_inc(stored.handle, 16)
                sp.wait_ge(stored.handle, stored.at(16))


def second_block(core, out, debug):
    def mod(layer, i, s):
        at = layer * 48 + i * KD
        return core.mod[:, at:at + KD, s]

    def streams(layer, gain, i, both):
        g = lambda: core.col(gain, layer * KD, KD)
        lat = [(0, SEQ, g(), mod(layer, i + 1, 0), mod(layer, i, 0))]
        return lat + ([(SEQ, CTX, g(), mod(layer, i + 1, 1), mod(layer, i, 1))] if both else [])

    norm_stage(core, "norm_h", streams(0, "norm1_w_2", 0, True))
    hyena_stage(core, [mod(0, 2, 0), mod(0, 2, 1)])
    if debug: debug(core, 'hyena')
    norm_stage(core, "norm_e", streams(0, "norm2_w_2", 3, True))
    moe(core, 0, True, [mod(0, 5, 0), mod(0, 5, 1)])
    if debug: debug(core, 'moe0')
    norm_stage(core, "norm_s", streams(1, "norm1_w_2", 0, True))
    attention_layer(core, mod(1, 2, 0))
    if debug: debug(core, 'swa')
    norm_stage(core, "norm_f", streams(1, "norm2_w_2", 3, False))
    moe(core, 1, False, [mod(1, 5, 0)])
    if debug: debug(core, 'moe1')
    norm_stage(core, "norm_l", [(0, SEQ, core.col("final_norm_w_2"), None, None)])
    store_stage(core, out)


def build(nc, ins, consts, out, debug=None):
    with ExitStack() as ctx:
        core = Core(nc, ins, consts, ctx)
        chunks = []
        for layer in range(2):
            chunks += [column_chunk(ins["ada_w_2"][layer], c * CW, CW) for c in range(12)]
        chunks += [column_chunk(ins["w_in"][0], c * CW, min(CW, IN_COLS - c * CW)) for c in range(5)]
        chunks += [column_chunk(ins["w_o"][0], c * CW, CW) for c in range(2)]
        chunks += [column_chunk(ins["w_up"][0], c * CW, CW) for c in range(FF // CW)]
        chunks += [row_chunk(ins["w_down"][0], c * CW) for c in range(FF // CW)]
        chunks += [place(q) for q in range(TURNS) for place in hyena_chunks(core)]
        experts = lambda layer: [place(first) for first in range(0, N_EXP, EXPERTS_PER_TURN) for place in expert_chunks(core, layer)]
        chunks += experts(0)
        chunks += [column_chunk(ins["sw_w_in_2"], c * CW, CW) for c in range(3)]
        chunks += [column_chunk(ins["sw_w_out_2"], c * CW, CW) for c in range(2)]
        chunks += experts(1)
        core.set_chunks(chunks)
        load_stage(core)
        modulation_stage(core)
        if debug: debug(core, 'load')
        first_block(core)
        if debug: debug(core, 'first')
        second_block(core, out, debug)


def constants():
    f = np.float32
    c = {"ident": np.eye(P, dtype=f)}
    inv = f(1.0) / (f(10000.0) ** (np.arange(0, 32, 2, dtype=f) / f(32)))
    ang = np.arange(SEQ, dtype=f)[:, None] * inv[None, :]
    tile = lambda a: np.ascontiguousarray(a.reshape(-1, P, a.shape[-1]).transpose(1, 0, 2))
    c["rope_cos"], c["rope_sin"] = tile(np.cos(ang)), tile(np.sin(ang))
    dist = np.arange(P)[:, None] + (SEQ - P) - np.arange(SEQ)[None, :]
    idx = np.arange(1, 3 * HEADS + 1, dtype=f).reshape(HEADS, 3)
    slopes = np.exp2(f(-8.0) * idx / f(3 * HEADS)).astype(f)
    causal = dist >= 0
    count = (dist <= 128).astype(f) + (dist % 4 == 0) + (dist % 16 == 0)
    bias = np.full((4, P, HEADS, SEQ), NEG, f)
    for h in range(HEADS):
        for g, (valid, col) in enumerate(((causal, 0), (causal, None), (causal & (count > 0), 1), (causal & (dist < 128), 2))):
            b = np.zeros_like(dist, dtype=f) if col is None else -slopes[h, col] * dist.astype(f)
            if g == 2:
                b = b + np.log(np.maximum(count, 1))
            bias[g, :, h, :] = np.where(valid, b, NEG)
    c["bias"] = bias
    deltas = np.abs(np.linspace(np.log(1e-2) / 1.5, np.log(1e-2) / 0.3, D, dtype=f))
    z_all, win_all = [], []
    for name, L in (("l", SEQ), ("c", CTX)):
        order = np.concatenate([np.arange(0, L, 2), np.arange(1, L, 2)])
        t = np.linspace(0.0, 1.0, L, dtype=f)[:, None]
        w = f(2.0 * np.pi) * np.arange(L, dtype=f)[:, None] / f(L)
        bands = np.linspace(1e-4, 15, 16, dtype=f)[None, :]
        z = np.concatenate([t, np.cos(bands * w), -np.sin(bands * w)], axis=-1).astype(f)
        z_all.append(z[order].T)
        window = np.exp(-t * deltas) + f(0.05)
        both = np.stack([window, window], axis=1)
        both[0, 1, :] = 0.0
        win_all.append(both[order].reshape(-1, P, 2, D).transpose(1, 0, 2, 3))
        half = L // 2
        freq = np.arange(half) + 0.5
        pos = [np.arange(0, L, 2), np.arange(1, L, 2)]
        fwd = [fn(np.pi * pos[par][:, None] * freq[None, :] / L) for fn in (np.cos, np.sin) for par in (0, 1)]
        inv = [m.T / L for m in fwd]
        pack = lambda ms: np.ascontiguousarray(np.stack([m.reshape(-1, P, half).transpose(1, 0, 2) for m in ms], axis=1)).astype(f)
        c["dft_" + name], c["idft_" + name] = pack(fwd), pack(inv)
    c["filter_z"] = np.ascontiguousarray(np.concatenate(z_all, axis=1)).astype(f)
    c["window"] = np.ascontiguousarray(np.concatenate(win_all, axis=1)).astype(f)
    row = np.repeat(np.arange(SEQ // 64, dtype=f), 64)
    col = np.tile(np.arange(64, dtype=f), SEQ // 64)
    inv = f(10000.0) ** (-np.arange(16, dtype=f) / f(16))
    ang = np.concatenate([row[:, None] * inv, col[:, None] * inv], axis=-1)
    c["axial_cos"], c["axial_sin"] = tile(np.cos(ang)), tile(np.sin(ang))
    gap = np.arange(P)[:, None] + P - np.arange(3 * P)[None, :]
    c["band"] = np.where(np.abs(gap) <= 128, f(0), f(NEG)).astype(f)
    c["slot_number"] = np.broadcast_to(np.arange(1, CAP_L + 1, dtype=f), (P, CAP_L)).copy()
    return c


_UNUSED = ("gd_", "hg_")


def kernel(**inputs):
    import concourse.bacc as bacc
    from concourse.bass_utils import run_bass_kernel_spmd

    nc = bacc.Bacc("TRN2", target_bir_lowering=False, num_devices=1)
    arrays, ins, consts = {}, {}, {}

    def place(name, a):
        a = np.ascontiguousarray(a)
        arrays[name] = a
        return nc.dram_tensor(name, a.shape, mybir.dt.from_np(a.dtype), kind="ExternalInput").ap()

    for name, a in inputs.items():
        if not name.startswith(_UNUSED):
            ins[name] = place("in_" + name, a)
    for name, a in constants().items():
        consts[name] = place("table_" + name, a)
    out = nc.dram_tensor("out", (1, SEQ, D), F32, kind="ExternalOutput").ap()
    build(nc, ins, consts, out)
    r = run_bass_kernel_spmd(nc, [arrays], core_ids=[0])
    return r.results[0]["out"]
```

```python
from contextlib import ExitStack

import numpy as np

import concourse.bass as bass
from concourse import mybir

ALU = mybir.AluOpType
ACT = mybir.ActivationFunctionType
F32 = mybir.dt.float32
F32R = mybir.dt.float32r
AX_X = mybir.AxisListType.X

P = 128
D = 1024
KD = D // P
SEQ = 512
CTX = 256
TOK = SEQ + CTX
LT, CT = SEQ // P, CTX // P
FF = 4096
EPS = 1e-6
NEG = -1e30
HD = 64
IN_COLS = 2464
HEADS = 4
MLA_DIM = 96
N_EXP = 16
CAP_L, CAP_C = 2 * SEQ // N_EXP, 2 * CTX // N_EXP
NS = 3
CW = 512
TWO_PI = 2.0 * np.pi
TWO_PI_HI = float(np.float32(TWO_PI))
TWO_PI_LO = float(TWO_PI - np.float64(np.float32(TWO_PI)))
ROUND_MAGIC = float(1.5 * 2 ** 23)
SIN_MAX = 3.1415925

A_Q, A_K, A_V, B_QL, B_KVL, B_KR, C_Q, C_K, C_V, D_Q, D_K, D_V = (
    0, 256, 512, 768, 1024, 1152, 1184, 1440, 1696, 1952, 2208, 2336)

VEC_ROWS = [
    [("ada_b_2", 96), ("c_2", 8), ("c_ctx_2", 8), ("attn_norm_g", 8), ("group_out_g", 8)],
    [("hy_b_in_2", 24), ("hy_short_w_2", 72), ("hy_short_b_2", 24), ("hy_b_out_2", 8)],
    [("norm1_w_2", 16), ("norm2_w_2", 16), ("final_norm_w_2", 8), ("mlp_norm_g", 8),
     ("hy_filter_bias_2", 16), ("mla_qlat_g", 2), ("mla_kvlat_g", 1)],
]
VEC_AT = {}
for _t, _rows in enumerate(VEC_ROWS):
    _r = 0
    for _name, _n in _rows:
        VEC_AT[_name] = (_t * P + _r, _n)
        _r += _n


class Counter:

    def __init__(self, handle):
        self.handle = handle
        self.base = 0

    def at(self, n):
        return n + self.base


class Link:

    def __init__(self, eng, signal, start=0):
        self.eng, self.counter, self.start, self.n = eng, signal, start, 0

    def __call__(self, ins):
        self.n += 1
        ins.then_inc(self.counter.handle, 1)
        self.eng.wait_ge(self.counter.handle, self.counter.at(self.start + self.n))


class Stage:

    def __init__(self, core, name):
        core.stages += 1
        self.core, self.name = core, f"{name}{core.stages}"
        self.mem = ExitStack()
        self.used = []

    def sb(self, name, shape, dt=F32):
        return self.mem.enter_context(self.core.nc.sbuf_tensor(f"{self.name}_{name}", shape, dt))

    def ps(self, name, banks=1):
        return self.mem.enter_context(self.core.nc.psum_tensor(f"{self.name}_{name}", [P, banks * 512], F32))

    def counter(self, name, total):
        s = self.core.counter(name)
        self.used.append((s, total))
        return s

    def __enter__(self):
        return self

    def run(self):
        return self.core.nc.Block()

    def __exit__(self, *e):
        self.mem.__exit__(*e)
        for s, total in self.used:
            s.base += total


class Core:

    def __init__(self, nc, ins, consts, ctx):
        self.nc, self.ins, self.consts, self.ctx = nc, ins, consts, ctx
        self.counters = {}
        self.stages = 0
        sb = lambda n, s: ctx.enter_context(nc.sbuf_tensor(n, s, F32))
        self.x = sb("residual", [P, KD, TOK])
        self.h = sb("normed", [P, KD, TOK])
        self.ring = [sb(f"ring{i}", [P, KD * CW]) for i in range(NS)]
        self.ident = sb("ident", [P, P])
        self.ones = sb("ones", [P, P])
        self.vec = sb("vec", [P, 3 * P])
        self.mod = sb("mod", [P, 96, 2])
        self.loaded = [self.counter(f"ring_loaded{i}") for i in range(NS)]
        self.freed = self.counter("ring_freed")
        self.chunks = []
        self.issued = 0
        self.reserved = 0
        self.used = 0

    def counter(self, name):
        if name not in self.counters:
            self.counters[name] = Counter(self.ctx.enter_context(self.nc.semaphore(name)))
        return self.counters[name]

    def col(self, name, i=0, n=None):
        at, size = VEC_AT[name]
        return self.vec[:, at + i:at + i + (size - i if n is None else n)]

    def slot(self, n):
        return self.ring[n % NS]

    def set_chunks(self, chunks):
        self.chunks = chunks
        self.arrival, so_far = [], [0] * NS
        for n, place in enumerate(chunks):
            so_far[n % NS] += 16 * len(place(self.slot(n)))
            self.arrival.append(so_far[n % NS])

    def issue(self, sp, n, place):
        for dst, src in place(self.slot(n)):
            sp.dma_start(dst, src).then_inc(self.loaded[n % NS].handle, 16)

    def load_chunk(self, sp, n):
        if n >= NS:
            sp.wait_ge(self.freed.handle, n - NS + 1)
        self.issue(sp, n, self.chunks[n])

    def stream(self, sp, used):
        while self.issued < min(used + NS - self.reserved, len(self.chunks)):
            self.load_chunk(sp, self.issued)
            self.issued += 1

    def await_chunk(self, eng, n, it=0, per=0):
        if per:
            each = self.arrival[n + per] - self.arrival[n]
            eng.wait_ge(self.loaded[n % NS].handle, it * each + self.arrival[n])
            return
        eng.wait_ge(self.loaded[n % NS].handle, self.arrival[n])


def column_chunk(w, c0, width):
    def place(slot):
        return [(slot[:, 0:KD * width].rearrange("p (k n) -> p k n", k=KD),
                 w[:, c0:c0 + width].rearrange("(k p) n -> p k n", p=P))]
    return place


def row_chunk(w, r0, tiles=4):
    def place(slot):
        return [(slot[:, 0:tiles * D].rearrange("p (k n) -> p k n", k=tiles),
                 w[r0:r0 + tiles * P, :].rearrange("(k p) n -> p k n", p=P))]
    return place


def by_k(slot, width=CW, k=KD):
    return slot[:, 0:k * width].rearrange("p (k n) -> p k n", k=k)


def tokens_in(core):
    return core.h[:].rearrange("p k n -> p (k n)").rearrange("p (t d) -> p t d", d=D)


def load_stage(core):
    nc, ins = core.nc, core.ins
    with Stage(core, "load") as st:
        rows = st.sb("rows", [P, 3, P])
        tok = tokens_in(core)
        pv = st.ps("pv")
        rows_loaded = st.counter("rows_loaded", 16 * sum(len(r) for r in VEC_ROWS))
        x_loaded = st.counter("x_loaded", 32)
        id_loaded = st.counter("id_loaded", 16)
        vec_turned = st.counter("vec_turned", 1)
        with st.run() as block:
            @block.sync
            def _(sp):
                sp.dma_start(core.ident[:], core.consts["ident"]).then_inc(id_loaded.handle, 16)
                sp.wait_ge(rows_loaded.handle, rows_loaded.at(16 * sum(len(r) for r in VEC_ROWS)))
                sp.dma_start(tok[:, 0:LT], ins["x"][0].rearrange("(t p) d -> p t d", p=P)).then_inc(x_loaded.handle, 16)
                sp.dma_start(tok[:, LT:LT + CT], ins["ctx_2"][0].rearrange("(t p) d -> p t d", p=P)).then_inc(x_loaded.handle, 16)
                core.stream(sp, core.used)

            @block.gpsimd
            def _(pool):
                nc.gpsimd.memset(core.ones[:], 1.0 / D)

            @block.scalar
            def _(act):
                for t, group in enumerate(VEC_ROWS):
                    r = 0
                    for name, n in group:
                        a = ins[name]
                        while len(a.shape) > 1:
                            a = a.rearrange("a b ... -> (a b) ...") if len(a.shape) > 2 else a.rearrange("a b -> (a b)")
                        act.dma_start(rows[r:r + n, t, :], a.rearrange("(r c) -> r c", c=P)).then_inc(rows_loaded.handle, 16)
                        r += n

            @block.tensor
            def _(pe):
                pe.wait_ge(id_loaded.handle, id_loaded.at(16))
                pe.wait_ge(rows_loaded.handle, rows_loaded.at(16 * sum(len(r) for r in VEC_ROWS)))
                for t, group in enumerate(VEC_ROWS):
                    n = sum(c for _, c in group)
                    last = nc.tensor.transpose(pv[:, t * P:t * P + n], rows[0:n, t, :], core.ident[0:n, 0:n])
                last.then_inc(vec_turned.handle, 1)

            @block.vector
            def _(dve):
                dve.wait_ge(vec_turned.handle, vec_turned.at(1))
                n = 2 * P + sum(c for _, c in VEC_ROWS[2])
                nc.vector.tensor_copy(core.vec[:, 0:n], pv[:, 0:n])


def modulation_stage(core):
    nc = core.nc
    n0 = core.used
    per = 12
    turns = 24 // per
    pieces = KD * per
    B = 6
    amid = 4
    with Stage(core, "mod") as st:
        cs = st.sb("cs", [P, KD, 2])
        c_parts = st.sb("c_parts", [P, KD, 4], F32R)
        fold = st.sb("fold", [4, 2])
        w_hi = st.sb("w_hi", [P, B, CW], F32R)
        w_lo = st.sb("w_lo", [P, B, CW], F32R)
        row = st.sb("row", [4, 2, CW])
        pr = [st.ps(f"pr{i}") for i in range(2)]
        pt = [st.ps(f"pt{i}") for i in range(2)]
        px = [st.ps(f"px{i}") for i in range(2)]
        pc = [st.ps(f"pc{i}") for i in range(2)]
        tok = tokens_in(core)
        x_loaded = st.counter("x_loaded", 0)
        lat_turned = st.counter("lat_turned", KD)
        ctx_turned = st.counter("ctx_turned", KD)
        lat_kept = st.counter("lat_kept", KD)
        ctx_kept = st.counter("ctx_kept", KD)
        silu_done = st.counter("silu_done", 2)
        c_high = st.counter("c_high", 1)
        c_split = st.counter("c_split", 1)
        fold_made = st.counter("fold_made", 1)
        w_high = st.counter("prod_w_high", pieces * turns)
        w_low = st.counter("prod_w_low", pieces * turns)
        w_used = st.counter("prod_w_used", pieces * turns + B)
        row_kept = st.counter("row_kept", 24)
        row_turned = st.counter("row_turned", 24 + 2)
        col_kept = st.counter("col_kept", 24 + 2)
        with st.run() as block:
            @block.sync
            def _(sp):
                core.used = n0 + 24
                core.stream(sp, core.used)

            @block.scalar
            def _(act):
                def high(it, r, k):
                    n = KD * r + k
                    if k == 0:
                        core.await_chunk(act, n0 + r, it, per)
                    act.wait_ge(w_used.handle, it * pieces + w_used.at(n + 1))
                    nc.scalar.copy(w_hi[:, n % B, :], by_k(core.slot(n0 + r))[:, k, :]).then_inc(w_high.handle, 1)

                def take_out(it, r):
                    act.wait_ge(w_used.handle, it * pieces + w_used.at(KD * (r + 1) + B))
                    act.wait_ge(row_turned.handle, it * per + row_turned.at(r + 1))
                    nc.scalar.copy(row[:, r % 2, :], pr[r % 2][0:4, 0:CW]).then_inc(row_kept.handle, 1)

                nc.scalar.activation(cs[:, :, 0], core.col("c_2"), ACT.Silu).then_inc(silu_done.handle, 1)
                nc.scalar.activation(cs[:, :, 1], core.col("c_ctx_2"), ACT.Silu).then_inc(silu_done.handle, 1)
                act.wait_ge(silu_done.handle, silu_done.at(2))
                nc.scalar.copy(c_parts[:, :, 0:2], cs[:]).then_inc(c_high.handle, 1)
                for k in range(KD):
                    act.wait_ge(ctx_turned.handle, ctx_turned.at(k + 1))
                    nc.scalar.copy(core.x[:, k, SEQ:TOK], pc[k % 2][:, 0:CTX]).then_inc(ctx_kept.handle, 1)
                with act.Fori(0, turns) as it:
                    for r in range(per):
                        for k in range(KD):
                            high(it, r, k)
                            if r and k == amid:
                                take_out(it, r - 1)
                    take_out(it, per - 1)

            @block.tensor
            def _(pe):
                def turn(it, r):
                    pe.wait_ge(row_kept.handle, it * per + row_kept.at(r + 1))
                    pe.wait_ge(col_kept.handle, it * per + col_kept.at(r + 1))
                    for j in range(4):
                        last = nc.tensor.matmul(pt[r % 2][:, 2 * j:2 * j + 2], row[:, r % 2, j * P:(j + 1) * P], fold[:], start=True, stop=True)
                    last.then_inc(row_turned.handle, 1)

                pe.wait_ge(x_loaded.handle, x_loaded.at(0))
                for k in range(KD):
                    if k >= 2:
                        pe.wait_ge(lat_kept.handle, lat_kept.at(k - 1))
                        pe.wait_ge(ctx_kept.handle, ctx_kept.at(k - 1))
                    for t in range(LT):
                        last = nc.tensor.transpose(px[k % 2][:, t * P:(t + 1) * P], tok[:, t, k * P:(k + 1) * P], core.ident[:])
                    last.then_inc(lat_turned.handle, 1)
                    for t in range(CT):
                        last = nc.tensor.transpose(pc[k % 2][:, t * P:(t + 1) * P], tok[:, LT + t, k * P:(k + 1) * P], core.ident[:])
                    last.then_inc(ctx_turned.handle, 1)
                pe.sem_inc(w_used.handle, B)
                pe.sem_inc(row_turned.handle, 2)
                pe.wait_ge(c_split.handle, c_split.at(1))
                pe.wait_ge(fold_made.handle, fold_made.at(1))
                with pe.Fori(0, turns) as it:
                    for r in range(per):
                        for k in range(KD):
                            n = KD * r + k
                            pe.wait_ge(w_low.handle, it * pieces + w_low.at(n + 1))
                            nc.tensor.matmul(pr[r % 2][0:4, 0:CW], c_parts[:, k, :], w_hi[:, n % B, :], start=(k == 0), stop=False)
                            nc.tensor.matmul(pr[r % 2][0:4, 0:CW], c_parts[:, k, :], w_lo[:, n % B, :], start=False, stop=(k == KD - 1)).then_inc(w_used.handle, 1)
                        if r:
                            turn(it, r - 1)
                    turn(it, per - 1)

            @block.vector
            def _(dve):
                def low(it, r, k):
                    n = KD * r + k
                    dve.wait_ge(w_high.handle, it * pieces + w_high.at(n + 1))
                    nc.vector.tensor_tensor(w_lo[:, n % B, :], by_k(core.slot(n0 + r))[:, k, :], w_hi[:, n % B, :], ALU.subtract).then_inc(w_low.handle, 1)

                def take_out(it, r):
                    dve.wait_ge(row_turned.handle, it * per + row_turned.at(r + 1 + 2))
                    nc.vector.tensor_copy(core.mod[:, bass.ds(it * (per * 4) + r * 4, 4), :],
                                          pt[r % 2][:, 0:8].rearrange("p (j s) -> p j s", s=2)).then_inc(col_kept.handle, 1)

                dve.sem_inc(col_kept.handle, 2)
                nc.vector.tensor_tensor(fold[:], core.ident[0:4, 0:2], core.ident[0:4, 2:4], ALU.add).then_inc(fold_made.handle, 1)
                dve.wait_ge(c_high.handle, c_high.at(1))
                nc.vector.tensor_tensor(c_parts[:, :, 2:4], cs[:], c_parts[:, :, 0:2], ALU.subtract).then_inc(c_split.handle, 1)
                for k in range(KD):
                    dve.wait_ge(lat_turned.handle, lat_turned.at(k + 1))
                    nc.vector.tensor_copy(core.x[:, k, 0:SEQ], px[k % 2][:]).then_inc(lat_kept.handle, 1)
                with dve.Fori(0, turns) as it:
                    for r in range(per):
                        for k in range(KD):
                            low(it, r, k)
                            if r >= 2 and k == amid:
                                take_out(it, r - 2)
                    take_out(it, per - 2)
                    take_out(it, per - 1)
                dve.wait_ge(col_kept.handle, col_kept.at(26))
                nc.vector.tensor_tensor(core.mod[:], core.mod[:], core.col("ada_b_2").unsqueeze(2).to_broadcast([P, 96, 2]), ALU.add)

            @block.gpsimd
            def _(pool):
                with pool.Fori(0, turns) as it:
                    for r in range(per):
                        pool.wait_ge(w_low.handle, it * pieces + w_low.at(KD * (r + 1)))
                        pool.sem_inc(core.freed.handle, 1)


def norm_stage(core, name, streams, dst=None):
    nc = core.nc
    x, h = core.x, core.h
    with Stage(core, name) as st:
        ms = [st.ps(f"ms{i}") for i in range(2)]
        var = st.sb("var", [P, 2, 512])
        rstd = st.sb("rstd", [P, 2, 512])
        gain = st.sb("gain", [P, 2, KD])
        total = KD * len(streams)
        width = sum(s[1] for s in streams)
        odd = st.sb("odd", [P, 2, width])
        squared = st.counter("norm_squared", KD // 2)
        odd_made = st.counter("norm_odd_made", KD // 2)
        paired = st.counter("norm_paired", KD // 2)
        summed = st.counter("norm_summed", len(streams))
        inverted = st.counter("norm_inverted", len(streams))
        rooted = st.counter("norm_rooted", len(streams))
        scaled = st.counter("norm_scaled", total)
        chain = st.counter("norm_chain", 4 * len(streams))
        with st.run() as block:
            @block.sync
            def _(sp):
                core.stream(sp, core.used)

            @block.scalar
            def _(act):
                for k in range(0, KD, 2):
                    nc.scalar.activation(h[:, k, 0:width], x[:, k, 0:width], ACT.Square).then_inc(squared.handle, 1)
                for i, (c0, n, g, sc, sh) in enumerate(streams):
                    act.wait_ge(inverted.handle, inverted.at(i + 1))
                    nc.scalar.activation(rstd[:, i, 0:n], var[:, i, 0:n], ACT.Sqrt).then_inc(rooted.handle, 1)
                for i, (c0, n, g, sc, sh) in enumerate(streams):
                    if sh is not None:
                        for k in range(KD):
                            act.wait_ge(scaled.handle, scaled.at(i * KD + k + 1))
                            nc.scalar.activation(h[:, k, c0:c0 + n], h[:, k, c0:c0 + n], ACT.Identity, bias=sh[:, k:k + 1])

            @block.tensor
            def _(pe):
                for i, (c0, n, g, sc, sh) in enumerate(streams):
                    for k in range(0, KD, 2):
                        pe.wait_ge(paired.handle, paired.at(k // 2 + 1))
                        last = nc.tensor.matmul(ms[i][:, 0:n], core.ones[:], h[:, k, c0:c0 + n], start=(k == 0), stop=(k == KD - 2))
                    last.then_inc(summed.handle, 1)

            @block.vector
            def _(dve):
                link = Link(dve, chain)
                for i, (c0, n, g, sc, sh) in enumerate(streams):
                    if sc is None:
                        link(nc.vector.tensor_copy(gain[:, i, :], g))
                    else:
                        link(nc.vector.scalar_tensor_tensor(out=gain[:, i, :], in0=sc, scalar=1.0, in1=g, op0=ALU.add, op1=ALU.mult))
                for j in range(KD // 2):
                    o, e = odd[:, j % 2, :], h[:, 2 * j, 0:width]
                    nc.vector.tensor_tensor(o, x[:, 2 * j + 1, 0:width], x[:, 2 * j + 1, 0:width], ALU.mult).then_inc(odd_made.handle, 1)
                    dve.wait_ge(odd_made.handle, odd_made.at(j + 1))
                    dve.wait_ge(squared.handle, squared.at(j + 1))
                    nc.vector.tensor_tensor(e, e, o, ALU.add).then_inc(paired.handle, 1)
                for i, (c0, n, g, sc, sh) in enumerate(streams):
                    dve.wait_ge(summed.handle, summed.at(i + 1))
                    link(nc.vector.tensor_scalar(var[:, i, 0:n], ms[i][:, 0:n], EPS, None, ALU.add))
                    nc.vector.reciprocal(var[:, i, 0:n], var[:, i, 0:n]).then_inc(inverted.handle, 1)
                for i, (c0, n, g, sc, sh) in enumerate(streams):
                    dve.wait_ge(rooted.handle, rooted.at(i + 1))
                    for k in range(KD):
                        nc.vector.scalar_tensor_tensor(out=h[:, k, c0:c0 + n], in0=x[:, k, c0:c0 + n], scalar=gain[:, i, k:k + 1],
                                                       in1=rstd[:, i, 0:n], op0=ALU.mult, op1=ALU.mult).then_inc(scaled.handle, 1)
        st.used[-1] = (chain, 2 * len(streams))


BUFS = 3


def product_stage(core, name, widths, tokens, tiles, move, by, take, then=None):
    nc = core.nc
    n0 = core.used
    items = [(c, t) for c in range(len(widths)) for t in tiles[c]]
    of = [[i for i, item in enumerate(items) if item[0] == c] for c in range(len(widths))]
    rank = [sum(by(j) == by(i) for j in range(i)) for i in range(len(items))]
    NB = 8
    amid = BUFS - 2
    with Stage(core, name) as st:
        h_hi = st.sb("h_hi", [P, KD, tokens], F32R)
        h_lo = st.sb("h_lo", [P, KD, tokens], F32R)
        w_hi = st.sb("w_hi", [P, BUFS, CW], F32R)
        w_lo = st.sb("w_lo", [P, BUFS, CW], F32R)
        acc = [st.ps(f"acc{i}") for i in range(NB)]
        pieces = KD * len(widths)
        h_high = st.counter("prod_h_high", KD)
        h_low = st.counter("prod_h_low", KD)
        w_high = st.counter("prod_w_high", pieces)
        w_low = st.counter("prod_w_low", pieces)
        w_used = st.counter("prod_w_used", pieces)
        kept = {e: st.counter(f"prod_kept_{e}", sum(by(i) == e for i in range(len(items)))) for e in ("act", "dve")}

        def await_kept(eng, i):
            eng.wait_ge(kept[by(i)].handle, kept[by(i)].at(rank[i] + 1))

        def bank(i):
            c, t = items[i]
            return acc[i % NB][:, 0:widths[c] if move else tokens]

        def await_outputs(eng, c):
            eng.wait_ge(w_used.handle, w_used.at(KD * (c + 1)))

        with st.run() as block:
            @block.sync
            def _(sp):
                core.used = n0 + len(widths)
                core.stream(sp, core.used)

            @block.gpsimd
            def _(pool):
                for c in range(len(widths)):
                    pool.wait_ge(w_low.handle, w_low.at(KD * (c + 1)))
                    pool.sem_inc(core.freed.handle, 1)

            @block.tensor
            def _(pe):
                for c, width in enumerate(widths):
                    for i in of[c]:
                        if i >= NB:
                            await_kept(pe, i - NB)
                    for k in range(KD):
                        n = KD * c + k
                        if c == 0:
                            pe.wait_ge(h_low.handle, h_low.at(k + 1))
                        pe.wait_ge(w_low.handle, w_low.at(n + 1))
                        for i in of[c]:
                            o = slice(items[i][1] * P, (items[i][1] + 1) * P)
                            if move:
                                s_hi, s_lo, m_hi, m_lo = h_hi[:, k, o], h_lo[:, k, o], w_hi[:, n % BUFS, 0:width], w_lo[:, n % BUFS, 0:width]
                            else:
                                s_hi, s_lo, m_hi, m_lo = w_hi[:, n % BUFS, o], w_lo[:, n % BUFS, o], h_hi[:, k, :], h_lo[:, k, :]
                            nc.tensor.matmul(bank(i), s_hi, m_hi, start=(k == 0), stop=False)
                            nc.tensor.matmul(bank(i), s_hi, m_lo, start=False, stop=False)
                            last = nc.tensor.matmul(bank(i), s_lo, m_hi, start=False, stop=(k == KD - 1))
                        last.then_inc(w_used.handle, 1)

            @block.scalar
            def _(act):
                def take_out(c):
                    if any(by(i) == "act" for i in of[c]):
                        await_outputs(act, c)
                    for i in of[c]:
                        if by(i) == "act":
                            take("act", *items[i], bank(i)).then_inc(kept["act"].handle, 1)

                for c, width in enumerate(widths):
                    for k in range(KD):
                        n = KD * c + k
                        if c == 0:
                            nc.scalar.copy(h_hi[:, k, :], core.h[:, k, 0:tokens]).then_inc(h_high.handle, 1)
                        if k == 0:
                            core.await_chunk(act, n0 + c)
                        if n >= BUFS:
                            act.wait_ge(w_used.handle, w_used.at(n - BUFS + 1))
                        nc.scalar.copy(w_hi[:, n % BUFS, 0:width], by_k(core.slot(n0 + c), width)[:, k, :]).then_inc(w_high.handle, 1)
                        if c and k == amid:
                            take_out(c - 1)
                take_out(len(widths) - 1)

            @block.vector
            def _(dve):
                def take_out(c):
                    if any(by(i) == "dve" for i in of[c]):
                        await_outputs(dve, c)
                    for i in of[c]:
                        if by(i) == "dve":
                            take("dve", *items[i], bank(i)).then_inc(kept["dve"].handle, 1)
                    if then is not None:
                        for i in of[c]:
                            await_kept(dve, i)
                            then(*items[i])

                for c, width in enumerate(widths):
                    for k in range(KD):
                        n = KD * c + k
                        if c == 0:
                            dve.wait_ge(h_high.handle, h_high.at(k + 1))
                            nc.vector.tensor_tensor(h_lo[:, k, :], core.h[:, k, 0:tokens], h_hi[:, k, :], ALU.subtract).then_inc(h_low.handle, 1)
                        dve.wait_ge(w_high.handle, w_high.at(n + 1))
                        nc.vector.tensor_tensor(w_lo[:, n % BUFS, 0:width], by_k(core.slot(n0 + c), width)[:, k, :], w_hi[:, n % BUFS, 0:width],
                                                ALU.subtract).then_inc(w_low.handle, 1)
                        if c and k == amid:
                            take_out(c - 1)
                take_out(len(widths) - 1)


def project_stage(core, name, tiles, widths, keep):
    nc = core.nc

    def take(engine, c, t, bank):
        return nc.scalar.copy(keep(t, c), bank) if engine == "act" else nc.vector.tensor_copy(keep(t, c), bank)

    product_stage(core, name, widths, P * (1 + max(max(t) for t in tiles)), tiles, True, lambda i: ("act", "dve")[i % 2], take)


def residual_stage(core, name, gate=None):
    nc = core.nc

    def take(engine, c, t, bank):
        j = 4 * c + t
        row = core.x[:, j, 0:SEQ]
        if gate is None:
            return nc.vector.tensor_tensor(row, bank, row, ALU.add)
        return nc.vector.scalar_tensor_tensor(out=row, in0=bank, scalar=gate[:, j:j + 1], in1=row, op0=ALU.mult, op1=ALU.add)

    product_stage(core, name, [CW] * 2, SEQ, [range(4)] * 2, False, lambda i: "dve", take)


def mlp_stage(core):
    nc = core.nc
    n_up = FF // CW
    with Stage(core, "mlp") as outer:
        u = outer.sb("u", [P, FF // P, SEQ])

        def take(engine, c, t, bank):
            return nc.scalar.activation(u[:, 4 * c + t, :], bank, ACT.Relu)

        def square(c, t):
            v = u[:, 4 * c + t, :]
            nc.vector.tensor_tensor(v, v, v, ALU.mult)

        product_stage(core, "up", [CW] * n_up, SEQ, [range(4)] * n_up, False, lambda i: "act", take, square)
        down_stage(core, u)


def down_stage(core, u):
    nc = core.nc
    n0 = core.used
    tiles = FF // P
    chunks = tiles // 4
    pieces = 2 * tiles
    B = 6
    with Stage(core, "down") as st:
        u_hi = st.sb("u_hi", [P, BUFS, SEQ], F32R)
        u_lo = st.sb("u_lo", [P, BUFS, SEQ], F32R)
        w_hi = st.sb("w_hi", [P, B, CW], F32R)
        w_lo = st.sb("w_lo", [P, B, CW], F32R)
        acc = [st.ps(f"acc{i}") for i in range(KD)]
        u_high = st.counter("prod_h_high", tiles)
        u_low = st.counter("prod_h_low", tiles)
        w_high = st.counter("prod_w_high", pieces)
        w_low = st.counter("prod_w_low", pieces)
        w_used = st.counter("prod_w_used", pieces)

        def raw(n):
            f, half = n // 2, n % 2
            return by_k(core.slot(n0 + f // 4), D, 4)[:, f % 4, half * CW:(half + 1) * CW]

        with st.run() as block:
            @block.sync
            def _(sp):
                core.used = n0 + chunks
                core.stream(sp, core.used)

            @block.gpsimd
            def _(pool):
                for c in range(chunks):
                    pool.wait_ge(w_low.handle, w_low.at(8 * (c + 1)))
                    pool.sem_inc(core.freed.handle, 1)

            @block.tensor
            def _(pe):
                for n in range(pieces):
                    f, half = n // 2, n % 2
                    if half == 0:
                        pe.wait_ge(u_low.handle, u_low.at(f + 1))
                    pe.wait_ge(w_low.handle, w_low.at(n + 1))
                    for j in range(4):
                        out, o = acc[4 * half + j][:], slice(j * P, (j + 1) * P)
                        nc.tensor.matmul(out, w_hi[:, n % B, o], u_hi[:, f % BUFS, :], start=(f == 0), stop=False)
                        nc.tensor.matmul(out, w_hi[:, n % B, o], u_lo[:, f % BUFS, :], start=False, stop=False)
                        last = nc.tensor.matmul(out, w_lo[:, n % B, o], u_hi[:, f % BUFS, :], start=False, stop=(f == tiles - 1))
                    last.then_inc(w_used.handle, 1)

            @block.scalar
            def _(act):
                for n in range(pieces):
                    f, half = n // 2, n % 2
                    if half == 0:
                        if f >= BUFS:
                            act.wait_ge(w_used.handle, w_used.at(2 * (f - BUFS + 1)))
                        nc.scalar.copy(u_hi[:, f % BUFS, :], u[:, f, :]).then_inc(u_high.handle, 1)
                    if n % 8 == 0:
                        core.await_chunk(act, n0 + n // 8)
                    if n >= B:
                        act.wait_ge(w_used.handle, w_used.at(n - B + 1))
                    nc.scalar.copy(w_hi[:, n % B, :], raw(n)).then_inc(w_high.handle, 1)

            @block.vector
            def _(dve):
                for n in range(pieces):
                    f, half = n // 2, n % 2
                    if half == 0:
                        dve.wait_ge(u_high.handle, u_high.at(f + 1))
                        nc.vector.tensor_tensor(u_lo[:, f % BUFS, :], u[:, f, :], u_hi[:, f % BUFS, :], ALU.subtract).then_inc(u_low.handle, 1)
                    dve.wait_ge(w_high.handle, w_high.at(n + 1))
                    nc.vector.tensor_tensor(w_lo[:, n % B, :], raw(n), w_hi[:, n % B, :], ALU.subtract).then_inc(w_low.handle, 1)
                for j in range(KD):
                    dve.wait_ge(w_used.handle, w_used.at(pieces - 1 + j // 4))
                    nc.vector.tensor_tensor(core.x[:, j, 0:SEQ], acc[j][:], core.x[:, j, 0:SEQ], ALU.add)


def rms_rows(nc, act, squares, x, scratch, signal):
    nc.scalar.activation(scratch, x, ACT.Square).then_inc(signal.handle, 1)


def head_norm_stage(core, cols):
    nc = core.nc
    spans = [(A_Q, 8, HD), (C_Q, 8, HD), (D_Q, 6, HD), (B_QL, 1, 256), (B_KVL, 1, 128)]
    with Stage(core, "heads") as st:
        square = st.sb("square", [P, 2, 512])
        ss = st.sb("ss", [P, LT, 24])
        rstd = st.sb("rstd", [P, LT, 24])
        n = LT * len(spans)
        squared = st.counter("head_squared", n)
        reduced = st.counter("head_reduced", n)
        inverted = st.counter("head_inverted", 1)
        rooted = st.counter("head_rooted", 1)
        chain = st.counter("head_chain", 2)
        at, offs = 0, []
        for _, heads, _ in spans:
            offs.append(at)
            at += heads
        todo = [(t, s) for t in range(LT) for s in range(len(spans))]
        with st.run() as block:
            @block.scalar
            def _(act):
                for i, (t, s) in enumerate(todo):
                    c, heads, w = spans[s]
                    if i >= 2:
                        act.wait_ge(reduced.handle, reduced.at(i - 1))
                    nc.scalar.activation(square[:, i % 2, 0:heads * w], cols[:, t, c:c + heads * w], ACT.Square,
                                         scale=float(w) ** -0.5).then_inc(squared.handle, 1)
                act.wait_ge(inverted.handle, inverted.at(1))
                nc.scalar.activation(rstd[:], ss[:], ACT.Sqrt).then_inc(rooted.handle, 1)

            @block.vector
            def _(dve):
                link = Link(dve, chain)
                for i, (t, s) in enumerate(todo):
                    c, heads, w = spans[s]
                    dve.wait_ge(squared.handle, squared.at(i + 1))
                    nc.vector.tensor_reduce(ss[:, t, offs[s]:offs[s] + heads],
                                            square[:, i % 2, 0:heads * w].rearrange("p (h w) -> p h w", w=w),
                                            AX_X, ALU.add).then_inc(reduced.handle, 1)
                dve.wait_ge(reduced.handle, reduced.at(n))
                link(nc.vector.tensor_scalar(ss[:], ss[:], EPS, None, ALU.add))
                nc.vector.reciprocal(ss[:], ss[:]).then_inc(inverted.handle, 1)
                dve.wait_ge(rooted.handle, rooted.at(1))
                for t, s in todo:
                    c, heads, w = spans[s]
                    v = cols[:, t, c:c + heads * w].rearrange("p (h w) -> p h w", w=w)
                    nc.vector.tensor_tensor(v, v, rstd[:, t, offs[s]:offs[s] + heads].unsqueeze(2).to_broadcast([P, heads, w]), ALU.mult)
        st.used[-1] = (chain, 1)


def mla_stage(core, cols, q, kf, ukv):
    nc, ins = core.nc, core.ins
    with Stage(core, "mla") as st:
        uq = st.sb("uq", [P, 2, HEADS * MLA_DIM])
        uk = st.sb("uk", [P, 512])
        gains = st.sb("gains", [P, 2, MLA_DIM])
        rope = st.sb("rope", [P, 2, LT, 16])
        lat = st.sb("lat", [P, 3, SEQ])
        square = st.sb("square", [P, 16 * MLA_DIM])
        ss = st.sb("ss", [P, 2, 16])
        rstd = st.sb("rstd", [P, 2, 16])
        tmp = st.sb("tmp", [P, 4, LT, HEADS, 16])
        pl = [st.ps(f"pl{i}") for i in range(3)]
        pq = [st.ps(f"pq{i}") for i in range(2)]
        pk = [st.ps(f"pk{i}") for i in range(2)]
        loaded = st.counter("mla_loaded", 16 * 6)
        turned = st.counter("mla_turned", 3)
        lat_kept = st.counter("mla_lat_kept", 3)
        up_q = st.counter("mla_up_q", LT)
        up_k = st.counter("mla_up_k", LT)
        q_kept = st.counter("mla_q_kept", LT)
        k_kept = st.counter("mla_k_kept", LT)
        k_built = st.counter("mla_k_built", 2 * LT)
        squared = st.counter("mla_squared", 2)
        inverted = st.counter("mla_inverted", 1)
        rooted = st.counter("mla_rooted", 1)
        reduced = st.counter("mla_reduced", 2)
        chain = st.counter("mla_chain", 8 + 3)
        with st.run() as block:
            @block.sync
            def _(sp):
                sp.dma_start(uq[:], ins["mla_w_uq"][0].rearrange("(k p) n -> p k n", p=P)).then_inc(loaded.handle, 16)
                sp.dma_start(uk[:], ins["mla_w_ukv"][0]).then_inc(loaded.handle, 16)
                sp.dma_start(gains[:, 0, :], ins["mla_q_g"][0].partition_broadcast(P)).then_inc(loaded.handle, 16)
                sp.dma_start(gains[:, 1, :], ins["mla_k_g"][0].partition_broadcast(P)).then_inc(loaded.handle, 16)
                sp.dma_start(rope[:, 0], core.consts["rope_cos"]).then_inc(loaded.handle, 16)
                sp.dma_start(rope[:, 1], core.consts["rope_sin"]).then_inc(loaded.handle, 16)

            @block.tensor
            def _(pe):
                for j, c in enumerate((B_QL, B_QL + P, B_KVL)):
                    for t in range(LT):
                        last = nc.tensor.transpose(pl[j][:, t * P:(t + 1) * P], cols[:, t, c:c + P], core.ident[:])
                    last.then_inc(turned.handle, 1)
                pe.wait_ge(loaded.handle, loaded.at(96))
                pe.wait_ge(lat_kept.handle, lat_kept.at(3))
                for t in range(LT):
                    if t >= 2:
                        pe.wait_ge(q_kept.handle, q_kept.at(t - 1))
                        pe.wait_ge(k_kept.handle, k_kept.at(t - 1))
                    for j in range(2):
                        last = nc.tensor.matmul(pq[t % 2][:, 0:HEADS * MLA_DIM], lat[:, j, t * P:(t + 1) * P], uq[:, j, :], start=(j == 0), stop=(j == 1))
                    last.then_inc(up_q.handle, 1)
                    nc.tensor.matmul(pk[t % 2][:], lat[:, 2, t * P:(t + 1) * P], uk[:], start=True, stop=True).then_inc(up_k.handle, 1)

            @block.scalar
            def _(act):
                for t in range(LT):
                    act.wait_ge(up_k.handle, up_k.at(t + 1))
                    nc.scalar.copy(ukv[:, t, :], pk[t % 2][:]).then_inc(k_kept.handle, 1)
                for i, (v, ready, n) in enumerate(((q, q_kept, LT), (kf, k_built, 2 * LT))):
                    act.wait_ge(ready.handle, ready.at(n))
                    if i:
                        act.wait_ge(reduced.handle, reduced.at(1))
                    nc.scalar.activation(square[:], v[:].rearrange("p t h w -> p (t h w)"), ACT.Square, scale=float(MLA_DIM) ** -0.5).then_inc(squared.handle, 1)
                act.wait_ge(inverted.handle, inverted.at(1))
                nc.scalar.activation(rstd[:], ss[:], ACT.Sqrt).then_inc(rooted.handle, 1)

            @block.gpsimd
            def _(pool):
                for t in range(LT):
                    pool.wait_ge(k_kept.handle, k_kept.at(t + 1))
                    nc.gpsimd.tensor_copy(kf[:, t, :, 0:HD], ukv[:, t, :].rearrange("p (h w) -> p h w", h=HEADS)[:, :, 0:HD]).then_inc(k_built.handle, 1)
                    nc.gpsimd.tensor_copy(kf[:, t, :, HD:MLA_DIM], cols[:, t, B_KR:B_KR + 32].unsqueeze(1).to_broadcast([P, HEADS, 32])).then_inc(k_built.handle, 1)

            @block.vector
            def _(dve):
                link = Link(dve, chain)
                for j, g in enumerate((core.col("mla_qlat_g", 0, 1), core.col("mla_qlat_g", 1, 1), core.col("mla_kvlat_g"))):
                    dve.wait_ge(turned.handle, turned.at(j + 1))
                    nc.vector.tensor_scalar(lat[:, j, :], pl[j][:], g, None, ALU.mult).then_inc(lat_kept.handle, 1)
                for t in range(LT):
                    dve.wait_ge(up_q.handle, up_q.at(t + 1))
                    nc.vector.tensor_copy(q[:, t].rearrange("p h w -> p (h w)"), pq[t % 2][:, 0:HEADS * MLA_DIM]).then_inc(q_kept.handle, 1)
                for i in range(2):
                    dve.wait_ge(squared.handle, squared.at(i + 1))
                    nc.vector.tensor_reduce(ss[:, i, :], square[:].rearrange("p (g w) -> p g w", w=MLA_DIM), AX_X, ALU.add).then_inc(reduced.handle, 1)
                dve.wait_ge(reduced.handle, reduced.at(2))
                link(nc.vector.tensor_scalar(ss[:], ss[:], EPS, None, ALU.add))
                nc.vector.reciprocal(ss[:], ss[:]).then_inc(inverted.handle, 1)
                dve.wait_ge(rooted.handle, rooted.at(1))
                for i, v in enumerate((q, kf)):
                    flat = v[:].rearrange("p t h w -> p (t h) w")
                    link(nc.vector.tensor_tensor(flat, flat, rstd[:, i, :].unsqueeze(2).to_broadcast([P, 16, MLA_DIM]), ALU.mult))
                    link(nc.vector.tensor_tensor(flat, flat, gains[:, i, :].unsqueeze(1).to_broadcast([P, 16, MLA_DIM]), ALU.mult))
                    x1, x2 = v[:, :, :, HD:HD + 16], v[:, :, :, HD + 16:MLA_DIM]
                    cos, sin = (rope[:, j].unsqueeze(2).to_broadcast([P, LT, HEADS, 16]) for j in range(2))
                    nc.vector.tensor_tensor(tmp[:, 0], x1, cos, ALU.mult)
                    nc.vector.tensor_tensor(tmp[:, 1], x2, sin, ALU.mult)
                    nc.vector.tensor_tensor(tmp[:, 2], x1, sin, ALU.mult)
                    link(nc.vector.tensor_tensor(tmp[:, 3], x2, cos, ALU.mult))
                    nc.vector.tensor_tensor(x1, tmp[:, 0], tmp[:, 1], ALU.subtract)
                    link(nc.vector.tensor_tensor(x2, tmp[:, 2], tmp[:, 3], ALU.add))
        st.used[-1] = (chain, 9)


def turn_heads_stage(core, name, jobs, zero=(), extra=None):
    nc = core.nc
    with Stage(core, name) as st:
        bank = [st.ps(f"bank{i}", 2) for i in range(4)]
        by = ["act" if i % 2 and (gain is None or scale == 1.0) else "dve" for i, (_, _, _, _, gain, scale) in enumerate(jobs)]
        turned = st.counter("turn_turned", len(jobs))
        kept = {e: st.counter(f"turn_kept_{e}", by.count(e)) for e in ("act", "dve")}
        loaded = st.counter("turn_loaded", 16 * (0 if extra is None else extra(None, None)))
        with st.run() as block:
            if extra is not None:
                @block.sync
                def _(sp):
                    extra(sp, loaded)

            @block.gpsimd
            def _(pool):
                for z in zero:
                    nc.gpsimd.memset(z, 0.0)

            @block.tensor
            def _(pe):
                for i, (src, tiles, w, dst, gain, scale) in enumerate(jobs):
                    if i >= 4:
                        e = by[i - 4]
                        pe.wait_ge(kept[e].handle, kept[e].at(by[:i - 3].count(e)))
                    for t in range(tiles):
                        last = nc.tensor.transpose(bank[i % 4][0:w, t * P:(t + 1) * P], src(t), core.ident[:])
                    last.then_inc(turned.handle, 1)

            @block.scalar
            def _(act):
                if extra is not None:
                    act.wait_ge(loaded.handle, loaded.at(16 * extra(None, None)))
                for i, (src, tiles, w, dst, gain, scale) in enumerate(jobs):
                    if by[i] == "act":
                        act.wait_ge(turned.handle, turned.at(i + 1))
                        nc.scalar.activation(dst, bank[i % 4][0:w, 0:tiles * P], ACT.Copy, scale=scale if gain is None else gain).then_inc(kept["act"].handle, 1)

            @block.vector
            def _(dve):
                if extra is not None:
                    dve.wait_ge(loaded.handle, loaded.at(16 * extra(None, None)))
                for i, (src, tiles, w, dst, gain, scale) in enumerate(jobs):
                    if by[i] == "dve":
                        dve.wait_ge(turned.handle, turned.at(i + 1))
                        s = bank[i % 4][0:w, 0:tiles * P]
                        if gain is None:
                            ins_ = nc.vector.tensor_scalar(dst, s, scale, None, ALU.mult)
                        else:
                            ins_ = nc.vector.tensor_scalar(dst, s, gain, scale, ALU.mult, ALU.mult)
                        ins_.then_inc(kept["dve"].handle, 1)


def attention_stage(core, name, turns, per, dim, q_tiles, keys, q, k_of, v_of, bias_of, out_of, sink_of=None):
    nc = core.nc
    steps = per * q_tiles
    pieces = [keys(i) for i in range(q_tiles)]
    width = max(sum(n for _, n, _ in p) for p in pieces)
    npc = max(len(p) for p in pieces)
    with Stage(core, name) as st:
        q_now = st.sb("q_now", [dim, 2, q_tiles * P])
        s = st.sb("s", [P, 2, width + 1])
        p = st.sb("p", [P, 2, width + 1])
        pt = st.sb("pt", [P, 2, width])
        top = st.sb("top", [P, 2])
        total = st.sb("total", [P, 4])
        inv = st.sb("inv", [P, 2])
        ps_s = [st.ps(f"scores{i}", npc) for i in range(2)]
        nt = 1 if width > 512 else 2
        ps_t = [st.ps(f"turned{i}", 2 // nt) for i in range(nt)]
        ps_o = [st.ps(f"out{i}") for i in range(2)]
        N = turns * steps
        q_staged = st.counter("att_q_staged", turns * per)
        held = 2 * q_tiles
        scored = st.counter("att_scored", N + held)
        biased = st.counter("att_biased", N + 2)
        topped = st.counter("att_topped", N)
        raised = st.counter("att_raised", N + 2)
        turned = st.counter("att_turned", N)
        copied = st.counter("att_copied", N + nt)
        weighed = st.counter("att_weighed", N + 2)
        normed = st.counter("att_normed", N + 4)
        summed = st.counter("att_summed", N)
        off = 0 if sink_of is None else 1
        n_of = [sum(n for _, n, _ in pc) for pc in pieces]

        def run(eng, turn_of_heads):
            if turns == 1:
                turn_of_heads(0)
            else:
                with eng.Fori(0, turns) as it:
                    turn_of_heads(it)

        with st.run() as block:
            @block.sync
            def _(sp):
                core.stream(sp, core.used)

            @block.gpsimd
            def _(pool):
                def turn_of_heads(it):
                    for r in range(per):
                        pool.wait_ge(scored.handle, it * steps + scored.at((r + 1) * q_tiles))
                        nc.gpsimd.tensor_copy(q_now[:, r % 2, :], q[:, bass.ds(it * per + r, 1), :].rearrange("p a n -> p (a n)")).then_inc(q_staged.handle, 1)

                run(pool, turn_of_heads)

            @block.tensor
            def _(pe):
                def score(it, g):
                    r, i = divmod(g, q_tiles)
                    if i == 0:
                        pe.wait_ge(q_staged.handle, it * per + q_staged.at(r + 1))
                    pe.wait_ge(biased.handle, it * steps + biased.at(g + 1))
                    for b, (k0, n, _) in enumerate(pieces[i]):
                        last = nc.tensor.matmul(ps_s[g % 2][:, b * 512:b * 512 + n], q_now[:, r % 2, i * P:(i + 1) * P], k_of(it, r, k0, n), start=True, stop=True)
                    last.then_inc(scored.handle, 1)

                def turn(it, g):
                    i = g % q_tiles
                    pe.wait_ge(raised.handle, it * steps + raised.at(g + 3))
                    pe.wait_ge(copied.handle, it * steps + copied.at(g + 1))
                    for j in range(n_of[i] // P):
                        last = nc.tensor.transpose(ps_t[g % nt][:, j * P:(j + 1) * P], p[:, g % 2, off + j * P:off + (j + 1) * P], core.ident[:])
                    last.then_inc(turned.handle, 1)

                def weigh(it, g):
                    r, i = divmod(g, q_tiles)
                    pe.wait_ge(copied.handle, it * steps + copied.at(g + 1 + nt))
                    pe.wait_ge(normed.handle, it * steps + normed.at(g + 3))
                    tiles = [(k0 + j * P) // P for k0, n, _ in pieces[i] for j in range(n // P)]
                    for j, kt in enumerate(tiles):
                        last = nc.tensor.matmul(ps_o[g % 2][:, 0:HD], pt[:, g % 2, j * P:(j + 1) * P], v_of(it, r, kt), start=(j == 0), stop=(j == len(tiles) - 1))
                    last.then_inc(weighed.handle, 1)

                pe.sem_inc(scored.handle, held)
                pe.sem_inc(weighed.handle, 2)
                def turn_of_heads(it):
                    score(it, 0)
                    score(it, 1)
                    for g in range(steps):
                        turn(it, g)
                        if g + 2 < steps:
                            score(it, g + 2)
                        if g:
                            weigh(it, g - 1)
                    weigh(it, steps - 1)

                run(pe, turn_of_heads)

            @block.vector
            def _(dve):
                def bias(it, g):
                    r, i = divmod(g, q_tiles)
                    dve.wait_ge(scored.handle, it * steps + scored.at(g + 1 + held))
                    dve.wait_ge(raised.handle, it * steps + raised.at(g + 1))
                    at = off
                    if off:
                        nc.vector.tensor_scalar(s[:, g % 2, 0:1], sink_of(it, r), 1.0, None, ALU.mult)
                    for b, (k0, n, bs) in enumerate(pieces[i]):
                        src = ps_s[g % 2][:, b * 512:b * 512 + n]
                        if bs is None:
                            last = nc.vector.tensor_copy(s[:, g % 2, at:at + n], src)
                        else:
                            last = nc.vector.tensor_tensor(s[:, g % 2, at:at + n], src, bias_of(it, r, *bs), ALU.add)
                        at += n
                    last.then_inc(biased.handle, 1)
                    dve.wait_ge(biased.handle, it * steps + biased.at(g + 3))
                    nc.vector.tensor_reduce(top[:, g % 2:g % 2 + 1], s[:, g % 2, 0:at], AX_X, ALU.max, negate=True).then_inc(topped.handle, 1)

                def norm(it, g):
                    r, i = divmod(g, q_tiles)
                    dve.wait_ge(weighed.handle, it * steps + weighed.at(g + 3))
                    dve.wait_ge(raised.handle, it * steps + raised.at(g + 3))
                    nc.vector.reciprocal(inv[:, g % 2:g % 2 + 1], total[:, g % 4:g % 4 + 1]).then_inc(summed.handle, 1)
                    dve.wait_ge(summed.handle, it * steps + summed.at(g + 1))
                    nc.vector.tensor_scalar(out_of(it, r, i), ps_o[g % 2][:, 0:HD], inv[:, g % 2:g % 2 + 1], None, ALU.mult).then_inc(normed.handle, 1)

                dve.sem_inc(biased.handle, 2)
                dve.sem_inc(normed.handle, 4)
                def turn_of_heads(it):
                    bias(it, 0)
                    bias(it, 1)
                    for g in range(steps):
                        if g + 2 < steps:
                            bias(it, g + 2)
                        if g:
                            norm(it, g - 1)
                    norm(it, steps - 1)

                run(dve, turn_of_heads)

            @block.scalar
            def _(act):
                def exp(it, g):
                    n = n_of[g % q_tiles] + off
                    act.wait_ge(topped.handle, it * steps + topped.at(g + 1))
                    act.wait_ge(normed.handle, it * steps + normed.at(g + 1))
                    nc.scalar.activation(p[:, g % 2, 0:n], s[:, g % 2, 0:n], ACT.Exp, bias=top[:, g % 2:g % 2 + 1],
                                         accum_out=total[:, g % 4:g % 4 + 1]).then_inc(raised.handle, 1)

                act.sem_inc(copied.handle, nt)
                act.sem_inc(raised.handle, 2)
                def turn_of_heads(it):
                    exp(it, 0)
                    for g in range(steps):
                        if g + 1 < steps:
                            exp(it, g + 1)
                        n = n_of[g % q_tiles]
                        act.wait_ge(turned.handle, it * steps + turned.at(g + 1))
                        act.wait_ge(weighed.handle, it * steps + weighed.at(g + 1))
                        nc.scalar.copy(pt[:, g % 2, 0:n], ps_t[g % nt][:, 0:n]).then_inc(copied.handle, 1)

                run(act, turn_of_heads)


def group_norm_stage(core, o):
    nc = core.nc
    G, W = 4, 256
    with Stage(core, "groups") as st:
        square = st.sb("square", [P, LT * G, W])
        ss = st.sb("ss", [P, LT * G])
        rstd = st.sb("rstd", [P, LT * G])
        bank = [st.ps(f"bank{i}") for i in range(2)]
        squared = st.counter("group_squared", 1)
        inverted = st.counter("group_inverted", 1)
        rooted = st.counter("group_rooted", 1)
        scaled = st.counter("group_scaled", LT * G)
        turned = st.counter("group_turned", KD)
        kept = st.counter("group_kept", KD)
        chain = st.counter("group_chain", 1)
        with st.run() as block:
            @block.scalar
            def _(act):
                for t in range(LT):
                    for g in range(G):
                        last = nc.scalar.activation(square[:, t * G + g, :], o[:, t, g * W:(g + 1) * W], ACT.Square, scale=float(W) ** -0.5,
                                                    accum_out=ss[:, t * G + g:t * G + g + 1])
                last.then_inc(squared.handle, 1)
                act.wait_ge(inverted.handle, inverted.at(1))
                nc.scalar.activation(rstd[:], ss[:], ACT.Sqrt).then_inc(rooted.handle, 1)

            @block.vector
            def _(dve):
                link = Link(dve, chain)
                dve.wait_ge(squared.handle, squared.at(1))
                link(nc.vector.tensor_scalar(ss[:], ss[:], EPS, None, ALU.add))
                nc.vector.reciprocal(ss[:], ss[:]).then_inc(inverted.handle, 1)
                dve.wait_ge(rooted.handle, rooted.at(1))
                for g in range(G):
                    for t in range(LT):
                        v = o[:, t, g * W:(g + 1) * W]
                        nc.vector.tensor_scalar(v, v, rstd[:, t * G + g:t * G + g + 1], None, ALU.mult).then_inc(scaled.handle, 1)
                for k in range(KD):
                    dve.wait_ge(turned.handle, turned.at(k + 1))
                    nc.vector.tensor_scalar(core.h[:, k, 0:SEQ], bank[k % 2][:], core.col("group_out_g", k, 1), None, ALU.mult).then_inc(kept.handle, 1)

            @block.tensor
            def _(pe):
                for k in range(KD):
                    pe.wait_ge(scaled.handle, scaled.at(LT * (k // 2 + 1)))
                    if k >= 2:
                        pe.wait_ge(kept.handle, kept.at(k - 1))
                    for t in range(LT):
                        last = nc.tensor.transpose(bank[k % 2][:, t * P:(t + 1) * P], o[:, t, k * P:(k + 1) * P], core.ident[:])
                    last.then_inc(turned.handle, 1)


def turn_tokens_stage(core, name, src, dst, tiles):
    nc = core.nc
    with Stage(core, name) as st:
        bank = [st.ps(f"bank{i}") for i in range(4)]
        todo = [(t, j) for t in tiles for j in range(2)]
        turned = st.counter("back_turned", len(todo))
        kept = [st.counter("back_kept_act", len(todo) // 2), st.counter("back_kept_dve", len(todo) // 2)]
        with st.run() as block:
            @block.tensor
            def _(pe):
                for i, (t, j) in enumerate(todo):
                    if i >= 4:
                        pe.wait_ge(kept[i % 2].handle, kept[i % 2].at((i - 4) // 2 + 1))
                    for k in range(4):
                        last = nc.tensor.transpose(bank[i % 4][:, k * P:(k + 1) * P], src[:, 4 * j + k, t * P:(t + 1) * P], core.ident[:])
                    last.then_inc(turned.handle, 1)

            @block.scalar
            def _(act):
                for i, (t, j) in enumerate(todo):
                    if i % 2 == 0:
                        act.wait_ge(turned.handle, turned.at(i + 1))
                        nc.scalar.copy(dst[:, t, j * 512:(j + 1) * 512], bank[i % 4][:]).then_inc(kept[0].handle, 1)

            @block.vector
            def _(dve):
                for i, (t, j) in enumerate(todo):
                    if i % 2 == 1:
                        dve.wait_ge(turned.handle, turned.at(i + 1))
                        nc.vector.tensor_copy(dst[:, t, j * 512:(j + 1) * 512], bank[i % 4][:]).then_inc(kept[1].handle, 1)


def first_block(core):
    nc, ins = core.nc, core.ins
    norm_stage(core, "norm_a", [(0, SEQ, core.col("attn_norm_g"), None, None)])
    with Stage(core, "mixers") as mx:
        cols = mx.sb("cols", [P, LT, IN_COLS])
        widths = [CW] * 4 + [IN_COLS - 4 * CW]
        project_stage(core, "w_in", [range(LT)] * len(widths), widths, lambda t, c: cols[:, t, c * CW:c * CW + widths[c]])
        o = mx.sb("o", [P, LT, D])
        head_norm_stage(core, cols)
        spare = core.h[:].rearrange("p k n -> p (k n)")
        n = HEADS * MLA_DIM
        q96 = spare[:, 0:LT * n].rearrange("p (t h w) -> p t h w", t=LT, h=HEADS)
        k96 = spare[:, LT * n:2 * LT * n].rearrange("p (t h w) -> p t h w", t=LT, h=HEADS)
        ukv = spare[:, 2 * LT * n:2 * LT * n + LT * 512].rearrange("p (t w) -> p t w", t=LT)
        mla_stage(core, cols, q96, k96, ukv)
        for g, (name, dim) in enumerate((("moba", HD), ("mla", MLA_DIM), ("dil", HD), ("swa", HD))):
            with Stage(core, f"g_{name}") as gs:
                qT = gs.sb("qT", [MLA_DIM, HEADS, SEQ])
                kv = 2 if name == "swa" else HEADS
                kT = gs.sb("kT", [MLA_DIM, kv, SEQ])
                table = gs.sb("table", [P, HEADS, SEQ])
                gain = gs.sb("gain", [HD, 2])
                sink = gs.sb("sink", [P, HEADS])

                def extra(sp, loaded, name=name, g=g, gain=gain, table=table, sink=sink):
                    todo = [(table[:], core.consts["bias"][g])]
                    if name != "mla":
                        for j in range(2):
                            todo.append((gain[:, j:j + 1], ins[f"{name}_{'qk'[j]}_g"][0].unsqueeze(1)))
                    if name == "swa":
                        todo.append((sink[:], ins["swa_sinks"][0].partition_broadcast(P)))
                    if sp is not None:
                        for d, s in todo:
                            sp.dma_start(d, s).then_inc(loaded.handle, 16)
                    return len(todo)

                jobs = []
                for hd in range(HEADS):
                    for dst, at, heads, j in ((qT, (A_Q, 0, C_Q, D_Q)[g], HEADS, 0), (kT, (A_K, 0, C_K, D_K)[g], kv, 1)):
                        if hd >= heads:
                            continue
                        if name == "mla":
                            src = lambda t, v=(q96, k96)[j], hd=hd: v[:, t, hd, :]
                            jobs.append((src, LT, dim, dst[0:dim, hd, :], None, float(dim) ** -0.5 if j == 0 else 1.0))
                        else:
                            src = lambda t, c=at + hd * HD: cols[:, t, c:c + HD]
                            jobs.append((src, LT, dim, dst[0:dim, hd, :], gain[:, j:j + 1], float(dim) ** -0.5 if j == 0 else 1.0))
                turn_heads_stage(core, f"turn_{name}", jobs, zero=[] if dim == MLA_DIM else [qT[dim:MLA_DIM], kT[dim:MLA_DIM]], extra=extra)
                per = HEADS

                def k_of(it, r, k0, n, kT=kT, name=name):
                    head = it * per + r
                    if name == "swa":
                        head = r // 2
                    return kT[:, bass.ds(head, 1), k0:k0 + n].rearrange("p a n -> p (a n)")

                def v_of(it, r, kt, name=name):
                    if name == "mla":
                        return ukv[:, kt, bass.ds(it * (2 * per * HD) + (r * 2 * HD + HD), HD)]
                    if name == "swa":
                        return cols[:, kt, D_V + r // 2 * HD:D_V + (r // 2 + 1) * HD]
                    return cols[:, kt, bass.ds(it * (per * HD) + ((A_V if name == "moba" else C_V) + r * HD), HD)]

                attention_stage(
                    core, f"att_{name}", HEADS // per, per, MLA_DIM, LT,
                    lambda i: [(0, (i + 1) * P, (SEQ - (i + 1) * P, SEQ))], qT, k_of, v_of,
                    lambda it, r, a, b, table=table: table[:, bass.ds(it * per + r, 1), a:b].rearrange("p a n -> p (a n)"),
                    lambda it, r, i, g=g: o[:, i, bass.ds(it * (per * HD) + (g * 256 + r * HD), HD)],
                    (lambda it, r, sink=sink: sink[:, bass.ds(it * per + r, 1)]) if name == "swa" else None)
        group_norm_stage(core, o)
    residual_stage(core, "w_o")
    norm_stage(core, "norm_m", [(0, SEQ, core.col("mlp_norm_g"), None, None)])
    mlp_stage(core)


QC = 256
TURNS = D // QC
UP = 772
CTX_AT = SEQ + 2


def hyena_chunks(core):
    w = core.ins["hy_w_in_2"].rearrange("(k p) (s c) -> p k s c", p=P, s=3)
    out = core.ins["hy_w_out_2"].rearrange("(q k p) n -> q p k n", p=P, k=2)

    def first(q):
        return lambda slot: [(slot[:].rearrange("p (k s c) -> p k s c", k=KD, s=2)[:, :, s], w[:, :, s, q * QC:(q + 1) * QC]) for s in range(2)]

    def second(q):
        return lambda slot: [(slot[:, 0:KD * QC].rearrange("p (k c) -> p k c", k=KD), w[:, :, 2, q * QC:(q + 1) * QC])]

    def third(q):
        return lambda slot: [(slot[:, 0:2 * D].rearrange("p (k n) -> p k n", k=2), out[q])]

    chunks = [first(0), second(0)]
    for q in range(1, TURNS):
        chunks += [first(q), second(q), third(q - 1)]
    return chunks + [third(TURNS - 1)]


def hyena_stage(core, gate):
    nc, ins = core.nc, core.ins
    n0 = core.used
    x, h = core.x, core.h
    with Stage(core, "hyena") as st:
        h2 = st.sb("h2", [64, TOK])
        net_w1 = st.sb("net_w1", [33, 64])
        net_w2 = st.sb("net_w2", [64, 64])
        net_col = st.sb("net_col", [64, 4])
        tables = {n: st.sb(n, [P, 4, k, w]) for n, k, w in (("dft_l", 2, 256), ("idft_l", 2, 256), ("dft_c", 1, P), ("idft_c", 1, P))}
        spare = [core.slot(n0 + i)[:, KD * QC:KD * QC + 2 * UP].rearrange("p (i n) -> p i n", i=2) for i in (1, 0)]
        raws = [st.sb("raw", [P, 2, UP])[:]] + spare
        raw = lambda i: raws[i // 2][:, i % 2]
        u = st.sb("u", [P, 6, UP])
        v_tok = st.sb("v_tok", [P, 6, QC])
        ab = st.sb("ab", [P, 2, 2, 3, QC])
        taps = ab[:].rearrange("p a b c n -> p a (b c) n")
        pq = st.sb("pq", [P, 2, 2, 3, QC])
        win = st.sb("win", [P, 6, 2, QC])
        w3 = st.sb("w3", [64, 4, QC])
        even = st.sb("even", [P, 2, QC])
        t1 = st.sb("t1", [P, TOK])
        t2 = st.sb("t2", [P, TOK])
        t3 = st.sb("t3", [P, TOK])
        t4 = st.sb("t4", [P, TOK])
        lat = [st.ps(f"lat{i}") for i in range(2)]
        ctx = [st.ps(f"ctx{i}") for i in range(2)]
        spec = [st.ps(f"spec{i}") for i in range(4)]

        FULL = [("proj", 0), ("proj", 1), ("tok", 0), ("tok", 1), ("proj", 2), ("proj", 3), ("back", 0), ("back", 1), ("proj", 4), ("tok", 2), ("tok", 3),
                ("proj", 5), ("back", 2), ("back", 3)] + [("out", j) for j in range(KD)]
        LAST = [item for item in FULL if item[0] != "proj"]
        NI, ND, NP, SP = len(FULL), 4 + KD, 6, 36
        ip_done = st.counter("hy_ip_done", NP * TURNS + len(LAST) * TURNS)
        raw_kept = st.counter("hy_raw_kept", NP * TURNS)
        tok_kept = st.counter("hy_tok_kept", 4 * TURNS)
        ip_dve = st.counter("hy_ip_dve", ND * TURNS + 2)
        sp_done = st.counter("hy_sp_done", SP * TURNS)
        sp_free = st.counter("hy_sp_free", SP * TURNS + 4)
        net_arg, net_turns, net_h1, net_z = t1[0:64], t2[0:64], t3[0:64], t4[0:33]
        net_acc = [spec[0:2], spec[2:4]]
        net_spans = ((0, SEQ), (SEQ, CTX))
        net_loaded = st.counter("hy_net_loaded", 16 * 7)
        net_done = st.counter("hy_net_done", 2)
        net_reduced = st.counter("hy_net_reduced", 2)
        net_bent = st.counter("hy_net_bent", 2)
        even_kept = st.counter("hy_even_kept", 24 * TURNS)
        convolved = st.counter("hy_convolved", NP * TURNS)
        taps_made = st.counter("hy_taps_made", 12 * TURNS)
        multiplied = st.counter("hy_multiplied", 8 * TURNS)
        combined = st.counter("hy_combined", 2 * TURNS)
        gated = st.counter("hy_gated", 2 * TURNS)
        win_loaded = st.counter("hy_win_loaded", 32 * TURNS)
        tab_loaded = st.counter("hy_tab_loaded", 64)
        pads = st.counter("hy_pads", 3)
        chain = st.counter("hy_chain", 0)

        def parity(tile, c0, n):
            return tile[:, c0:c0 + n].rearrange("p (i a) -> p a i", a=2)

        links = []

        def flat(v):
            return v.rearrange("p f n -> p (f n)")

        with st.run() as block:
            def order(it):
                return LAST if isinstance(it, int) and it == TURNS - 1 else FULL

            @block.sync
            def _(sp):
                core.used = n0 + 3 * TURNS
                for dst, src in ((net_z, core.consts["filter_z"]), (net_w1[:], ins["hy_ffn_w1_2"]), (net_w2[:], ins["hy_ffn_w2_2"]),
                                 (net_col[:, 0:1], ins["hy_ffn_b1_2"].unsqueeze(1)), (net_col[:, 1:2], ins["hy_ffn_b2_2"].unsqueeze(1)),
                                 (net_col[:, 2:3], ins["hy_sin_freq_2"][0].unsqueeze(1)), (net_col[:, 3:4], ins["hy_sin_freq_2"][1].unsqueeze(1))):
                    sp.dma_start(dst, src).then_inc(net_loaded.handle, 16)
                for q in range(TURNS):
                    if q:
                        sp.wait_ge(taps_made.handle, taps_made.at(12 * q))
                    sp.dma_start(win[:], core.consts["window"][:, :, :, q * QC:(q + 1) * QC]).then_inc(win_loaded.handle, 16)
                    sp.dma_start(w3[:], ins["hy_ffn_w3_2"].rearrange("a (o c) -> a o c", o=4)[:, :, q * QC:(q + 1) * QC]).then_inc(win_loaded.handle, 16)
                    if q == 0:
                        for name, t in tables.items():
                            sp.dma_start(t[:], core.consts[name]).then_inc(tab_loaded.handle, 16)
                    if q == TURNS - 1:
                        core.reserved = 1
                    core.stream(sp, n0 + 3 * (q + 1))

            @block.tensor
            def _(pe):
                def take(it, what, n):
                    seq = order(it)
                    i = seq.index((what, n))
                    if i < 2:
                        pe.wait_ge(raw_kept.handle, raw_kept.at(NP))
                        pe.wait_ge(ip_dve.handle, it * ND + ip_dve.at(i + 1))
                    elif seq[i - 2][0] == "proj":
                        pe.wait_ge(raw_kept.handle, it * NP + raw_kept.at(NP + seq[i - 2][1] + 1))
                    elif seq[i - 2][0] == "tok":
                        pe.wait_ge(tok_kept.handle, it * 4 + tok_kept.at(seq[i - 2][1] + 1))
                    else:
                        j = seq[i - 2][1] + (4 if seq[i - 2][0] == "out" else 0)
                        pe.wait_ge(ip_dve.handle, it * ND + ip_dve.at(j + 1 + 2))
                    return lat[i % 2], ctx[i % 2]

                def project(bl, bc, i, n):
                    w, o = (by_k(core.slot(n)), i * P) if i < 4 else (by_k(core.slot(n), QC), (i - 4) * P)
                    for k in range(KD):
                        nc.tensor.matmul(bl[:], w[:, k, o:o + P], h[:, k, 0:SEQ], start=(k == 0), stop=(k == KD - 1))
                    for k in range(KD):
                        last = nc.tensor.matmul(bc[:, 0:CTX], w[:, k, o:o + P], h[:, k, SEQ:TOK], start=(k == 0), stop=(k == KD - 1))
                    last.then_inc(ip_done.handle, 1)

                def next_projection(it, i):
                    if ("proj", i) in order(it):
                        n = n0 + (2 if i < 4 else 3)
                        if i in (0, 4):
                            core.await_chunk(pe, n, it, 3)
                        project(*take(it, "proj", i), i, n)

                def take_spec(it, m):
                    pe.wait_ge(sp_free.handle, it * SP + sp_free.at(m + 1))
                    return spec[m % 4]

                def filters(it, o):
                    for t in range(6):
                        b = take_spec(it, 18 * o + t)
                        for d in range(2):
                            last = nc.tensor.matmul(b[:, d * QC:(d + 1) * QC], h2[:, t * P:(t + 1) * P], w3[:, 2 * o + d, :], start=True, stop=True)
                        last.then_inc(sp_done.handle, 1)

                def transform(it, m0, src):
                    for a in range(2):
                        for f in range(3):
                            b = take_spec(it, m0 + 3 * a + f)
                            table, o, base, kn = (tables["dft_l"], f * P, 0, 2) if f < 2 else (tables["dft_c"], 0, 4, 1)
                            for par in range(2):
                                for k in range(kn):
                                    last = nc.tensor.matmul(b[:, par * QC:(par + 1) * QC], table[:, 2 * a + par, k, o:o + P],
                                                            src(a)[:, base + kn * par + k, :], start=(k == 0), stop=(k == kn - 1))
                            last.then_inc(sp_done.handle, 1)

                def turn_tokens(it, o):
                    for j in range(2):
                        bl, bc = take(it, "tok", 2 * o + j)
                        for par in range(2):
                            for k in range(2):
                                nc.tensor.transpose(bl[:, (2 * par + k) * P:(2 * par + k + 1) * P],
                                                    parity(u[:, j], 0, SEQ)[:, par, k * P:(k + 1) * P], core.ident[:])
                            last = nc.tensor.transpose(bc[:, par * P:(par + 1) * P], parity(u[:, j], CTX_AT, CTX)[:, par, :], core.ident[:])
                        last.then_inc(ip_done.handle, 1)

                def back(it, o):
                    pe.wait_ge(combined.handle, it * 2 + combined.at(o + 1))
                    for j in range(2):
                        bl, bc = take(it, "back", 2 * o + j)
                        for b, table, tiles, n in ((bl, tables["idft_l"], (0, 1), 256), (bc, tables["idft_c"], (2,), P)):
                            for par in range(2):
                                steps = [(a, k, f) for a in range(2) for k, f in enumerate(tiles)]
                                for s, (a, k, f) in enumerate(steps):
                                    last = nc.tensor.matmul(b[:, par * n:(par + 1) * n], pq[:, a, par, f, j * P:(j + 1) * P],
                                                            table[:, 2 * a + par, k, :], start=(s == 0), stop=(s == len(steps) - 1))
                        last.then_inc(ip_done.handle, 1)

                def sine_layer(layer, w, z):
                    for b, (c0, n) in enumerate(net_spans):
                        last = nc.tensor.matmul(net_acc[layer][b][0:64, 0:n], w[:], z[:, c0:c0 + n], start=True, stop=True)
                    last.then_inc(net_done.handle, 1)

                for i in range(NP):
                    if i in (0, 4):
                        core.await_chunk(pe, n0 + i // 4)
                    if i >= 2:
                        pe.wait_ge(raw_kept.handle, raw_kept.at(i - 1))
                    project(lat[i % 2], ctx[i % 2], i, n0 + i // 4)
                    if i == 0:
                        pe.wait_ge(net_loaded.handle, net_loaded.at(112))
                        sine_layer(0, net_w1, net_z)
                    elif i == 2:
                        pe.wait_ge(net_bent.handle, net_bent.at(1))
                        sine_layer(1, net_w2, net_h1)
                pe.wait_ge(net_bent.handle, net_bent.at(2))
                pe.wait_ge(tab_loaded.handle, tab_loaded.at(64))

                def turn(it):
                    next_projection(it, 0)
                    pe.wait_ge(win_loaded.handle, it * 32 + win_loaded.at(32))
                    filters(it, 0)
                    next_projection(it, 1)
                    for o in range(2):
                        if o == 0:
                            pe.wait_ge(convolved.handle, it * NP + convolved.at(2))
                        else:
                            pe.wait_ge(gated.handle, it * 2 + gated.at(1))
                        turn_tokens(it, o)
                        pe.wait_ge(taps_made.handle, it * 12 + taps_made.at(6 * o + 6))
                        transform(it, 18 * o + 6, lambda a: taps[:, a])
                        pe.wait_ge(tok_kept.handle, it * 4 + tok_kept.at(2 * o + 2))
                        transform(it, 18 * o + 12, lambda a: v_tok[:])
                        if o == 0:
                            next_projection(it, 2)
                            next_projection(it, 3)
                            back(it, 0)
                            filters(it, 1)
                            next_projection(it, 4)
                        else:
                            next_projection(it, 5)
                            back(it, 1)
                    n = n0 + 4 if order(it) is FULL else n0 + 3 * TURNS - 1
                    if order(it) is FULL:
                        core.await_chunk(pe, n, it, 3)
                    else:
                        core.await_chunk(pe, n)
                    pe.wait_ge(gated.handle, it * 2 + gated.at(2))
                    w = by_k(core.slot(n), D, 2)
                    for j in range(KD):
                        bl, bc = take(it, "out", j)
                        for k in range(2):
                            nc.tensor.matmul(bl[:], w[:, k, j * P:(j + 1) * P], u[:, k, 0:SEQ], start=(k == 0), stop=(k == 1))
                        for k in range(2):
                            last = nc.tensor.matmul(bc[:, 0:CTX], w[:, k, j * P:(j + 1) * P], u[:, k, CTX_AT:CTX_AT + CTX], start=(k == 0), stop=(k == 1))
                        last.then_inc(ip_done.handle, 1)

                with pe.Fori(0, TURNS - 1) as it:
                    turn(it)
                turn(TURNS - 1)

            def await_item(eng, it, what, n):
                i = order(it).index((what, n))
                eng.wait_ge(ip_done.handle, it * NI + ip_done.at(NP + i + 1))
                return i

            @block.gpsimd
            def _(pool):
                nc.gpsimd.memset(raws[0], 0.0).then_inc(pads.handle, 1)
                nc.gpsimd.memset(raws[1], 0.0).then_inc(pads.handle, 1)
                pool.wait_ge(ip_done.handle, ip_done.at(4))
                nc.gpsimd.memset(raws[2], 0.0).then_inc(pads.handle, 1)
                pool.sem_inc(core.freed.handle, 1)
                pool.wait_ge(ip_done.handle, ip_done.at(6))
                pool.sem_inc(core.freed.handle, 1)
                def multiply(it, o):
                    A, B, Pc, Qs = (flat(v[:, a, 1]) for v in (ab, pq) for a in range(2))
                    pool.wait_ge(sp_free.handle, it * SP + sp_free.at(18 * o + 18 + 4))
                    nc.gpsimd.tensor_tensor(t3[:], A, Pc, ALU.mult).then_inc(multiplied.handle, 1)
                    nc.gpsimd.tensor_tensor(t4[:], B, Qs, ALU.mult).then_inc(multiplied.handle, 1)
                    nc.gpsimd.tensor_tensor(A, A, Qs, ALU.mult).then_inc(multiplied.handle, 1)
                    nc.gpsimd.tensor_tensor(B, B, Pc, ALU.mult).then_inc(multiplied.handle, 1)

                with pool.Fori(0, TURNS - 1) as it:
                    multiply(it, 0)
                    await_item(pool, it, "proj", 3)
                    pool.sem_inc(core.freed.handle, 1)
                    multiply(it, 1)
                    pool.wait_ge(convolved.handle, it * NP + convolved.at(2 * NP))
                    pool.sem_inc(core.freed.handle, 1)
                    await_item(pool, it, "out", KD - 1)
                    pool.sem_inc(core.freed.handle, 1)
                for o in range(2):
                    multiply(TURNS - 1, o)
                await_item(pool, TURNS - 1, "out", KD - 1)
                pool.sem_inc(core.freed.handle, 1)

            @block.scalar
            def _(act):
                def keep_even(it, m0, e0):
                    for s in range(6):
                        act.wait_ge(sp_done.handle, it * SP + sp_done.at(m0 + s + 1))
                        act.wait_ge(sp_free.handle, it * SP + sp_free.at(m0 + s - 2 + 1 + 4))
                        nc.scalar.copy(even[:, s % 2, :], spec[(m0 + s) % 4][:, 0:QC]).then_inc(even_kept.handle, 1)

                def keep_tokens(it, o):
                    for j in range(2):
                        i = await_item(act, it, "tok", 2 * o + j)
                        nc.scalar.copy(v_tok[:, 0:4, j * P:(j + 1) * P], lat[i % 2][:].rearrange("p (t n) -> p t n", n=P))
                        last = nc.scalar.copy(v_tok[:, 4:6, j * P:(j + 1) * P], ctx[i % 2][:, 0:CTX].rearrange("p (t n) -> p t n", n=P))
                        last.then_inc(tok_kept.handle, 1)

                def keep_projection(q, i, bank):
                    b = core.vec[:, bass.ds(q * 2 + (VEC_AT["hy_b_in_2"][0] + (i // 2) * KD + i % 2), 1)]
                    nc.scalar.activation(raw(i)[:, 1:1 + SEQ], lat[bank][:], ACT.Identity, bias=b)
                    nc.scalar.activation(raw(i)[:, SEQ + 3:UP - 1], ctx[bank][:, 0:CTX], ACT.Identity, bias=b).then_inc(raw_kept.handle, 1)

                def next_projection(it, i):
                    if ("proj", i) in order(it):
                        n = await_item(act, it, "proj", i)
                        act.wait_ge(convolved.handle, it * NP + convolved.at(i + 1))
                        keep_projection(it + 1, i, n % 2)

                def turn(it):
                    next_projection(it, 0)
                    next_projection(it, 1)
                    for o in range(2):
                        keep_tokens(it, o)
                        keep_even(it, 18 * o + 6, 12 * o)
                        keep_even(it, 18 * o + 12, 12 * o + 6)
                        for i in (2, 3, 4) if o == 0 else (5,):
                            next_projection(it, i)

                for i in range(NP):
                    if i % 2 == 0:
                        act.wait_ge(pads.handle, pads.at(i // 2 + 1))
                    act.wait_ge(ip_done.handle, ip_done.at(i + 1))
                    keep_projection(0, i, i % 2)
                    if i in (1, 3):
                        layer = i // 2
                        act.wait_ge(net_reduced.handle, net_reduced.at(layer + 1))
                        nc.scalar.activation((net_h1, h2[:])[layer], net_arg, ACT.Sin).then_inc(net_bent.handle, 1)
                with act.Fori(0, TURNS - 1) as it:
                    turn(it)
                turn(TURNS - 1)

            @block.vector
            def _(dve):

                def combine(it, link, m0, e0, dst):
                    for a in range(2):
                        for f in range(3):
                            s = 3 * a + f
                            m = m0 + s
                            dve.wait_ge(sp_done.handle, it * SP + sp_done.at(m + 1))
                            dve.wait_ge(even_kept.handle, it * 24 + even_kept.at(e0 + s + 1))
                            odd = spec[m % 4][:, QC:2 * QC]
                            nc.vector.tensor_tensor(dst[:, a, 0, f, :], even[:, s % 2, :], odd, ALU.add)
                            if a == 0:
                                last = nc.vector.tensor_tensor(dst[:, a, 1, f, :], even[:, s % 2, :], odd, ALU.subtract)
                            else:
                                last = nc.vector.tensor_tensor(dst[:, a, 1, f, :], odd, even[:, s % 2, :], ALU.subtract)
                            last.then_inc(sp_free.handle, 1)

                def make_taps(it, link, o):
                    for t in range(6):
                        m = 18 * o + t
                        dve.wait_ge(sp_done.handle, it * SP + sp_done.at(m + 1))
                        link(nc.vector.tensor_tensor(t1[:, 0:2 * QC], spec[m % 4][:], win[:, t].rearrange("p d n -> p (d n)"), ALU.mult))
                        nc.vector.tensor_tensor(taps[:, 0, t, :], t1[:, 0:QC], t1[:, QC:2 * QC], ALU.add).then_inc(sp_free.handle, 1)
                        nc.vector.tensor_tensor(taps[:, 1, t, :], t1[:, 0:QC], t1[:, QC:2 * QC], ALU.subtract).then_inc(taps_made.handle, 1)
                        dve.wait_ge(taps_made.handle, it * 12 + taps_made.at(6 * o + t + 1))

                def products(it, link, o):
                    for s in range(2):
                        A, B = flat(ab[:, 0, s]), flat(ab[:, 1, s])
                        Pc, Qs = flat(pq[:, 0, s]), flat(pq[:, 1, s])
                        p1, p2 = (t1, t2) if s == 0 else (t3, t4)
                        if s == 0:
                            nc.vector.tensor_tensor(p1[:], A, Pc, ALU.mult)
                            link(nc.vector.tensor_tensor(p2[:], B, Qs, ALU.mult))
                            nc.vector.tensor_tensor(A, A, Qs, ALU.mult)
                            link(nc.vector.tensor_tensor(B, B, Pc, ALU.mult))
                        else:
                            dve.wait_ge(multiplied.handle, it * 8 + multiplied.at(4 * o + 4))
                        link(nc.vector.tensor_tensor(B, A, B, ALU.add))
                        link(nc.vector.tensor_tensor(A, p1[:], p2[:], ALU.subtract))
                    lo, hi = [flat(ab[:, a, 0]) for a in range(2)], [flat(ab[:, a, 1]) for a in range(2)]
                    nc.vector.tensor_tensor(flat(pq[:, 0, 0]), lo[0], hi[0], ALU.add)
                    nc.vector.tensor_tensor(flat(pq[:, 0, 1]), lo[0], hi[0], ALU.subtract)
                    nc.vector.tensor_tensor(flat(pq[:, 1, 0]), lo[1], hi[1], ALU.subtract)
                    nc.vector.tensor_tensor(flat(pq[:, 1, 1]), lo[1], hi[1], ALU.add).then_inc(combined.handle, 1)

                def gates(it, link, o):
                    for j in range(2):
                        i = await_item(dve, it, "back", 2 * o + j)
                        b = core.vec[:, bass.ds(it * 2 + (VEC_AT["hy_filter_bias_2"][0] + o * KD + j), 1)]
                        y = lambda tile, n: tile[:, 0:n].rearrange("p (a i) -> p a i", a=2)
                        nc.vector.scalar_tensor_tensor(out=y(t1[:], SEQ), in0=parity(u[:, j], 0, SEQ), scalar=b, in1=y(lat[i % 2][:], SEQ), op0=ALU.mult, op1=ALU.add)
                        ins_ = nc.vector.scalar_tensor_tensor(out=y(t2[:], CTX), in0=parity(u[:, j], CTX_AT, CTX), scalar=b, in1=y(ctx[i % 2][:], CTX), op0=ALU.mult, op1=ALU.add)
                        ins_.then_inc(ip_dve.handle, 1)
                        dve.wait_ge(ip_dve.handle, it * ND + ip_dve.at(2 * o + j + 1 + 2))
                        xo = u[:, 2 + 2 * o + j]
                        nc.vector.tensor_tensor(parity(u[:, j], 0, SEQ), y(t1[:], SEQ), parity(xo, 0, SEQ), ALU.mult)
                        last = nc.vector.tensor_tensor(parity(u[:, j], CTX_AT, CTX), y(t2[:], CTX), parity(xo, CTX_AT, CTX), ALU.mult)
                        if j == 0:
                            link(last)
                        else:
                            last.then_inc(gated.handle, 1)
                            dve.wait_ge(gated.handle, it * 2 + gated.at(o + 1))

                gb = even[:, 0, 0:2 * KD].rearrange("p (s k) -> p s k", s=2)
                pre = Link(dve, chain)
                for s in range(2):
                    pre(nc.vector.tensor_tensor(gb[:, s], gate[s], core.col("hy_b_out_2"), ALU.mult))
                for s, (c0, n) in enumerate(((0, SEQ), (SEQ, CTX))):
                    for k in range(KD):
                        last = nc.vector.tensor_scalar(x[:, k, c0:c0 + n], x[:, k, c0:c0 + n], gb[:, s, k:k + 1], None, ALU.add)
                pre(last)
                dve.wait_ge(net_loaded.handle, net_loaded.at(112))
                for layer in range(2):
                    dve.wait_ge(net_done.handle, net_done.at(layer + 1))
                    for b, (c0, n) in enumerate(net_spans):
                        last = nc.vector.tensor_scalar(net_arg[:, c0:c0 + n], net_acc[layer][b][0:64, 0:n], net_col[:, layer:layer + 1],
                                                       net_col[:, 2 + layer:3 + layer], ALU.add, ALU.mult)
                    pre(last)
                    pre(nc.vector.tensor_scalar(net_turns, net_arg, 1.0 / TWO_PI, ROUND_MAGIC, ALU.mult, ALU.add))
                    pre(nc.vector.tensor_scalar(net_turns, net_turns, -ROUND_MAGIC, None, ALU.add))
                    pre(nc.vector.scalar_tensor_tensor(out=net_arg, in0=net_turns, scalar=-TWO_PI_HI, in1=net_arg, op0=ALU.mult, op1=ALU.add))
                    pre(nc.vector.scalar_tensor_tensor(out=net_arg, in0=net_turns, scalar=-TWO_PI_LO, in1=net_arg, op0=ALU.mult, op1=ALU.add))
                    nc.vector.tensor_scalar(net_arg, net_arg, SIN_MAX, -SIN_MAX, ALU.min, ALU.max).then_inc(net_reduced.handle, 1)
                    dve.wait_ge(net_bent.handle, net_bent.at(layer + 1))
                dve.sem_inc(ip_dve.handle, 2)
                dve.sem_inc(sp_free.handle, 4)
                n_pre = pre.n

                def convolve(it, link, i):
                    dve.wait_ge(raw_kept.handle, it * NP + raw_kept.at(i + 1))
                    r = raw(i)
                    col = lambda name, tap=0: core.vec[:, bass.ds(it * 2 + (VEC_AT[name][0] + tap * 24 + (i // 2) * KD + i % 2), 1)]
                    m = UP - 2
                    dst = u[:, i, 0:m]
                    link(nc.vector.tensor_scalar(dst, r[:, 1:1 + m], col("hy_short_w_2", 1), col("hy_short_b_2"), ALU.mult, ALU.add))
                    link(nc.vector.scalar_tensor_tensor(out=dst, in0=r[:, 0:m], scalar=col("hy_short_w_2", 0), in1=dst, op0=ALU.mult, op1=ALU.add))
                    nc.vector.scalar_tensor_tensor(out=dst, in0=r[:, 2:2 + m], scalar=col("hy_short_w_2", 2), in1=dst, op0=ALU.mult, op1=ALU.add).then_inc(convolved.handle, 1)

                def turn(it):
                    link = Link(dve, chain, it * LINKS_PER_TURN + n_pre)
                    for i in range(2):
                        convolve(it, link, i)
                    dve.wait_ge(win_loaded.handle, it * 32 + win_loaded.at(32))
                    make_taps(it, link, 0)
                    for i in range(2, NP):
                        convolve(it, link, i)
                    dve.wait_ge(convolved.handle, it * NP + convolved.at(NP))
                    for o in range(2):
                        if o:
                            make_taps(it, link, 1)
                        combine(it, link, 18 * o + 6, 12 * o, pq)
                        combine(it, link, 18 * o + 12, 12 * o + 6, ab)
                        dve.wait_ge(sp_free.handle, it * SP + sp_free.at(18 * o + 18 + 4))
                        products(it, link, o)
                        gates(it, link, o)
                    for j in range(KD):
                        i = await_item(dve, it, "out", j)
                        dve.wait_ge(ip_dve.handle, it * ND + ip_dve.at(4 + j + 2))
                        nc.vector.scalar_tensor_tensor(out=x[:, j, 0:SEQ], in0=lat[i % 2][:], scalar=gate[0][:, j:j + 1], in1=x[:, j, 0:SEQ], op0=ALU.mult, op1=ALU.add)
                        nc.vector.scalar_tensor_tensor(out=x[:, j, SEQ:TOK], in0=ctx[i % 2][:, 0:CTX], scalar=gate[1][:, j:j + 1], in1=x[:, j, SEQ:TOK], op0=ALU.mult, op1=ALU.add).then_inc(ip_dve.handle, 1)
                    links.append(link.n)

                with dve.Fori(0, TURNS - 1) as it:
                    turn(it)
                turn(TURNS - 1)
                assert links == [LINKS_PER_TURN] * 2, links
                links[:] = [n_pre + TURNS * LINKS_PER_TURN]
        st.used = [(s, n) if s is not chain else (chain, links[0]) for s, n in st.used]


LINKS_PER_TURN = 2 * (6 + 4 + 2 + 1) + 12


def route_stage(core, layer, ctx, xe_l, xe_c, sp_l, sp_c):
    nc, ins = core.nc, core.ins
    tiles = LT + (CT if ctx else 0)
    cols = tiles * P
    E = N_EXP
    with Stage(core, "route") as st:
        tok_hi = st.sb("tok_hi", [P, LT, D], F32R)
        tok_lo = st.sb("tok_lo", [P, LT, D], F32R)
        flat = sp_l[:].rearrange("p j n -> p (j n)")
        if ctx:
            rows, work, pos = (flat[0:E, i * cols:(i + 1) * cols] for i in range(3))
            one = flat[0:E, 3 * cols:3 * cols + SEQ]
            tok_ctx = [flat[:, 3 * cols + SEQ:3 * cols + SEQ + D], sp_c[:].rearrange("p j n -> p (j n)")]
        else:
            rows, work, pos = (st.sb(n, [E, cols])[:] for n in ("rows", "work", "pos"))
            one = st.sb("one", [E, SEQ])[:]
        router = st.sb("router", [P, KD, E])
        number = st.sb("number", [P, CAP_L])
        aff = st.sb("aff", [P, tiles, E])
        top = st.sb("top", [P, tiles])
        total = st.sb("total", [P, tiles])
        best = st.sb("best", [E, 8])
        sel = rows
        at = st.sb("at", [P, tiles, E])
        pick_l = st.sb("pick_l", [P, LT, E, CAP_L], F32R)
        assert core.reserved == (1 if ctx else 0)
        gated_l = (core.slot(core.used + NS - 1)[:] if ctx else core.h[:].rearrange("p k n -> p (k n)")[:, 0:LT * E * CAP_L]).rearrange(
            "p (t e s) -> p t e s", t=LT, e=E)
        pick_c = st.sb("pick_c", [P, CT, E, CAP_C]) if ctx else None
        pl = st.ps("logits")
        pr = st.ps("by_expert", 2)
        pa = st.ps("places")
        bank = [st.ps(f"bank{i}") for i in range(4)]
        halves = [(t, j) for t in range(tiles) for j in range(2)]
        tok_turned = st.counter("route_tok_turned", len(halves))
        tok_kept = st.counter("route_tok_kept", len(halves))
        tok_split = st.counter("route_tok_split", 2 * LT)
        loaded = st.counter("route_loaded", 32)
        scored = st.counter("route_scored", 1)
        scores_kept = st.counter("route_scores_kept", 1)
        scores_turned = st.counter("route_scores_turned", 1)
        shifted = st.counter("route_shifted", 1)
        raised = st.counter("route_raised", 1)
        softmaxed = st.counter("route_softmaxed", 1)
        rowed = st.counter("route_rowed", 1)
        placed = st.counter("route_placed", 1)
        turned = st.counter("route_turned", 1)
        picked = st.counter("route_picked", 1)
        gathers = [(d, c, "l") for d in range(KD) for c in range(2)] + ([(d, 0, "c") for d in range(KD)] if ctx else [])
        ng = len(gathers)
        gathered = st.counter("route_gathered", ng)
        kept = [st.counter("route_kept_act", ng // 2), st.counter("route_kept_dve", ng // 2)]
        gated = st.counter("route_gated", 2 if ctx else 1)
        scatters = [("l", j) for j in range(E // 2)] + ([("c", j) for j in range(E // 4)] if ctx else [])
        spread = st.counter("route_spread", len(scatters))
        spread_kept = st.counter("route_spread_kept", len(scatters))
        chain = st.counter("route_chain", 0)
        spans = [(0, SEQ, CAP_L)] + ([(SEQ, CTX, CAP_C)] if ctx else [])
        n_links = []
        with st.run() as block:
            @block.sync
            def _(sp):
                sp.dma_start(router[:], ins["moe_router_2"][layer].rearrange("(k p) e -> p k e", p=P)).then_inc(loaded.handle, 16)
                sp.dma_start(number[:], core.consts["slot_number"]).then_inc(loaded.handle, 16)

            @block.tensor
            def _(pe):
                pe.wait_ge(loaded.handle, loaded.at(32))
                for c0, n, _ in spans:
                    for k in range(KD):
                        last = nc.tensor.matmul(pr[0:E, c0:c0 + n], router[:, k, :], core.h[:, k, c0:c0 + n], start=(k == 0), stop=(k == KD - 1))
                last.then_inc(scored.handle, 1)
                for i, (t, j) in enumerate(halves):
                    if i >= 4:
                        pe.wait_ge(tok_split.handle, tok_split.at(i - 3))
                    for k in range(4):
                        last = nc.tensor.transpose(bank[i % 4][:, k * P:(k + 1) * P], core.h[:, 4 * j + k, t * P:(t + 1) * P], core.ident[:])
                    last.then_inc(tok_turned.handle, 1)
                    if i == 0:
                        pe.wait_ge(scores_kept.handle, scores_kept.at(1))
                        for tt in range(tiles):
                            last = nc.tensor.transpose(pl[:, tt * E:(tt + 1) * E], rows[:, tt * P:(tt + 1) * P], core.ident[0:E, 0:E])
                        last.then_inc(scores_turned.handle, 1)
                    if i == 3:
                        pe.wait_ge(softmaxed.handle, softmaxed.at(1))
                        for tt in range(tiles):
                            last = nc.tensor.transpose(pr[0:E, tt * P:(tt + 1) * P], aff[:, tt, :], core.ident[:])
                        last.then_inc(rowed.handle, 1)
                pe.wait_ge(placed.handle, placed.at(1))
                for t in range(tiles):
                    last = nc.tensor.transpose(pa[:, t * E:(t + 1) * E], pos[:, t * P:(t + 1) * P], core.ident[0:E, 0:E])
                last.then_inc(turned.handle, 1)
                pe.wait_ge(picked.handle, picked.at(1))
                pe.wait_ge(tok_split.handle, tok_split.at(2 * LT))
                pe.wait_ge(tok_kept.handle, tok_kept.at(len(halves)))
                for i, (d, c, s) in enumerate(gathers):
                    if i >= 4:
                        pe.wait_ge(kept[i % 2].handle, kept[i % 2].at((i - 4) // 2 + 1))
                    tt = range(LT) if s == "l" else range(CT)
                    for t in tt:
                        rhs = pick_l[:, t, 8 * c:8 * c + 8, :] if s == "l" else pick_c[:, t]
                        parts = (tok_hi[:, t], tok_lo[:, t]) if s == "l" else (tok_ctx[t],)
                        for n, part in enumerate(parts):
                            last = nc.tensor.matmul(bank[i % 4][:], part[:, d * P:(d + 1) * P], rhs.rearrange("p e s -> p (e s)"),
                                                    start=(t == 0 and n == 0), stop=(t == tt[-1] and n == len(parts) - 1))
                    last.then_inc(gathered.handle, 1)
                pe.wait_ge(gated.handle, gated.at(2 if ctx else 1))
                for i in (0, 1):
                    pe.wait_ge(kept[i].handle, kept[i].at(ng // 2))
                for i, (s, j) in enumerate(scatters):
                    if i >= 4:
                        pe.wait_ge(spread_kept.handle, spread_kept.at(i - 3))
                    for t in range(LT if s == "l" else CT):
                        src = gated_l[:, t, 2 * j:2 * j + 2, :] if s == "l" else pick_c[:, t, 4 * j:4 * j + 4, :]
                        last = nc.tensor.transpose(bank[i % 4][:, t * P:(t + 1) * P], src.rearrange("p e s -> p (e s)"), core.ident[:])
                    last.then_inc(spread.handle, 1)

            def keep(i):
                d, c, s = gathers[i]
                if s == "l":
                    return xe_l[:, 8 * c:8 * c + 8, d, :], bank[i % 4][:].rearrange("p (e s) -> p e s", s=CAP_L)
                return xe_c[:, :, d, :], bank[i % 4][:].rearrange("p (e s) -> p e s", s=CAP_C)

            @block.scalar
            def _(act):
                for i, (t, j) in enumerate(halves):
                    if i == 3:
                        act.wait_ge(shifted.handle, shifted.at(1))
                        nc.scalar.activation(aff[:], aff[:], ACT.Exp).then_inc(raised.handle, 1)
                    act.wait_ge(tok_turned.handle, tok_turned.at(i + 1))
                    dst = tok_hi[:, t] if t < LT else tok_ctx[t - LT]
                    nc.scalar.copy(dst[:, j * 512:(j + 1) * 512], bank[i % 4][:]).then_inc(tok_kept.handle, 1)
                for i in range(0, ng, 2):
                    act.wait_ge(gathered.handle, gathered.at(i + 1))
                    dst, src = keep(i)
                    nc.scalar.copy(dst, src).then_inc(kept[0].handle, 1)

            @block.vector
            def _(dve):
                def low(first, last):
                    for i, (t, j) in list(enumerate(halves))[first:last]:
                        dve.wait_ge(tok_kept.handle, tok_kept.at(i + 1))
                        o = slice(j * 512, (j + 1) * 512)
                        nc.vector.tensor_tensor(tok_lo[:, t, o], bank[i % 4][:], tok_hi[:, t, o], ALU.subtract).then_inc(tok_split.handle, 1)

                link = Link(dve, chain)
                dve.wait_ge(scored.handle, scored.at(1))
                nc.vector.tensor_copy(rows, pr[0:E, 0:cols]).then_inc(scores_kept.handle, 1)
                dve.wait_ge(scores_turned.handle, scores_turned.at(1))
                logits = pl[:, 0:tiles * E].rearrange("p (t e) -> p t e", e=E)
                link(nc.vector.tensor_reduce(top[:], logits, AX_X, ALU.max))
                nc.vector.tensor_tensor(aff[:], logits, top[:].unsqueeze(2).to_broadcast([P, tiles, E]), ALU.subtract).then_inc(shifted.handle, 1)
                dve.wait_ge(raised.handle, raised.at(1))
                link(nc.vector.tensor_reduce(total[:], aff[:], AX_X, ALU.add))
                link(nc.vector.reciprocal(total[:], total[:]))
                nc.vector.tensor_tensor(aff[:], aff[:], total[:].unsqueeze(2).to_broadcast([P, tiles, E]), ALU.mult).then_inc(softmaxed.handle, 1)
                low(0, 3)
                nc.vector.memset(one, 1.0)
                dve.wait_ge(rowed.handle, rowed.at(1))
                link(nc.vector.tensor_copy(rows, pr[0:E, 0:cols]))
                for c0, n, cap in spans:
                    src = rows
                    for _r in range(cap // 8):
                        link(nc.vector.max(best[:], src[:, c0:c0 + n]))
                        link(nc.vector.match_replace(work[:, c0:c0 + n], best[:], src[:, c0:c0 + n], -1.0))
                        src = work
                link(nc.vector.tensor_scalar(sel, work, 0.0, None, ALU.is_lt))
                for c0, n, cap in spans:
                    last = nc.vector.tensor_tensor_scan(pos[:, c0:c0 + n], one[:, 0:n], sel[:, c0:c0 + n], 0.0, ALU.mult, ALU.add)
                link(last)
                nc.vector.tensor_tensor(pos, pos, sel, ALU.mult).then_inc(placed.handle, 1)
                low(3, 2 * LT)
                dve.wait_ge(turned.handle, turned.at(1))
                link(nc.vector.tensor_copy(at[:], pa[:, 0:tiles * E].rearrange("p (t e) -> p t e", e=E)))
                dve.wait_ge(loaded.handle, loaded.at(32))
                sets = [(pick_l[:, t], gated_l[:, t], t, CAP_L) for t in range(LT)] + ([(pick_c[:, t], pick_c[:, t], LT + t, CAP_C) for t in range(CT)] if ctx else [])
                for v, _, t, cap in sets:
                    last = nc.vector.tensor_tensor(v, number[:, 0:cap].unsqueeze(1).to_broadcast([P, E, cap]),
                                                   at[:, t, :].unsqueeze(2).to_broadcast([P, E, cap]), ALU.is_equal)
                last.then_inc(picked.handle, 1)
                dve.wait_ge(picked.handle, picked.at(1))

                def gates(some):
                    for v, g, t, cap in some:
                        last = nc.vector.tensor_tensor(g, v, aff[:, t, :].unsqueeze(2).to_broadcast([P, E, cap]), ALU.mult)
                    last.then_inc(gated.handle, 1)

                gates(sets[:LT])
                for i in range(1, ng, 2):
                    dve.wait_ge(gathered.handle, gathered.at(i + 1))
                    dst, src = keep(i)
                    nc.vector.tensor_copy(dst, src).then_inc(kept[1].handle, 1)
                if ctx:
                    dve.wait_ge(gathered.handle, gathered.at(ng))
                    gates(sets[LT:])
                for i, (s, j) in enumerate(scatters):
                    dve.wait_ge(spread.handle, spread.at(i + 1))
                    dst = sp_l[:, j, :] if s == "l" else sp_c[:, j, :]
                    nc.vector.tensor_copy(dst, bank[i % 4][:, 0:SEQ if s == "l" else CTX]).then_inc(spread_kept.handle, 1)
                n_links.append(link.n)
        st.used = [(s, n) if s is not chain else (chain, n_links[0]) for s, n in st.used]


EXPERTS_PER_TURN = 4
EXPERT_ORDER = []
for _r in range(EXPERTS_PER_TURN):
    EXPERT_ORDER += [(_r, "gate", 0), (_r, "up", 0)] + ([(_r - 1, "down", 1)] if _r else []) + [(_r, "gate", 1), (_r, "up", 1), (_r, "down", 0)]
EXPERT_ORDER.append((EXPERTS_PER_TURN - 1, "down", 1))


def expert_chunks(core, layer):
    def place(r, what, half):
        w = core.ins[f"moe_w_{what}_2"][layer]

        def of(first):
            def at(slot):
                a = w[bass.ds(first + r, 1)]
                if what == "down":
                    return [(slot[:].rearrange("p (k n) -> p k n", k=4),
                             a.rearrange("e (h k p) n -> h p (e k) n", p=P, h=2)[half])]
                return [(slot[:].rearrange("p (k n) -> p k n", k=KD),
                         a.rearrange("e (k p) n -> p (e k) n", p=P)[:, :, half * CW:(half + 1) * CW])]
            return at
        return of
    return [place(*c) for c in EXPERT_ORDER]


PIECES = 8
SPLIT_BUFS = 6
AMID = 5


def experts_stage(core, layer, ctx, xe_l, xe_c, sp_l, sp_c, gate):
    nc = core.nc
    n0 = core.used
    E, H = EXPERTS_PER_TURN, N_EXP // EXPERTS_PER_TURN
    S = CAP_L + (CAP_C if ctx else 0)
    NC = len(EXPERT_ORDER)
    NP = NC * PIECES
    stack = 2 * S <= P
    R = 2 * S if stack else S
    pool_pieces = (2, 5) if stack else (2,)
    dve_pieces = [q for q in range(PIECES) if q not in pool_pieces]
    ND, NG = len(dve_pieces), len(pool_pieces)
    M = 24 if ctx else 16
    nb = 3 if ctx else 2
    x = core.x
    W = KD * CW // PIECES
    with Stage(core, "experts") as st:
        x_parts = st.sb("x_parts", [P, 2, KD, 2, S], F32R)
        x_hi, x_lo = x_parts[:, :, :, 0], x_parts[:, :, :, 1]
        w_hi = st.sb("w_hi", [P, SPLIT_BUFS, W], F32R)
        w_lo = st.sb("w_lo", [P, SPLIT_BUFS, W], F32R)
        act_ = st.sb("act", [S, 2, CW])
        hid = st.sb("hid", [S, 2, CW])
        hid_parts = st.sb("hid_parts", [P, KD, 2, S], F32R)
        hid_hi, hid_lo = hid_parts[:, :, 0], hid_parts[:, :, 1]
        if stack:
            gate_low = st.sb("gate_low", [S, CW])
            up_low = st.sb("up_low", [S, CW])
            y_low = st.sb("y_low", [S, D])
            gate_sum = st.sb("gate_sum", [S, CW])
            up_sum = st.sb("up_sum", [S, CW])
        y_l = core.h[:].rearrange("p k n -> p (k n)")[:, N_EXP * KD * CAP_C:].rearrange("p (j d) -> p j d", j=2)
        y_c = st.sb("y_c", [P, D]) if ctx else None
        pg, pu, pt = st.ps("pg"), st.ps("pu"), st.ps("pt")
        py = st.ps("py", 2)
        psc = [st.ps(f"psc{i}") for i in range(nb)]
        per_stage = 2 if ctx else 1
        x_high = st.counter("ex_x_high", per_stage * E * H)
        x_high_seen = st.counter("ex_x_high_seen", per_stage * E * H)
        staged = st.counter("ex_staged", per_stage * E * H)
        c_used, c_silu, c_hid, c_turn, c_low, c_yl, c_sc, c_add = NP, 1, 2, 2, 1, 1, M, nb
        w_high = st.counter("ex_w_high", NP * H)
        w_low = st.counter("ex_w_low", ND * NC * H)
        w_low_pool = st.counter("ex_w_low_pool", NG * NC * H)
        w_used = st.counter("ex_w_used", NP * H + c_used)
        silu_done = st.counter("ex_silu_done", 2 * E * H + c_silu)
        gate_lowered = st.counter("ex_gate_lowered", 2 * E * H if stack else 0)
        gate_summed = st.counter("ex_gate_summed", 2 * E * H + 1 if stack else 0)
        up_lowered = st.counter("ex_up_lowered", 2 * E * H if stack else 0)
        up_summed = st.counter("ex_up_summed", 2 * E * H + 1 if stack else 0)
        y_lowered = st.counter("ex_y_lowered", E * H if stack else 0)
        hid_made = st.counter("ex_hid_made", 2 * E * H + c_hid)
        hid_turned = st.counter("ex_hid_turned", 2 * E * H + c_turn)
        hid_high = st.counter("ex_hid_high", 2 * E * H)
        hid_low = st.counter("ex_hid_low", 2 * E * H + c_low)
        yl_kept = st.counter("ex_yl_kept", E * H + c_yl)
        yc_kept = st.counter("ex_yc_kept", E * H + c_yl if ctx else c_yl)
        sc_done = st.counter("ex_sc_done", M * H + c_sc)
        sc_added = st.counter("ex_sc_added", M * H + c_add)
        place = expert_chunks(core, layer)

        def raw(j, q):
            return core.slot(n0 + j)[:, q * W:(q + 1) * W]

        def await_product(eng, it, r, what, half):
            j = EXPERT_ORDER.index((r % E, what, half)) - (NC if r < 0 else 0)
            eng.wait_ge(w_used.handle, it * NP + w_used.at(PIECES * (j + 1) + c_used))

        late = [(8, 11), (11, 14), (14, 17), (17, 20), (20, 22), (22, 24)] if ctx else [(8, 10), (10, 12), (12, 14), (14, 16)]
        late_after = [(0, "gate", 1), (0, "up", 1), (0, "down", 0), (1, "gate", 0), (1, "up", 0), (0, "down", 1)]
        early = [(0, 2), (2, 4), (4, 6), (6, 8)]
        early_after = [(2, "gate", 1), (2, "up", 1), (2, "down", 0), (3, "gate", 0)]

        def scattered_after(first, *chunk):
            if chunk in early_after:
                return [(*early[early_after.index(chunk)], 0)]
            if not first and chunk in late_after[:len(late)]:
                return [(*late[late_after.index(chunk)], 1)]
            return []

        def in_order(it, piece, after):
            for j, c in enumerate(EXPERT_ORDER):
                for q in range(PIECES):
                    piece(it, j, q)
                    if q == AMID:
                        after(it, *c)

        with st.run() as block:
            @block.sync
            def _(sp):
                def split(it, j):
                    sp.wait_ge(w_low.handle, it * (ND * NC) + w_low.at(ND * (j + 1)))
                    sp.sem_inc(core.freed.handle, 1)

                core.reserved = 0
                core.stream(sp, n0)

                def load(first, j):
                    core.issue(sp, n0 + j, place[j % NC](first + j // NC * E))

                with sp.Fori(0, H - 1) as it:
                    first = sp.snap(it * E)
                    for j in range(NC):
                        split(it, j)
                        load(first, j + NS)
                for j in range(NC):
                    split(H - 1, j)
                    if j + NS < NC:
                        load((H - 1) * E, j + NS)
                core.used = core.issued = n0 + NC * H
                core.stream(sp, core.used)

            @block.gpsimd
            def _(pool):
                def stage(it, r):
                    await_product(pool, it, r - 2, "up", 1)
                    for i, (part, c0, n) in enumerate(((xe_l, 0, CAP_L), (xe_c, CAP_L, CAP_C))[:per_stage]):
                        src = part[:, bass.ds(it * E + r, 1)].rearrange("p e k s -> p (e k) s")
                        nc.gpsimd.tensor_copy(x_hi[:, r % 2, :, c0:c0 + n], src).then_inc(x_high.handle, 1)
                        pool.wait_ge(x_high.handle, it * (E * per_stage) + x_high.at(r * per_stage + i + 1))
                        pool.sem_inc(x_high_seen.handle, 1)
                        nc.gpsimd.tensor_tensor(x_lo[:, r % 2, :, c0:c0 + n], src, x_hi[:, r % 2, :, c0:c0 + n], ALU.subtract).then_inc(staged.handle, 1)

                def low(it, j, q):
                    if q in pool_pieces:
                        b = (j * PIECES + q) % SPLIT_BUFS
                        pool.wait_ge(w_high.handle, it * NP + w_high.at(j * PIECES + q + 1))
                        nc.gpsimd.tensor_tensor(w_lo[:, b, :], raw(j, q), w_hi[:, b, :], ALU.subtract).then_inc(w_low_pool.handle, 1)

                def after(it, r, what, half):
                    if (what, half) == ("gate", 1) and r + 1 < E:
                        stage(it, r + 1)

                with pool.Fori(0, H) as it:
                    stage(it, 0)
                    in_order(it, low, after)

            @block.tensor
            def _(pe):
                def part(it, j, q):
                    if q in pool_pieces:
                        pe.wait_ge(w_low_pool.handle, it * (NG * NC) + w_low_pool.at(NG * j + pool_pieces.index(q) + 1))
                    else:
                        pe.wait_ge(w_low.handle, it * (ND * NC) + w_low.at(ND * j + dve_pieces.index(q) + 1))
                    b = (j * PIECES + q) % SPLIT_BUFS
                    return w_hi[:, b, :], w_lo[:, b, :]

                def product(out, parts, w_h, w_l, start, stop):
                    if stack:
                        both = parts.rearrange("p a s -> p (a s)")
                        nc.tensor.matmul(out, both, w_h, start=start, stop=False)
                        return nc.tensor.matmul(out, both, w_l, start=False, stop=stop)
                    hi, lo = parts[:, 0], parts[:, 1]
                    nc.tensor.matmul(out, hi, w_h, start=start, stop=False)
                    nc.tensor.matmul(out, hi, w_l, start=False, stop=False)
                    return nc.tensor.matmul(out, lo, w_h, start=False, stop=stop)

                def into_hidden(it, r, what, c):
                    j = EXPERT_ORDER.index((r, what, c))
                    if what == "gate":
                        acc = pg
                        if stack:
                            pe.wait_ge(gate_summed.handle, it * (2 * E) + gate_summed.at(2 * r + c + 1))
                        else:
                            pe.wait_ge(silu_done.handle, it * (2 * E) + silu_done.at(2 * r + c + c_silu))
                    else:
                        acc = pu
                        pe.wait_ge(hid_made.handle, it * (2 * E) + hid_made.at(2 * r + c + c_hid))
                    for k in range(KD):
                        product(acc[0:R, :], x_parts[:, r % 2, k], *part(it, j, k), k == 0, k == KD - 1).then_inc(w_used.handle, 1)

                def turn(it, r, c):
                    s = 2 * r + c
                    pe.wait_ge(hid_made.handle, it * (2 * E) + hid_made.at(s + 1 + c_hid))
                    pe.wait_ge(hid_low.handle, it * (2 * E) + hid_low.at(s + c_low))
                    for f in range(4):
                        last = nc.tensor.matmul(pt[:, f * S:(f + 1) * S], hid[:, c, f * P:(f + 1) * P], core.ident[0:S, 0:S], start=True, stop=True)
                    last.then_inc(hid_turned.handle, 1)

                def down_of(it, r, c):
                    j = EXPERT_ORDER.index((r, "down", c))
                    pe.wait_ge(hid_low.handle, it * (2 * E) + hid_low.at(2 * r + c + 1 + c_low))
                    if c == 0:
                        pe.wait_ge(yl_kept.handle, it * E + yl_kept.at(r + c_yl))
                        if ctx:
                            pe.wait_ge(yc_kept.handle, it * E + yc_kept.at(r + c_yl))
                    for q in range(PIECES):
                        f, half = 4 * c + q // 2, q % 2
                        product(py[0:R, half * CW:(half + 1) * CW], hid_parts[:, f], *part(it, j, q), f == 0, f == KD - 1).then_inc(w_used.handle, 1)

                def scatter(it, m0, m1, lag):
                    for m in range(m0, m1):
                        if m in (0, 8):
                            pe.wait_ge(yl_kept.handle, it * E + yl_kept.at(2 * (m // 8) + 2 + c_yl - lag * E))
                        if m == 16:
                            pe.wait_ge(yc_kept.handle, it * E + yc_kept.at(E + c_yl - lag * E))
                        pe.wait_ge(sc_added.handle, it * M + sc_added.at(m + 1 - lag * M))
                        d = m % 8
                        if m < 16:
                            rhs = sp_l[:, bass.ds(it * 2 + (m // 8 - 2 * lag), 1), :].rearrange("p a n -> p (a n)")
                            last = nc.tensor.matmul(psc[m % nb][:], y_l[:, m // 8, d * P:(d + 1) * P], rhs, start=True, stop=True)
                        else:
                            rhs = sp_c[:, bass.ds(it - lag, 1), :].rearrange("p a n -> p (a n)")
                            last = nc.tensor.matmul(psc[m % nb][:, 0:CTX], y_c[:, d * P:(d + 1) * P], rhs, start=True, stop=True)
                        last.then_inc(sc_done.handle, 1)

                pe.sem_inc(w_used.handle, c_used)
                pe.sem_inc(hid_turned.handle, c_turn)
                pe.sem_inc(sc_done.handle, c_sc)
                def turn_of(it, first):
                    def then_scatter(*chunk):
                        for m0, m1, lag in scattered_after(first, *chunk):
                            scatter(it, m0, m1, lag)

                    for r in range(E):
                        pe.wait_ge(staged.handle, it * (E * per_stage) + staged.at((r + 1) * per_stage))
                        into_hidden(it, r, "gate", 0)
                        then_scatter(r, "gate", 0)
                        into_hidden(it, r, "up", 0)
                        then_scatter(r, "up", 0)
                        if r:
                            down_of(it, r - 1, 1)
                            then_scatter(r - 1, "down", 1)
                        into_hidden(it, r, "gate", 1)
                        then_scatter(r, "gate", 1)
                        turn(it, r, 0)
                        into_hidden(it, r, "up", 1)
                        then_scatter(r, "up", 1)
                        down_of(it, r, 0)
                        then_scatter(r, "down", 0)
                        turn(it, r, 1)
                    down_of(it, E - 1, 1)

                turn_of(0, True)
                with pe.Fori(1, H) as it:
                    turn_of(it, False)
                scatter(H, 8, M, 1)

            @block.scalar
            def _(act):
                def high(it, j, q):
                    i = j * PIECES + q
                    if q == 0:
                        core.await_chunk(act, n0 + j, it, NC)
                    act.wait_ge(w_used.handle, it * NP + w_used.at(i + 1 - SPLIT_BUFS + c_used))
                    nc.scalar.copy(w_hi[:, i % SPLIT_BUFS, :], raw(j, q)).then_inc(w_high.handle, 1)

                def silu(it, r, c):
                    s = 2 * r + c
                    if stack:
                        act.wait_ge(gate_summed.handle, it * (2 * E) + gate_summed.at(s + 1 + 1))
                    else:
                        await_product(act, it, r, "gate", c)
                    act.wait_ge(hid_made.handle, it * (2 * E) + hid_made.at(s + 1))
                    nc.scalar.activation(act_[:, c, :], gate_sum[:] if stack else pg[0:S, :], ACT.Silu).then_inc(silu_done.handle, 1)

                def lower(it, r, c, what):
                    s = 2 * r + c
                    await_product(act, it, r, what, c)
                    if what == "gate":
                        act.wait_ge(gate_summed.handle, it * (2 * E) + gate_summed.at(s + 1))
                        nc.scalar.copy(gate_low[:], pg[S:R, :]).then_inc(gate_lowered.handle, 1)
                    else:
                        act.wait_ge(up_summed.handle, it * (2 * E) + up_summed.at(s + 1))
                        nc.scalar.copy(up_low[:], pu[S:R, :]).then_inc(up_lowered.handle, 1)

                def turned(it, r, c):
                    act.wait_ge(hid_turned.handle, it * (2 * E) + hid_turned.at(2 * r + c + 1 + c_turn))
                    await_product(act, it, r - 1, "down", c)
                    nc.scalar.copy(hid_hi[:, 4 * c:4 * c + 4, :], pt[:, 0:4 * S].rearrange("p (f s) -> p f s", f=4)).then_inc(hid_high.handle, 1)

                def keep(it, r):
                    await_product(act, it, r, "down", 1)
                    if stack:
                        act.wait_ge(yl_kept.handle, it * E + yl_kept.at(r + c_yl))
                        nc.scalar.copy(y_low[:], py[S:R, :]).then_inc(y_lowered.handle, 1)
                        return
                    act.wait_ge(sc_done.handle, it * M + sc_done.at(8 * (r // 2) + 8 if r >= 0 else 16 - M))
                    o = (r % 2) * CAP_L
                    nc.scalar.copy(y_l[o:o + CAP_L, r // 2 % 2, :], py[0:CAP_L, :]).then_inc(yl_kept.handle, 1)

                def after(it, r, what, half, first):
                    if (what, half) == ("up", 0):
                        (lower(it, r, 0, "gate") if stack else silu(it, r, 0))
                    elif (what, half) == ("gate", 0) and r:
                        turned(it, r - 1, 1)
                    elif (what, half) == ("gate", 1):
                        if stack and r == 0:
                            silu(it, 0, 0)
                            lower(it, 0, 0, "up")
                        if r or not first:
                            keep(it, r - 1)
                    elif (what, half) == ("up", 1):
                        (lower(it, r, 1, "gate") if stack else silu(it, r, 1))
                        turned(it, r, 0)
                    elif stack and (what, half) == ("down", 0):
                        silu(it, r, 1)
                        lower(it, r, 1, "up")
                    elif (what, half) == ("down", 1):
                        if r == E - 1:
                            turned(it, r, 1)
                        elif stack:
                            silu(it, r + 1, 0)
                            lower(it, r + 1, 0, "up")

                act.sem_inc(silu_done.handle, c_silu)
                if not stack:
                    act.sem_inc(yl_kept.handle, c_yl)
                in_order(0, high, lambda *at: after(*at, True))
                with act.Fori(1, H) as it:
                    in_order(it, high, lambda *at: after(*at, False))
                keep(H, -1)

            @block.vector
            def _(dve):
                def low(it, j, q):
                    if q in dve_pieces:
                        b = (j * PIECES + q) % SPLIT_BUFS
                        dve.wait_ge(w_high.handle, it * NP + w_high.at(j * PIECES + q + 1))
                        if q == PIECES - 1:
                            dve.wait_ge(w_low_pool.handle, it * (NG * NC) + w_low_pool.at(NG * (j + 1)))
                        nc.vector.tensor_tensor(w_lo[:, b, :], raw(j, q), w_hi[:, b, :], ALU.subtract).then_inc(w_low.handle, 1)

                def product(it, r, c):
                    s = 2 * r + c
                    await_product(dve, it, r, "up", c)
                    if stack:
                        dve.wait_ge(up_lowered.handle, it * (2 * E) + up_lowered.at(s + 1))
                        dve.wait_ge(hid_made.handle, it * (2 * E) + hid_made.at(s + c_hid))
                        nc.vector.tensor_tensor(up_sum[:], pu[0:S, :], up_low[:], ALU.add).then_inc(up_summed.handle, 1)
                        dve.wait_ge(up_summed.handle, it * (2 * E) + up_summed.at(s + 1 + 1))
                    dve.wait_ge(silu_done.handle, it * (2 * E) + silu_done.at(s + 1 + c_silu))
                    dve.wait_ge(hid_turned.handle, it * (2 * E) + hid_turned.at(s + 1))
                    nc.vector.tensor_tensor(hid[:, c, :], act_[:, c, :], up_sum[:] if stack else pu[0:S, :], ALU.mult).then_inc(hid_made.handle, 1)

                def turned(it, r, c):
                    dve.wait_ge(hid_high.handle, it * (2 * E) + hid_high.at(2 * r + c + 1))
                    at = slice(4 * c, 4 * c + 4)
                    nc.vector.tensor_tensor(hid_lo[:, at, :], pt[:, 0:4 * S].rearrange("p (f s) -> p f s", f=4), hid_hi[:, at, :], ALU.subtract).then_inc(hid_low.handle, 1)

                def sum_gate(it, r, c):
                    s = 2 * r + c
                    dve.wait_ge(gate_lowered.handle, it * (2 * E) + gate_lowered.at(s + 1))
                    dve.wait_ge(silu_done.handle, it * (2 * E) + silu_done.at(s + c_silu))
                    nc.vector.tensor_tensor(gate_sum[:], pg[0:S, :], gate_low[:], ALU.add).then_inc(gate_summed.handle, 1)

                def keep(it, r):
                    if stack:
                        dve.wait_ge(y_lowered.handle, it * E + y_lowered.at(r + 1))
                        dve.wait_ge(sc_done.handle, it * M + sc_done.at(8 * (r // 2) + 8 if r >= 0 else 16 - M))
                        o = (r % 2) * CAP_L
                        nc.vector.tensor_tensor(y_l[o:o + CAP_L, r // 2 % 2, :], py[0:S, :], y_low[:], ALU.add).then_inc(yl_kept.handle, 1)
                    if ctx:
                        await_product(dve, it, r, "down", 1)
                        dve.wait_ge(sc_done.handle, it * M + sc_done.at(M if r >= 0 else 0))
                        dve.wait_ge(yl_kept.handle, it * E + yl_kept.at(r + 1 + c_yl))
                        nc.vector.tensor_copy(y_c[r % E * CAP_C:(r % E + 1) * CAP_C, :], py[CAP_L:S, :]).then_inc(yc_kept.handle, 1)

                def add(it, m0, m1, lag):
                    for m in range(m0, m1):
                        dve.wait_ge(sc_done.handle, it * M + sc_done.at(m + 1 + c_sc - lag * M))
                        dve.wait_ge(sc_added.handle, it * M + sc_added.at(m + c_add - lag * M))
                        d = m % 8
                        c0, n, s = (0, SEQ, 0) if m < 16 else (SEQ, CTX, 1)
                        nc.vector.scalar_tensor_tensor(out=x[:, d, c0:c0 + n], in0=psc[m % nb][:, 0:n], scalar=gate[s][:, d:d + 1], in1=x[:, d, c0:c0 + n],
                                                       op0=ALU.mult, op1=ALU.add).then_inc(sc_added.handle, 1)

                def after(it, r, what, half, first):
                    before = EXPERT_ORDER[EXPERT_ORDER.index((r, what, half)) - 1]
                    if (what, half) == ("gate", 0) and r:
                        turned(it, r - 1, 1)
                    elif (what, half) == ("up", 0) and stack:
                        sum_gate(it, r, 0)
                    elif (what, half) == ("down", 1) and r < E - 1:
                        product(it, r + 1, 0)
                    elif (what, half) == ("gate", 1) and r == 0:
                        product(it, 0, 0)
                    elif (what, half) == ("up", 1):
                        if stack:
                            sum_gate(it, r, 1)
                        turned(it, r, 0)
                    elif (what, half) == ("down", 0):
                        product(it, r, 1)
                    elif (what, half) == ("down", 1) and r == E - 1:
                        turned(it, r, 1)
                    for m0, m1, lag in scattered_after(first, *before):
                        add(it, m0, m1, lag)
                    if (what, half) == ("gate", 1) and (r or not first):
                        keep(it, r - 1)

                if stack:
                    dve.sem_inc(gate_summed.handle, 1)
                    dve.sem_inc(up_summed.handle, 1)
                    dve.sem_inc(yl_kept.handle, c_yl)
                dve.sem_inc(hid_made.handle, c_hid)
                dve.sem_inc(hid_low.handle, c_low)
                dve.sem_inc(yc_kept.handle, c_yl)
                dve.sem_inc(sc_added.handle, c_add)
                in_order(0, low, lambda *at: after(*at, True))
                with dve.Fori(1, H) as it:
                    in_order(it, low, lambda *at: after(*at, False))
                keep(H, -1)
                add(H, 8, M, 1)


def moe(core, layer, ctx, gate):
    with Stage(core, "moe") as st:
        xe_l = st.sb("xe_l", [P, N_EXP, KD, CAP_L])
        sp_l = st.sb("sp_l", [P, N_EXP // 2, SEQ])
        sp_c = st.sb("sp_c", [P, N_EXP // 4, CTX]) if ctx else None
        spare = core.h[:].rearrange("p k n -> p (k n)")[:, 0:N_EXP * KD * CAP_C]
        xe_c = spare.rearrange("p (e k s) -> p e k s", e=N_EXP, k=KD) if ctx else None
        route_stage(core, layer, ctx, xe_l, xe_c, sp_l, sp_c)
        experts_stage(core, layer, ctx, xe_l, xe_c, sp_l, sp_c, gate)


def axial_rope_stage(core, cols):
    nc = core.nc
    H = 20
    with Stage(core, "axial") as st:
        rope = st.sb("rope", [P, 2, LT, 32])
        tmp = [st.sb(f"tmp{i}", [P, 4, H, 32]) for i in range(2)]
        loaded = st.counter("axial_loaded", 32)
        chain = st.counter("axial_chain", 2 * (LT - 1))
        pool_chain = st.counter("axial_pool_chain", 2)
        with st.run() as block:
            @block.sync
            def _(sp):
                sp.dma_start(rope[:, 0], core.consts["axial_cos"]).then_inc(loaded.handle, 16)
                sp.dma_start(rope[:, 1], core.consts["axial_sin"]).then_inc(loaded.handle, 16)

            def turn(ops, link, t):
                v = cols[:, t, 0:H * HD].rearrange("p (h w) -> p h w", w=HD)
                x1, x2 = v[:, :, 0:32], v[:, :, 32:HD]
                cos, sin = (rope[:, j, t, :].unsqueeze(1).to_broadcast([P, H, 32]) for j in range(2))
                s = tmp[0 if t < LT - 1 else 1]
                ops.tensor_tensor(s[:, 0], x1, cos, ALU.mult)
                ops.tensor_tensor(s[:, 1], x2, sin, ALU.mult)
                ops.tensor_tensor(s[:, 2], x2, cos, ALU.mult)
                link(ops.tensor_tensor(s[:, 3], x1, sin, ALU.mult))
                ops.tensor_tensor(x1, s[:, 0], s[:, 1], ALU.subtract)
                link(ops.tensor_tensor(x2, s[:, 2], s[:, 3], ALU.add))

            @block.vector
            def _(dve):
                link = Link(dve, chain)
                dve.wait_ge(loaded.handle, loaded.at(32))
                for t in range(LT - 1):
                    turn(nc.vector, link, t)

            @block.gpsimd
            def _(pool):
                link = Link(pool, pool_chain)
                pool.wait_ge(loaded.handle, loaded.at(32))
                turn(nc.gpsimd, link, LT - 1)


def attention_layer(core, gate):
    nc, ins = core.nc, core.ins
    KV, REP, W = 4, 4, 1536
    with Stage(core, "swa2") as st:
        cols = st.sb("cols", [P, LT + CT, W])
        lat, both = list(range(LT)), list(range(LT + CT))
        project_stage(core, "w_in2", [lat, lat, both], [CW] * 3, lambda t, c: cols[:, t, c * CW:(c + 1) * CW])
        o = st.sb("o", [P, LT, D])
        axial_rope_stage(core, cols)
        qT = st.sb("qT", [MLA_DIM, KV * REP, SEQ])
        kT = core.h[0:MLA_DIM].rearrange("p k n -> p (k n)")[:, 0:KV * TOK].rearrange("p (h n) -> p h n", h=KV)
        band = st.sb("band", [P, 3 * P])
        sink = st.sb("sink", [P, KV * REP])
        jobs = [(lambda t, c=hd * HD: cols[:, t, c:c + HD], LT, HD, qT[0:HD, hd, :], None, HD ** -0.5) for hd in range(KV * REP)]
        order = [LT, LT + 1, 0, 1, 2, 3]
        jobs += [(lambda t, c=D + hd * HD: cols[:, order[t], c:c + HD], 6, HD, kT[0:HD, hd, :], None, 1.0) for hd in range(KV)]

        def extra(sp, loaded):
            if sp is not None:
                sp.dma_start(band[:], core.consts["band"]).then_inc(loaded.handle, 16)
                sp.dma_start(sink[:], ins["sw_sink_2"].partition_broadcast(P)).then_inc(loaded.handle, 16)
            return 2

        turn_heads_stage(core, "turn2", jobs, zero=[qT[HD:MLA_DIM], kT[HD:MLA_DIM]], extra=extra)

        def keys(i):
            lo, hi = max(0, i - 1), min(LT, i + 2)
            return [(0, CTX, None), (CTX + lo * P, (hi - lo) * P, ((lo - i + 1) * P, (hi - i + 1) * P))]

        attention_stage(
            core, "att2", KV // 2, 2 * REP, MLA_DIM, LT, keys, qT,
            lambda it, r, k0, n: kT[:, bass.ds(it * 2 + r // REP, 1), k0:k0 + n].rearrange("p a n -> p (a n)"),
            lambda it, r, kt: cols[:, order[kt], bass.ds(it * (2 * HD) + (D + KV * HD + r // REP * HD), HD)],
            lambda it, r, a, b: band[:, a:b],
            lambda it, r, i: o[:, i, bass.ds(it * (2 * REP * HD) + r * HD, HD)],
            lambda it, r: sink[:, bass.ds(it * (2 * REP) + r, 1)])
        turn_heads_stage(core, "turn3", [(lambda t, k=k: o[:, t, k * P:(k + 1) * P], LT, P, core.h[:, k, 0:SEQ], None, 1.0) for k in range(KD)])
    residual_stage(core, "w_out2", gate)


def store_stage(core, out):
    with Stage(core, "final") as st:
        tok = st.sb("tok", [P, LT, D])
        turn_tokens_stage(core, "last", core.h, tok, range(LT))
        stored = st.counter("stored", 16)
        with st.run() as block:
            @block.sync
            def _(sp):
                sp.dma_start(out[0].rearrange("(t p) d -> p t d", p=P), tok[:]).then_inc(stored.handle, 16)
                sp.wait_ge(stored.handle, stored.at(16))


def second_block(core, out, debug):
    def mod(layer, i, s):
        at = layer * 48 + i * KD
        return core.mod[:, at:at + KD, s]

    def streams(layer, gain, i, both):
        g = lambda: core.col(gain, layer * KD, KD)
        lat = [(0, SEQ, g(), mod(layer, i + 1, 0), mod(layer, i, 0))]
        return lat + ([(SEQ, CTX, g(), mod(layer, i + 1, 1), mod(layer, i, 1))] if both else [])

    norm_stage(core, "norm_h", streams(0, "norm1_w_2", 0, True))
    hyena_stage(core, [mod(0, 2, 0), mod(0, 2, 1)])
    if debug: debug(core, 'hyena')
    norm_stage(core, "norm_e", streams(0, "norm2_w_2", 3, True))
    moe(core, 0, True, [mod(0, 5, 0), mod(0, 5, 1)])
    if debug: debug(core, 'moe0')
    norm_stage(core, "norm_s", streams(1, "norm1_w_2", 0, True))
    attention_layer(core, mod(1, 2, 0))
    if debug: debug(core, 'swa')
    norm_stage(core, "norm_f", streams(1, "norm2_w_2", 3, False))
    moe(core, 1, False, [mod(1, 5, 0)])
    if debug: debug(core, 'moe1')
    norm_stage(core, "norm_l", [(0, SEQ, core.col("final_norm_w_2"), None, None)])
    store_stage(core, out)


def build(nc, ins, consts, out, debug=None):
    with ExitStack() as ctx:
        core = Core(nc, ins, consts, ctx)
        chunks = []
        for layer in range(2):
            chunks += [column_chunk(ins["ada_w_2"][layer], c * CW, CW) for c in range(12)]
        chunks += [column_chunk(ins["w_in"][0], c * CW, min(CW, IN_COLS - c * CW)) for c in range(5)]
        chunks += [column_chunk(ins["w_o"][0], c * CW, CW) for c in range(2)]
        chunks += [column_chunk(ins["w_up"][0], c * CW, CW) for c in range(FF // CW)]
        chunks += [row_chunk(ins["w_down"][0], c * CW) for c in range(FF // CW)]
        chunks += hyena_chunks(core)
        experts = lambda layer: [place(first) for first in range(0, N_EXP, EXPERTS_PER_TURN) for place in expert_chunks(core, layer)]
        chunks += experts(0)
        chunks += [column_chunk(ins["sw_w_in_2"], c * CW, CW) for c in range(3)]
        chunks += [column_chunk(ins["sw_w_out_2"], c * CW, CW) for c in range(2)]
        chunks += experts(1)
        core.set_chunks(chunks)
        load_stage(core)
        modulation_stage(core)
        if debug: debug(core, 'load')
        first_block(core)
        if debug: debug(core, 'first')
        second_block(core, out, debug)


def constants():
    f = np.float32
    c = {"ident": np.eye(P, dtype=f)}
    inv = f(1.0) / (f(10000.0) ** (np.arange(0, 32, 2, dtype=f) / f(32)))
    ang = np.arange(SEQ, dtype=f)[:, None] * inv[None, :]
    tile = lambda a: np.ascontiguousarray(a.reshape(-1, P, a.shape[-1]).transpose(1, 0, 2))
    c["rope_cos"], c["rope_sin"] = tile(np.cos(ang)), tile(np.sin(ang))
    dist = np.arange(P)[:, None] + (SEQ - P) - np.arange(SEQ)[None, :]
    idx = np.arange(1, 3 * HEADS + 1, dtype=f).reshape(HEADS, 3)
    slopes = np.exp2(f(-8.0) * idx / f(3 * HEADS)).astype(f)
    causal = dist >= 0
    count = (dist <= 128).astype(f) + (dist % 4 == 0) + (dist % 16 == 0)
    bias = np.full((4, P, HEADS, SEQ), NEG, f)
    for h in range(HEADS):
        for g, (valid, col) in enumerate(((causal, 0), (causal, None), (causal & (count > 0), 1), (causal & (dist < 128), 2))):
            b = np.zeros_like(dist, dtype=f) if col is None else -slopes[h, col] * dist.astype(f)
            if g == 2:
                b = b + np.log(np.maximum(count, 1))
            bias[g, :, h, :] = np.where(valid, b, NEG)
    c["bias"] = bias
    deltas = np.abs(np.linspace(np.log(1e-2) / 1.5, np.log(1e-2) / 0.3, D, dtype=f))
    z_all, win_all = [], []
    for name, L in (("l", SEQ), ("c", CTX)):
        order = np.concatenate([np.arange(0, L, 2), np.arange(1, L, 2)])
        t = np.linspace(0.0, 1.0, L, dtype=f)[:, None]
        w = f(2.0 * np.pi) * np.arange(L, dtype=f)[:, None] / f(L)
        bands = np.linspace(1e-4, 15, 16, dtype=f)[None, :]
        z = np.concatenate([t, np.cos(bands * w), -np.sin(bands * w)], axis=-1).astype(f)
        z_all.append(z[order].T)
        window = np.exp(-t * deltas) + f(0.05)
        both = np.stack([window, window], axis=1)
        both[0, 1, :] = 0.0
        win_all.append(both[order].reshape(-1, P, 2, D).transpose(1, 0, 2, 3))
        half = L // 2
        freq = np.arange(half) + 0.5
        pos = [np.arange(0, L, 2), np.arange(1, L, 2)]
        fwd = [fn(np.pi * pos[par][:, None] * freq[None, :] / L) for fn in (np.cos, np.sin) for par in (0, 1)]
        inv = [m.T / L for m in fwd]
        pack = lambda ms: np.ascontiguousarray(np.stack([m.reshape(-1, P, half).transpose(1, 0, 2) for m in ms], axis=1)).astype(f)
        c["dft_" + name], c["idft_" + name] = pack(fwd), pack(inv)
    c["filter_z"] = np.ascontiguousarray(np.concatenate(z_all, axis=1)).astype(f)
    c["window"] = np.ascontiguousarray(np.concatenate(win_all, axis=1)).astype(f)
    row = np.repeat(np.arange(SEQ // 64, dtype=f), 64)
    col = np.tile(np.arange(64, dtype=f), SEQ // 64)
    inv = f(10000.0) ** (-np.arange(16, dtype=f) / f(16))
    ang = np.concatenate([row[:, None] * inv, col[:, None] * inv], axis=-1)
    c["axial_cos"], c["axial_sin"] = tile(np.cos(ang)), tile(np.sin(ang))
    gap = np.arange(P)[:, None] + P - np.arange(3 * P)[None, :]
    c["band"] = np.where(np.abs(gap) <= 128, f(0), f(NEG)).astype(f)
    c["slot_number"] = np.broadcast_to(np.arange(1, CAP_L + 1, dtype=f), (P, CAP_L)).copy()
    return c


_UNUSED = ("gd_", "hg_")


def kernel(**inputs):
    import concourse.bacc as bacc
    from concourse.bass_utils import run_bass_kernel_spmd

    nc = bacc.Bacc("TRN2", target_bir_lowering=False, num_devices=1)
    arrays, ins, consts = {}, {}, {}

    def place(name, a):
        a = np.ascontiguousarray(a)
        arrays[name] = a
        return nc.dram_tensor(name, a.shape, mybir.dt.from_np(a.dtype), kind="ExternalInput").ap()

    for name, a in inputs.items():
        if not name.startswith(_UNUSED):
            ins[name] = place("in_" + name, a)
    for name, a in constants().items():
        consts[name] = place("table_" + name, a)
    out = nc.dram_tensor("out", (1, SEQ, D), F32, kind="ExternalOutput").ap()
    build(nc, ins, consts, out)
    r = run_bass_kernel_spmd(nc, [arrays], core_ids=[0])
    return r.results[0]["out"]
```
